# Optimizing a Trainium2 kernel written in Bass

```python
import math
import jax, jax.numpy as jnp
from jax import lax
import numpy as np

D_MODEL = 1024
BATCH = 1
SEQ = 512
DEPTH = 1

HEAD_DIM = 64
N_META = 16
BLOCK_Q = 128
SB_HEADS = 4
SP_HEADS = 4
IDX_HEADS = 8
IDX_DIM = 32
TOPK_MAX = 256
DF_HEADS = 4
N_BUCKETS = 32
MAX_DISTANCE = 128
N_BIAS_HEADS = SP_HEADS + DF_HEADS
D_FF = 2816
CONV_WIDTH = 3
EPS = 1e-6
NEG_INF = -1e30

SB_W = SB_HEADS * HEAD_DIM
SP_W = SP_HEADS * HEAD_DIM
DF_W = DF_HEADS * 2 * HEAD_DIM
SPLITS = (SB_W, SB_W, SB_W,
          SP_W, SP_W, SP_W,
          IDX_HEADS * IDX_DIM, IDX_DIM, IDX_HEADS,
          DF_W, DF_W, DF_W,
          D_MODEL, D_MODEL, D_MODEL)
D_IN = sum(SPLITS)


def _rmsnorm(a, gain):
    af = a.astype(jnp.float32)
    af = af * lax.rsqrt(jnp.mean(af * af, axis=-1, keepdims=True) + EPS)
    return (af * gain.astype(jnp.float32)).astype(a.dtype)

def _split_cols(z):
    out, off = [], 0
    for w in SPLITS:
        out.append(z[..., off:off + w])
        off += w
    return out

def _to_blocks(a):
    b, tp = a.shape[:2]
    return jnp.moveaxis(a.reshape((b, tp // BLOCK_Q, BLOCK_Q) + a.shape[2:]), 1, 0)

def _from_blocks(a):
    nb, b = a.shape[:2]
    return jnp.moveaxis(a, 0, 1).reshape((b, nb * BLOCK_Q) + a.shape[3:])

def _t5_bucket(rel):
    n = jnp.maximum(rel, 0)
    max_exact = N_BUCKETS // 2
    nf = jnp.maximum(n, 1).astype(jnp.float32)
    large = max_exact + (jnp.log(nf / max_exact) / math.log(MAX_DISTANCE / max_exact)
                         * (N_BUCKETS - max_exact)).astype(jnp.int32)
    return jnp.where(n < max_exact, n, jnp.minimum(large, N_BUCKETS - 1))

def _stick_breaking(q, k, v):
    tp, dh = q.shape[1], q.shape[-1]
    scale = dh ** -0.5
    kf, vf = k.astype(jnp.float32), v.astype(jnp.float32)
    key_pos = jnp.arange(tp)

    def block(args):
        qb, start = args
        qpos = start + jnp.arange(BLOCK_Q)
        z = jnp.einsum('bqhd,bkhd->bhqk', qb.astype(jnp.float32), kf) * scale
        mask = key_pos[None, :] < qpos[:, None]
        log_1m_beta = jnp.where(mask, jax.nn.log_sigmoid(-z), 0.0)
        between = lax.cumsum(log_1m_beta, axis=3, reverse=True) - log_1m_beta
        w = jnp.where(mask, jnp.exp(jax.nn.log_sigmoid(z) + between), 0.0)
        return jnp.einsum('bhqk,bkhd->bqhd', w, vf)

    nb = tp // BLOCK_Q
    out = lax.map(block, (_to_blocks(q), jnp.arange(nb) * BLOCK_Q))
    return _from_blocks(out).astype(v.dtype)

def _indexed_sparse_attention(q, k, v, q_ix, k_ix, w_ix, bias_table, top_k):
    tp, h, dh = q.shape[1], q.shape[2], q.shape[3]
    scale = dh ** -0.5
    k_ixf = k_ix.astype(jnp.float32)
    key_pos = jnp.arange(tp)
    table = bias_table.astype(jnp.float32)

    def block(args):
        qb, qib, wb, start = args
        qpos = start + jnp.arange(BLOCK_Q)
        dots = jnp.einsum('bqjd,bkd->bqjk', qib.astype(jnp.float32), k_ixf)
        score = jnp.einsum('bqj,bqjk->bqk', wb.astype(jnp.float32), jax.nn.relu(dots))
        score = jnp.where((key_pos[None, :] <= qpos[:, None])[None], score, NEG_INF)
        _, sel = lax.top_k(score, top_k)
        rel = qpos[None, :, None] - sel
        valid = rel >= 0
        k_sel = jax.vmap(lambda kk, ii: kk[ii])(k, sel)
        v_sel = jax.vmap(lambda vv, ii: vv[ii])(v, sel)
        s = jnp.einsum('bqhd,bqkhd->bhqk', qb.astype(jnp.float32),
                       k_sel.astype(jnp.float32)) * scale
        s = s + jnp.moveaxis(table[_t5_bucket(rel)], -1, 1)
        s = jnp.where(valid[:, None], s, NEG_INF)
        p = jax.nn.softmax(s, axis=-1)
        return jnp.einsum('bhqk,bqkhd->bqhd', p, v_sel.astype(jnp.float32))

    nb = tp // BLOCK_Q
    out = lax.map(block, (_to_blocks(q), _to_blocks(q_ix), _to_blocks(w_ix),
                          jnp.arange(nb) * BLOCK_Q))
    return _from_blocks(out).astype(v.dtype)

def _differential_attention(q1, q2, k1, k2, v, lam, bias_table):
    tp, dh = q1.shape[1], q1.shape[-1]
    scale = dh ** -0.5
    k1f, k2f, vf = k1.astype(jnp.float32), k2.astype(jnp.float32), v.astype(jnp.float32)
    key_pos = jnp.arange(tp)
    table = bias_table.astype(jnp.float32)

    def block(args):
        q1b, q2b, start = args
        qpos = start + jnp.arange(BLOCK_Q)
        mask = key_pos[None, :] <= qpos[:, None]
        bias = jnp.moveaxis(table[_t5_bucket(qpos[:, None] - key_pos[None, :])], -1, 0)

        def attn_map(qb, kf):
            s = jnp.einsum('bqhd,bkhd->bhqk', qb.astype(jnp.float32), kf) * scale + bias
            return jax.nn.softmax(jnp.where(mask, s, NEG_INF), axis=-1)

        p = attn_map(q1b, k1f) - lam * attn_map(q2b, k2f)
        return jnp.einsum('bhqk,bkhd->bqhd', p, vf)

    nb = tp // BLOCK_Q
    out = lax.map(block, (_to_blocks(q1), _to_blocks(q2), jnp.arange(nb) * BLOCK_Q))
    return _from_blocks(out).astype(v.dtype)

def _mixer(u, layer, w_in, b_gate, q_norm_sp, k_norm_sp, q_norm_df, k_norm_df,
           lam_q1, lam_k1, lam_q2, lam_k2, subln_df, w_br_sb, w_br_sp, w_br_df, w_out,
           rel_bias, top_k):
    b, tp, _ = u.shape
    (q_sb, k_sb, v_sb, q_sp, k_sp, v_sp, q_ix, k_ix, w_ix,
     q_df, k_df, v_df, g_sb, g_sp, g_df) = _split_cols(u @ w_in)

    def hd(a, n):
        return a.reshape(b, tp, n, -1)

    y_sb = _stick_breaking(hd(q_sb, SB_HEADS), hd(k_sb, SB_HEADS), hd(v_sb, SB_HEADS))
    y_sp = _indexed_sparse_attention(_rmsnorm(hd(q_sp, SP_HEADS), q_norm_sp),
                                     _rmsnorm(hd(k_sp, SP_HEADS), k_norm_sp),
                                     hd(v_sp, SP_HEADS), hd(q_ix, IDX_HEADS), k_ix, w_ix,
                                     rel_bias[:, :SP_HEADS], top_k)
    q_df = _rmsnorm(q_df.reshape(b, tp, DF_HEADS, 2, HEAD_DIM), q_norm_df)
    k_df = _rmsnorm(k_df.reshape(b, tp, DF_HEADS, 2, HEAD_DIM), k_norm_df)
    lam_init = 0.8 - 0.6 * math.exp(-0.3 * layer)
    lam = (jnp.exp(jnp.sum(lam_q1.astype(jnp.float32) * lam_k1.astype(jnp.float32)))
           - jnp.exp(jnp.sum(lam_q2.astype(jnp.float32) * lam_k2.astype(jnp.float32)))
           + lam_init)
    y_df = _differential_attention(q_df[..., 0, :], q_df[..., 1, :], k_df[..., 0, :],
                                   k_df[..., 1, :], hd(v_df, DF_HEADS), lam,
                                   rel_bias[:, SP_HEADS:])
    y_df = _rmsnorm(y_df, subln_df) * (1.0 - lam_init)

    merged = (jax.nn.sigmoid(g_sb + b_gate[:D_MODEL]) * (y_sb.reshape(b, tp, -1) @ w_br_sb)
              + jax.nn.sigmoid(g_sp + b_gate[D_MODEL:2 * D_MODEL]) * (y_sp.reshape(b, tp, -1) @ w_br_sp)
              + jax.nn.sigmoid(g_df + b_gate[2 * D_MODEL:]) * (y_df.reshape(b, tp, -1) @ w_br_df))
    return merged @ w_out

def _conv_ffn(u, w_up, conv_w, conv_b, w_down):
    tp = u.shape[1]
    z = u @ w_up
    gate, val = z[..., :D_FF], z[..., D_FF:]
    gp = jnp.pad(gate, ((0, 0), (CONV_WIDTH - 1, 0), (0, 0)))
    conv = conv_b + sum(gp[:, i:i + tp] * conv_w[i] for i in range(CONV_WIDTH))
    return (jax.nn.silu(conv) * val) @ w_down

def first_inputs(seed: int = 0) -> dict:
    key = jax.random.key(seed)
    ks = jax.random.split(key, 24)

    def n(k, shape, s):
        return jax.random.normal(k, shape, jnp.float32) * s

    return {
        'x': n(ks[0], (BATCH, SEQ, D_MODEL), 1.0),
        'meta_tokens': n(ks[1], (N_META, D_MODEL), 1.0),
        'rel_bias': n(ks[2], (N_BUCKETS, N_BIAS_HEADS), 0.5),
        'attn_norm': 1.0 + n(ks[3], (DEPTH, D_MODEL), 0.01),
        'w_in': n(ks[4], (DEPTH, D_MODEL, D_IN), D_MODEL ** -0.5),
        'b_gate': n(ks[5], (DEPTH, 3 * D_MODEL), 0.02),
        'q_norm_sp': 1.0 + n(ks[6], (DEPTH, HEAD_DIM), 0.01),
        'k_norm_sp': 1.0 + n(ks[7], (DEPTH, HEAD_DIM), 0.01),
        'q_norm_df': 1.0 + n(ks[8], (DEPTH, HEAD_DIM), 0.01),
        'k_norm_df': 1.0 + n(ks[9], (DEPTH, HEAD_DIM), 0.01),
        'lam_q1': n(ks[10], (DEPTH, HEAD_DIM), 0.1),
        'lam_k1': n(ks[11], (DEPTH, HEAD_DIM), 0.1),
        'lam_q2': n(ks[12], (DEPTH, HEAD_DIM), 0.1),
        'lam_k2': n(ks[13], (DEPTH, HEAD_DIM), 0.1),
        'subln_df': 1.0 + n(ks[14], (DEPTH, 2 * HEAD_DIM), 0.01),
        'w_br_sb': n(ks[15], (DEPTH, SB_W, D_MODEL), SB_W ** -0.5),
        'w_br_sp': n(ks[16], (DEPTH, SP_W, D_MODEL), SP_W ** -0.5),
        'w_br_df': n(ks[17], (DEPTH, DF_W, D_MODEL), DF_W ** -0.5),
        'w_out': n(ks[18], (DEPTH, D_MODEL, D_MODEL), D_MODEL ** -0.5),
        'ffn_norm': 1.0 + n(ks[19], (DEPTH, D_MODEL), 0.01),
        'w_up': n(ks[20], (DEPTH, D_MODEL, 2 * D_FF), D_MODEL ** -0.5),
        'conv_w': n(ks[21], (DEPTH, CONV_WIDTH, D_FF), CONV_WIDTH ** -0.5),
        'conv_b': n(ks[22], (DEPTH, D_FF), 0.02),
        'w_down': n(ks[23], (DEPTH, D_FF, D_MODEL), D_FF ** -0.5),
    }

def first_block(x, meta_tokens, rel_bias, attn_norm, w_in, b_gate, q_norm_sp, k_norm_sp,
              q_norm_df, k_norm_df, lam_q1, lam_k1, lam_q2, lam_k2, subln_df, w_br_sb,
              w_br_sp, w_br_df, w_out, ffn_norm, w_up, conv_w, conv_b, w_down):
    b, s, d = x.shape
    t = N_META + s
    tp = -(-t // BLOCK_Q) * BLOCK_Q
    top_k = min(TOPK_MAX, t // 4)
    meta = jnp.broadcast_to(meta_tokens[None].astype(x.dtype), (b, N_META, d))
    h = jnp.concatenate([meta, x, jnp.zeros((b, tp - t, d), x.dtype)], axis=1)
    for l in range(DEPTH):
        h = h + _mixer(_rmsnorm(h, attn_norm[l]), l, w_in[l], b_gate[l], q_norm_sp[l],
                       k_norm_sp[l], q_norm_df[l], k_norm_df[l], lam_q1[l], lam_k1[l],
                       lam_q2[l], lam_k2[l], subln_df[l], w_br_sb[l], w_br_sp[l],
                       w_br_df[l], w_out[l], rel_bias, top_k)
        h = h + _conv_ffn(_rmsnorm(h, ffn_norm[l]), w_up[l], conv_w[l], conv_b[l], w_down[l])
    return h[:, N_META:t]


_first_inputs = first_inputs


def first_inputs(seed=0):
    import zlib

    import numpy as np

    out = dict(_first_inputs(seed))
    spreads = {}
    factors = {'attn_norm': 4.909,
     'b_gate': 8.0,
     'q_norm_sp': 8.0,
     'k_norm_sp': 8.0,
     'q_norm_df': 8.0,
     'k_norm_df': 8.0,
     'lam_q1': 8.0,
     'subln_df': 8.0,
     'ffn_norm': 8.0,
     'conv_b': 6.173}
    for name, (base, spread) in spreads.items():
        noise = np.random.default_rng([zlib.crc32(name.encode()), seed]).standard_normal(out[name].shape)
        drawn = base * np.exp(spread * noise) if base else spread * noise
        out[name] = __import__('jax').numpy.asarray(drawn.astype(out[name].dtype))
    for name, factor in factors.items():
        out[name] = (out[name] * factor).astype(out[name].dtype)
    return out


_narrow_inputs = first_inputs


def first_inputs(seed=0):

    out = dict(_narrow_inputs(seed))
    wider = {'lam_q2': 4.72, 'subln_df': 6.65, 'ffn_norm': 4.52, 'conv_b': 4.2}
    for name, times in wider.items():
        mean = out[name].mean()
        out[name] = (mean + times * (out[name] - mean)).astype(out[name].dtype)
    return out


NSA_HEADS = 6
NSA_KV_HEADS = 2
NSA_GROUP = NSA_HEADS // NSA_KV_HEADS
RWKV_HEADS = 4
MOBA_HEADS = 6
D_NSA = NSA_HEADS * HEAD_DIM
D_NSA_KV = NSA_KV_HEADS * HEAD_DIM
D_RWKV = RWKV_HEADS * HEAD_DIM
D_MOBA = MOBA_HEADS * HEAD_DIM
D_MIX = D_NSA + D_RWKV + D_MOBA

CMP_LEN = 32
CMP_STRIDE = 16
CMP_HIDDEN = 256
SLC_BLOCK = 64
SLC_TOPK = 16
WINDOW = 512
N_BRANCH = 3
RW_DECAY_LORA = 32
RW_AAA_LORA = 32
RW_GATE_LORA = 64
RW_DECAY_SCALE = 0.606531
RW_LN_EPS = 64e-5
MOBA_BLOCK = 256
MOBA_TOPK = 3
Q_CHUNK = 128
NORM_EPS = 1e-6
BIG = 1e9

N_IN_NSA = D_NSA + 6 * D_NSA_KV + NSA_HEADS * N_BRANCH
N_IN_RWKV = 3 * D_RWKV + RW_DECAY_LORA + RW_AAA_LORA + RW_GATE_LORA
N_IN_MOBA = 3 * D_MOBA
N_IN = N_IN_NSA + N_IN_RWKV + N_IN_MOBA


def _rmsnorm_2(x, g):
    xf = x.astype(jnp.float32)
    y = xf * lax.rsqrt(jnp.mean(xf * xf, axis=-1, keepdims=True) + NORM_EPS)
    return (y * g.astype(jnp.float32)).astype(x.dtype)

def _head_rmsnorm(o, g):
    b, s, d = o.shape
    oh = o.reshape(b, s, d // HEAD_DIM, HEAD_DIM)
    return _rmsnorm_2(oh, g.reshape(d // HEAD_DIM, HEAD_DIM)).reshape(b, s, d)

def _masked_softmax(s, mask):
    s = jnp.where(mask, s.astype(jnp.float32), -jnp.inf)
    m = jnp.max(s, axis=-1, keepdims=True)
    m = jnp.where(jnp.isfinite(m), m, 0.0)
    p = jnp.exp(s - m)
    return p / jnp.maximum(jnp.sum(p, axis=-1, keepdims=True), 1e-30)

def _split(a, sizes):
    return jnp.split(a, [int(i) for i in np.cumsum(sizes)[:-1]], axis=-1)

def _nsa_compress(kv, pos, w1, w2):
    b, s, g, d = kv.shape
    n_cmp = (s - CMP_LEN) // CMP_STRIDE + 1
    idx = np.arange(n_cmp)[:, None] * CMP_STRIDE + np.arange(CMP_LEN)[None, :]
    blk = kv[:, idx] + pos[:, None, :]
    blk = jnp.transpose(blk, (0, 3, 1, 2, 4)).reshape(b, g, n_cmp, CMP_LEN * d)
    return jax.nn.gelu(blk @ w1) @ w2

def _cmp_to_slc(n_cmp, n_slc):
    r = SLC_BLOCK // CMP_STRIDE
    c = CMP_LEN // CMP_STRIDE
    i = (r * np.arange(n_slc)[:, None, None] - np.arange(r)[None, :, None] - np.arange(c)[None, None, :]).reshape(n_slc, -1)
    m = (i[:, :, None] == np.arange(n_cmp)[None, None, :]).sum(1)
    return jnp.asarray(m.T, jnp.float32)

def _nsa_mixer(p, cmp_pos, cmp_w1, cmp_w2):
    b, s, _ = p.shape
    q, kc, vc, ks, vs, kw, vw, gt = _split(p, [D_NSA] + [D_NSA_KV] * 6 + [NSA_HEADS * N_BRANCH])
    kvh = lambda t: t.reshape(b, s, NSA_KV_HEADS, HEAD_DIM)
    hf = lambda t: jnp.transpose(kvh(t), (0, 2, 1, 3))
    q = jnp.transpose(q.reshape(b, s, NSA_KV_HEADS, NSA_GROUP, HEAD_DIM), (0, 2, 3, 1, 4))
    gt = jnp.transpose(jax.nn.sigmoid(gt.reshape(b, s, NSA_KV_HEADS, NSA_GROUP, N_BRANCH)), (0, 2, 3, 1, 4))
    kc = _nsa_compress(kvh(kc), cmp_pos[0], cmp_w1[0], cmp_w2[0])
    vc = _nsa_compress(kvh(vc), cmp_pos[1], cmp_w1[1], cmp_w2[1])
    n_cmp = kc.shape[2]
    n_slc = s // SLC_BLOCK
    k_slc = min(SLC_TOPK, n_slc)
    ks = hf(ks).reshape(b, NSA_KV_HEADS, n_slc, SLC_BLOCK, HEAD_DIM)
    vs = hf(vs).reshape(b, NSA_KV_HEADS, n_slc, SLC_BLOCK, HEAD_DIM)
    kw = jnp.pad(hf(kw), ((0, 0), (0, 0), (WINDOW, 0), (0, 0)))
    vw = jnp.pad(hf(vw), ((0, 0), (0, 0), (WINDOW, 0), (0, 0)))
    cmp_map = _cmp_to_slc(n_cmp, n_slc)
    cmp_end = jnp.asarray(np.arange(n_cmp) * CMP_STRIDE + CMP_LEN - 1)
    blk_id = jnp.arange(n_slc)
    bi = jnp.arange(b)[:, None, None, None]
    gi = jnp.arange(NSA_KV_HEADS)[None, :, None, None]
    scale = HEAD_DIM ** -0.5

    def chunk(c):
        t0 = c * Q_CHUNK
        tpos = t0 + jnp.arange(Q_CHUNK)
        qc = lax.dynamic_slice_in_dim(q, t0, Q_CHUNK, axis=3)
        gc = lax.dynamic_slice_in_dim(gt, t0, Q_CHUNK, axis=3)
        pc = _masked_softmax(jnp.einsum('bgrqd,bgnd->bgrqn', qc, kc) * scale, cmp_end[None, :] <= tpos[:, None])
        oc = jnp.einsum('bgrqn,bgnd->bgrqd', pc.astype(vc.dtype), vc)
        imp = jnp.einsum('bgrqn,nj->bgqj', pc, cmp_map)
        cur = tpos // SLC_BLOCK
        forced = (blk_id[None, :] == 0) | (blk_id[None, :] == cur[:, None]) | (blk_id[None, :] == cur[:, None] - 1)
        causal = blk_id[None, :] * SLC_BLOCK <= tpos[:, None]
        imp = jnp.where(forced, BIG, jnp.where(causal, imp, -BIG))
        _, sel = lax.top_k(imp, k_slc)
        kg = ks[bi, gi, sel].reshape(b, NSA_KV_HEADS, Q_CHUNK, k_slc * SLC_BLOCK, HEAD_DIM)
        vg = vs[bi, gi, sel].reshape(b, NSA_KV_HEADS, Q_CHUNK, k_slc * SLC_BLOCK, HEAD_DIM)
        kpos = (sel[..., None] * SLC_BLOCK + jnp.arange(SLC_BLOCK)).reshape(b, NSA_KV_HEADS, Q_CHUNK, k_slc * SLC_BLOCK)
        ps = _masked_softmax(jnp.einsum('bgrqd,bgqkd->bgrqk', qc, kg) * scale, (kpos <= tpos[:, None])[:, :, None])
        osl = jnp.einsum('bgrqk,bgqkd->bgrqd', ps.astype(vg.dtype), vg)
        kwc = lax.dynamic_slice_in_dim(kw, t0, Q_CHUNK + WINDOW, axis=2)
        vwc = lax.dynamic_slice_in_dim(vw, t0, Q_CHUNK + WINDOW, axis=2)
        wpos = t0 - WINDOW + jnp.arange(Q_CHUNK + WINDOW)
        dist = tpos[:, None] - wpos[None, :]
        mw = (dist >= 0) & (dist < WINDOW) & (wpos[None, :] >= 0)
        pw = _masked_softmax(jnp.einsum('bgrqd,bgkd->bgrqk', qc, kwc) * scale, mw)
        ow = jnp.einsum('bgrqk,bgkd->bgrqd', pw.astype(vwc.dtype), vwc)
        return gc[..., 0:1] * oc + gc[..., 1:2] * osl + gc[..., 2:3] * ow

    o = lax.map(chunk, jnp.arange(s // Q_CHUNK))
    return jnp.transpose(o, (1, 0, 4, 2, 3, 5)).reshape(b, s, D_NSA)

def _rwkv7_mixer(p, mu, w0, w2, a0, a2, g2, k_k, k_a, r_k, lnx_w, lnx_b):
    b, s, _ = p.shape
    f32 = jnp.float32
    p_prev = jnp.pad(p, ((0, 0), (1, 0), (0, 0)))[:, :-1]
    p = p + (p_prev - p) * mu
    r, k, v, xw, xa, xg = _split(p, [D_RWKV] * 3 + [RW_DECAY_LORA, RW_AAA_LORA, RW_GATE_LORA])
    w = jnp.exp(-RW_DECAY_SCALE * jax.nn.sigmoid((w0 + jnp.tanh(xw) @ w2).astype(f32)))
    a = jax.nn.sigmoid(a0 + xa @ a2)
    g = jax.nn.sigmoid(xg) @ g2
    heads = lambda t: t.reshape(b, s, RWKV_HEADS, HEAD_DIM).astype(f32)
    kk = heads(k * k_k)
    kk = kk / jnp.maximum(jnp.sqrt(jnp.sum(kk * kk, axis=-1, keepdims=True)), 1e-12)
    k = k * (1.0 + (a - 1.0) * k_a)
    r_h, w_h, k_h, v_h, a_h = heads(r), heads(w), heads(k), heads(v), heads(a)

    def step(state, inp):
        r_t, w_t, k_t, v_t, kk_t, a_t = inp
        sa = jnp.einsum('bhvk,bhk->bhv', state, -kk_t)
        state = state * w_t[:, :, None, :] + sa[..., None] * (kk_t * a_t)[:, :, None, :] + v_t[..., None] * k_t[:, :, None, :]
        return state, jnp.einsum('bhvk,bhk->bhv', state, r_t)

    xs = tuple(jnp.moveaxis(t, 1, 0) for t in (r_h, w_h, k_h, v_h, kk, a_h))
    _, out = lax.scan(step, jnp.zeros((b, RWKV_HEADS, HEAD_DIM, HEAD_DIM), f32), xs)
    out = jnp.moveaxis(out, 0, 1)
    mean = jnp.mean(out, axis=-1, keepdims=True)
    var = jnp.mean(jnp.square(out - mean), axis=-1, keepdims=True)
    out = ((out - mean) * lax.rsqrt(var + RW_LN_EPS)).reshape(b, s, D_RWKV) * lnx_w + lnx_b
    bonus = jnp.sum(r_h * k_h * r_k, axis=-1, keepdims=True) * v_h
    out = (out + bonus.reshape(b, s, D_RWKV)) * g
    return out.astype(p.dtype)

def _moba_mixer(p):
    b, s, _ = p.shape
    q, k, v = [jnp.transpose(t.reshape(b, s, MOBA_HEADS, HEAD_DIM), (0, 2, 1, 3)) for t in _split(p, [D_MOBA] * 3)]
    n_blk = -(-s // MOBA_BLOCK)
    pad = n_blk * MOBA_BLOCK - s
    k = jnp.pad(k, ((0, 0), (0, 0), (0, pad), (0, 0)))
    v = jnp.pad(v, ((0, 0), (0, 0), (0, pad), (0, 0)))
    kb = k.reshape(b, MOBA_HEADS, n_blk, MOBA_BLOCK, HEAD_DIM)
    vb = v.reshape(b, MOBA_HEADS, n_blk, MOBA_BLOCK, HEAD_DIM)
    kmean = jnp.mean(kb.astype(jnp.float32), axis=3)
    n_sel = min(MOBA_TOPK, max(n_blk - 1, 1))
    n_g = n_sel * MOBA_BLOCK
    blk_id = jnp.arange(n_blk)
    bi = jnp.arange(b)[:, None, None, None]
    hi = jnp.arange(MOBA_HEADS)[None, :, None, None]
    scale = HEAD_DIM ** -0.5

    def chunk(c):
        t0 = c * Q_CHUNK
        tpos = t0 + jnp.arange(Q_CHUNK)
        cur = t0 // MOBA_BLOCK
        qc = lax.dynamic_slice_in_dim(q, t0, Q_CHUNK, axis=2)
        gate = jnp.einsum('bhqd,bhnd->bhqn', qc.astype(jnp.float32), kmean)
        gate = jnp.where(blk_id < cur, gate, -jnp.inf)
        _, sel = lax.top_k(gate, n_sel)
        kg = kb[bi, hi, sel].reshape(b, MOBA_HEADS, Q_CHUNK, n_g, HEAD_DIM)
        vg = vb[bi, hi, sel].reshape(b, MOBA_HEADS, Q_CHUNK, n_g, HEAD_DIM)
        mg = jnp.repeat(sel < cur, MOBA_BLOCK, axis=-1)
        ko = lax.dynamic_slice_in_dim(k, cur * MOBA_BLOCK, MOBA_BLOCK, axis=2)
        vo = lax.dynamic_slice_in_dim(v, cur * MOBA_BLOCK, MOBA_BLOCK, axis=2)
        mo = (cur * MOBA_BLOCK + jnp.arange(MOBA_BLOCK))[None, :] <= tpos[:, None]
        s_g = jnp.einsum('bhqd,bhqkd->bhqk', qc, kg)
        s_o = jnp.einsum('bhqd,bhkd->bhqk', qc, ko)
        mask = jnp.concatenate([mg, jnp.broadcast_to(mo, s_o.shape)], axis=-1)
        prob = _masked_softmax(jnp.concatenate([s_g, s_o], axis=-1) * scale, mask).astype(v.dtype)
        return jnp.einsum('bhqk,bhqkd->bhqd', prob[..., :n_g], vg) + jnp.einsum('bhqk,bhkd->bhqd', prob[..., n_g:], vo)

    o = lax.map(chunk, jnp.arange(s // Q_CHUNK))
    return jnp.transpose(o, (1, 0, 3, 2, 4)).reshape(b, s, D_MOBA)

def _conv_glu(h, w_in, conv_w, conv_b, w_out):
    u, gt = jnp.split(h @ w_in, 2, axis=-1)
    gt = lax.conv_general_dilated(gt, conv_w[:, None, :], window_strides=(1,), padding=[(CONV_WIDTH - 1, 0)], dimension_numbers=('NWC', 'WIO', 'NWC'), feature_group_count=D_FF) + conv_b
    return (jax.nn.silu(gt) * u) @ w_out

def second_inputs(seed: int = 0) -> dict:
    key = jax.random.key(seed)
    ks = iter(jax.random.split(key, 32))
    nrm = lambda shape, sc: jax.random.normal(next(ks), shape, jnp.float32) * sc
    gain = lambda shape: 1.0 + nrm(shape, 0.02)
    L = DEPTH
    resid = (2 * DEPTH) ** -0.5
    return {
        'x': nrm((BATCH, SEQ, D_MODEL), 1.0),
        'attn_norm': gain((L, D_MODEL)),
        'w_in': nrm((L, D_MODEL, N_IN), D_MODEL ** -0.5),
        'nsa_cmp_pos': nrm((L, 2, CMP_LEN, HEAD_DIM), 0.1),
        'nsa_cmp_w1': nrm((L, 2, CMP_LEN * HEAD_DIM, CMP_HIDDEN), (CMP_LEN * HEAD_DIM) ** -0.5),
        'nsa_cmp_w2': nrm((L, 2, CMP_HIDDEN, HEAD_DIM), CMP_HIDDEN ** -0.5),
        'nsa_out_gain': gain((L, D_NSA)),
        'rw_mu': jax.random.uniform(next(ks), (L, N_IN_RWKV), jnp.float32),
        'rw_w0': nrm((L, D_RWKV), 0.5),
        'rw_w2': nrm((L, RW_DECAY_LORA, D_RWKV), 0.5 * RW_DECAY_LORA ** -0.5),
        'rw_a0': nrm((L, D_RWKV), 0.5),
        'rw_a2': nrm((L, RW_AAA_LORA, D_RWKV), 0.5 * RW_AAA_LORA ** -0.5),
        'rw_g2': nrm((L, RW_GATE_LORA, D_RWKV), RW_GATE_LORA ** -0.5),
        'rw_k_k': 1.0 + nrm((L, D_RWKV), 0.1),
        'rw_k_a': 1.0 + nrm((L, D_RWKV), 0.1),
        'rw_r_k': nrm((L, RWKV_HEADS, HEAD_DIM), 0.1),
        'rw_lnx_w': gain((L, D_RWKV)),
        'rw_lnx_b': nrm((L, D_RWKV), 0.01),
        'moba_out_gain': gain((L, D_MOBA)),
        'w_out': nrm((L, D_MIX, D_MODEL), D_MIX ** -0.5 * resid),
        'ffn_norm': gain((L, D_MODEL)),
        'ffn_w_in': nrm((L, D_MODEL, 2 * D_FF), D_MODEL ** -0.5),
        'ffn_conv_w': nrm((L, CONV_WIDTH, D_FF), CONV_WIDTH ** -0.5),
        'ffn_conv_b': nrm((L, D_FF), 0.01),
        'ffn_w_out': nrm((L, D_FF, D_MODEL), D_FF ** -0.5 * resid),
        'final_norm': gain((D_MODEL,)),
    }

def second_block(x, attn_norm, w_in, nsa_cmp_pos, nsa_cmp_w1, nsa_cmp_w2, nsa_out_gain, rw_mu, rw_w0, rw_w2, rw_a0, rw_a2, rw_g2, rw_k_k, rw_k_a, rw_r_k, rw_lnx_w, rw_lnx_b, moba_out_gain, w_out, ffn_norm, ffn_w_in, ffn_conv_w, ffn_conv_b, ffn_w_out, final_norm):
    for l in range(DEPTH):
        h = _rmsnorm_2(x, attn_norm[l])
        proj = h @ w_in[l]
        p_nsa, p_rw, p_moba = _split(proj, [N_IN_NSA, N_IN_RWKV, N_IN_MOBA])
        o_nsa = _head_rmsnorm(_nsa_mixer(p_nsa, nsa_cmp_pos[l], nsa_cmp_w1[l], nsa_cmp_w2[l]), nsa_out_gain[l])
        o_rw = _rwkv7_mixer(p_rw, rw_mu[l], rw_w0[l], rw_w2[l], rw_a0[l], rw_a2[l], rw_g2[l], rw_k_k[l], rw_k_a[l], rw_r_k[l], rw_lnx_w[l], rw_lnx_b[l])
        o_moba = _head_rmsnorm(_moba_mixer(p_moba), moba_out_gain[l])
        x = x + jnp.concatenate([o_nsa, o_rw, o_moba], axis=-1) @ w_out[l]
        x = x + _conv_glu(_rmsnorm_2(x, ffn_norm[l]), ffn_w_in[l], ffn_conv_w[l], ffn_conv_b[l], ffn_w_out[l])
    return _rmsnorm_2(x, final_norm)


_first_inputs_2 = second_inputs


def second_inputs(seed=0):
    import zlib

    import numpy as np

    out = dict(_first_inputs_2(seed))
    spreads = {}
    factors = {'attn_norm': 2.959,
     'nsa_out_gain': 6.578,
     'rw_w2': 5.598,
     'rw_k_k': 8.0,
     'rw_k_a': 2.879,
     'rw_lnx_w': 8.0,
     'rw_lnx_b': 8.0,
     'moba_out_gain': 7.339,
     'ffn_norm': 6.102,
     'ffn_conv_b': 8.0,
     'final_norm': 2.808}
    for name, (base, spread) in spreads.items():
        noise = np.random.default_rng([zlib.crc32(name.encode()), seed]).standard_normal(out[name].shape)
        drawn = base * np.exp(spread * noise) if base else spread * noise
        out[name] = __import__('jax').numpy.asarray(drawn.astype(out[name].dtype))
    for name, factor in factors.items():
        out[name] = (out[name] * factor).astype(out[name].dtype)
    return out


_narrow_inputs_2 = second_inputs


def second_inputs(seed=0):

    out = dict(_narrow_inputs_2(seed))
    wider = {'nsa_out_gain': 3.66,
     'rw_k_k': 6.58,
     'rw_lnx_w': 7.02,
     'rw_lnx_b': 12.0,
     'moba_out_gain': 3.67,
     'ffn_conv_b': 5.07,
     'final_norm': 3.15}
    for name, times in wider.items():
        mean = out[name].mean()
        out[name] = (mean + times * (out[name] - mean)).astype(out[name].dtype)
    return out


CHUNK = 64
GMLP_BLOCK = 128
GMLP_WIDTH = D_MODEL
GMLP_GROUPS = 8
GMLP_GROUP_DIM = GMLP_WIDTH // GMLP_GROUPS
MLSTM_HEADS = 4
MLSTM_HEAD_DIM = 256
MLSTM_WIDTH = MLSTM_HEADS * MLSTM_HEAD_DIM
CONV_K = 4
FFN_DIM = 4 * D_MODEL

OFF_U = 0
OFF_V = OFF_U + GMLP_WIDTH
OFF_Q = OFF_V + GMLP_WIDTH
OFF_K = OFF_Q + MLSTM_WIDTH
OFF_MV = OFF_K + MLSTM_WIDTH
OFF_O = OFF_MV + MLSTM_WIDTH
OFF_I = OFF_O + MLSTM_WIDTH
OFF_F = OFF_I + MLSTM_HEADS
OFF_GA = OFF_F + MLSTM_HEADS
OFF_GB = OFF_GA + D_MODEL
IN_COLS = OFF_GB + D_MODEL


def rmsnorm(x, g):
    xf = x.astype(jnp.float32)
    y = xf * lax.rsqrt(jnp.mean(xf * xf, axis=-1, keepdims=True) + EPS)
    return y.astype(x.dtype) * g

def layernorm(x, g, b):
    xf = x.astype(jnp.float32)
    mu = jnp.mean(xf, axis=-1, keepdims=True)
    var = jnp.mean(jnp.square(xf - mu), axis=-1, keepdims=True)
    y = (xf - mu) * lax.rsqrt(var + EPS)
    return y.astype(x.dtype) * g + b

def modulate(xn, shift, scale):
    return xn * (1.0 + scale[:, None, :]) + shift[:, None, :]

def causal_dwconv(x, w, b):
    C = x.shape[-1]
    y = lax.conv_general_dilated(x, w[:, None, :], window_strides=(1,),
                                 padding=[(CONV_K - 1, 0)],
                                 dimension_numbers=('NWC', 'WIO', 'NWC'),
                                 feature_group_count=C)
    return y + b

def gmlp_branch(z_u, z_v, ln_g, ln_b, w_s, b_s):
    u = jax.nn.gelu(z_u)
    v = layernorm(jax.nn.gelu(z_v), ln_g, ln_b)
    B, S, _ = v.shape
    nb = S // GMLP_BLOCK
    v = v.reshape(B, nb, GMLP_BLOCK, GMLP_GROUPS, GMLP_GROUP_DIM)
    cid = jnp.arange(GMLP_BLOCK) // CHUNK
    mask = cid[None, :] <= cid[:, None]
    ws = jnp.where(mask[None], w_s, jnp.zeros_like(w_s))
    mixed = jnp.einsum('gts,bnsgc->bntgc', ws, v) + b_s.T[None, None, :, :, None]
    return u * mixed.reshape(B, S, GMLP_WIDTH)

def mlstm_branch(q, k, v, o_pre, i_pre, f_pre, hn_g):
    out_dtype = q.dtype
    B, S, _ = q.shape
    H, dh, L = MLSTM_HEADS, MLSTM_HEAD_DIM, CHUNK
    nc = S // L

    def heads(t):
        return t.astype(jnp.float32).reshape(B, nc, L, H, dh).transpose(1, 0, 3, 2, 4)

    def gates(t):
        return t.astype(jnp.float32).reshape(B, nc, L, H).transpose(1, 0, 3, 2)

    qh = heads(q) * (dh ** -0.5)
    kh = heads(k)
    vh = heads(v)
    li = gates(i_pre)
    lf = jax.nn.log_sigmoid(gates(f_pre))
    causal = jnp.tril(jnp.ones((L, L), dtype=bool))

    def step(carry, xs):
        C, n, m = carry
        qc, kc, vc, lic, lfc = xs
        bcum = jnp.cumsum(lfc, axis=-1)
        dmat = bcum[..., :, None] - bcum[..., None, :] + lic[..., None, :]
        dmat = jnp.where(causal, dmat, -jnp.inf)
        m_inter = bcum + m[..., None]
        m_t = jnp.maximum(m_inter, jnp.max(dmat, axis=-1))
        wts = jnp.exp(dmat - m_t[..., None])
        s = jnp.einsum('bhtd,bhsd->bhts', qc, kc) * wts
        inter = jnp.exp(m_inter - m_t)
        num = (jnp.einsum('bhts,bhsv->bhtv', s, vc)
               + inter[..., None] * jnp.einsum('bhtk,bhkv->bhtv', qc, C))
        den = jnp.sum(s, axis=-1) + inter * jnp.einsum('bhtk,bhk->bht', qc, n)
        h = num / jnp.maximum(jnp.abs(den), jnp.exp(-m_t))[..., None]
        b_last = bcum[..., -1]
        g = b_last[..., None] - bcum + lic
        m_new = jnp.maximum(b_last + m, jnp.max(g, axis=-1))
        decay = jnp.exp(b_last + m - m_new)
        wk = jnp.exp(g - m_new[..., None])[..., None] * kc
        C = decay[..., None, None] * C + jnp.einsum('bhsk,bhsv->bhkv', wk, vc)
        n = decay[..., None] * n + jnp.sum(wk, axis=2)
        return (C, n, m_new), h

    init = (jnp.zeros((B, H, dh, dh), jnp.float32),
            jnp.zeros((B, H, dh), jnp.float32),
            jnp.zeros((B, H), jnp.float32))
    _, h = lax.scan(step, init, (qh, kh, vh, li, lf))
    h = h.transpose(1, 0, 3, 2, 4).reshape(B, S, H, dh)
    mu = jnp.mean(h, axis=-1, keepdims=True)
    var = jnp.mean(jnp.square(h - mu), axis=-1, keepdims=True)
    h = (h - mu) * lax.rsqrt(var + EPS) * hn_g.astype(jnp.float32).reshape(H, dh)
    h = h.reshape(B, S, MLSTM_WIDTH) * jax.nn.sigmoid(o_pre.astype(jnp.float32))
    return h.astype(out_dtype)

def third_inputs(seed: int = 0) -> dict:
    key = jax.random.key(seed)
    ks = jax.random.split(key, 24)
    f32 = jnp.float32
    D = D_MODEL

    def nrm(k, shape, scale):
        return jax.random.normal(k, shape, f32) * scale

    f_bias = jnp.broadcast_to(jnp.linspace(3.0, 6.0, MLSTM_HEADS, dtype=f32), (DEPTH, MLSTM_HEADS))
    gate_b = jnp.stack([nrm(ks[7], (DEPTH, MLSTM_HEADS), 0.1),
                        f_bias + nrm(ks[8], (DEPTH, MLSTM_HEADS), 0.1)], axis=1)
    return {
        "x": nrm(ks[0], (BATCH, SEQ, D), 1.0),
        "c": nrm(ks[1], (BATCH, D), 1.0),
        "w_ada": nrm(ks[2], (DEPTH, D, 6 * D), 0.5 * D ** -0.5),
        "b_ada": nrm(ks[3], (DEPTH, 6 * D), 0.02),
        "norm1_g": 1.0 + nrm(ks[4], (DEPTH, D), 0.02),
        "w_in": nrm(ks[5], (DEPTH, D, IN_COLS), D ** -0.5),
        "conv_w": nrm(ks[6], (DEPTH, CONV_K, 2 * MLSTM_WIDTH), CONV_K ** -0.5),
        "conv_b": nrm(ks[9], (DEPTH, 2 * MLSTM_WIDTH), 0.02),
        "mlstm_gate_b": gate_b,
        "gmlp_ln_g": 1.0 + nrm(ks[10], (DEPTH, GMLP_WIDTH), 0.02),
        "gmlp_ln_b": nrm(ks[11], (DEPTH, GMLP_WIDTH), 0.02),
        "gmlp_ws": nrm(ks[12], (DEPTH, GMLP_GROUPS, GMLP_BLOCK, GMLP_BLOCK), 0.5 * GMLP_BLOCK ** -0.5),
        "gmlp_bs": 1.0 + nrm(ks[13], (DEPTH, GMLP_GROUPS, GMLP_BLOCK), 0.1),
        "mlstm_hn_g": 1.0 + nrm(ks[14], (DEPTH, MLSTM_WIDTH), 0.02),
        "w_out": nrm(ks[15], (DEPTH, D, D), D ** -0.5),
        "norm2_g": 1.0 + nrm(ks[16], (DEPTH, D), 0.02),
        "w_ff1": nrm(ks[17], (DEPTH, D, FFN_DIM), D ** -0.5),
        "w_ff2": nrm(ks[18], (DEPTH, FFN_DIM, D), FFN_DIM ** -0.5),
        "final_g": 1.0 + nrm(ks[19], (D,), 0.02),
    }

def third_block(x, c, w_ada, b_ada, norm1_g, w_in, conv_w, conv_b, mlstm_gate_b,
              gmlp_ln_g, gmlp_ln_b, gmlp_ws, gmlp_bs, mlstm_hn_g, w_out,
              norm2_g, w_ff1, w_ff2, final_g):
    h = x
    c_act = jax.nn.silu(c)
    for l in range(DEPTH):
        mod = c_act @ w_ada[l] + b_ada[l]
        sh1, sc1, g1, sh2, sc2, g2 = jnp.split(mod, 6, axis=-1)

        xn = modulate(rmsnorm(h, norm1_g[l]), sh1, sc1)
        p = xn @ w_in[l]
        qk = jax.nn.silu(causal_dwconv(p[..., OFF_Q:OFF_MV], conv_w[l], conv_b[l]))
        q, k = jnp.split(qk, 2, axis=-1)
        y_a = gmlp_branch(p[..., OFF_U:OFF_V], p[..., OFF_V:OFF_Q],
                          gmlp_ln_g[l], gmlp_ln_b[l], gmlp_ws[l], gmlp_bs[l])
        y_b = mlstm_branch(q, k, p[..., OFF_MV:OFF_O], p[..., OFF_O:OFF_I],
                           p[..., OFF_I:OFF_F] + mlstm_gate_b[l, 0],
                           p[..., OFF_F:OFF_GA] + mlstm_gate_b[l, 1],
                           mlstm_hn_g[l])
        merged = (jax.nn.sigmoid(p[..., OFF_GA:OFF_GB]) * y_a
                  + jax.nn.sigmoid(p[..., OFF_GB:IN_COLS]) * y_b)
        h = h + g1[:, None, :] * (merged @ w_out[l])

        xn = modulate(rmsnorm(h, norm2_g[l]), sh2, sc2)
        ff = jnp.square(jax.nn.relu(xn @ w_ff1[l])) @ w_ff2[l]
        h = h + g2[:, None, :] * ff
    return rmsnorm(h, final_g)


_first_inputs_3 = third_inputs


def third_inputs(seed=0):
    import zlib

    import numpy as np

    out = dict(_first_inputs_3(seed))
    spreads = {}
    factors = {'norm1_g': 8.0,
     'conv_b': 64.0,
     'gmlp_ln_g': 35.681,
     'gmlp_ln_b': 33.141,
     'gmlp_bs': 4.535,
     'mlstm_hn_g': 64.0,
     'norm2_g': 18.431,
     'final_g': 8.123,
     'conv_w': 6.234}
    for name, (base, spread) in spreads.items():
        noise = np.random.default_rng([zlib.crc32(name.encode()), seed]).standard_normal(out[name].shape)
        drawn = base * np.exp(spread * noise) if base else spread * noise
        out[name] = __import__('jax').numpy.asarray(drawn.astype(out[name].dtype))
    for name, factor in factors.items():
        out[name] = (out[name] * factor).astype(out[name].dtype)
    return out


_narrow_inputs_3 = third_inputs


def third_inputs(seed=0):

    out = dict(_narrow_inputs_3(seed))
    wider = {'conv_b': 12.0, 'gmlp_ln_g': 3.35, 'gmlp_ln_b': 3.3, 'mlstm_hn_g': 6.52, 'final_g': 3.21}
    for name, times in wider.items():
        mean = out[name].mean()
        out[name] = (mean + times * (out[name] - mean)).astype(out[name].dtype)
    return out


def setup_inputs(seed=0):
    out = dict(first_inputs(seed))
    for name, value in second_inputs(seed + 1).items():
        if name != "x":
            out[name + "_2"] = value
    for name, value in third_inputs(seed + 2).items():
        if name != "x":
            out[name + "_3"] = value
    return out


def reference(
    x, meta_tokens, rel_bias, attn_norm, w_in, b_gate, q_norm_sp, k_norm_sp, q_norm_df,
    k_norm_df, lam_q1, lam_k1, lam_q2, lam_k2, subln_df, w_br_sb, w_br_sp, w_br_df, w_out,
    ffn_norm, w_up, conv_w, conv_b, w_down, attn_norm_2, w_in_2, nsa_cmp_pos_2, nsa_cmp_w1_2,
    nsa_cmp_w2_2, nsa_out_gain_2, rw_mu_2, rw_w0_2, rw_w2_2, rw_a0_2, rw_a2_2, rw_g2_2,
    rw_k_k_2, rw_k_a_2, rw_r_k_2, rw_lnx_w_2, rw_lnx_b_2, moba_out_gain_2, w_out_2, ffn_norm_2,
    ffn_w_in_2, ffn_conv_w_2, ffn_conv_b_2, ffn_w_out_2, final_norm_2, c_3, w_ada_3, b_ada_3,
    norm1_g_3, w_in_3, conv_w_3, conv_b_3, mlstm_gate_b_3, gmlp_ln_g_3, gmlp_ln_b_3, gmlp_ws_3,
    gmlp_bs_3, mlstm_hn_g_3, w_out_3, norm2_g_3, w_ff1_3, w_ff2_3, final_g_3,
):
    x = first_block(
        x, meta_tokens, rel_bias, attn_norm, w_in, b_gate, q_norm_sp, k_norm_sp, q_norm_df,
        k_norm_df, lam_q1, lam_k1, lam_q2, lam_k2, subln_df, w_br_sb, w_br_sp, w_br_df, w_out,
        ffn_norm, w_up, conv_w, conv_b, w_down,
    )
    x = second_block(
        x, attn_norm_2, w_in_2, nsa_cmp_pos_2, nsa_cmp_w1_2, nsa_cmp_w2_2, nsa_out_gain_2,
        rw_mu_2, rw_w0_2, rw_w2_2, rw_a0_2, rw_a2_2, rw_g2_2, rw_k_k_2, rw_k_a_2, rw_r_k_2,
        rw_lnx_w_2, rw_lnx_b_2, moba_out_gain_2, w_out_2, ffn_norm_2, ffn_w_in_2, ffn_conv_w_2,
        ffn_conv_b_2, ffn_w_out_2, final_norm_2,
    )
    return third_block(
        x, c_3, w_ada_3, b_ada_3, norm1_g_3, w_in_3, conv_w_3, conv_b_3, mlstm_gate_b_3,
        gmlp_ln_g_3, gmlp_ln_b_3, gmlp_ws_3, gmlp_bs_3, mlstm_hn_g_3, w_out_3, norm2_g_3,
        w_ff1_3, w_ff2_3, final_g_3,
    )


_drawn_inputs = setup_inputs


def setup_inputs(seed=0):
    import zlib

    import numpy as np

    out = dict(_drawn_inputs(seed))
    spreads = {}
    factors = {'nsa_cmp_pos_2': 8.0,
     'nsa_out_gain_2': 4.444,
     'rw_w0_2': 4.581,
     'rw_k_k_2': 5.001,
     'rw_lnx_w_2': 3.308,
     'rw_lnx_b_2': 4.381,
     'moba_out_gain_2': 4.379,
     'conv_b_3': 6.391,
     'norm2_g_3': 2.782}
    for name, (base, spread) in spreads.items():
        noise = np.random.default_rng([zlib.crc32(name.encode()), seed]).standard_normal(out[name].shape)
        drawn = base * np.exp(spread * noise) if base else spread * noise
        out[name] = __import__('jax').numpy.asarray(drawn.astype(out[name].dtype))
    for name, factor in factors.items():
        out[name] = (out[name] * factor).astype(out[name].dtype)
    return out
```

```python
from contextlib import ExitStack
import math

import numpy as np
import concourse.bass as bass
from concourse import mybir

F32 = mybir.dt.float32
ALU = mybir.AluOpType
ACT = mybir.ActivationFunctionType
AX = mybir.AxisListType.X

P = 128
D = 1024
NC = D // P
META = 16
SEQ = 512
T1 = META + SEQ
D_FF = 2816
FT = D_FF // P
RING = 4
ARENA = 37200
NEG = -1e30
EPS = 1e-6
TOPK = T1 // 4
STRIP = 640
DIAG = 512
NR = STRIP + P - 1
BUCKETS = 32
NCMP = (SEQ - 32) // 16 + 1
CH = 32

SB_Q, SB_K, SB_V, SP_Q, SP_K, SP_V, IX_Q, IX_K, DF_Q, DF_K, DF_V, N1 = 0, 2, 4, 6, 8, 10, 12, 14, 15, 19, 23, 27
NQ, NKC, NVC, NKS, NVS, NKW, NVW, NG, RR, RK, RV, RL, MQ, MK, MV, N2 = (
    0, 3, 4, 5, 6, 7, 8, 9, 10, 12, 14, 16, 17, 20, 23, 26)


def pack_units(w):
    k, n = w.shape
    ku, nt = -(-k // D), -(-n // P)
    full = np.zeros((ku * D, nt * P), w.dtype)
    full[:k, :n] = w
    return full.reshape(ku, NC, P, nt, P).transpose(3, 0, 2, 1, 4).reshape(nt * ku, P, D)


def interleave(*parts):
    return np.stack(parts, 1).reshape(-1, P, D)


def columns(v):
    v = np.asarray(v).reshape(-1)
    m = -(-v.size // P)
    full = np.zeros(m * P, v.dtype)
    full[:v.size] = v
    return full.reshape(m, P).T


PARAMS = [
    ("attn_norm", 8), ("b_gate", 24), ("q_norm_sp", 1), ("k_norm_sp", 1), ("q_norm_df", 1), ("k_norm_df", 1),
    ("subln_df", 1), ("ffn_norm", 8), ("conv_w", 66), ("conv_b", 22),
    ("attn_norm_2", 8), ("nsa_out_gain_2", 3), ("rw_mu_2", 7), ("rw_w0_2", 2), ("rw_a0_2", 2), ("rw_k_k_2", 2),
    ("rw_k_a_2", 2), ("rw_r_k_2", 2), ("rw_lnx_w_2", 2), ("rw_lnx_b_2", 2), ("moba_out_gain_2", 3),
    ("ffn_norm_2", 8), ("ffn_conv_w_2", 66), ("ffn_conv_b_2", 22), ("final_norm_2", 8),
    ("c_3", 8), ("b_ada_3", 48), ("norm1_g_3", 8), ("conv_w_3", 64), ("conv_b_3", 16), ("mlstm_gate_b_3", 1),
    ("gmlp_ln_g_3", 8), ("gmlp_ln_b_3", 8), ("mlstm_hn_g_3", 8), ("norm2_g_3", 8), ("final_g_3", 8),
]
PCOL, NPAR = {}, 0
for _name, _m in PARAMS:
    PCOL[_name] = NPAR
    NPAR += _m


def params(a):
    v = {n: a[n] for n, _ in PARAMS}
    for n in ("q_norm_sp", "k_norm_sp", "q_norm_df", "k_norm_df"):
        v[n] = np.concatenate([a[n].reshape(-1)] * 2)
    g = a["mlstm_gate_b_3"].reshape(2, 4)
    rows = np.zeros(P, g.dtype)
    rows[0:4], rows[32:36] = g[0], g[1]
    v["mlstm_gate_b_3"] = rows
    return np.concatenate([columns(v[n]) for n, _ in PARAMS], 1)


CONSTS = [("ident", P), ("ones", P), ("pair64", P), ("flip", P), ("causal", STRIP), ("strict", P), ("strict_neg", P),
          ("heads", 4 * P), ("upper", P), ("eps6", 1), ("eps_rw", 1), ("zero", 1)]
NSA_CONSTS = [("cmp_bias", 24 * NCMP), ("cmp_keep", 24 * NCMP), ("gates", 9 * P)]
RWKV_CONSTS = [("mask32", 512), ("restart", SEQ), ("eye16", 512)]
WIDTH = dict(CONSTS + NSA_CONSTS + RWKV_CONSTS)
NCON = sum(m for _, m in CONSTS)


def constants():
    p, c = np.arange(P)[:, None], np.arange(P)[None, :]
    k = {}
    k["ident"] = p == c
    k["ones"] = np.ones((P, P))
    k["pair64"] = p // 64 == c // 64
    k["flip"] = p + c == P - 1
    k["causal"] = np.where(np.arange(STRIP)[None, :] <= p + DIAG, 0.0, NEG)
    k["strict"] = c < p
    k["strict_neg"] = np.where(c < p, 0.0, NEG)
    heads = np.zeros((P, 4, P))
    for h in range(4):
        heads[h, h], heads[32 + h, h] = 1, 1
    k["heads"] = heads.reshape(P, -1)
    q = np.arange(4)[None, :, None, None] * P + np.arange(P)[:, None, None, None]
    seen = (np.arange(NCMP) * 16 + 31 <= q) & np.ones((1, 1, 6, 1), bool)
    k["cmp_bias"] = np.where(seen, 0.0, NEG).reshape(P, -1)
    k["cmp_keep"] = seen.reshape(P, -1)
    b, t, f = np.arange(3)[None, :, None, None], np.arange(3)[None, None, :, None], np.arange(P)[None, None, None, :]
    k["gates"] = (np.arange(P)[:, None, None, None] == (2 * t + f // 64) * 3 + b).reshape(P, -1)
    s, t = np.arange(P)[:, None, None], np.arange(CH)[None, None, :]
    m = np.concatenate([s < t, s <= t], 1) & (s < CH)
    k["mask32"] = (m[:, None] & np.ones((1, 8, 1, 1), bool)).reshape(P, -1)
    k["restart"] = np.arange(SEQ)[None, :] % CH != 0
    k["restart"] = k["restart"] & np.ones((P, 1), bool)
    k["eye16"] = (np.arange(CH)[None, :, None] == 16 * (np.arange(P)[:, None, None] // 64) + np.arange(16)[None, None, :]).reshape(P, -1)
    k["upper"] = p <= c
    k["eps6"], k["eps_rw"], k["zero"] = np.full(P, EPS), np.full(P, 64e-5), np.zeros(P)
    return [np.concatenate([np.asarray(k[n], np.float32).reshape(P, -1) for n, _ in names], 1)
            for names in (CONSTS, NSA_CONSTS, RWKV_CONSTS)]


def bucket_rows():
    n = STRIP - 1 - np.arange(NR)
    m = np.maximum(n, 1).astype(np.float32)
    large = 16 + (np.log(m / np.float32(16)) / np.float32(math.log(8)) * 16).astype(np.int32)
    b = np.where(n < 16, np.maximum(n, 0), np.minimum(large, 31))
    out = np.zeros((BUCKETS + 1, NR), np.float32)
    out[b, np.arange(NR)] = 1
    out[:BUCKETS, n < 0] = 0
    out[BUCKETS] = n < 0
    return out


def lay_out(a):
    w = a["w_in"][0]
    cut = np.cumsum([0, 256, 256, 256, 256, 256, 256, 256, 32, 8, 512, 512, 512, D, D, D])
    col = [w[:, cut[i]:cut[i + 1]] for i in range(15)]
    units = [pack_units(c) for c in col[:7]]
    units += [pack_units(np.concatenate(col[7:9], 1))]
    units += [pack_units(c) for c in col[9:12]]
    br = np.concatenate([a["w_br_sb"][0], a["w_br_sp"][0], a["w_br_df"][0]], 0)
    units += [interleave(*[pack_units(c) for c in col[12:15]], pack_units(br))]
    units += [pack_units(a["w_out"][0])]
    up = a["w_up"][0]
    units += [interleave(pack_units(up[:, :D_FF]), pack_units(up[:, D_FF:]))]
    units += [pack_units(a["w_down"][0])]
    w = a["w_in_2"][0]
    cut = np.cumsum([0, 384, 128, 128, 128, 128, 128, 128, 18, 256, 256, 256, 128, 384, 384, 384])
    units += [pack_units(w[:, cut[i]:cut[i + 1]]) for i in range(15)]
    units += [pack_units(a["w_out_2"][0])]
    up = a["ffn_w_in_2"][0]
    units += [interleave(pack_units(up[:, D_FF:]), pack_units(up[:, :D_FF]))]
    units += [pack_units(a["ffn_w_out_2"][0])]
    units += [pack_units(a["w_ada_3"][0])]
    w = a["w_in_3"][0]
    u, v, qk, mv, o = w[:, :D], w[:, D:2 * D], w[:, 2 * D:4 * D], w[:, 4 * D:5 * D], w[:, 5 * D:6 * D]
    fi = np.zeros((D, P), w.dtype)
    fi[:, 0:4], fi[:, 32:36] = w[:, 6 * D:6 * D + 4], w[:, 6 * D + 4:6 * D + 8]
    ga, gb = w[:, 6 * D + 8:7 * D + 8], w[:, 7 * D + 8:]
    units += [pack_units(c) for c in (v, u, ga, qk, mv, fi, o, gb)]
    units += [pack_units(a[n][0]) for n in ("w_out_3", "w_ff1_3", "w_ff2_3")]
    fixed = constants()
    seq = np.concatenate([a["meta_tokens"], a["x"][0]], 0)
    return {
        "weights": np.concatenate(units, 0),
        "x": np.ascontiguousarray(seq.T.reshape(NC, P, T1).transpose(1, 0, 2)).reshape(P, -1),
        "params": params(a),
        "consts": fixed[0],
        "nsa_consts": fixed[1],
        "rwkv_consts": fixed[2],
        "bucket": bucket_rows(),
        "rel_bias": a["rel_bias"],
        "lam": np.concatenate([a[n].reshape(1, 64) for n in ("lam_q1", "lam_q2", "lam_k1", "lam_k2")], 1),
        "cmp_pos": a["nsa_cmp_pos_2"][0].reshape(2, 16, 2, 64).transpose(2, 3, 0, 1).reshape(P, 32),
        "cmp_w1": a["nsa_cmp_w1_2"][0].reshape(2, 16, P, 256).transpose(0, 2, 1, 3).reshape(2, P, 4096),
        "cmp_w2": a["nsa_cmp_w2_2"][0].reshape(2, 2, P, 64).transpose(2, 0, 1, 3).reshape(P, 256),
        "lora": np.concatenate([a["rw_w2_2"][0], a["rw_a2_2"][0], a["rw_g2_2"][0]], 0),
        "gmlp_ws": a["gmlp_ws_3"][0].transpose(2, 0, 1).reshape(P, -1),
        "gmlp_bs": a["gmlp_bs_3"][0].reshape(1, -1),
    }


class Signal:

    def __init__(self, sem, unit=1):
        self.sem, self.unit, self.base = sem, unit, 0

    def at(self, k):
        return self.base + self.unit * k

    def passed(self, k):
        self.base += self.unit * k


class Chain:

    def __init__(self, sem):
        self.sem, self.value = sem, 0

    def do(self, eng, ins):
        self.value += 1
        ins.then_inc(self.sem, 1)
        eng.wait_ge(self.sem, self.value)


def tile_loop(eng, n, tb, body):
    full = n // tb
    for j in range(min(tb, n)):
        body(0, j)
    if full > 2:
        with eng.Fori(1, full) as i:
            for j in range(tb):
                body(i, j)
    elif full == 2:
        for j in range(tb):
            body(1, j)
    if full:
        for j in range(n % tb):
            body(full, j)


def halves(T):
    return [(0, 264), (264, 264)] if T == T1 else [(0, T)]


class Core:

    def __init__(self, nc, ctx, dram):
        self.nc, self.ctx, self.dram = nc, ctx, dram
        self.signals = {}
        self.h_all = self.sb("h", [P, NC, T1])
        self.h = self.h_all[:, :, :]
        self.xn = self.sb("xn", [P, NC, T1])
        self.ring = self.sb("ring", [P, RING, NC, P])
        self.con = self.sb("con", [P, NCON])
        self.where = {}
        self.place(CONSTS, self.con)
        self.par = self.sb("par", [P, NPAR])
        self.arena = self.sb("arena", [P, ARENA])
        self.ps = ctx.enter_context(nc.psum_tensor("ps", [P, 8, 512], F32))
        self.flat = self.ps[:, :, :].rearrange("p b n -> p (b n)")
        self.arrived = [self.sem(f"weights_arrived{i}") for i in range(RING)]
        self.used = self.sem("weights_used")
        self.issued, self.taken = 0, 0
        self.total = dram["weights"].shape[0]
        self.vec = Chain(self.sem("vector_step"))
        self.act = Chain(self.sem("scalar_step"))
        self.pool = Chain(self.sem("pool_step"))

    def sb(self, name, shape):
        return self.ctx.enter_context(self.nc.sbuf_tensor(name, shape, F32))

    def sem(self, name):
        return self.ctx.enter_context(self.nc.semaphore(name))

    def sig(self, name, unit=1):
        if name not in self.signals:
            self.signals[name] = Signal(self.sem(name), unit)
        return self.signals[name]

    def place(self, names, area):
        o = 0
        for n, m in names:
            self.where[n] = area[:, o:o + m]
            o += m

    def c(self, name, n=None):
        return self.where[name][:, 0:n or WIDTH[name]]

    def p(self, name, j=0):
        o = PCOL[name]
        return self.par[:, bass.ds(o + j, 1)] if not isinstance(j, int) else self.par[:, o + j:o + j + 1]

    def area(self, start, *dims):
        n = int(np.prod(dims))
        assert start + n <= ARENA, (start, dims)
        v = self.arena[:, start:start + n]
        if len(dims) == 1:
            return v
        names = "abcd"[:len(dims)]
        return v.rearrange(f"p ({' '.join(names)}) -> p {' '.join(names)}", **dict(zip(names[1:], dims[1:])))

    def load_units(self, sp, units):
        a, b = self.issued, min(self.taken + units + RING, self.total)
        w = self.dram["weights"]

        def load(u, j, i):
            slot = u % RING
            if not isinstance(i, int) or u >= RING:
                sp.wait_ge(self.used, u - RING + 1 + i * RING)
            src = w[u:u + 1] if isinstance(i, int) else w[bass.ds(u + i * RING, 1)]
            sp.dma_start(self.ring[:, slot:slot + 1], src.rearrange("o p (c n) -> p o c n", c=NC)).then_inc(
                self.arrived[slot], 16)

        u = a
        while u < min(b, RING):
            load(u, 0, 0)
            u += 1
        rounds = (b - u) // RING
        if rounds > 1:
            with sp.Fori(0, rounds) as i:
                for j in range(RING):
                    load(u + j, j, i)
            u += rounds * RING
        while u < b:
            load(u, 0, 0)
            u += 1
        self.issued = max(b, a)

    def unit(self, pe, off, i=0, per=0):
        u = self.taken + off
        pe.wait_ge(self.arrived[u % RING], 16 * (u // RING + 1) + i * (16 * per // RING))
        return self.ring[:, u % RING]



def tile_of(buf, t, T):
    s = len(halves(T))
    if isinstance(t, int):
        return buf[:, t, 0:T].rearrange("p (s n) -> p s n", s=s)
    return buf[:, bass.ds(t, 1), 0:T].rearrange("p o (s n) -> p (o s) n", s=s)


def banks(core, slot, T):
    s, w = len(halves(T)), halves(T)[0][1]
    return core.ps[:, slot:slot + s, 0:w]


def out_slot(j, bank=0):
    return bank + 2 * (j % 2)


def gemm(core, pe, n, tb, upt, kc, rhs, T, free=None, free2=None):
    def body(i, j):
        t = i * tb + j
        if not isinstance(i, int) or t >= 2:
            if free2 is None:
                pe.wait_ge(free.sem, free.at(t - 1))
            else:
                own = free2 if j % 2 else free
                pe.wait_ge(own.sem, own.at(i * (tb // 2) + j // 2))
        for u in range(upt):
            w = core.unit(pe, j * upt + u, i, tb * upt)
            m = min(NC, kc - u * NC)
            for k in range(m):
                for s, (o, n_) in enumerate(halves(T)):
                    last = pe.matmul(core.ps[:, out_slot(j) + s, 0:n_], w[:, k, :], rhs[:, u * NC + k, o:o + n_],
                                     start=(u == 0 and k == 0), stop=(u == upt - 1 and k == m - 1))
            last.then_inc(core.used, 1)
    tile_loop(pe, n, tb, body)


def tile_done(core, eng, i, j, tb, upt=1):
    eng.wait_ge(core.used, core.taken + upt * (j + 1) + i * (upt * tb))


def project(core, n, dst, T, func=ACT.Copy, bias=None):
    free = core.sig("tile_free")
    with core.nc.Block() as block:
        @block.sync
        def _(sp):
            core.load_units(sp, n)

        @block.tensor
        def _(pe):
            gemm(core, pe, n, 4, 1, NC, core.xn, T, free)

        @block.scalar
        def _(act):
            def body(i, j):
                tile_done(core, act, i, j, 4)
                act.activation(tile_of(dst, i * 4 + j, T), banks(core, out_slot(j), T), func,
                               bias=core.p(bias) if bias else 0.0).then_inc(free.sem, 1)
            tile_loop(act, n, 4, body)
    free.passed(n)
    core.taken += n


def add_product(core, upt, kc, src, T, scale=None):
    free = core.sig("tile_free")
    tb = 4 if upt < 4 else 2
    with core.nc.Block() as block:
        @block.sync
        def _(sp):
            core.load_units(sp, NC * upt)

        @block.tensor
        def _(pe):
            gemm(core, pe, NC, tb, upt, kc, src, T, free)

        @block.vector
        def _(dve):
            def body(i, j):
                t = i * tb + j
                tile_done(core, dve, i, j, tb, upt)
                out, got = tile_of(core.h, t, T), banks(core, out_slot(j), T)
                if scale is None:
                    dve.tensor_tensor(out, got, out, ALU.add).then_inc(free.sem, 1)
                else:
                    dve.scalar_tensor_tensor(out=out, in0=got, scalar=scale(t), in1=out, op0=ALU.mult,
                                             op1=ALU.add).then_inc(free.sem, 1)
            tile_loop(dve, NC, tb, body)
    free.passed(NC)
    core.taken += NC * upt


def conv_glu_up(core, dst, tmp, T, conv_w, conv_b):
    free, gate_in, conv_out, act_out = (core.sig(n) for n in ("tile_free", "gate_in", "conv_out", "silu_out"))
    gate = core.area(tmp, 2, T + 2)
    mid = core.area(tmp + 2 * (T + 2), 2, 3, T)
    step = core.vec
    with core.nc.Block() as block:
        @block.sync
        def _(sp):
            core.load_units(sp, 2 * FT)

        @block.tensor
        def _(pe):
            gemm(core, pe, 2 * FT, 4, 1, NC, core.xn, T, gate_in, free)

        @block.scalar
        def _(act):
            core.act.do(act, act.activation(gate[:, :, 0:2], core.c("ones", 4).rearrange("p (b n) -> p b n", b=2),
                                            ACT.Copy, scale=0.0))

            def body(i, j):
                p = i * 2 + j
                act.wait_ge(core.used, core.taken + 2 * j + 1 + i * 4)
                if not isinstance(p, int) or p >= 2:
                    act.wait_ge(conv_out.sem, conv_out.at(p - 1))
                o = gate[:, j, 2:2 + T].rearrange("p (s n) -> p s n", s=len(halves(T)))
                act.activation(o, banks(core, out_slot(0), T), ACT.Copy).then_inc(gate_in.sem, 1)
                act.wait_ge(conv_out.sem, conv_out.at(p + 1))
                act.activation(mid[:, j, 2], mid[:, j, 1], ACT.Silu).then_inc(act_out.sem, 1)
            tile_loop(act, FT, 2, body)

        @block.vector
        def _(dve):
            base = step.value

            def body(i, j):
                p = i * 2 + j

                def ordered(k, ins):
                    ins.then_inc(step.sem, 1)
                    dve.wait_ge(step.sem, base + 2 * p + k)
                dve.wait_ge(gate_in.sem, gate_in.at(p + 1))
                ordered(1, dve.tensor_scalar(mid[:, j, 0], gate[:, j, 2:2 + T], core.p(conv_w, 2 * FT + p),
                                             core.p(conv_b, p), ALU.mult, ALU.add))
                ordered(2, dve.scalar_tensor_tensor(out=mid[:, j, 1], in0=gate[:, j, 1:1 + T],
                                                    scalar=core.p(conv_w, FT + p), in1=mid[:, j, 0], op0=ALU.mult,
                                                    op1=ALU.add))
                dve.scalar_tensor_tensor(out=mid[:, j, 1], in0=gate[:, j, 0:T], scalar=core.p(conv_w, p),
                                         in1=mid[:, j, 1], op0=ALU.mult, op1=ALU.add).then_inc(conv_out.sem, 1)
                dve.wait_ge(act_out.sem, act_out.at(p + 1))
                dve.wait_ge(core.used, core.taken + 2 * j + 2 + i * 4)
                s = mid[:, j, 2].rearrange("p (s n) -> p s n", s=len(halves(T)))
                dve.tensor_tensor(tile_of(dst, p, T), banks(core, out_slot(1), T), s, ALU.mult).then_inc(free.sem, 1)
            tile_loop(dve, FT, 2, body)
            step.value = base + 2 * FT
    for s in (free, gate_in, conv_out, act_out):
        s.passed(FT)
    core.taken += 2 * FT


def act_mul(core, parts, T, tmp, tiles=NC):
    free, mul = core.sig("tile_free"), core.sig("multiplied")
    mid = core.area(tmp, 2, T)
    prod = core.area(tmp + 2 * T, 2, T)
    S = len(halves(T))

    for func, other, dst, add in parts:
        with core.nc.Block() as block:
            @block.sync
            def _(sp):
                core.load_units(sp, tiles)

            @block.tensor
            def _(pe):
                gemm(core, pe, tiles, 4, 1, NC, core.xn, T, free)

            @block.scalar
            def _(act):
                def body(i, j):
                    t = i * 4 + j
                    tile_done(core, act, i, j, 4)
                    if not isinstance(t, int) or t >= 2:
                        act.wait_ge(mul.sem, mul.at(t - 1))
                    act.activation(mid[:, j % 2].rearrange("p (s n) -> p s n", s=S), banks(core, out_slot(j), T), func).then_inc(free.sem, 1)
                tile_loop(act, tiles, 4, body)

            @block.vector
            def _(dve):
                base = core.vec.value

                def body(i, j):
                    t = i * 4 + j
                    dve.wait_ge(free.sem, free.at(t + 1))
                    m = mid[:, j % 2].rearrange("p (s n) -> p s n", s=S)
                    o = m if other is None else tile_of(other, t, T)
                    if not add:
                        dve.tensor_tensor(tile_of(dst, t, T), m, o, ALU.mult).then_inc(mul.sem, 1)
                        return
                    pr = prod[:, j % 2].rearrange("p (s n) -> p s n", s=S)
                    dve.tensor_tensor(pr, m, o, ALU.mult).then_inc(mul.sem, 1)
                    dve.wait_ge(mul.sem, mul.at(t + 1))
                    out = tile_of(dst, t, T)
                    dve.tensor_tensor(out, out, pr, ALU.add)
                tile_loop(dve, tiles, 4, body)
        free.passed(tiles)
        mul.passed(tiles)
        core.taken += tiles


def norm(core, items, T, inv_n, tmp, eps="eps6", ones="ones", least=None):
    sq_ready, sq_used, sum_used, root_used = (core.sig(n) for n in ("square_ready", "square_used", "sum_used", "root_used"))
    sq = core.area(tmp, 2, T)
    r = core.area(tmp + 2 * T, 2, T)
    tiles = sum(len(x[0]) for x in items)
    with core.nc.Block() as block:
        @block.scalar
        def _(act):
            def root(n, t):
                act.wait_ge(sq_used.sem, sq_used.at(t))
                if n >= 2:
                    act.wait_ge(root_used.sem, root_used.at(n - 1))
                act.activation(r[:, n % 2].rearrange("p (s n) -> p s n", s=len(halves(T))), banks(core, out_slot(n), T),
                               ACT.Sqrt, bias=core.c(eps), scale=inv_n).then_inc(sum_used.sem, 1)

            t = 0
            for n, (x, _, _, _) in enumerate(items):
                for k, a in enumerate(x):
                    if t >= 2:
                        act.wait_ge(sq_used.sem, sq_used.at(t - 1))
                    act.activation(sq[:, t % 2], a, ACT.Square).then_inc(sq_ready.sem, 1)
                    t += 1
                    if n and k == 0:
                        root(n - 1, t - 1)
            root(len(items) - 1, t)

        @block.tensor
        def _(pe):
            t = 0
            for n, (x, _, _, _) in enumerate(items):
                if n >= 2:
                    pe.wait_ge(sum_used.sem, sum_used.at(n - 1))
                for k in range(len(x)):
                    pe.wait_ge(sq_ready.sem, sq_ready.at(t + 1))
                    for s, (o, w) in enumerate(halves(T)):
                        last = pe.matmul(core.ps[:, out_slot(n) + s, 0:w], core.c(ones), sq[:, t % 2, o:o + w],
                                         start=(k == 0), stop=(k == len(x) - 1))
                    last.then_inc(sq_used.sem, 1)
                    t += 1

        @block.vector
        def _(dve):
            do = lambda ins: core.vec.do(dve, ins)
            for n, (x, out, gains, shifts) in enumerate(items):
                rn = r[:, n % 2]
                dve.wait_ge(sum_used.sem, sum_used.at(n + 1))
                if least is not None:
                    do(dve.tensor_scalar(rn, rn, least, None, ALU.max))
                do(dve.reciprocal(rn, rn))
                for k, a in enumerate(x):
                    if gains is None:
                        ins = dve.tensor_tensor(out[k], a, rn, ALU.mult)
                    else:
                        ins = dve.scalar_tensor_tensor(out=out[k], in0=a, scalar=gains[k], in1=rn, op0=ALU.mult,
                                                       op1=ALU.mult)
                    if shifts is not None:
                        do(ins)
                        ins = dve.tensor_scalar(out[k], out[k], shifts[k], None, ALU.add)
                    if k < len(x) - 1:
                        do(ins)
                    else:
                        ins.then_inc(root_used.sem, 1)
    sq_ready.passed(tiles)
    sq_used.passed(tiles)
    sum_used.passed(len(items))
    root_used.passed(len(items))


def layer_norm_input(core, gain, T, tmp):
    x = [core.h[:, k, 0:T] for k in range(NC)]
    out = [core.xn[:, k, 0:T] for k in range(NC)]
    norm(core, [(x, out, [core.p(gain, k) for k in range(NC)], None)], T, 1.0 / D, tmp)


def load_small(core):
    d, got = core.dram, core.sig("loaded", 16)
    with core.nc.Block() as block:
        @block.sync
        def _(sp):
            sp.dma_start(core.h.rearrange("p c t -> p (c t)"), d["x"]).then_inc(got.sem, 16)
            sp.dma_start(core.con[:, :], d["consts"]).then_inc(got.sem, 16)
            sp.dma_start(core.par[:, :], d["params"]).then_inc(got.sem, 16)
            core.load_units(sp, 0)
            sp.wait_ge(got.sem, got.at(3))
    got.passed(3)


def q_tiles(T):
    return [(q, min(P, T - q), min(q + P, T)) for q in range(0, T, P)]


def to_tokens(core, pairs, T):
    turned, turned_used = core.sig("turned"), core.sig("turned_used")
    nj = len(q_tiles(T))
    with core.nc.Block() as block:
        @block.tensor
        def _(pe):
            n = 0
            for tiles, _ in pairs:
                for q, nq, _ in q_tiles(T):
                    if n >= 2:
                        pe.wait_ge(turned_used.sem, turned_used.at(n - 1))
                    for m, a in enumerate(tiles):
                        last = pe.transpose(core.ps[0:nq, 4 + n % 2, m * P:(m + 1) * P], a[:, q:q + nq], core.c("ident"))
                    last.then_inc(turned.sem, 1)
                    n += 1

        @block.vector
        def _(dve):
            n = 0
            for tiles, dst in pairs:
                for j, (q, nq, _) in enumerate(q_tiles(T)):
                    dve.wait_ge(turned.sem, turned.at(n + 1))
                    dve.tensor_copy(dst(j)[0:nq], core.ps[0:nq, 4 + n % 2, 0:len(tiles) * P]).then_inc(turned_used.sem, 1)
                    n += 1
    turned.passed(nj * len(pairs))
    turned_used.passed(nj * len(pairs))


class Head:

    def __init__(self, maps, values, out, strip=None, chosen=None):
        self.maps, self.values, self.out, self.strip, self.chosen = maps, values, out, strip, chosen


def attention(core, kind, heads, T, tmp, neg_lam=None):
    names = ("scores", "scores_used", "shifted", "exps", "probs", "turned", "turned_used", "out_ready", "out_used")
    scores, scores_used, shifted, exps, probs, turned, turned_used, out_ready, out_used = (core.sig(n) for n in names)
    nm = len(heads[0].maps)
    steps = [(h, i) for h in heads for i in range(len(q_tiles(T)))]
    N = len(steps)
    X = core.area(tmp, 2, nm, T)
    Y = core.area(tmp + 2 * nm * T, 2, T)
    PT = core.area(tmp + 2 * nm * T + 2 * T, 2, 512)
    stat = core.area(tmp + 2 * nm * T + 2 * T + 1024, 2, 2, 8)

    def psum_scores(s, m, nq, nk):
        b = 2 * ((s * nm + m) % 2)
        return core.flat[0:nq, b * 512:b * 512 + nk]

    with core.nc.Block() as block:
        @block.tensor
        def _(pe):
            def score(s):
                h, i = steps[s]
                q0, nq, nk = q_tiles(T)[i]
                for m, (q, k) in enumerate(h.maps):
                    n = s * nm + m
                    if n >= 2:
                        pe.wait_ge(scores_used.sem, scores_used.at(n - 1))
                    dst = psum_scores(s, m, nq, nk)
                    for o in range(0, nk, 512):
                        w = min(512, nk - o)
                        last = pe.matmul(dst[:, o:o + w], q[:, q0:q0 + nq], k[:, o:o + w], start=True, stop=True)
                    last.then_inc(scores.sem, 1)

            def turn(s):
                h, i = steps[s]
                q0, nq, nk = q_tiles(T)[i]
                pe.wait_ge(probs.sem, probs.at(s + 1))
                if s >= 2:
                    pe.wait_ge(turned_used.sem, turned_used.at(s - 1))
                for j, o in enumerate(range(0, nk, P)):
                    w = min(P, nk - o)
                    last = pe.transpose(core.ps[0:w, 4 + s % 2, j * nq:(j + 1) * nq], X[0:nq, s % 2, 0, o:o + w],
                                        core.c("ident")[0:nq, 0:nq])
                last.then_inc(turned.sem, 1)

            def weigh(s):
                h, i = steps[s]
                q0, nq, nk = q_tiles(T)[i]
                pe.wait_ge(turned_used.sem, turned_used.at(s + 1))
                if s >= 2:
                    pe.wait_ge(out_used.sem, out_used.at(s - 1))
                lo, n = h.out[0], h.out[1]
                for j, o in enumerate(range(0, nk, P)):
                    w = min(P, nk - o)
                    last = pe.matmul(core.ps[lo:lo + n, 6 + s % 2, 0:nq], h.values(j, w), PT[0:w, s % 2, j * nq:(j + 1) * nq],
                                     start=(j == 0), stop=(o + P >= nk))
                last.then_inc(out_ready.sem, 1)

            score(0)
            for s in range(N):
                if s + 1 < N:
                    score(s + 1)
                turn(s)
                if s:
                    weigh(s - 1)
            weigh(N - 1)

        @block.vector
        def _(dve):
            do = lambda ins: core.vec.do(dve, ins)

            def before(s):
                h, i = steps[s]
                q0, nq, nk = q_tiles(T)[i]
                o = DIAG - q0
                if s >= 2:
                    dve.wait_ge(turned.sem, turned.at(s - 1))
                for m in range(nm):
                    n = s * nm + m
                    x, got, st = X[0:nq, s % 2, m, 0:nk], psum_scores(s, m, nq, nk), stat[0:nq, s % 2, m]
                    if kind == "stick":
                        y = Y[0:nq, s % 2, 0:nk]
                        dve.wait_ge(exps.sem, exps.at(s + 1))
                        do(dve.scalar_tensor_tensor(out=y, in0=got, scalar=0.0, in1=y, op0=ALU.max, op1=ALU.add))
                        do(dve.tensor_tensor(y[:, q0:nk], y[:, q0:nk], core.c("strict")[0:nq, 0:nk - q0], ALU.mult))
                        do(dve.tensor_tensor_scan(x[:, ::-1], y[:, ::-1], y[:, ::-1], 0.0, ALU.add, ALU.bypass))
                        dve.tensor_tensor(x, got, x, ALU.subtract).then_inc(scores_used.sem, 1)
                        dve.wait_ge(scores_used.sem, scores_used.at(n + 1))
                        dve.tensor_tensor(x[:, q0:nk], x[:, q0:nk], core.c("strict_neg")[0:nq, 0:nk - q0],
                                          ALU.add).then_inc(shifted.sem, 1)
                        continue
                    strip = h.strip[0:nq, o:o + nk]
                    dve.wait_ge(scores.sem, scores.at(n + 1))
                    if h.chosen is not None and i:
                        dve.tensor_tensor(x, got, strip, ALU.add).then_inc(scores_used.sem, 1)
                        dve.wait_ge(scores_used.sem, scores_used.at(n + 1))
                        do(dve.tensor_tensor(x, x, h.chosen(i)[0:nq, 0:nk], ALU.add))
                    else:
                        dve.tensor_tensor(x, got, strip, ALU.add).then_inc(scores_used.sem, 1)
                        dve.wait_ge(scores_used.sem, scores_used.at(n + 1))
                    do(dve.tensor_reduce(st[:, 0:1], x, AX, ALU.max))
                    dve.tensor_scalar(st[:, 1:2], st[:, 0:1], -1.0, None, ALU.mult).then_inc(shifted.sem, 1)

            def after(s):
                h, i = steps[s]
                q0, nq, nk = q_tiles(T)[i]
                for m in range(nm):
                    x, st = X[0:nq, s % 2, m, 0:nk], stat[0:nq, s % 2, m]
                    dve.wait_ge(exps.sem, exps.at(s * nm + m + 1))
                    do(dve.reciprocal(st[:, 3:4], st[:, 2:3]))
                    if m == 0:
                        ins = dve.tensor_scalar(x, x, st[:, 3:4], None, ALU.mult)
                        if nm == 2:
                            do(ins)
                        else:
                            ins.then_inc(probs.sem, 1)
                    else:
                        do(dve.tensor_scalar(st[:, 4:5], st[:, 3:4], neg_lam[0:nq, 0:1], None, ALU.mult))
                        x0 = X[0:nq, s % 2, 0, 0:nk]
                        dve.scalar_tensor_tensor(out=x0, in0=x, scalar=st[:, 4:5], in1=x0, op0=ALU.mult,
                                                 op1=ALU.add).then_inc(probs.sem, 1)

            before(0)
            for s in range(N):
                if s + 1 < N:
                    before(s + 1)
                if kind != "stick":
                    after(s)

        @block.scalar
        def _(act):
            do = lambda ins: core.act.do(act, ins)

            def softplus(s):
                h, i = steps[s]
                q0, nq, nk = q_tiles(T)[i]
                got, y = psum_scores(s, 0, nq, nk), Y[0:nq, s % 2, 0:nk]
                act.wait_ge(scores.sem, scores.at(s + 1))
                if s >= 2:
                    act.wait_ge(scores_used.sem, scores_used.at(s - 1))
                do(act.activation(y, got, ACT.Abs))
                do(act.activation(y, y, ACT.Exp, scale=-1.0))
                act.activation(y, y, ACT.Ln, bias=1.0).then_inc(exps.sem, 1)

            def exp(s):
                h, i = steps[s]
                q0, nq, nk = q_tiles(T)[i]
                for m in range(nm):
                    x, st = X[0:nq, s % 2, m, 0:nk], stat[0:nq, s % 2, m]
                    act.wait_ge(shifted.sem, shifted.at(s * nm + m + 1))
                    if kind == "stick":
                        act.activation(x, x, ACT.Exp).then_inc(probs.sem, 1)
                    else:
                        act.activation(x, x, ACT.Exp, bias=st[:, 1:2], accum_out=st[:, 2:3]).then_inc(exps.sem, 1)

            def copy_turned(s):
                h, i = steps[s]
                q0, nq, nk = q_tiles(T)[i]
                act.wait_ge(turned.sem, turned.at(s + 1))
                if s >= 2:
                    act.wait_ge(out_ready.sem, out_ready.at(s - 1))
                full, rest = nk // P * nq, nk % P
                ins = act.activation(PT[:, s % 2, 0:full], core.ps[:, 4 + s % 2, 0:full], ACT.Copy)
                if rest:
                    core.act.do(act, ins)
                    ins = act.activation(PT[0:rest, s % 2, full:full + nq], core.ps[0:rest, 4 + s % 2, full:full + nq], ACT.Copy)
                ins.then_inc(turned_used.sem, 1)

            def copy_out(s):
                h, i = steps[s]
                q0, nq, nk = q_tiles(T)[i]
                lo, n, out = h.out
                act.wait_ge(out_ready.sem, out_ready.at(s + 1))
                act.activation(out[lo:lo + n, q0:q0 + nq], core.ps[lo:lo + n, 6 + s % 2, 0:nq], ACT.Copy).then_inc(out_used.sem, 1)

            if kind == "stick":
                softplus(0)
            for s in range(N):
                if kind == "stick" and s + 1 < N:
                    softplus(s + 1)
                exp(s)
                if s >= 1:
                    copy_turned(s - 1)
                if s >= 2:
                    copy_out(s - 2)
            copy_turned(N - 1)
            copy_out(N - 2)
            copy_out(N - 1)
    exps.passed(N * nm)
    scores.passed(N * nm)
    scores_used.passed(N * nm)
    shifted.passed(N * nm)
    for x in (probs, turned, turned_used, out_ready, out_used):
        x.passed(N)


def bias_strips(core, strips, tmp):
    got, made, row, back = (core.sig(n, u) for n, u in (
        ("strip_inputs", 16), ("strip_made", 1), ("strip_row", 1), ("strip_stored", 16)))
    done = [core.sig(f"strip_back{i}", 16) for i in range(2)]
    table = core.area(tmp, 8)
    hot = core.area(tmp + 8, NR)
    rows = core.area(tmp + 8 + NR, NR)
    skew = core.area(tmp + 8 + 2 * NR, 2, STRIP)
    scratch = core.dram["strip_scratch"]
    flipped, used = core.sig("strip_flipped"), core.sig("strip_used")
    with core.nc.Block() as block:
        @block.vector
        def _(dve):
            dve.memset(table[0:64, :], NEG).then_inc(made.sem, 1)
            dve.wait_ge(row.sem, row.at(1))
            dve.tensor_copy(rows[0:8, :], core.flat[0:8, 0:NR]).then_inc(row.sem, 1)
            for h in range(8):
                dve.wait_ge(flipped.sem, flipped.at(h + 1))
                dve.tensor_copy(strips[:, h, :].rearrange("p (s n) -> p s n", s=2),
                                core.ps[:, 2 + 2 * (h % 2):4 + 2 * (h % 2), 0:STRIP // 2]).then_inc(used.sem, 1)

        @block.sync
        def _(sp):
            sp.dma_start(hot[0:BUCKETS + 1, :], core.dram["bucket"]).then_inc(got.sem, 16)
            sp.wait_ge(made.sem, made.at(1))
            sp.dma_start(table[0:BUCKETS, :], core.dram["rel_bias"]).then_inc(got.sem, 16)
            sp.wait_ge(row.sem, row.at(2))
            sp.dma_start(scratch[:, :], rows[0:8, :]).then_inc(back.sem, 16)
            sp.wait_ge(back.sem, back.at(1))
            for h in range(8):
                if h >= 2:
                    sp.wait_ge(flipped.sem, flipped.at(h - 1))
                src = bass.AP(scratch.tensor, scratch.offset + h * NR, [[1, P], [1, STRIP]])
                sp.dma_start(skew[:, h % 2], src).then_inc(done[h % 2].sem, 16)

        @block.tensor
        def _(pe):
            pe.wait_ge(got.sem, got.at(2))
            for o in range(0, NR, 512):
                w = min(512, NR - o)
                last = pe.matmul(core.flat[0:8, o:o + w], table[0:BUCKETS + 1, :], hot[0:BUCKETS + 1, o:o + w],
                                 start=True, stop=True)
            last.then_inc(row.sem, 1)
            for h in range(8):
                pe.wait_ge(done[h % 2].sem, done[h % 2].at(h // 2 + 1))
                if h >= 2:
                    pe.wait_ge(used.sem, used.at(h - 1))
                for s in range(2):
                    n = STRIP // 2
                    last = pe.matmul(core.ps[:, 2 + 2 * (h % 2) + s, 0:n], core.c("flip"), skew[:, h % 2, s * n:(s + 1) * n],
                                     start=True, stop=True)
                last.then_inc(flipped.sem, 1)
    got.passed(2), made.passed(1), row.passed(2), back.passed(1), done[0].passed(4), done[1].passed(4), flipped.passed(8), used.passed(8)


def choose_keys(core, P1, kx, chosen, tmp):
    copied, turned, weighed = core.sig("ix_copied"), core.sig("ix_turned"), core.sig("ix_weights")
    dots, dots_used, relus, relus_used = (core.sig(n) for n in ("ix_dots", "ix_dots_used", "ix_relus", "ix_relus_used"))
    w = core.area(tmp, 5, 8)
    R = core.area(tmp + 40, 2, T1)
    S = core.area(tmp + 40 + 2 * T1, T1)
    W = core.area(tmp + 40 + 3 * T1, T1)
    m8 = core.area(tmp + 40 + 4 * T1, 8)
    need = core.area(tmp + 48 + 4 * T1, 1)
    tiles = q_tiles(T1)
    steps = [(i, j) for i in range(1, 5) for j in range(8)]
    with core.nc.Block() as block:
        @block.gpsimd
        def _(pool):
            for g in range(4):
                ins = pool.tensor_copy(kx[32 * g:32 * g + 32, :], P1[0:32, IX_K, :])
                if g < 3:
                    core.pool.do(pool, ins)
            ins.then_inc(copied.sem, 1)

        @block.tensor
        def _(pe):
            for i, (q0, nq, _) in enumerate(tiles):
                last = pe.transpose(core.ps[0:nq, 4, 8 * i:8 * i + 8], P1[32:40, IX_K, q0:q0 + nq],
                                    core.c("ident")[32:40, 32:40])
            last.then_inc(turned.sem, 1)
            pe.wait_ge(copied.sem, copied.at(1))
            for n, (i, j) in enumerate(steps):
                q0, nq, nk = tiles[i]
                g = 32 * (j % 4)
                if n >= 2:
                    pe.wait_ge(dots_used.sem, dots_used.at(n - 1))
                b = 2 * (n % 2)
                for o in range(0, nk, 512):
                    v = min(512, nk - o)
                    last = pe.matmul(core.flat[0:nq, b * 512 + o:b * 512 + o + v], P1[g:g + 32, IX_Q + j // 4, q0:q0 + nq],
                                     kx[g:g + 32, o:o + v], start=True, stop=True)
                last.then_inc(dots.sem, 1)

        @block.scalar
        def _(act):
            for n, (i, j) in enumerate(steps):
                q0, nq, nk = tiles[i]
                act.wait_ge(dots.sem, dots.at(n + 1))
                if n >= 2:
                    act.wait_ge(relus_used.sem, relus_used.at(n - 1))
                b = 2 * (n % 2)
                act.activation(R[0:nq, n % 2, 0:nk], core.flat[0:nq, b * 512:b * 512 + nk], ACT.Relu).then_inc(dots_used.sem, 1)

        @block.vector
        def _(dve):
            do = lambda ins: core.vec.do(dve, ins)
            dve.wait_ge(turned.sem, turned.at(1))
            do(dve.tensor_copy(w[:, 0:4].rearrange("p a b -> p (a b)"), core.ps[:, 4, 0:32]))
            do(dve.tensor_copy(w[0:16, 4], core.ps[0:16, 4, 32:40]))
            for n, (i, j) in enumerate(steps):
                q0, nq, nk = tiles[i]
                s, wk, c = S[0:nq, 0:nk], W[0:nq, 0:nk], chosen(i)[0:nq, 0:nk]
                dve.wait_ge(dots_used.sem, dots_used.at(n + 1))
                prev = core.c("causal")[0:nq, DIAG - q0:DIAG - q0 + nk] if j == 0 else s
                dve.scalar_tensor_tensor(out=s, in0=R[0:nq, n % 2, 0:nk], scalar=w[0:nq, i, j:j + 1], in1=prev,
                                         op0=ALU.mult, op1=ALU.add).then_inc(relus_used.sem, 1)
                dve.wait_ge(relus_used.sem, relus_used.at(n + 1))
                if j < 7:
                    continue
                m, nd = m8[0:nq, :], need[0:nq, :]
                for k in range(TOPK // 8):
                    src = s if k == 0 else wk
                    do(dve.max(m, src))
                    do(dve.match_replace(wk, m, src, -3e38))
                do(dve.max(m, wk))
                t = m[:, TOPK % 8 - 1:TOPK % 8]
                do(dve.tensor_scalar(c, s, t, None, ALU.is_gt))
                do(dve.tensor_reduce(nd, c, AX, ALU.add))
                do(dve.tensor_scalar(nd, nd, -1.0, float(TOPK), ALU.mult, ALU.add))
                do(dve.tensor_scalar(s, s, t, None, ALU.is_equal))
                do(dve.tensor_tensor_scan(wk, s, s, 0.0, ALU.add, ALU.bypass))
                do(dve.scalar_tensor_tensor(out=s, in0=wk, scalar=nd, in1=s, op0=ALU.is_le, op1=ALU.mult))
                do(dve.tensor_tensor(c, c, s, ALU.add))
                do(dve.tensor_scalar(c, c, -NEG, NEG, ALU.mult, ALU.add))
    assert TOPK % 8
    for x in (copied, turned):
        x.passed(1)
    for x in (dots, dots_used, relus_used):
        x.passed(len(steps))


def difference_weight(core, neg_lam, tmp):
    got, sums, exps, lam, spread = (core.sig(n, u) for n, u in (
        ("lam_loaded", 16), ("lam_sums", 1), ("lam_exps", 1), ("lam_ready", 1), ("lam_spread", 1)))
    v, pr, s = core.area(tmp, 256), core.area(tmp + 256, 2, 64), core.area(tmp + 384, 8)
    init = 0.8 - 0.6 * math.exp(-0.3 * 0)
    with core.nc.Block() as block:
        @block.sync
        def _(sp):
            sp.dma_start(v[0:1, :], core.dram["lam"]).then_inc(got.sem, 16)

        @block.vector
        def _(dve):
            do = lambda ins: core.vec.do(dve, ins)
            dve.wait_ge(got.sem, got.at(1))
            do(dve.tensor_tensor(pr[0:1].rearrange("p a b -> p (a b)"), v[0:1, 0:128], v[0:1, 128:256], ALU.mult))
            dve.tensor_reduce(s[0:1, 0:2], pr[0:1], AX, ALU.add).then_inc(sums.sem, 1)
            dve.wait_ge(exps.sem, exps.at(1))
            do(dve.tensor_tensor(s[0:1, 4:5], s[0:1, 3:4], s[0:1, 2:3], ALU.subtract))
            dve.tensor_scalar(s[0:1, 5:6], s[0:1, 4:5], -init, None, ALU.add).then_inc(lam.sem, 1)
            dve.wait_ge(spread.sem, spread.at(1))
            do(dve.tensor_copy(neg_lam, core.ps[:, 0, 0:1]))
            do(dve.tensor_scalar(core.p("subln_df"), core.p("subln_df"), 1.0 - init, None, ALU.mult))
            do(dve.tensor_scalar(core.p("q_norm_sp"), core.p("q_norm_sp"), 0.125, None, ALU.mult))
            do(dve.tensor_scalar(core.p("q_norm_df"), core.p("q_norm_df"), 0.125, None, ALU.mult))

        @block.scalar
        def _(act):
            act.wait_ge(sums.sem, sums.at(1))
            act.activation(s[0:1, 2:4], s[0:1, 0:2], ACT.Exp).then_inc(exps.sem, 1)

        @block.tensor
        def _(pe):
            pe.wait_ge(lam.sem, lam.at(1))
            pe.matmul(core.ps[:, 0, 0:1], core.c("ones")[0:1, :], s[0:1, 5:6], start=True, stop=True).then_inc(spread.sem, 1)
    for x in (got, sums, exps, lam, spread):
        x.passed(1)


def scale_tiles(core, tiles, factor):
    with core.nc.Block() as block:
        @block.vector
        def _(dve):
            for a in tiles:
                dve.tensor_scalar(a, a, factor, None, ALU.mult)



def merge_branches(core, Y, merged, tmp):
    gate, branch, branch_used, merge = (core.sig(n) for n in ("gate_ready", "branch", "branch_used", "merge_step"))
    g = core.area(tmp, 2, 3, T1)
    m = core.area(tmp + 6 * T1, 2, T1)
    cuts = [(0, 2), (2, 4), (4, 8)]
    hv = halves(T1)
    parts = lambda a: a.rearrange("p (s n) -> p s n", s=2)

    with core.nc.Block() as block:
        @block.sync
        def _(sp):
            core.load_units(sp, 4 * NC)

        @block.tensor
        def _(pe):
            def body(i, j):
                t = 2 * i + j
                for b in range(3):
                    w = core.unit(pe, 4 * j + b, i, 8)
                    if not isinstance(t, int) or 3 * t + b >= 2:
                        pe.wait_ge(gate.sem, gate.at(3 * t + b - 1))
                    for k in range(NC):
                        for s, (o, n) in enumerate(hv):
                            last = pe.matmul(core.ps[:, out_slot(3 * j + b) + s, 0:n], w[:, k, :], core.xn[:, k, o:o + n],
                                             start=(k == 0), stop=(k == NC - 1))
                    last.then_inc(core.used, 1)
                w = core.unit(pe, 4 * j + 3, i, 8)
                for b, (lo, hi) in enumerate(cuts):
                    if not isinstance(t, int) or 3 * t + b >= 2:
                        pe.wait_ge(branch_used.sem, branch_used.at(3 * t + b - 1))
                    for k in range(lo, hi):
                        for s, (o, n) in enumerate(hv):
                            last = pe.matmul(core.ps[:, out_slot(3 * j + b, 4) + s, 0:n], w[:, k, :], Y[:, k, o:o + n],
                                             start=(k == lo), stop=(k == hi - 1))
                    if b < 2:
                        last.then_inc(branch.sem, 1)
                last.then_inc(core.used, 1)
            tile_loop(pe, NC, 2, body)

        @block.scalar
        def _(act):
            def body(i, j):
                t = 2 * i + j
                if not isinstance(t, int) or t >= 2:
                    act.wait_ge(merge.sem, merge.at(2 * t - 2))
                for b in range(3):
                    act.wait_ge(core.used, core.taken + 4 * j + b + 1 + i * 8)
                    act.activation(parts(g[:, j, b]), banks(core, out_slot(3 * j + b), T1), ACT.Sigmoid,
                                   bias=core.p("b_gate", t + NC * b)).then_inc(gate.sem, 1)
            tile_loop(act, NC, 2, body)

        @block.vector
        def _(dve):
            def body(i, j):
                t = 2 * i + j
                out = tile_of(merged, t, T1)
                for b in range(3):
                    dve.wait_ge(gate.sem, gate.at(3 * t + b + 1))
                    if b < 2:
                        dve.wait_ge(branch.sem, branch.at(2 * t + b + 1))
                    else:
                        dve.wait_ge(core.used, core.taken + 4 * j + 4 + i * 8)
                    to = out if b == 0 else parts(m[:, b - 1])
                    dve.tensor_tensor(to, banks(core, out_slot(3 * j + b, 4), T1), parts(g[:, j, b]),
                                      ALU.mult).then_inc(branch_used.sem, 1)
                    dve.wait_ge(branch_used.sem, branch_used.at(3 * t + b + 1))
                    if b:
                        dve.tensor_tensor(out, out, to, ALU.add).then_inc(merge.sem, 1)
                        dve.wait_ge(merge.sem, merge.at(2 * t + b))
            tile_loop(dve, NC, 2, body)
    gate.passed(3 * NC), branch.passed(2 * NC), branch_used.passed(3 * NC), merge.passed(2 * NC)
    core.taken += 4 * NC


def first_block(core, stop=None):
    T = T1
    P1 = core.area(0, N1, T)
    at = N1 * T
    strips = core.area(at, 8, STRIP)
    at += 8 * STRIP
    VT = core.area(at, 5, 8, P)
    at += 40 * P
    Y = core.area(at, NC, T)
    at += NC * T
    neg_lam = core.area(at, 1)
    tmp = at + 8
    layer_norm_input(core, "attn_norm", T, tmp)
    difference_weight(core, neg_lam, tmp)
    bias_strips(core, strips, tmp)
    project(core, N1, P1, T)

    to_tokens(core, [([P1[:, SB_V, :], P1[:, SB_V + 1, :], P1[:, SP_V, :], P1[:, SP_V + 1, :]],
                      lambda j: VT[:, j, 0:4].rearrange("p a b -> p (a b)")),
                     ([P1[:, DF_V + t, :] for t in range(4)],
                      lambda j: VT[:, j, 4:8].rearrange("p a b -> p (a b)"))], T)
    normed = [(SP_Q, 2, "q_norm_sp"), (SP_K, 2, "k_norm_sp"), (DF_Q, 4, "q_norm_df"), (DF_K, 4, "k_norm_df")]
    norm(core, [([P1[:, a + t, :]], [P1[:, a + t, :]], [core.p(g)], None) for a, n, g in normed for t in range(n)],
         T, 1.0 / 64, tmp, ones="pair64")
    scale_tiles(core, [P1[:, SB_Q + t, :] for t in range(2)], 0.125)

    kx = P1[:, SB_V, :]
    spots = {i: P1[:, DF_V + i - 1, :] for i in range(1, 5)}
    choose_keys(core, P1, kx, lambda i: spots[i], tmp)

    def half(t, h):
        lo = 64 * (h % 2)
        return lambda base: P1[lo:lo + 64, base + h // 2, :]

    def values(v, lo, n):
        return lambda j, w: VT[0:w, j, v, lo:lo + n]

    sb = [Head([(half(0, h)(SB_Q), half(0, h)(SB_K))], values(h // 2, 64 * (h % 2), 64), (64 * (h % 2), 64, Y[:, h // 2, :]))
          for h in range(4)]
    attention(core, "stick", sb, T, tmp)
    sp_ = [Head([(half(0, h)(SP_Q), half(0, h)(SP_K))], values(2 + h // 2, 64 * (h % 2), 64),
                (64 * (h % 2), 64, Y[:, 2 + h // 2, :]), strips[:, h, :], lambda i: spots[i]) for h in range(4)]
    attention(core, "soft", sp_, T, tmp)
    df = [Head([(P1[lo:lo + 64, DF_Q + h, :], P1[lo:lo + 64, DF_K + h, :]) for lo in (0, 64)], values(4 + h, 0, P),
               (0, P, Y[:, 4 + h, :]), strips[:, 4 + h, :]) for h in range(4)]
    attention(core, "diff", df, T, tmp, neg_lam)
    norm(core, [([Y[:, 4 + h, :]], [Y[:, 4 + h, :]], [core.p("subln_df")], None) for h in range(4)], T, 1.0 / P, tmp)
    if stop == "Y":
        return Y, P1, spots

    merged = core.area(0, NC, T)
    merge_branches(core, Y, merged, NC * T)
    add_product(core, 1, NC, merged, T)
    feed_forward(core, T, "ffn_norm", "conv_w", "conv_b")


def feed_forward(core, T, gain, conv_w, conv_b):
    hidden = core.area(0, FT, T)
    tmp = FT * T
    layer_norm_input(core, gain, T, tmp)
    conv_glu_up(core, hidden, tmp, T, conv_w, conv_b)
    add_product(core, 3, FT, hidden, T)


def load_constants(core, names, dram, area):
    got = core.sig("constants", 16)
    with core.nc.Block() as block:
        @block.sync
        def _(sp):
            sp.dma_start(area, core.dram[dram]).then_inc(got.sem, 16)
            sp.wait_ge(got.sem, got.at(1))
    got.passed(1)
    core.place(names, area)


def compress(core, P2, KC, VC, tmp):
    got, blocks, hidden, act_out, out, kept = (core.sig(n, u) for n, u in (
        ("cmp_loaded", 16), ("cmp_blocks", 1), ("cmp_hidden", 1), ("cmp_gelu", 1), ("cmp_out", 1), ("cmp_kept", 1)))
    w1 = core.area(tmp, 2, 16, 256)
    w2 = core.area(tmp + 8192, 2, 2, 64)
    pos = core.area(tmp + 8448, 2, 16)
    X = core.area(tmp + 8480, 2, 16, 2 * NCMP)
    H = core.area(tmp + 8480 + 64 * NCMP, 2, 2, 2 * NCMP)
    with core.nc.Block() as block:
        @block.sync
        def _(sp):
            for e in range(2):
                sp.dma_start(w1[:, e].rearrange("p a b -> p (a b)"), core.dram["cmp_w1"][e]).then_inc(got.sem, 16)
            sp.dma_start(w2.rearrange("p a b c -> p (a b c)"), core.dram["cmp_w2"]).then_inc(got.sem, 16)
            sp.dma_start(pos.rearrange("p a b -> p (a b)"), core.dram["cmp_pos"]).then_inc(got.sem, 16)

        @block.vector
        def _(dve):
            for e in range(2):
                for g in range(2):
                    v = P2[64 * g:64 * g + 64, NKC + e, :].rearrange("p (n l two) -> p two l n", l=8, two=2)
                    for half in range(2):
                        for late in range(2):
                            ins = dve.tensor_copy(
                                X[64 * half:64 * half + 64, e, 8 * late:8 * late + 8, g * NCMP:(g + 1) * NCMP],
                                v[:, half, :, late:late + NCMP])
                core.vec.do(dve, ins)
            dve.wait_ge(got.sem, got.at(4))
            for e in range(2):
                dve.tensor_tensor(X[:, e], X[:, e], pos[:, e].unsqueeze(2).broadcast_to([P, 16, 2 * NCMP]),
                                  ALU.add).then_inc(blocks.sem, 1)
            dve.wait_ge(out.sem, out.at(1))
            dve.tensor_copy(KC, core.ps[:, 4, 0:2 * NCMP]).then_inc(kept.sem, 1)
            dve.tensor_copy(VC[0:NCMP], core.ps[0:NCMP, 5, 0:P].rearrange("p (a b) -> p a b", a=2)).then_inc(kept.sem, 1)

        @block.tensor
        def _(pe):
            pe.wait_ge(got.sem, got.at(4))
            for e in range(2):
                pe.wait_ge(blocks.sem, blocks.at(e + 1))
                for c in range(2):
                    for l in range(16):
                        last = pe.matmul(core.ps[:, 2 * e + c, 0:2 * NCMP], w1[:, e, l, c * P:(c + 1) * P], X[:, e, l],
                                         start=(l == 0), stop=(l == 15))
                    last.then_inc(hidden.sem, 1)
            pe.wait_ge(act_out.sem, act_out.at(4))
            for lo in (0, 64):
                for c in range(2):
                    pe.matmul(core.ps[lo:lo + 64, 4, 0:2 * NCMP], w2[:, 0, c], H[:, 0, c], start=(c == 0), stop=(c == 1))
            for g in range(2):
                for c in range(2):
                    last = pe.matmul(core.ps[0:NCMP, 5, 64 * g:64 * g + 64], H[:, 1, c, g * NCMP:(g + 1) * NCMP], w2[:, 1, c],
                                     start=(c == 0), stop=(c == 1))
            last.then_inc(out.sem, 1)

        @block.scalar
        def _(act):
            for n in range(4):
                act.wait_ge(hidden.sem, hidden.at(n + 1))
                act.activation(H[:, n // 2, n % 2], core.ps[:, n, 0:2 * NCMP], ACT.Gelu_apprx_tanh).then_inc(act_out.sem, 1)
    got.passed(4), blocks.passed(2), hidden.passed(4), act_out.passed(4), out.passed(1), kept.passed(2)


def compressed_attention(core, P2, KC, VC, OC, tmp):
    scores, shifted, exps, probs, turned, pt, out, kept = (core.sig(n) for n in (
        "cmp_scores", "cmp_shifted", "cmp_exps", "cmp_probs", "cmp_turned", "cmp_pt", "cmp_weighed", "cmp_copied"))
    X = core.area(tmp, 24, NCMP)
    st = core.area(tmp + 24 * NCMP, 2, 24)
    PT = core.area(tmp + 24 * NCMP + 48, 2, 6 * P)
    wide = [P, 24, NCMP]
    with core.nc.Block() as block:
        @block.tensor
        def _(pe):
            for i in range(4):
                for h in range(6):
                    lo, g = 64 * (h % 2), h // 3
                    o = h // 2 * NCMP
                    last = pe.matmul(core.ps[:, 4 * (h % 2) + i, o:o + NCMP], P2[lo:lo + 64, NQ + h // 2, i * P:(i + 1) * P],
                                     KC[lo:lo + 64, g * NCMP:(g + 1) * NCMP], start=True, stop=True)
            last.then_inc(scores.sem, 1)
            pe.wait_ge(probs.sem, probs.at(1))
            for i in range(4):
                if i >= 1:
                    pe.wait_ge(pt.sem, pt.at(i))
                for h in range(6):
                    last = pe.transpose(core.flat[0:NCMP, 2048 + h * P:2048 + (h + 1) * P], X[:, i * 6 + h % 2 * 3 + h // 2], core.c("ident"))
                last.then_inc(turned.sem, 1)
                pe.wait_ge(pt.sem, pt.at(i + 1))
                if i >= 2:
                    pe.wait_ge(kept.sem, kept.at(i - 1))
                for h in range(6):
                    lo, g = 64 * (h % 2), h // 3
                    last = pe.matmul(core.ps[lo:lo + 64, 6 + i % 2, h // 2 * P:(h // 2 + 1) * P], VC[0:NCMP, g],
                                     PT[0:NCMP, i % 2, h * P:(h + 1) * P], start=True, stop=True)
                last.then_inc(out.sem, 1)

        @block.vector
        def _(dve):
            do = lambda ins: core.vec.do(dve, ins)
            dve.wait_ge(scores.sem, scores.at(1))
            for odd in range(2):
                ins = dve.tensor_tensor(X.rearrange("p (a o b) c -> p a o (b c)", a=4, o=2)[:, :, odd],
                                        core.ps[:, 4 * odd:4 * odd + 4, 0:3 * NCMP],
                                        core.c("cmp_bias").rearrange("p (a o b) -> p a o b", a=4, o=2)[:, :, odd], ALU.add)
            do(ins)
            do(dve.tensor_reduce(st[:, 0], X, AX, ALU.max))
            dve.tensor_tensor(X, X, st[:, 0].unsqueeze(2).broadcast_to(wide), ALU.subtract).then_inc(shifted.sem, 1)
            dve.wait_ge(exps.sem, exps.at(1))
            do(dve.tensor_tensor(X, X, core.c("cmp_keep").rearrange("p (a b) -> p a b", a=24), ALU.mult))
            do(dve.tensor_reduce(st[:, 1], X, AX, ALU.add))
            do(dve.tensor_scalar(st[:, 1], st[:, 1], 1e-30, None, ALU.max))
            do(dve.reciprocal(st[:, 1], st[:, 1]))
            dve.tensor_tensor(X, X, st[:, 1].unsqueeze(2).broadcast_to(wide), ALU.mult).then_inc(probs.sem, 1)
            for i in range(4):
                dve.wait_ge(out.sem, out.at(i + 1))
                dve.tensor_copy(OC[:, :, i * P:(i + 1) * P],
                                core.ps[:, 6 + i % 2, 0:3 * P].rearrange("p (a b) -> p a b", a=3)).then_inc(kept.sem, 1)

        @block.scalar
        def _(act):
            act.wait_ge(shifted.sem, shifted.at(1))
            act.activation(X, X, ACT.Exp).then_inc(exps.sem, 1)
            for i in range(4):
                act.wait_ge(turned.sem, turned.at(i + 1))
                if i >= 2:
                    act.wait_ge(out.sem, out.at(i - 1))
                act.activation(PT[0:NCMP, i % 2], core.flat[0:NCMP, 2048:2048 + 6 * P], ACT.Copy).then_inc(pt.sem, 1)
    for x in (scores, shifted, exps, probs):
        x.passed(1)
    for x in (turned, pt, out, kept):
        x.passed(4)


def cross_keys(core, P2, KX):
    with core.nc.Block() as block:
        @block.gpsimd
        def _(pool):
            for e, t in enumerate((NKS, NKW)):
                for g in range(2):
                    core.pool.do(pool, pool.tensor_copy(KX[64 - 64 * g:128 - 64 * g, e], P2[64 * g:64 * g + 64, t, :]))


def gate_branches(core, P2, branches, tmp):
    sig, spread, used = core.sig("nsa_gates"), core.sig("nsa_spread"), core.sig("nsa_spread_used")
    g = core.area(tmp, SEQ)
    with core.nc.Block() as block:
        @block.scalar
        def _(act):
            act.activation(g[0:18], P2[0:18, NG, :], ACT.Sigmoid).then_inc(sig.sem, 1)

        @block.tensor
        def _(pe):
            pe.wait_ge(sig.sem, sig.at(1))
            for n in range(9):
                if n >= 4:
                    pe.wait_ge(used.sem, used.at(n - 3))
                pe.matmul(core.ps[:, n % 4, :], core.c("gates")[0:18, n * P:(n + 1) * P], g[0:18], start=True,
                          stop=True).then_inc(spread.sem, 1)

        @block.vector
        def _(dve):
            for n in range(9):
                b, t = n // 3, n % 3
                dve.wait_ge(spread.sem, spread.at(n + 1))
                a = branches[b][:, t]
                dve.tensor_tensor(a, core.ps[:, n % 4, :], a, ALU.mult).then_inc(used.sem, 1)
                if b:
                    dve.wait_ge(used.sem, used.at(n + 1))
                    o = branches[0][:, t]
                    core.vec.do(dve, dve.tensor_tensor(o, o, a, ALU.add))
    sig.passed(1), spread.passed(9), used.passed(9)


def center(core, items, T, inv_n, ones):
    total, gone = core.sig("mean_ready"), core.sig("mean_used")
    with core.nc.Block() as block:
        @block.tensor
        def _(pe):
            for n, x in enumerate(items):
                if n >= 2:
                    pe.wait_ge(gone.sem, gone.at(n - 1))
                for k, a in enumerate(x):
                    last = pe.matmul(core.ps[:, n % 2, 0:T], core.c(ones), a, start=(k == 0), stop=(k == len(x) - 1))
                last.then_inc(total.sem, 1)

        @block.vector
        def _(dve):
            for n, x in enumerate(items):
                dve.wait_ge(total.sem, total.at(n + 1))
                for k, a in enumerate(x):
                    ins = dve.scalar_tensor_tensor(out=a, in0=core.ps[:, n % 2, 0:T], scalar=-inv_n, in1=a, op0=ALU.mult,
                                                   op1=ALU.add)
                ins.then_inc(gone.sem, 1)
    total.passed(len(items)), gone.passed(len(items))


def rwkv_prepare(core, R, K, V, L, A, G, KK, AR, B, KP, CE, bonus, tmp):
    got, up, lora, lora_used, decays, exps, sums, done = (core.sig(n, u) for n, u in (
        ("lora_loaded", 16), ("lora_in", 1), ("lora_out", 1), ("lora_used", 1), ("decay_sums", 1), ("decay_exps", 1),
        ("bonus_sum", 1), ("rwkv_ready", 1)))
    w = core.area(tmp, 256)
    LW = core.area(tmp + 256, 2, SEQ)
    CL = core.area(tmp + 256 + 1024, 2, SEQ)
    E = core.area(tmp + 256 + 2048, 3, 2, SEQ)
    D_ = core.area(tmp + 256 + 2048 + 3072, SEQ)
    tiles = [(R, 0), (R, 1), (K, 0), (K, 1), (V, 0), (V, 1), (L, 0)]
    with core.nc.Block() as block:
        @block.sync
        def _(sp):
            sp.dma_start(w, core.dram["lora"]).then_inc(got.sem, 16)

        @block.vector
        def _(dve):
            do = lambda ins: core.vec.do(dve, ins)
            for n in [6, 0, 1, 2, 3, 4, 5]:
                a, t = tiles[n]
                x = a[:, t]
                do(dve.tensor_scalar(D_[:, 0:1], x[:, 0:1], -1.0, None, ALU.mult))
                do(dve.tensor_tensor(D_[:, 1:], x[:, :-1], x[:, 1:], ALU.subtract))
                ins = dve.scalar_tensor_tensor(out=x, in0=D_, scalar=core.p("rw_mu_2", n), in1=x, op0=ALU.mult, op1=ALU.add)
                if n == 6:
                    ins.then_inc(up.sem, 1)
                    dve.wait_ge(up.sem, up.at(1))
                else:
                    do(ins)
            for t in range(2):
                dve.wait_ge(lora_used.sem, lora_used.at(t + 1))
                do(dve.tensor_scalar(LW[:, t], LW[:, t], -0.606531, None, ALU.mult))
                do(dve.tensor_tensor_scan(CL[:, t], core.c("restart"), LW[:, t], 0.0, ALU.mult, ALU.add))
                dve.tensor_tensor(LW[:, t], CL[:, t], LW[:, t], ALU.subtract).then_inc(decays.sem, 1)
            dve.wait_ge(lora_used.sem, lora_used.at(4))
            for t in range(2):
                do(dve.tensor_scalar(KK[:, t], K[:, t], core.p("rw_k_k_2", t), None, ALU.mult))
                do(dve.tensor_scalar(D_, A[:, t], 1.0, core.p("rw_k_a_2", t), ALU.subtract, ALU.mult))
                do(dve.scalar_tensor_tensor(out=K[:, t], in0=D_, scalar=1.0, in1=K[:, t], op0=ALU.add, op1=ALU.mult))
                do(dve.scalar_tensor_tensor(out=D_, in0=R[:, t], scalar=core.p("rw_r_k_2", t), in1=K[:, t],
                                            op0=ALU.mult, op1=ALU.mult))
                dve.tensor_copy(bonus[:, t], D_).then_inc(done.sem, 1)
                dve.wait_ge(done.sem, done.at(t + 1))
            for t in range(2):
                dve.wait_ge(sums.sem, sums.at(t + 1))
                do(dve.tensor_tensor(bonus[:, t], core.ps[:, 6 + t, :], V[:, t], ALU.mult))
            dve.wait_ge(exps.sem, exps.at(6))
            for t in range(2):
                c, c0, ic = E[:, 0, t], E[:, 1, t], E[:, 2, t]
                by = lambda a: a.rearrange("p (c t) -> p c t", t=CH)
                do(dve.tensor_tensor(AR[:, t, :, 1], by(c), by(R[:, t]), ALU.mult))
                do(dve.tensor_copy(AR[:, t, :, 0], by(c0)))
                do(dve.tensor_tensor(KP[:, t], ic, K[:, t], ALU.mult))
                do(dve.tensor_tensor(B[:, t], ic, A[:, t], ALU.mult))
                do(dve.tensor_copy(CE[:, t], by(c)[:, :, CH - 1]))

        @block.scalar
        def _(act):
            act.wait_ge(up.sem, up.at(1))
            x = L[:, 0]
            act.activation(x[0:32], x[0:32], ACT.Tanh)
            act.activation(x[64:128], x[64:128], ACT.Sigmoid).then_inc(up.sem, 1)
            for n, (dst, bias) in enumerate([(LW, "rw_w0_2"), (A, "rw_a0_2"), (G, None)]):
                for t in range(2):
                    act.wait_ge(lora.sem, lora.at(2 * n + t + 1))
                    got_ = core.ps[:, 2 * n + t, :]
                    if bias:
                        ins = act.activation(dst[:, t], got_, ACT.Sigmoid, bias=core.p(bias, t))
                    else:
                        ins = act.activation(dst[:, t], got_, ACT.Copy)
                    ins.then_inc(lora_used.sem, 1)
            for t in range(2):
                act.wait_ge(decays.sem, decays.at(t + 1))
                act.activation(E[:, 0, t], CL[:, t], ACT.Exp).then_inc(exps.sem, 1)
                act.activation(E[:, 1, t], LW[:, t], ACT.Exp).then_inc(exps.sem, 1)
                act.activation(E[:, 2, t], CL[:, t], ACT.Exp, scale=-1.0).then_inc(exps.sem, 1)

        @block.tensor
        def _(pe):
            pe.wait_ge(got.sem, got.at(1))
            pe.wait_ge(up.sem, up.at(2))
            for n, (lo, hi) in enumerate([(0, 32), (32, 64), (64, 128)]):
                for t in range(2):
                    pe.matmul(core.ps[:, 2 * n + t, :], w[lo:hi, t * P:(t + 1) * P], L[lo:hi, 0], start=True,
                              stop=True).then_inc(lora.sem, 1)
            for t in range(2):
                pe.wait_ge(done.sem, done.at(t + 1))
                pe.matmul(core.ps[:, 6 + t, :], core.c("pair64"), bonus[:, t], start=True, stop=True).then_inc(sums.sem, 1)
    got.passed(1), up.passed(2), lora.passed(6), lora_used.passed(6), decays.passed(2), exps.passed(6), sums.passed(2)
    done.passed(2)


def rwkv_factors(core, KK, AR, B):
    with core.nc.Block() as block:
        @block.vector
        def _(dve):
            for t in range(2):
                by = KK[:, t].rearrange("p (c t) -> p c t", t=CH)
                core.vec.do(dve, dve.tensor_tensor(AR[:, t, :, 0], AR[:, t, :, 0], by, ALU.mult))
                core.vec.do(dve, dve.tensor_tensor(B[:, t], B[:, t], KK[:, t], ALU.mult))


def rwkv_matrices(core, V, AR, B, KP, MM, TOK):
    made, used, turned, kept = (core.sig(n) for n in ("chunk_products", "chunk_masked", "chunk_turned", "chunk_kept"))
    NCH = SEQ // CH
    with core.nc.Block() as block:
        @block.tensor
        def _(pe):
            for c in range(NCH):
                if c >= 2:
                    pe.wait_ge(used.sem, used.at(c - 1))
                t0 = c * CH
                for h in range(4):
                    lo, t = 64 * (h % 2), h // 2
                    for e, F in enumerate((B, KP)):
                        o = (t * 2 + e) * 64
                        last = pe.matmul(core.ps[0:CH, 2 * (c % 2) + h % 2, o:o + 64], F[lo:lo + 64, t, t0:t0 + CH],
                                         AR[lo:lo + 64, t, c].rearrange("p a b -> p (a b)"), start=True, stop=True)
                last.then_inc(made.sem, 1)
                if c >= 2:
                    pe.wait_ge(kept.sem, kept.at(c - 1))
                for e, F in enumerate((B, KP, V)):
                    for t in range(2):
                        o = (4 + 2 * (c % 2)) * 512 + e * 256 + t * P
                        last = pe.transpose(core.flat[0:CH, o:o + P], F[:, t, t0:t0 + CH], core.c("ident"))
                last.then_inc(turned.sem, 1)

        @block.vector
        def _(dve):
            for c in range(NCH):
                dve.wait_ge(made.sem, made.at(c + 1))
                two = lambda a: a.rearrange("p (o n) -> p o n", o=2)
                dve.tensor_tensor(two(MM[0:CH, c]), core.ps[0:CH, 2 * (c % 2):2 * (c % 2) + 2, 0:256],
                                  two(core.c("mask32")[0:CH]), ALU.mult).then_inc(used.sem, 1)

        @block.scalar
        def _(act):
            for c in range(NCH):
                act.wait_ge(turned.sem, turned.at(c + 1))
                o = (4 + 2 * (c % 2)) * 512
                for e in range(3):
                    ins = act.activation(TOK[e][0:CH, c], core.flat[0:CH, o + 256 * e:o + 256 * e + 256], ACT.Copy)
                ins.then_inc(kept.sem, 1)
    for x in (made, used, turned, kept):
        x.passed(NCH)


def rwkv_inverse(core, MM, TT, tmp, rd):
    out, back, solved, out2, back2 = (core.sig(n, u) for n, u in (
        ("chunks_stored", 16), ("chunks_back", 16), ("chunks_solved", 1), ("inverse_stored", 16), ("inverse_back", 16)))
    NP = SEQ // CH * 4
    AT = core.area(tmp, CH, CH)
    Yv = core.area(tmp + CH * CH, CH, 16)
    pr = core.area(tmp + CH * CH + CH * 16, 16 * CH)
    a_dram, y_dram = core.dram["chunk_scratch"], core.dram["inverse_scratch"]
    with core.nc.Block() as block:
        @block.sync
        def _(sp):
            m = MM.rearrange("p c (h e f t) -> p c h e f t", h=4, e=2, f=2)
            for c in range(SEQ // CH):
                sp.dma_start(a_dram[4 * c:4 * c + 4].rearrange("n s t -> s n t"), m[0:CH, c, :, 0, 0, :]).then_inc(out.sem, 16)
            sp.wait_ge(out.sem, out.at(SEQ // CH))
            for half in range(2):
                sp.dma_start(AT[64 * half:64 * half + 64].rearrange("p s t -> p (s t)"),
                             a_dram.rearrange("n s t -> n (s t)")).then_inc(back.sem, 16)
            sp.wait_ge(solved.sem, solved.at(1))
            for half in range(2):
                sp.dma_start(y_dram[:, :, 16 * half:16 * half + 16], Yv[64 * half:64 * half + 64]).then_inc(out2.sem, 16)
            sp.wait_ge(out2.sem, out2.at(2))
            sp.dma_start(TT[0:CH], y_dram.rearrange("n s i -> s n i")).then_inc(back2.sem, 16)
            sp.wait_ge(back2.sem, back2.at(1))

        @block.vector
        def _(dve):
            do = lambda ins: core.vec.do(dve, ins)
            do(dve.tensor_copy(Yv.rearrange("p s i -> p (s i)"), core.c("eye16")))
            dve.wait_ge(back.sem, back.at(2))
            for s in range(CH - 2, -1, -1):
                n = CH - 1 - s
                p3 = pr[:, 0:16 * n].rearrange("p (i t) -> p i t", i=16)
                do(dve.tensor_tensor(p3, Yv[:, s + 1:, :].rearrange("p t i -> p i t"),
                                     AT[:, s, s + 1:].unsqueeze(1).broadcast_to([P, 16, n]), ALU.mult))
                do(dve.tensor_reduce(rd, p3, AX, ALU.add))
                ins = dve.tensor_tensor(Yv[:, s, :], Yv[:, s, :], rd, ALU.subtract)
                if s:
                    do(ins)
                else:
                    ins.then_inc(solved.sem, 1)
    out.passed(SEQ // CH), back.passed(2), solved.passed(1), out2.passed(2), back2.passed(1)
    assert NP == 64


def rwkv_chunks(core, AR, MM, TOK, TT, CE, RO, tmp):
    init, x_ready, x_kept, u_ready, u_kept, o_ready, o_kept, s_ready, s_kept = (core.sig(n) for n in (
        "state_zero", "x_ready", "x_kept", "u_ready", "u_kept", "o_ready", "o_kept", "s_ready", "s_kept"))
    NCH = SEQ // CH
    ST = core.area(tmp, 2, 64)
    SC = core.area(tmp + 128, 2, 64)
    X = core.area(tmp + 256, 256)
    U = core.area(tmp + 512, 256)
    order = lambda h: h % 2 * 2 + h // 2
    with core.nc.Block() as block:
        @block.tensor
        def _(pe):
            pe.wait_ge(s_kept.sem, s_kept.at(1))
            for c in range(NCH):
                m = MM[0:CH, c].rearrange("p (h e f t) -> p h e f t", h=4, e=2, f=2)
                tok = [a[0:CH, c] for a in TOK]
                if c:
                    pe.wait_ge(s_kept.sem, s_kept.at(c + 1))
                    pe.wait_ge(x_kept.sem, x_kept.at(c))
                for h in range(4):
                    lo, t, o = 64 * (h % 2), h // 2, 64 * h
                    dst = core.ps[0:CH, h % 2, t * 64:t * 64 + 64]
                    pe.matmul(dst, m[:, order(h), 1, 0], tok[2][:, o:o + 64], start=True, stop=False)
                    last = pe.matmul(dst, AR[lo:lo + 64, t, c, 0], ST[lo:lo + 64, t], start=False,
                                     stop=True)
                last.then_inc(x_ready.sem, 1)
                pe.wait_ge(x_kept.sem, x_kept.at(c + 1))
                for h in range(4):
                    o = 64 * order(h)
                    last = pe.matmul(core.ps[0:CH, 3, o:o + 64], TT[0:CH, 4 * c + order(h)], X[0:CH, o:o + 64], start=True,
                                     stop=True)
                last.then_inc(u_ready.sem, 1)
                pe.wait_ge(u_kept.sem, u_kept.at(c + 1))
                for h in range(4):
                    lo, t, o = 64 * (h % 2), h // 2, 64 * h
                    dst = core.ps[lo:lo + 64, 2, t * 64:t * 64 + 64]
                    pe.matmul(dst, tok[1][:, o:o + 64], tok[2][:, o:o + 64], start=True, stop=False)
                    last = pe.matmul(dst, tok[0][:, o:o + 64], U[0:CH, 64 * order(h):64 * order(h) + 64], start=False, stop=True)
                if c >= 2:
                    pe.wait_ge(o_kept.sem, o_kept.at(c - 1))
                for h in range(4):
                    lo, t, o = 64 * (h % 2), h // 2, 64 * h
                    dst = core.ps[lo:lo + 64, 4 + c % 2, t * CH:(t + 1) * CH]
                    pe.matmul(dst, ST[lo:lo + 64, t], AR[lo:lo + 64, t, c, 1], start=True, stop=False)
                    pe.matmul(dst, tok[2][:, o:o + 64], m[:, order(h), 1, 1], start=False, stop=False)
                    last = pe.matmul(dst, U[0:CH, 64 * order(h):64 * order(h) + 64], m[:, order(h), 0, 1], start=False, stop=True)
                last.then_inc(s_ready.sem, 1)

        @block.vector
        def _(dve):
            do = lambda ins: core.vec.do(dve, ins)
            dve.memset(ST, 0.0).then_inc(s_kept.sem, 1)
            dve.wait_ge(s_kept.sem, s_kept.at(1))
            for c in range(NCH):
                for t in range(2):
                    ins = dve.tensor_scalar(SC[:, t], ST[:, t], CE[:, t, c:c + 1], None, ALU.mult)
                do(ins)
                dve.wait_ge(x_ready.sem, x_ready.at(c + 1))
                dve.tensor_scalar(X[0:CH].rearrange("p (o n) -> p o n", o=2), core.ps[0:CH, 0:2, 0:128], -1.0, None, ALU.mult).then_inc(x_kept.sem, 1)
                dve.wait_ge(u_ready.sem, u_ready.at(c + 1))
                dve.tensor_copy(U[0:CH], core.ps[0:CH, 3, 0:256]).then_inc(u_kept.sem, 1)
                dve.wait_ge(s_ready.sem, s_ready.at(c + 1))
                for t in range(2):
                    ins = dve.scalar_tensor_tensor(out=ST[:, t], in0=core.ps[:, 2, t * 64:t * 64 + 64], scalar=CE[:, t, c:c + 1],
                                                   in1=SC[:, t], op0=ALU.mult, op1=ALU.add)
                ins.then_inc(s_kept.sem, 1)
                dve.wait_ge(s_kept.sem, s_kept.at(c + 2))

        @block.scalar
        def _(act):
            for c in range(NCH):
                act.wait_ge(s_ready.sem, s_ready.at(c + 1))
                act.activation(RO[:, :, c * CH:(c + 1) * CH], core.ps[:, 4 + c % 2, 0:2 * CH].rearrange("p (a b) -> p a b", a=2),
                               ACT.Copy).then_inc(o_kept.sem, 1)
    s_kept.passed(NCH + 1)
    for x in (x_ready, x_kept, u_ready, u_kept, o_kept, s_ready):
        x.passed(NCH)


def second_block(core, stop=None):
    T = SEQ
    P2 = core.area(0, N2, T)
    at = N2 * T
    Y = core.area(at, NC, T)
    at += NC * T
    VT = core.area(at, 4, 5, P)
    at += 20 * P
    KX = core.area(at, 2, T)
    OC, OS = core.area(at + 2 * T, 3, T), core.area(at + 5 * T, 3, T)
    KC, VC = core.area(at + 8 * T, 2 * NCMP), core.area(at + 8 * T + 2 * NCMP, 2, 64)
    late = at + 8 * T + 2 * NCMP + P
    tmp = late + sum(m for _, m in NSA_CONSTS)
    core.h = core.h_all[:, :, META:META + SEQ]
    layer_norm_input(core, "attn_norm_2", T, tmp)
    project(core, N2, P2, T)
    to_tokens(core, [([P2[:, t, :] for t in (NVS, NVW, MV, MV + 1)], lambda j: VT[:, j, 0:4].rearrange("p a b -> p (a b)")),
                     ([P2[:, MV + 2, :]], lambda j: VT[:, j, 4])], T)
    scale_tiles(core, [P2[:, t, :] for t in (NQ, NQ + 1, NQ + 2, MQ, MQ + 1, MQ + 2)], 0.125)
    compress(core, P2, KC, VC, late)
    load_constants(core, NSA_CONSTS, "nsa_consts", core.area(late, tmp - late))
    cross_keys(core, P2, KX)
    compressed_attention(core, P2, KC, VC, OC, tmp)
    causal = core.c("causal")

    def values(v, lo):
        return lambda j, w: VT[0:w, j, v, lo:lo + 64]

    for e, (kt, out) in enumerate(((NKS, OS), (NKW, Y))):
        heads = []
        for h in range(6):
            lo, g = 64 * (h % 2), h // 3
            k = P2[lo:lo + 64, kt, :] if h % 2 == g else KX[lo:lo + 64, e]
            heads.append(Head([(P2[lo:lo + 64, NQ + h // 2, :], k)], values(e, 64 * g), (lo, 64, out[:, h // 2]), causal))
        attention(core, "soft", heads, T, tmp)
    gate_branches(core, P2, [OC, OS, Y], tmp)
    heads = []
    for h in range(6):
        lo = 64 * (h % 2)
        heads.append(Head([(P2[lo:lo + 64, MQ + h // 2, :], P2[lo:lo + 64, MK + h // 2, :])], values(2 + h // 2, lo),
                          (lo, 64, Y[:, 5 + h // 2]), causal))
    attention(core, "soft", heads, T, tmp)
    norm(core, [([OC[:, t]], [Y[:, t]], [core.p("nsa_out_gain_2", t)], None) for t in range(3)]
         + [([Y[:, 5 + t]], [Y[:, 5 + t]], [core.p("moba_out_gain_2", t)], None) for t in range(3)], T, 1.0 / 64, tmp,
         ones="pair64")

    R, K, V, L = (P2[:, a:b, :] for a, b in ((RR, RR + 2), (RK, RK + 2), (RV, RV + 2), (RL, RL + 1)))
    A, KK, G, B, KP = (core.area(i * 2 * T, 2, T) for i in range(5))
    at = (N2 + NC) * T
    bonus = core.area(at, 2, T)
    RO = core.area(at + 2 * T, 2, T)
    AR = core.area(at + 4 * T, 2, SEQ // CH, 2, CH)
    MM = core.area(at + 8 * T, SEQ // CH, 512)
    tmp = at + 24 * T
    late = tmp + 8 * T
    end = late + 3 * 512
    spare = core.xn[:, :, :].rearrange("p a b -> p (a b)")
    TOK = [core.area((RL + 1) * T, SEQ // CH, 256), core.area(tmp, SEQ // CH, 256),
           spare[:, 0:16 * 256].rearrange("p (c n) -> p c n", n=256)]
    CE = spare[:, 4096:4096 + 32].rearrange("p (a b) -> p a b", a=2)
    rd = spare[:, 4128:4144]
    TT = core.area(0, SEQ // CH * 4, CH)
    load_constants(core, RWKV_CONSTS, "rwkv_consts", core.area(late, end - late))
    rwkv_prepare(core, R, K, V, L, A, G, KK, AR, B, KP, CE, bonus, at + 8 * T)
    norm(core, [([KK[:, t]], [KK[:, t]], None, None) for t in range(2)], T, 1.0, tmp, eps="zero", ones="pair64", least=1e-12)
    rwkv_factors(core, KK, AR, B)
    rwkv_matrices(core, V, AR, B, KP, MM, TOK)
    rwkv_inverse(core, MM, TT, 6 * T, rd)
    rwkv_chunks(core, AR, MM, TOK, TT, CE, RO, end)
    center(core, [[RO[:, t]] for t in range(2)], T, 1.0 / 64, "pair64")
    norm(core, [([RO[:, t]], [RO[:, t]], [core.p("rw_lnx_w_2", t)], [core.p("rw_lnx_b_2", t)]) for t in range(2)], T, 1.0 / 64,
         tmp, eps="eps_rw", ones="pair64")
    rwkv_output(core, RO, bonus, G, Y[:, 3:5, :])
    if stop == "Y":
        return Y
    add_product(core, 1, NC, Y, T)
    feed_forward(core, T, "ffn_norm_2", "ffn_conv_w_2", "ffn_conv_b_2")
    x = [core.h[:, k] for k in range(NC)]
    norm(core, [(x, x, [core.p("final_norm_2", k) for k in range(NC)], None)], T, 1.0 / D, 0)


def rwkv_output(core, RO, bonus, G, Y):
    with core.nc.Block() as block:
        @block.vector
        def _(dve):
            core.vec.do(dve, dve.tensor_tensor(RO, RO, bonus, ALU.add))
            dve.tensor_tensor(Y, RO, G, ALU.mult)


def modulation(core, mod, tmp):
    ready = core.sig("c_ready")
    ca = core.area(tmp, NC)
    n = 6 * NC
    with core.nc.Block() as block:
        @block.sync
        def _(sp):
            core.load_units(sp, n)

        @block.scalar
        def _(act):
            o = PCOL["c_3"]
            act.activation(ca, core.par[:, o:o + NC], ACT.Silu).then_inc(ready.sem, 1)

        @block.tensor
        def _(pe):
            pe.wait_ge(ready.sem, ready.at(1))

            def body(i, j):
                t = i * 4 + j
                w = core.unit(pe, j, i, 4)
                out = core.ps[:, 0, t:t + 1] if isinstance(t, int) else core.ps[:, 0, bass.ds(t, 1)]
                for k in range(NC):
                    last = pe.matmul(out, w[:, k, :], ca[:, k:k + 1], start=(k == 0), stop=(k == NC - 1))
                last.then_inc(core.used, 1)
            tile_loop(pe, n, 4, body)

        @block.vector
        def _(dve):
            do = lambda ins: core.vec.do(dve, ins)
            dve.wait_ge(core.used, core.taken + n)
            b = PCOL["b_ada_3"]
            do(dve.tensor_tensor(mod, core.ps[:, 0, 0:n], core.par[:, b:b + n], ALU.add))
            for at, name in ((NC, "norm1_g_3"), (4 * NC, "norm2_g_3")):
                g = PCOL[name]
                do(dve.scalar_tensor_tensor(out=mod[:, at:at + NC], in0=mod[:, at:at + NC], scalar=1.0,
                                            in1=core.par[:, g:g + NC], op0=ALU.add, op1=ALU.mult))
    ready.passed(1)
    core.taken += n


def mix_tokens(core, VT, MX, tmp):
    got, ready, mixed, kept = (core.sig(n, u) for n, u in (("ws_loaded", 16), ("ws_masked", 1), ("mixed", 1), ("mixed_kept", 1)))
    WS = core.area(tmp, NC, P)
    BS = core.area(tmp + NC * P, NC, P)
    with core.nc.Block() as block:
        @block.sync
        def _(sp):
            sp.dma_start(WS.rearrange("p a b -> p (a b)"), core.dram["gmlp_ws"]).then_inc(got.sem, 16)
            sp.dma_start(BS[0:1].rearrange("p a b -> p (a b)"), core.dram["gmlp_bs"]).then_inc(got.sem, 16)

        @block.vector
        def _(dve):
            dve.wait_ge(got.sem, got.at(2))
            dve.memset(WS[64:128, :, 0:64], 0.0).then_inc(ready.sem, 1)

        @block.tensor
        def _(pe):
            pe.wait_ge(ready.sem, ready.at(1))
            for g in range(NC):
                if g >= 2:
                    pe.wait_ge(kept.sem, kept.at(g - 1))
                for n in range(4):
                    dst = core.ps[:, g % 2, n * P:(n + 1) * P]
                    pe.matmul(dst, VT[:, n, g], WS[:, g], start=True, stop=False)
                    last = pe.matmul(dst, core.c("ones")[0:1, :], BS[0:1, g], start=False, stop=True)
                last.then_inc(mixed.sem, 1)

        @block.scalar
        def _(act):
            for g in range(NC):
                act.wait_ge(mixed.sem, mixed.at(g + 1))
                act.activation(MX[:, g], core.ps[:, g % 2, :], ACT.Copy).then_inc(kept.sem, 1)
    got.passed(2), ready.passed(1), mixed.passed(NC), kept.passed(NC)


def project_conv(core, n, dst, tmp):
    T = SEQ
    copied, conv, act_out = core.sig("tile_free"), core.sig("conv_out"), core.sig("silu_out")
    pad = core.area(tmp, 2, T + 3)
    mid = core.area(tmp + 2 * (T + 3), 2, 2, T)
    step = core.vec
    with core.nc.Block() as block:
        @block.sync
        def _(sp):
            core.load_units(sp, n)

        @block.tensor
        def _(pe):
            gemm(core, pe, n, 4, 1, NC, core.xn, T, copied)

        @block.scalar
        def _(act):
            core.act.do(act, act.activation(pad[:, :, 0:3], core.c("ones", 6).rearrange("p (b n) -> p b n", b=2),
                                            ACT.Copy, scale=0.0))

            def body(i, j):
                t = i * 4 + j
                tile_done(core, act, i, j, 4)
                if not isinstance(t, int) or t >= 2:
                    act.wait_ge(conv.sem, conv.at(t - 1))
                act.activation(pad[:, j % 2, 3:], core.ps[:, out_slot(j), :], ACT.Copy).then_inc(copied.sem, 1)
                act.wait_ge(conv.sem, conv.at(t + 1))
                out = dst[:, t] if isinstance(t, int) else dst[:, bass.ds(t, 1)].rearrange("p o n -> p (o n)")
                act.activation(out, mid[:, j % 2, 1], ACT.Silu).then_inc(act_out.sem, 1)
            tile_loop(act, n, 4, body)

        @block.vector
        def _(dve):
            base = step.value

            def body(i, j):
                t = i * 4 + j
                x, y, z = pad[:, j % 2], mid[:, j % 2, 0], mid[:, j % 2, 1]

                def ordered(k, ins):
                    ins.then_inc(step.sem, 1)
                    dve.wait_ge(step.sem, base + 3 * t + k)
                dve.wait_ge(copied.sem, copied.at(t + 1))
                ordered(1, dve.tensor_scalar(y, x[:, 3:], core.p("conv_w_3", 48 + t), core.p("conv_b_3", t), ALU.mult, ALU.add))
                ordered(2, dve.scalar_tensor_tensor(out=y, in0=x[:, 2:2 + T], scalar=core.p("conv_w_3", 32 + t), in1=y,
                                                    op0=ALU.mult, op1=ALU.add))
                ordered(3, dve.scalar_tensor_tensor(out=y, in0=x[:, 1:1 + T], scalar=core.p("conv_w_3", 16 + t), in1=y,
                                                    op0=ALU.mult, op1=ALU.add))
                if not isinstance(t, int) or t >= 2:
                    dve.wait_ge(act_out.sem, act_out.at(t - 1))
                dve.scalar_tensor_tensor(out=z, in0=x[:, 0:T], scalar=core.p("conv_w_3", t), in1=y, op0=ALU.mult,
                                         op1=ALU.add).then_inc(conv.sem, 1)
                dve.wait_ge(conv.sem, conv.at(t + 1))
            tile_loop(dve, n, 4, body)
            step.value = base + 3 * n
    for x in (copied, conv, act_out):
        x.passed(n)
    core.taken += n


def mlstm_gates(core, FI, M4, EB, GC, tmp):
    soft, rows, turned, spread, kept = (core.sig(n) for n in ("f_softplus", "gate_rows", "g_turned", "m_spread", "m_kept"))
    T = SEQ
    S, F, G, FM = (core.area(tmp + i * T, T) for i in range(4))
    with core.nc.Block() as block:
        @block.scalar
        def _(act):
            do = lambda ins: core.act.do(act, ins)
            f = FI[32:36, 0]
            do(act.activation(S[32:36], f, ACT.Abs))
            do(act.activation(S[32:36], S[32:36], ACT.Exp, scale=-1.0))
            act.activation(S[32:36], S[32:36], ACT.Ln, bias=1.0).then_inc(soft.sem, 1)
            for h in range(4):
                act.wait_ge(spread.sem, spread.at(h + 1))
                act.activation(EB[:, h], core.ps[:, h % 2, :], ACT.Exp, scale=-1.0).then_inc(kept.sem, 1)

        @block.vector
        def _(dve):
            do = lambda ins: core.vec.do(dve, ins)
            dve.wait_ge(soft.sem, soft.at(1))
            lf = S[32:36]
            do(dve.scalar_tensor_tensor(out=lf, in0=FI[32:36, 0], scalar=0.0, in1=lf, op0=ALU.min, op1=ALU.subtract))
            do(dve.tensor_tensor_scan(F[32:36], lf, lf, 0.0, ALU.add, ALU.bypass))
            do(dve.tensor_copy(F[0:4], F[32:36]))
            do(dve.tensor_tensor(G[0:4], FI[0:4, 0], F[0:4], ALU.subtract))
            do(dve.tensor_tensor_scan(M4[0:4], G[0:4], G[0:4], 0.0, ALU.max, ALU.bypass))
            dve.tensor_tensor(FM[0:4], F[0:4], M4[0:4], ALU.add).then_inc(rows.sem, 1)
            dve.wait_ge(turned.sem, turned.at(1))
            do(dve.tensor_copy(GC.rearrange("p a b -> p (a b)"), core.ps[:, 2, 0:16]))

        @block.tensor
        def _(pe):
            pe.wait_ge(rows.sem, rows.at(1))
            for j in range(4):
                last = pe.transpose(core.ps[:, 2, 4 * j:4 * j + 4], G[0:4, j * P:(j + 1) * P], core.c("ident")[0:4, 0:4])
            last.then_inc(turned.sem, 1)
            for h in range(4):
                if h >= 2:
                    pe.wait_ge(kept.sem, kept.at(h - 1))
                pe.matmul(core.ps[:, h % 2, :], core.c("heads")[0:4, h * P:(h + 1) * P], FM[0:4], start=True,
                          stop=True).then_inc(spread.sem, 1)
    soft.passed(1), rows.passed(1), turned.passed(1), spread.passed(4), kept.passed(4)


def mlstm(core, Q, K, VT, M4, EB, GC, H, tmp):
    spread, arg, exps, scores, probs, sums, absd, done = (core.sig(n) for n in (
        "m_rows", "weight_arg", "weight_exp", "key_scores", "key_probs", "head_sums", "norm_abs", "head_done"))
    T = SEQ
    MB = core.area(tmp, 2, T)
    W = core.area(tmp + 2 * T, 2, T)
    PT = core.area(tmp + 4 * T, 2, T)
    N = core.area(tmp + 6 * T, 2, T)
    steps = [(h, j) for h in range(4) for j in range(4)]
    with core.nc.Block() as block:
        @block.tensor
        def _(pe):
            def score(n):
                h, j = steps[n]
                if j == 0:
                    if h:
                        pe.wait_ge(spread.sem, spread.at(2 * h))
                    pe.matmul(core.ps[:, 2, :], core.c("heads")[0:4, h * P:(h + 1) * P], M4[0:4], start=True,
                              stop=True).then_inc(spread.sem, 1)
                if n >= 2:
                    pe.wait_ge(probs.sem, probs.at(n - 1))
                for e in range(2):
                    last = pe.matmul(core.ps[:, n % 2, 0:T - j * P], K[:, 2 * h + e, j * P:(j + 1) * P], Q[:, 2 * h + e, j * P:],
                                     start=(e == 0), stop=(e == 1))
                last.then_inc(scores.sem, 1)

            def add(n):
                h, j = steps[n]
                w = T - j * P
                pe.wait_ge(probs.sem, probs.at(n + 1))
                if j == 0 and h:
                    pe.wait_ge(done.sem, done.at(h))
                p = PT[:, n % 2, 0:w]
                for b, lhs in ((3, core.c("ones")), (4, VT[:, j, 2 * h]), (5, VT[:, j, 2 * h + 1])):
                    last = pe.matmul(core.ps[:, b, j * P:], lhs, p, start=(j == 0), stop=(j == 3))
                last.then_inc(sums.sem, 1)

            score(0)
            for n in range(16):
                if n + 1 < 16:
                    score(n + 1)
                add(n)

        @block.vector
        def _(dve):
            do = lambda ins: core.vec.do(dve, ins)

            def argument(n):
                h, j = steps[n]
                w = T - j * P
                if j == 0:
                    dve.wait_ge(spread.sem, spread.at(2 * h + 1))
                    dve.tensor_copy(MB[:, h % 2], core.ps[:, 2, :]).then_inc(spread.sem, 1)
                    dve.wait_ge(spread.sem, spread.at(2 * h + 2))
                dve.tensor_scalar(W[:, n % 2, 0:w], MB[:, h % 2, j * P:], GC[:, j, h:h + 1], 0.0, ALU.subtract,
                                  ALU.max).then_inc(arg.sem, 1)

            argument(0)
            for n, (h, j) in enumerate(steps):
                w = T - j * P
                if n + 1 < 16:
                    if n >= 1:
                        dve.wait_ge(probs.sem, probs.at(n))
                    argument(n + 1)
                dve.wait_ge(exps.sem, exps.at(n + 1))
                dve.wait_ge(scores.sem, scores.at(n + 1))
                if n >= 2:
                    dve.wait_ge(sums.sem, sums.at(n - 1))
                wt, p = W[:, n % 2, 0:w], PT[:, n % 2, 0:w]
                do(dve.tensor_tensor(wt[:, 0:P], wt[:, 0:P], core.c("upper"), ALU.mult))
                dve.scalar_tensor_tensor(out=p, in0=core.ps[:, n % 2, 0:w], scalar=1.0 / 16, in1=wt, op0=ALU.mult,
                                         op1=ALU.mult).then_inc(probs.sem, 1)
                if j < 3:
                    continue
                nh = N[:, h % 2]
                dve.wait_ge(absd.sem, absd.at(h + 1))
                do(dve.tensor_tensor(nh, nh, EB[:, h], ALU.max))
                do(dve.reciprocal(nh, nh))
                do(dve.tensor_tensor(H[:, 2 * h], core.ps[:, 4, :], nh, ALU.mult))
                dve.tensor_tensor(H[:, 2 * h + 1], core.ps[:, 5, :], nh, ALU.mult).then_inc(done.sem, 1)

        @block.scalar
        def _(act):
            for n, (h, j) in enumerate(steps):
                w = T - j * P
                act.wait_ge(arg.sem, arg.at(n + 1))
                act.activation(W[:, n % 2, 0:w], W[:, n % 2, 0:w], ACT.Exp, scale=-1.0).then_inc(exps.sem, 1)
                if j == 0 and h:
                    act.wait_ge(sums.sem, sums.at(4 * h))
                    if h >= 3:
                        act.wait_ge(done.sem, done.at(h - 2))
                    act.activation(N[:, (h - 1) % 2], core.ps[:, 3, :], ACT.Abs).then_inc(absd.sem, 1)
            act.wait_ge(sums.sem, sums.at(16))
            act.activation(N[:, 1], core.ps[:, 3, :], ACT.Abs).then_inc(absd.sem, 1)
    spread.passed(8)
    for x in (arg, exps, scores, probs, sums):
        x.passed(16)
    absd.passed(4), done.passed(4)


def third_block(core, stop=None):
    T = SEQ
    merged = core.area(0, NC, T)
    QK = core.area(NC * T, 2 * NC, T)
    V = core.area(3 * NC * T, NC, T)
    VT = core.area(4 * NC * T, 4, NC, P)
    at = 5 * NC * T
    mod = core.area(at, 6 * NC)
    EB, M4, GC, FI = core.area(at + 64, 4, T), core.area(at + 64 + 4 * T, T), core.area(at + 64 + 5 * T, 4, 4), core.area(
        at + 80 + 5 * T, 1, T)
    tmp = at + 96 + 6 * T
    cols = lambda o: [mod[:, o + k:o + k + 1] for k in range(NC)]
    x, xn = [core.h[:, k] for k in range(NC)], [core.xn[:, k, 0:T] for k in range(NC)]
    modulation(core, mod, tmp)
    norm(core, [(x, xn, cols(NC), cols(0))], T, 1.0 / D, tmp)

    project(core, NC, V, T, ACT.Gelu_apprx_tanh)
    v = [V[:, k] for k in range(NC)]
    center(core, [v], T, 1.0 / D, "ones")
    norm(core, [(v, v, [core.p("gmlp_ln_g_3", k) for k in range(NC)], [core.p("gmlp_ln_b_3", k) for k in range(NC)])], T,
         1.0 / D, tmp)
    quads = lambda a: [([a[:, 4 * g + k] for k in range(4)], lambda j, g=g: VT[:, j, 4 * g:4 * g + 4].rearrange("p a b -> p (a b)"))
                       for g in range(2)]
    to_tokens(core, quads(V), T)
    mix_tokens(core, VT, merged, tmp)
    act_mul(core, [(ACT.Gelu_apprx_tanh, merged, merged, False), (ACT.Sigmoid, merged, merged, False)], T, tmp)

    project_conv(core, 2 * NC, QK, tmp)
    project(core, NC, V, T)
    to_tokens(core, quads(V), T)
    project(core, 1, FI, T, ACT.Identity, "mlstm_gate_b_3")
    mlstm_gates(core, FI, M4, EB, GC, tmp)
    mlstm(core, QK[:, 0:NC], QK[:, NC:2 * NC], VT, M4, EB, GC, V, tmp)
    center(core, [[V[:, 2 * h], V[:, 2 * h + 1]] for h in range(4)], T, 1.0 / 256, "ones")
    norm(core, [([V[:, 2 * h], V[:, 2 * h + 1]],) * 2 + ([core.p("mlstm_hn_g_3", 2 * h + e) for e in range(2)], None)
                for h in range(4)], T, 1.0 / 256, tmp)
    act_mul(core, [(ACT.Sigmoid, V, V, False), (ACT.Sigmoid, V, merged, True)], T, tmp)
    add_product(core, 1, NC, merged, T, lambda t: column(mod, 2 * NC, t))

    norm(core, [(x, xn, cols(4 * NC), cols(3 * NC))], T, 1.0 / D, tmp)
    hidden = core.area(0, 4 * NC, T)
    act_mul(core, [(ACT.Relu, None, hidden, False)], T, tmp, 4 * NC)
    add_product(core, 4, 4 * NC, hidden, T, lambda t: column(mod, 5 * NC, t))
    norm(core, [(x, xn, [core.p("final_g_3", k) for k in range(NC)], None)], T, 1.0 / D, tmp)


def column(a, o, t):
    return a[:, o + t:o + t + 1] if isinstance(t, int) else a[:, bass.ds(o + t, 1)]


def store(core, out):
    got = core.sig("stored", 16)
    with core.nc.Block() as block:
        @block.sync
        def _(sp):
            sp.dma_start(out, core.xn[:, :, 0:SEQ]).then_inc(got.sem, 16)
            sp.wait_ge(got.sem, got.at(1))
    got.passed(1)


def build(nc, dram, out):
    with ExitStack() as ctx:
        core = Core(nc, ctx, dram)
        load_small(core)
        first_block(core)
        second_block(core)
        third_block(core)
        store(core, out)


def kernel(**inputs):
    import concourse.bacc as bacc
    from concourse.bass_utils import run_bass_kernel_spmd

    arrays = {f"in_{n}": np.ascontiguousarray(v) for n, v in lay_out({n: np.asarray(v) for n, v in inputs.items()}).items()}
    nc = bacc.Bacc("TRN2", target_bir_lowering=False, num_devices=1)
    dram = {n[3:]: nc.dram_tensor(n, v.shape, F32, kind="ExternalInput").ap() for n, v in arrays.items()}
    for n, shape in (("strip_scratch", (8, NR)), ("chunk_scratch", (64, CH, CH)), ("inverse_scratch", (64, CH, CH))):
        dram[n] = nc.dram_tensor(n, shape, F32, kind="Internal").ap()
    out = nc.dram_tensor("out_features", (P, NC, SEQ), F32, kind="ExternalOutput").ap()
    build(nc, dram, out)
    r = run_bass_kernel_spmd(nc, [arrays], core_ids=[0])
    return r.results[0]["out_features"].transpose(2, 1, 0).reshape(1, SEQ, D)
```

```python
from contextlib import ExitStack
import math

import numpy as np
import concourse.bass as bass
from concourse import mybir

F32 = mybir.dt.float32
F32R = mybir.dt.float32r
ALU = mybir.AluOpType
ACT = mybir.ActivationFunctionType
AX = mybir.AxisListType.X

P = 128
D = 1024
NC = D // P
META = 16
SEQ = 512
T1 = META + SEQ
D_FF = 2816
FT = D_FF // P
NG_DOWN = -(-FT // NC)
RING = 4
MAIN = 29640
TAIL = 1 << 20
SMALL_TAIL = 4224
NEG = -1e30
EPS = 1e-6
TOPK = T1 // 4
STRIP = 640
DIAG = 512
NR = STRIP + P - 1
BUCKETS = 32
EXP_LN_TABLES = 6
NCMP = (SEQ - 32) // 16 + 1
CH = 32

SB_Q, SB_K, SB_V, SP_Q, SP_K, SP_V, IX_Q, IX_K, DF_Q, DF_K, DF_V, N1 = 0, 2, 4, 6, 8, 10, 12, 14, 15, 19, 23, 27
NQ, NKC, NVC, NKS, NVS, NKW, NVW, NG, RR, RK, RV, RL, MQ, MK, MV, N2 = (
    0, 3, 4, 5, 6, 7, 8, 9, 10, 12, 14, 16, 17, 20, 23, 26)
RAW0 = N1 + 3 * NC + 2 * NC + 2 * FT + NC * NG_DOWN + N2
RAW = 6 * NC


def pack_units(w):
    k, n = w.shape
    ku, nt = -(-k // D), -(-n // P)
    full = np.zeros((ku * D, nt * P), w.dtype)
    full[:k, :n] = w
    return full.reshape(ku, NC, P, nt, P).transpose(3, 0, 2, 1, 4).reshape(nt * ku, P, D)


def pack_groups(w):
    return np.concatenate([pack_units(w[k:k + D]) for k in range(0, w.shape[0], D)], 0)


def interleave(*parts):
    return np.stack(parts, 1).reshape(-1, P, D)


def columns(v):
    v = np.asarray(v).reshape(-1)
    m = -(-v.size // P)
    full = np.zeros(m * P, v.dtype)
    full[:v.size] = v
    return full.reshape(m, P).T


PARAMS = [
    ("attn_norm", 8), ("b_gate", 24), ("q_norm_sp", 1), ("k_norm_sp", 1), ("q_norm_df", 1), ("k_norm_df", 1),
    ("subln_df", 1), ("ffn_norm", 8), ("conv_w", 66), ("conv_b", 22),
    ("attn_norm_2", 8), ("nsa_out_gain_2", 3), ("rw_mu_2", 7), ("rw_w0_2", 2), ("rw_a0_2", 2), ("rw_k_k_2", 2),
    ("rw_k_a_2", 2), ("rw_r_k_2", 2), ("rw_lnx_w_2", 2), ("rw_lnx_b_2", 2), ("moba_out_gain_2", 3),
    ("ffn_norm_2", 8), ("ffn_conv_w_2", 66), ("ffn_conv_b_2", 22), ("final_norm_2", 8),
    ("b_ada_3", 48), ("norm1_g_3", 8), ("conv_w_3", 64), ("conv_b_3", 16), ("mlstm_gate_b_3", 1),
    ("gmlp_ln_g_3", 8), ("gmlp_ln_b_3", 8), ("mlstm_hn_g_3", 8), ("norm2_g_3", 8), ("final_g_3", 8),
]
PCOL, NPAR = {}, 0
for _name, _m in PARAMS:
    PCOL[_name] = NPAR
    NPAR += _m


def params(a):
    v = {n: a[n] for n, _ in PARAMS}
    for n in ("q_norm_sp", "k_norm_sp", "q_norm_df", "k_norm_df"):
        v[n] = np.concatenate([a[n].reshape(-1)] * 2)
    g = a["mlstm_gate_b_3"].reshape(2, 4)
    rows = np.zeros(P, g.dtype)
    rows[0:4], rows[32:36] = g[0], g[1]
    v["mlstm_gate_b_3"] = rows
    return np.concatenate([columns(v[n]) for n, _ in PARAMS], 1)


CONSTS = [("ident", P), ("ones", P), ("pair64", P), ("flip", P), ("causal", STRIP), ("strict", P), ("strict_neg", P),
          ("heads", 4 * P), ("upper", P), ("eps6", 1), ("eps_rw", 1), ("zero", 1)]
NSA_CONSTS = [("cmp_bias", 24 * NCMP), ("cmp_keep", 24 * NCMP), ("gates", 9 * P)]
RWKV_CONSTS = [("mask32", 512), ("restart", SEQ), ("eye16", 512)]
WIDTH = dict(CONSTS + NSA_CONSTS + RWKV_CONSTS)
NCON = sum(m for _, m in CONSTS)


def constants():
    p, c = np.arange(P)[:, None], np.arange(P)[None, :]
    k = {}
    k["ident"] = p == c
    k["ones"] = np.ones((P, P))
    k["pair64"] = p // 64 == c // 64
    k["flip"] = p + c == P - 1
    k["causal"] = np.where(np.arange(STRIP)[None, :] <= p + DIAG, 0.0, NEG)
    k["strict"] = c < p
    k["strict_neg"] = np.where(c < p, 0.0, NEG)
    heads = np.zeros((P, 4, P))
    for h in range(4):
        heads[h, h], heads[32 + h, h] = 1, 1
    k["heads"] = heads.reshape(P, -1)
    q = np.arange(4)[None, :, None, None] * P + np.arange(P)[:, None, None, None]
    seen = (np.arange(NCMP) * 16 + 31 <= q) & np.ones((1, 1, 6, 1), bool)
    k["cmp_bias"] = np.where(seen, 0.0, NEG).reshape(P, -1)
    k["cmp_keep"] = seen.reshape(P, -1)
    b, t, f = np.arange(3)[None, :, None, None], np.arange(3)[None, None, :, None], np.arange(P)[None, None, None, :]
    k["gates"] = (np.arange(P)[:, None, None, None] == (2 * t + f // 64) * 3 + b).reshape(P, -1)
    s, t = np.arange(P)[:, None, None], np.arange(CH)[None, None, :]
    m = np.concatenate([s < t, s <= t], 1) & (s < CH)
    k["mask32"] = (m[:, None] & np.ones((1, 8, 1, 1), bool)).reshape(P, -1)
    k["restart"] = np.arange(SEQ)[None, :] % CH != 0
    k["restart"] = k["restart"] & np.ones((P, 1), bool)
    k["eye16"] = (np.arange(CH)[None, :, None] == 16 * (np.arange(P)[:, None, None] // 64) + np.arange(16)[None, None, :]).reshape(P, -1)
    k["upper"] = p <= c
    k["eps6"], k["eps_rw"], k["zero"] = np.full(P, EPS), np.full(P, 64e-5), np.zeros(P)
    return [np.concatenate([np.asarray(k[n], np.float32).reshape(P, -1) for n, _ in names], 1)
            for names in (CONSTS, NSA_CONSTS, RWKV_CONSTS)]


def bucket_rows():
    n = STRIP - 1 - np.arange(NR)
    m = np.maximum(n, 1).astype(np.float32)
    large = 16 + (np.log(m / np.float32(16)) / np.float32(math.log(8)) * 16).astype(np.int32)
    b = np.where(n < 16, np.maximum(n, 0), np.minimum(large, 31))
    out = np.zeros((BUCKETS + 1, NR), np.float32)
    out[b, np.arange(NR)] = 1
    out[:BUCKETS, n < 0] = 0
    out[BUCKETS] = n < 0
    return out


def lay_out(a):
    w = a["w_in"][0]
    cut = np.cumsum([0, 256, 256, 256, 256, 256, 256, 256, 32, 8, 512, 512, 512, D, D, D])
    col = [w[:, cut[i]:cut[i + 1]] for i in range(15)]
    units = [pack_units(c) for c in col[:7]]
    units += [pack_units(np.concatenate(col[7:9], 1))]
    units += [pack_units(c) for c in col[9:12]]
    br = np.concatenate([a["w_br_sb"][0], a["w_br_sp"][0], a["w_br_df"][0]], 0)
    units += [pack_units(c) for c in col[12:15]] + [pack_units(br)]
    units += [pack_units(a["w_out"][0])]
    up = a["w_up"][0]
    units += [interleave(pack_units(up[:, :D_FF]), pack_units(up[:, D_FF:]))]
    units += [pack_groups(a["w_down"][0])]
    w = a["w_in_2"][0]
    cut = np.cumsum([0, 384, 128, 128, 128, 128, 128, 128, 18, 256, 256, 256, 128, 384, 384, 384])
    units += [pack_units(w[:, cut[i]:cut[i + 1]]) for i in range(15)]
    units += [a["w_ada_3"][0].T.reshape(RAW, P, D)]
    units += [pack_units(a["w_out_2"][0])]
    up = a["ffn_w_in_2"][0]
    units += [interleave(pack_units(up[:, D_FF:]), pack_units(up[:, :D_FF]))]
    units += [pack_groups(a["ffn_w_out_2"][0])]
    w = a["w_in_3"][0]
    u, v, qk, mv, o = w[:, :D], w[:, D:2 * D], w[:, 2 * D:4 * D], w[:, 4 * D:5 * D], w[:, 5 * D:6 * D]
    fi = np.zeros((D, P), w.dtype)
    fi[:, 0:4], fi[:, 32:36] = w[:, 6 * D:6 * D + 4], w[:, 6 * D + 4:6 * D + 8]
    ga, gb = w[:, 6 * D + 8:7 * D + 8], w[:, 7 * D + 8:]
    units += [pack_units(c) for c in (v, u, ga, qk, mv, fi, o, gb)]
    units += [pack_units(a["w_out_3"][0]), pack_units(a["w_ff1_3"][0]), pack_groups(a["w_ff2_3"][0])]
    fixed = constants()
    seq = np.concatenate([a["meta_tokens"], a["x"][0]], 0)
    return {
        "weights": np.concatenate(units, 0),
        "x": np.ascontiguousarray(seq.T.reshape(NC, P, T1).transpose(1, 0, 2)).reshape(P, -1),
        "params": params(a),
        "consts": fixed[0],
        "nsa_consts": fixed[1],
        "rwkv_consts": fixed[2],
        "c": a["c_3"].reshape(1, D),
        "bucket": bucket_rows(),
        "rel_bias": a["rel_bias"],
        "lam": np.concatenate([a[n].reshape(1, 64) for n in ("lam_q1", "lam_q2", "lam_k1", "lam_k2")], 1),
        "cmp_pos": a["nsa_cmp_pos_2"][0].reshape(2, 16, 2, 64).transpose(2, 3, 0, 1).reshape(P, 32),
        "cmp_w1": a["nsa_cmp_w1_2"][0].reshape(2, 16, P, 256).transpose(0, 2, 1, 3).reshape(2, P, 4096),
        "cmp_w2": a["nsa_cmp_w2_2"][0].reshape(2, 2, P, 64).transpose(2, 0, 1, 3).reshape(P, 256),
        "lora": np.concatenate([a["rw_w2_2"][0], a["rw_a2_2"][0], a["rw_g2_2"][0]], 0),
        "gmlp_ws": a["gmlp_ws_3"][0].transpose(2, 0, 1).reshape(P, -1),
        "gmlp_bs": a["gmlp_bs_3"][0].reshape(1, -1),
    }


class Signal:

    def __init__(self, sem, unit=1):
        self.sem, self.unit, self.base = sem, unit, 0

    def at(self, k):
        return self.base + self.unit * k

    def passed(self, k):
        self.base += self.unit * k


class Chain:

    def __init__(self, sem):
        self.sem, self.value = sem, 0

    def do(self, eng, ins):
        self.value += 1
        ins.then_inc(self.sem, 1)
        eng.wait_ge(self.sem, self.value)


def tile_loop(eng, n, tb, body):
    full = n // tb
    for j in range(min(tb, n)):
        body(0, j)
    if full > 3:
        with eng.Fori(1, full - 1) as i:
            for j in range(tb):
                body(i, j)
    elif full == 3:
        for j in range(tb):
            body(1, j)
    if full > 1:
        for j in range(tb):
            body(full - 1, j)
    if full:
        for j in range(n % tb):
            body(full, j)


def halves(T):
    return [(0, 264), (264, 264)] if T == T1 else [(0, T)]


class Core:

    def __init__(self, nc, ctx, dram):
        self.nc, self.ctx, self.dram = nc, ctx, dram
        self.signals = {}
        self.h_all = self.sb("h", [P, NC, T1])
        self.h = self.h_all[:, :, :]
        self.ring = self.sb("ring", [P, RING, NC, P])
        self.con = self.sb("con", [P, NCON])
        self.where = {}
        self.place(CONSTS, self.con)
        self.par = self.sb("par", [P, NPAR])
        self.mod = self.sb("mod", [P, 6 * NC])
        self.arena = self.sb("arena", [P, MAIN])
        self.inner, self.outer, self.tail = ExitStack(), ExitStack(), None
        self.ps = ctx.enter_context(nc.psum_tensor("ps", [P, 8, 512], F32))
        self.flat = self.ps[:, :, :].rearrange("p b n -> p (b n)")
        self.arrived = [self.sem(f"weights_arrived{i}") for i in range(RING)]
        self.used = self.sem("weights_used")
        self.split_done = self.sem("weights_split")
        self.hi_ready = self.sem("weights_hi_ready")
        self.raw_used = self.sem("raw_weights_used")
        self.issued, self.stream, self.taken, self.split, self.limit = 0, 0, 0, 0, 0
        self.total = dram["weights"].shape[0]
        self.vec = Chain(self.sem("vector_step"))
        self.act = Chain(self.sem("scalar_step"))
        self.pool = Chain(self.sem("pool_step"))

    def sb(self, name, shape):
        return self.ctx.enter_context(self.nc.sbuf_tensor(name, shape, F32))

    def sem(self, name):
        return self.ctx.enter_context(self.nc.semaphore(name))

    def sig(self, name, unit=1):
        if name not in self.signals:
            self.signals[name] = Signal(self.sem(name), unit)
        return self.signals[name]

    def place(self, names, area):
        o = 0
        for n, m in names:
            self.where[n] = area[:, o:o + m]
            o += m

    def c(self, name, n=None):
        return self.where[name][:, 0:n or WIDTH[name]]

    def p(self, name, j=0):
        o = PCOL[name]
        return self.par[:, bass.ds(o + j, 1)] if not isinstance(j, int) else self.par[:, o + j:o + j + 1]

    def area(self, start, *dims):
        n = int(np.prod(dims))
        if start >= TAIL:
            v = self.tail[:, start - TAIL:start - TAIL + n]
            assert start - TAIL + n <= self.tail_size, (start - TAIL, dims)
        else:
            assert start + n <= MAIN, (start, dims)
            v = self.arena[:, start:start + n]
        if len(dims) == 1:
            return v
        names = "abcd"[:len(dims)]
        return v.rearrange(f"p ({' '.join(names)}) -> p {' '.join(names)}", **dict(zip(names[1:], dims[1:])))

    def open_inputs(self):
        self.outer = ExitStack()
        self.xh, self.xl = (self.outer.enter_context(self.nc.sbuf_tensor(f"{n}{self.taken}", [P, NC, T1], F32R)) for n in ("xh", "xl"))

    def open_weights(self, units):
        self.inner = ExitStack()
        self.wh, self.wl = (self.inner.enter_context(self.nc.sbuf_tensor(f"{n}{self.taken}", [P, 2, NC, P], F32R)) for n in ("wh", "wl"))
        self.limit = self.taken + units

    def close(self, inputs=False):
        assert self.taken == self.split == self.limit
        self.inner.close()
        if inputs:
            self.outer.close()

    def open_tail(self, size):
        self.inner, self.tail_size = ExitStack(), size
        self.tail = self.inner.enter_context(self.nc.sbuf_tensor(f"tail{size}", [P, size], F32))

    def load_units(self, sp, units):
        a, b = self.issued, min(self.stream + units + RING, self.total)
        w = self.dram["weights"]

        def load(u, i):
            slot = u % RING
            old = u - RING
            if old >= 0:
                if old < RAW0:
                    sp.wait_ge(self.split_done, old + 1 + i * RING)
                elif old < RAW0 + RAW:
                    sp.wait_ge(self.raw_used, old - RAW0 + 1 + i * RING)
                else:
                    sp.wait_ge(self.split_done, old - RAW + 1 + i * RING)
            src = w[u:u + 1] if isinstance(i, int) else w[bass.ds(u + i * RING, 1)]
            sp.dma_start(self.ring[:, slot:slot + 1], src.rearrange("o p (c n) -> p o c n", c=NC)).then_inc(
                self.arrived[slot], 16)

        cuts = sorted({min(max(c, a), b) for c in (a, RING, RAW0 + RING, RAW0 + RAW + RING, b)})
        for u, end in zip(cuts, cuts[1:]):
            rounds = (end - u) // RING
            if rounds > 1 and u >= RING:
                with sp.Fori(0, rounds) as i:
                    for j in range(RING):
                        load(u + j, i)
                u += rounds * RING
            while u < end:
                load(u, 0)
                u += 1
        self.issued = max(b, a)

    def place_of(self, s):
        return s if s < RAW0 else s + RAW

    def split_hi(self, act, off, i=0, per=0):
        s = self.taken + off + 2
        if isinstance(i, int):
            s += i * per
            i = 0
            if s >= self.limit:
                return
        if s < self.split:
            return
        u = self.place_of(s)
        act.wait_ge(self.arrived[u % RING], 16 * (u // RING + 1) + i * (16 * per // RING))
        if s >= 2:
            act.wait_ge(self.used, s - 1 + i * per)
        flat = lambda a: a.rearrange("p c n -> p (c n)")
        act.activation(flat(self.wh[:, s % 2]), flat(self.ring[:, u % RING]), ACT.Copy).then_inc(self.hi_ready, 1)

    def split_lo(self, dve, off, i=0, per=0):
        s = self.taken + off + 2
        if isinstance(i, int):
            s += i * per
            i = 0
            if s >= self.limit:
                return
        if s < self.split:
            return
        u = self.place_of(s)
        dve.wait_ge(self.hi_ready, s + 1 + i * per)
        flat = lambda a: a.rearrange("p c n -> p (c n)")
        dve.tensor_tensor(flat(self.wl[:, s % 2]), flat(self.ring[:, u % RING]), flat(self.wh[:, s % 2]).bitcast(F32),
                          ALU.subtract).then_inc(self.split_done, 1)

    def split_first(self, eng, split):
        for off in range(2):
            split(eng, off - 2)

    def product(self, pe, out, T, off, i=0, per=0, chunks=NC, input_ready=None):
        s = self.taken + off
        pe.wait_ge(self.split_done, s + 1 + i * per)
        wh, wl = self.wh[:, s % 2], self.wl[:, s % 2]
        for k in range(chunks):
            if input_ready:
                input_ready(k)
            for n, (w, x) in enumerate(((wh, self.xh), (wh, self.xl), (wl, self.xh))):
                for e, (o, m) in enumerate(halves(T)):
                    last = pe.matmul(out(e), w[:, k, :], x[:, k, o:o + m], start=(k == 0 and n == 0),
                                     stop=(k == chunks - 1 and n == 2))
        return last

    def finished(self, units):
        self.split = max(self.split, min(self.taken + units + 2, self.limit))
        self.stream += units
        self.taken += units


def tile_of(buf, t, T):
    s = len(halves(T))
    if isinstance(t, int):
        return buf[:, t, 0:T].rearrange("p (s n) -> p s n", s=s)
    return buf[:, bass.ds(t, 1), 0:T].rearrange("p o (s n) -> p (o s) n", s=s)


def banks(core, slot, T):
    s, w = len(halves(T)), halves(T)[0][1]
    return core.ps[:, slot:slot + s, 0:w]


def out_slot(j, bank=0):
    return bank + 2 * (j % 2)


def gemm(core, pe, n, tb, T, free, free2=None, first=0, chunks=NC, input_ready=None):
    def body(i, j):
        t = i * tb + j + first
        if not isinstance(t, int) or t >= 2:
            if free2 is None:
                pe.wait_ge(free.sem, free.at(t - 1))
            else:
                own = free2 if j % 2 else free
                pe.wait_ge(own.sem, own.at(i * (tb // 2) + j // 2))
        core.product(pe, lambda s: core.ps[:, out_slot(j) + s, 0:halves(T)[s][1]], T, first + j, i, tb, chunks,
                     input_ready if isinstance(i, int) and i * tb + j == 0 else None).then_inc(core.used, 1)
    tile_loop(pe, n, tb, body)


def tile_done(core, eng, i, j, tb):
    eng.wait_ge(core.used, core.taken + j + 1 + i * tb)


def project(core, n, dst, T, func=ACT.Copy, bias=None):
    free = core.sig("tile_free")
    with core.nc.Block() as block:
        @block.sync
        def _(sp):
            core.load_units(sp, n)

        @block.tensor
        def _(pe):
            gemm(core, pe, n, 4, T, free)

        @block.scalar
        def _(act):
            core.split_first(act, core.split_hi)

            def body(i, j):
                t = i * 4 + j
                tile_done(core, act, i, j, 4)
                core.split_hi(act, j, i, 4)
                act.activation(tile_of(dst, t, T), banks(core, out_slot(j), T), func,
                               bias=core.p(bias, t) if bias else 0.0).then_inc(free.sem, 1)
            tile_loop(act, n, 4, body)

        @block.vector
        def _(dve):
            core.split_first(dve, core.split_lo)
            tile_loop(dve, n, 4, lambda i, j: core.split_lo(dve, j, i, 4))
    free.passed(n)
    core.finished(n)


def split_input(core, tiles, T):
    hi = core.sig("input_hi")
    with core.nc.Block() as block:
        @block.scalar
        def _(act):
            for k, a in enumerate(tiles):
                act.activation(core.xh[:, k, 0:T], a, ACT.Copy).then_inc(hi.sem, 1)

        @block.vector
        def _(dve):
            for k, a in enumerate(tiles):
                dve.wait_ge(hi.sem, hi.at(k + 1))
                dve.tensor_tensor(core.xl[:, k, 0:T], a, core.xh[:, k, 0:T].bitcast(F32), ALU.subtract)
    hi.passed(len(tiles))


def add_product(core, kc, src, T, scale=None):
    free, hi, lo = core.sig("tile_free"), core.sig("input_hi"), core.sig("input_lo")
    groups = [(g, min(NC, kc - g)) for g in range(0, kc, NC)]
    with core.nc.Block() as block:
        @block.sync
        def _(sp):
            core.load_units(sp, NC * len(groups))

        @block.tensor
        def _(pe):
            for g, m in groups:
                gemm(core, pe, NC, 4, T, free, first=g, chunks=m,
                     input_ready=lambda k, g=g: pe.wait_ge(lo.sem, lo.at(g + k + 1)))

        @block.scalar
        def _(act):
            core.split_first(act, core.split_hi)
            for g, m in groups:
                if g:
                    act.wait_ge(core.used, core.taken + g)
                for k in range(m):
                    act.activation(core.xh[:, k, 0:T], src[:, g + k, 0:T], ACT.Copy).then_inc(hi.sem, 1)
                tile_loop(act, NC, 4, lambda i, j: core.split_hi(act, g + j, i, 4))

        @block.vector
        def _(dve):
            core.split_first(dve, core.split_lo)
            for g, m in groups:
                for k in range(m):
                    dve.wait_ge(hi.sem, hi.at(g + k + 1))
                    dve.tensor_tensor(core.xl[:, k, 0:T], src[:, g + k, 0:T], core.xh[:, k, 0:T].bitcast(F32),
                                      ALU.subtract).then_inc(lo.sem, 1)

                def body(i, j):
                    t = i * 4 + j
                    dve.wait_ge(core.used, core.taken + g + j + 1 + i * 4)
                    out, got = tile_of(core.h, t, T), banks(core, out_slot(j), T)
                    if scale is None:
                        dve.tensor_tensor(out, got, out, ALU.add).then_inc(free.sem, 1)
                    else:
                        dve.scalar_tensor_tensor(out=out, in0=got, scalar=scale(t), in1=out, op0=ALU.mult,
                                                 op1=ALU.add).then_inc(free.sem, 1)
                    core.split_lo(dve, g + j, i, 4)
                tile_loop(dve, NC, 4, body)
    free.passed(NC * len(groups))
    hi.passed(kc)
    lo.passed(kc)
    core.finished(NC * len(groups))


def conv_glu_up(core, dst, tmp, T, conv_w, conv_b):
    free, gate_in, conv_out, act_out = (core.sig(n) for n in ("tile_free", "gate_in", "conv_out", "silu_out"))
    gate = core.area(tmp, 2, T + 2)
    mid = core.area(tmp + 2 * (T + 2), 2, 3, T)
    step = core.vec
    with core.nc.Block() as block:
        @block.sync
        def _(sp):
            core.load_units(sp, 2 * FT)

        @block.tensor
        def _(pe):
            gemm(core, pe, 2 * FT, 4, T, gate_in, free)

        @block.scalar
        def _(act):
            core.split_first(act, core.split_hi)
            core.act.do(act, act.activation(gate[:, :, 0:2], core.c("ones", 4).rearrange("p (b n) -> p b n", b=2),
                                            ACT.Copy, scale=0.0))

            def body(i, j):
                p = i * 2 + j
                act.wait_ge(core.used, core.taken + 2 * j + 1 + i * 4)
                core.split_hi(act, 2 * j, i, 4)
                if not isinstance(p, int) or p >= 2:
                    act.wait_ge(conv_out.sem, conv_out.at(p - 1))
                o = gate[:, j, 2:2 + T].rearrange("p (s n) -> p s n", s=len(halves(T)))
                act.activation(o, banks(core, out_slot(0), T), ACT.Copy).then_inc(gate_in.sem, 1)
                act.wait_ge(conv_out.sem, conv_out.at(p + 1))
                act.activation(mid[:, j, 2], mid[:, j, 1], ACT.Silu).then_inc(act_out.sem, 1)
                core.split_hi(act, 2 * j + 1, i, 4)
            tile_loop(act, FT, 2, body)

        @block.vector
        def _(dve):
            base = step.value
            core.split_first(dve, core.split_lo)

            def body(i, j):
                p = i * 2 + j

                def ordered(k, ins):
                    ins.then_inc(step.sem, 1)
                    dve.wait_ge(step.sem, base + 2 * p + k)
                core.split_lo(dve, 2 * j, i, 4)
                dve.wait_ge(gate_in.sem, gate_in.at(p + 1))
                ordered(1, dve.tensor_scalar(mid[:, j, 0], gate[:, j, 2:2 + T], core.p(conv_w, 2 * FT + p),
                                             core.p(conv_b, p), ALU.mult, ALU.add))
                ordered(2, dve.scalar_tensor_tensor(out=mid[:, j, 1], in0=gate[:, j, 1:1 + T],
                                                    scalar=core.p(conv_w, FT + p), in1=mid[:, j, 0], op0=ALU.mult,
                                                    op1=ALU.add))
                dve.scalar_tensor_tensor(out=mid[:, j, 1], in0=gate[:, j, 0:T], scalar=core.p(conv_w, p),
                                         in1=mid[:, j, 1], op0=ALU.mult, op1=ALU.add).then_inc(conv_out.sem, 1)
                dve.wait_ge(act_out.sem, act_out.at(p + 1))
                dve.wait_ge(core.used, core.taken + 2 * j + 2 + i * 4)
                s = mid[:, j, 2].rearrange("p (s n) -> p s n", s=len(halves(T)))
                dve.tensor_tensor(tile_of(dst, p, T), banks(core, out_slot(1), T), s, ALU.mult).then_inc(free.sem, 1)
                core.split_lo(dve, 2 * j + 1, i, 4)
            tile_loop(dve, FT, 2, body)
            step.value = base + 2 * FT
    for s in (free, gate_in, conv_out, act_out):
        s.passed(FT)
    core.finished(2 * FT)


def act_mul(core, parts, T, tmp, tiles=NC):
    free, mul = core.sig("tile_free"), core.sig("multiplied")
    mid = core.area(tmp, 2, T)
    prod = core.area(tmp + 2 * T, 2, T)
    S = len(halves(T))

    for func, other, dst, add in parts:
        with core.nc.Block() as block:
            @block.sync
            def _(sp):
                core.load_units(sp, tiles)

            @block.tensor
            def _(pe):
                gemm(core, pe, tiles, 4, T, free)

            @block.scalar
            def _(act):
                core.split_first(act, core.split_hi)

                def body(i, j):
                    t = i * 4 + j
                    tile_done(core, act, i, j, 4)
                    core.split_hi(act, j, i, 4)
                    if not isinstance(t, int) or t >= 2:
                        act.wait_ge(mul.sem, mul.at(t - 1))
                    act.activation(mid[:, j % 2].rearrange("p (s n) -> p s n", s=S), banks(core, out_slot(j), T),
                                   func).then_inc(free.sem, 1)
                tile_loop(act, tiles, 4, body)

            @block.vector
            def _(dve):
                core.split_first(dve, core.split_lo)

                def body(i, j):
                    t = i * 4 + j
                    core.split_lo(dve, j, i, 4)
                    dve.wait_ge(free.sem, free.at(t + 1))
                    m = mid[:, j % 2].rearrange("p (s n) -> p s n", s=S)
                    o = m if other is None else tile_of(other, t, T)
                    if not add:
                        dve.tensor_tensor(tile_of(dst, t, T), m, o, ALU.mult).then_inc(mul.sem, 1)
                        return
                    pr = prod[:, j % 2].rearrange("p (s n) -> p s n", s=S)
                    dve.tensor_tensor(pr, m, o, ALU.mult).then_inc(mul.sem, 1)
                    dve.wait_ge(mul.sem, mul.at(t + 1))
                    out = tile_of(dst, t, T)
                    dve.tensor_tensor(out, out, pr, ALU.add)
                tile_loop(dve, tiles, 4, body)
        free.passed(tiles)
        mul.passed(tiles)
        core.finished(tiles)


def norm(core, items, T, inv_n, tmp, eps="eps6", ones="ones", least=None):
    sq_ready, sq_used, sum_used, root_used = (core.sig(n) for n in ("square_ready", "square_used", "sum_used", "root_used"))
    sq = core.area(tmp, 2, T)
    r = core.area(tmp + 2 * T, 2, T)
    tiles = sum(len(x[0]) for x in items)
    with core.nc.Block() as block:
        @block.scalar
        def _(act):
            def root(n, t):
                act.wait_ge(sq_used.sem, sq_used.at(t))
                if n >= 2:
                    act.wait_ge(root_used.sem, root_used.at(n - 1))
                act.activation(r[:, n % 2].rearrange("p (s n) -> p s n", s=len(halves(T))), banks(core, out_slot(n), T),
                               ACT.Sqrt, bias=core.c(eps), scale=inv_n).then_inc(sum_used.sem, 1)

            t = 0
            for n, (x, _, _, _) in enumerate(items):
                for k, a in enumerate(x):
                    if t >= 2:
                        act.wait_ge(sq_used.sem, sq_used.at(t - 1))
                    act.activation(sq[:, t % 2], a, ACT.Square).then_inc(sq_ready.sem, 1)
                    t += 1
                    if n and k == 0:
                        root(n - 1, t - 1)
            root(len(items) - 1, t)

        @block.tensor
        def _(pe):
            t = 0
            for n, (x, _, _, _) in enumerate(items):
                if n >= 2:
                    pe.wait_ge(sum_used.sem, sum_used.at(n - 1))
                for k in range(len(x)):
                    pe.wait_ge(sq_ready.sem, sq_ready.at(t + 1))
                    for s, (o, w) in enumerate(halves(T)):
                        last = pe.matmul(core.ps[:, out_slot(n) + s, 0:w], core.c(ones), sq[:, t % 2, o:o + w],
                                         start=(k == 0), stop=(k == len(x) - 1))
                    last.then_inc(sq_used.sem, 1)
                    t += 1

        @block.vector
        def _(dve):
            do = lambda ins: core.vec.do(dve, ins)
            for n, (x, out, gains, shifts) in enumerate(items):
                rn = r[:, n % 2]
                dve.wait_ge(sum_used.sem, sum_used.at(n + 1))
                if least is not None:
                    do(dve.tensor_scalar(rn, rn, least, None, ALU.max))
                do(dve.reciprocal(rn, rn))
                for k, a in enumerate(x):
                    if gains is None:
                        ins = dve.tensor_tensor(out[k], a, rn, ALU.mult)
                    else:
                        ins = dve.scalar_tensor_tensor(out=out[k], in0=a, scalar=gains[k], in1=rn, op0=ALU.mult,
                                                       op1=ALU.mult)
                    if shifts is not None:
                        do(ins)
                        ins = dve.tensor_scalar(out[k], out[k], shifts[k], None, ALU.add)
                    if k < len(x) - 1:
                        do(ins)
                    else:
                        ins.then_inc(root_used.sem, 1)
    sq_ready.passed(tiles)
    sq_used.passed(tiles)
    sum_used.passed(len(items))
    root_used.passed(len(items))


def input_norm(core, gains, shifts, T, tmp):
    sq_ready, sq_used, root, made, hi = (core.sig(n) for n in (
        "square_ready", "square_used", "root_ready", "normed", "input_hi"))
    sq, r, out = core.area(tmp, 2, T), core.area(tmp + 2 * T, T), core.area(tmp + 3 * T, 2, T)
    x = lambda k: core.h[:, k, 0:T]
    S = len(halves(T))
    with core.nc.Block() as block:
        @block.sync
        def _(sp):
            core.load_units(sp, 0)

        @block.scalar
        def _(act):
            for k in range(NC):
                if k >= 2:
                    act.wait_ge(sq_used.sem, sq_used.at(k - 1))
                act.activation(sq[:, k % 2], x(k), ACT.Square).then_inc(sq_ready.sem, 1)
            act.wait_ge(sq_used.sem, sq_used.at(NC))
            act.activation(r.rearrange("p (s n) -> p s n", s=S), banks(core, 0, T), ACT.Sqrt, bias=core.c("eps6"),
                           scale=1.0 / D).then_inc(root.sem, 1)
            core.split_first(act, core.split_hi)
            for k in range(NC):
                act.wait_ge(made.sem, made.at(k + 1))
                act.activation(core.xh[:, k, 0:T], out[:, k % 2], ACT.Identity,
                               bias=shifts[k] if shifts else 0.0).then_inc(hi.sem, 1)

        @block.tensor
        def _(pe):
            for k in range(NC):
                pe.wait_ge(sq_ready.sem, sq_ready.at(k + 1))
                for s, (o, w) in enumerate(halves(T)):
                    last = pe.matmul(core.ps[:, s, 0:w], core.c("ones"), sq[:, k % 2, o:o + w], start=(k == 0),
                                     stop=(k == NC - 1))
                last.then_inc(sq_used.sem, 1)

        @block.vector
        def _(dve):
            def low(k):
                dve.wait_ge(hi.sem, hi.at(k + 1))
                to, a, b = core.xl[:, k, 0:T], out[:, k % 2], core.xh[:, k, 0:T].bitcast(F32)
                if shifts:
                    ins = dve.scalar_tensor_tensor(out=to, in0=a, scalar=shifts[k], in1=b, op0=ALU.add, op1=ALU.subtract)
                else:
                    ins = dve.tensor_tensor(to, a, b, ALU.subtract)
                core.vec.do(dve, ins)
            core.split_first(dve, core.split_lo)
            dve.wait_ge(root.sem, root.at(1))
            core.vec.do(dve, dve.reciprocal(r, r))
            for k in range(NC):
                if k >= 2:
                    low(k - 2)
                dve.scalar_tensor_tensor(out=out[:, k % 2], in0=x(k), scalar=gains[k], in1=r, op0=ALU.mult,
                                         op1=ALU.mult).then_inc(made.sem, 1)
            low(NC - 2)
            low(NC - 1)
    for a, n in ((sq_ready, NC), (sq_used, NC), (root, 1), (made, NC), (hi, NC)):
        a.passed(n)
    core.finished(0)


def layer_norm_input(core, gain, T, tmp):
    input_norm(core, [core.p(gain, k) for k in range(NC)], None, T, tmp)


def load_small(core):
    d, got = core.dram, core.sig("loaded", 16)
    with core.nc.Block() as block:
        @block.sync
        def _(sp):
            sp.dma_start(core.h.rearrange("p c t -> p (c t)"), d["x"]).then_inc(got.sem, 16)
            sp.dma_start(core.con[:, :], d["consts"]).then_inc(got.sem, 16)
            sp.dma_start(core.par[:, :], d["params"]).then_inc(got.sem, 16)
            core.load_units(sp, 0)
            sp.wait_ge(got.sem, got.at(3))
    got.passed(3)


def q_tiles(T):
    return [(q, min(P, T - q), min(q + P, T)) for q in range(0, T, P)]


def to_tokens(core, pairs, T):
    turned, turned_used = core.sig("turned"), core.sig("turned_used")
    nj = len(q_tiles(T))
    with core.nc.Block() as block:
        @block.tensor
        def _(pe):
            n = 0
            for tiles, _ in pairs:
                for q, nq, _ in q_tiles(T):
                    if n >= 2:
                        pe.wait_ge(turned_used.sem, turned_used.at(n - 1))
                    for m, a in enumerate(tiles):
                        last = pe.transpose(core.ps[0:nq, 4 + n % 2, m * P:(m + 1) * P], a[:, q:q + nq], core.c("ident"))
                    last.then_inc(turned.sem, 1)
                    n += 1

        @block.vector
        def _(dve):
            n = 0
            for tiles, dst in pairs:
                for j, (q, nq, _) in enumerate(q_tiles(T)):
                    dve.wait_ge(turned.sem, turned.at(n + 1))
                    dve.tensor_copy(dst(j)[0:nq], core.ps[0:nq, 4 + n % 2, 0:len(tiles) * P]).then_inc(turned_used.sem, 1)
                    n += 1
    turned.passed(nj * len(pairs))
    turned_used.passed(nj * len(pairs))


class Head:

    def __init__(self, maps, values, out, strip=None, chosen=None):
        self.maps, self.values, self.out, self.strip, self.chosen = maps, values, out, strip, chosen


def attention(core, kind, heads, T, tmp, neg_lam=None, beside=None):
    names = ("scores", "scores_used", "shifted", "exps", "probs", "turned", "turned_used", "out_ready", "out_used")
    scores, scores_used, shifted, exps, probs, turned, turned_used, out_ready, out_used = (core.sig(n) for n in names)
    nm = len(heads[0].maps)
    steps = [(h, i) for h in heads for i in range(len(q_tiles(T)))]
    N = len(steps)
    ahead, NX = (2, 3) if nm == 1 else (1, 2)
    softplus_size = 2 * T if kind == "stick" else 0
    X = core.area(tmp, NX, nm, T)
    Y = core.area(tmp + NX * nm * T, 2, T) if kind == "stick" else None
    PT = core.area(tmp + NX * nm * T + softplus_size, 2, 512)
    stat = core.area(tmp + NX * nm * T + softplus_size + 1024, NX, 2, 8)

    def psum_scores(s, m, nq, nk):
        b = 2 * ((s * nm + m) % 2)
        return core.flat[0:nq, b * 512:b * 512 + nk]

    with core.nc.Block() as block:
        if beside:
            @block.sync
            def _(sp):
                core.load_units(sp, N)

        @block.tensor
        def _(pe):
            def score(s):
                h, i = steps[s]
                q0, nq, nk = q_tiles(T)[i]
                for m, (q, k) in enumerate(h.maps):
                    n = s * nm + m
                    if n >= 2:
                        pe.wait_ge(scores_used.sem, scores_used.at(n - 1))
                    dst = psum_scores(s, m, nq, nk)
                    for o in range(0, nk, 512):
                        w = min(512, nk - o)
                        last = pe.matmul(dst[:, o:o + w], q[:, q0:q0 + nq], k[:, o:o + w], start=True, stop=True)
                    last.then_inc(scores.sem, 1)

            def turn(s):
                h, i = steps[s]
                q0, nq, nk = q_tiles(T)[i]
                pe.wait_ge(probs.sem, probs.at(s + 1))
                if s >= 2:
                    pe.wait_ge(turned_used.sem, turned_used.at(s - 1))
                for j, o in enumerate(range(0, nk, P)):
                    w = min(P, nk - o)
                    last = pe.transpose(core.ps[0:w, 4 + s % 2, j * nq:(j + 1) * nq], X[0:nq, s % NX, 0, o:o + w],
                                        core.c("ident")[0:nq, 0:nq])
                last.then_inc(turned.sem, 1)

            def weigh(s):
                h, i = steps[s]
                q0, nq, nk = q_tiles(T)[i]
                pe.wait_ge(turned_used.sem, turned_used.at(s + 1))
                if s >= 2:
                    pe.wait_ge(out_used.sem, out_used.at(s - 1))
                lo, n = h.out[0], h.out[1]
                for j, o in enumerate(range(0, nk, P)):
                    w = min(P, nk - o)
                    last = pe.matmul(core.ps[lo:lo + n, 6 + s % 2, 0:nq], h.values(j, w), PT[0:w, s % 2, j * nq:(j + 1) * nq],
                                     start=(j == 0), stop=(o + P >= nk))
                last.then_inc(out_ready.sem, 1)

            for s in range(ahead):
                score(s)
            for s in range(N):
                if s + ahead < N:
                    score(s + ahead)
                turn(s)
                if s:
                    weigh(s - 1)
            weigh(N - 1)

        @block.vector
        def _(dve):
            do = lambda ins: core.vec.do(dve, ins)

            def before(s):
                h, i = steps[s]
                q0, nq, nk = q_tiles(T)[i]
                o = DIAG - q0
                if s >= NX:
                    dve.wait_ge(turned.sem, turned.at(s - NX + 1))
                for m in range(nm):
                    n = s * nm + m
                    x, got, st = X[0:nq, s % NX, m, 0:nk], psum_scores(s, m, nq, nk), stat[0:nq, s % NX, m]
                    if kind == "stick":
                        y = Y[0:nq, s % 2, 0:nk]
                        dve.wait_ge(exps.sem, exps.at(s + 1))
                        do(dve.scalar_tensor_tensor(out=y, in0=got, scalar=0.0, in1=y, op0=ALU.max, op1=ALU.add))
                        do(dve.tensor_tensor(y[:, q0:nk], y[:, q0:nk], core.c("strict")[0:nq, 0:nk - q0], ALU.mult))
                        do(dve.tensor_tensor_scan(x[:, ::-1], y[:, ::-1], y[:, ::-1], 0.0, ALU.add, ALU.bypass))
                        dve.tensor_tensor(x, got, x, ALU.subtract).then_inc(scores_used.sem, 1)
                        dve.wait_ge(scores_used.sem, scores_used.at(n + 1))
                        dve.tensor_tensor(x[:, q0:nk], x[:, q0:nk], core.c("strict_neg")[0:nq, 0:nk - q0],
                                          ALU.add).then_inc(shifted.sem, 1)
                        continue
                    strip = h.strip[0:nq, o:o + nk]
                    dve.wait_ge(scores.sem, scores.at(n + 1))
                    if h.chosen is not None and i:
                        dve.tensor_tensor(x, got, strip, ALU.add).then_inc(scores_used.sem, 1)
                        dve.wait_ge(scores_used.sem, scores_used.at(n + 1))
                        do(dve.tensor_tensor(x, x, h.chosen(i)[0:nq, 0:nk], ALU.add))
                    else:
                        dve.tensor_tensor(x, got, strip, ALU.add).then_inc(scores_used.sem, 1)
                        dve.wait_ge(scores_used.sem, scores_used.at(n + 1))
                    do(dve.tensor_reduce(st[:, 0:1], x, AX, ALU.max))
                    dve.tensor_scalar(st[:, 1:2], st[:, 0:1], -1.0, None, ALU.mult).then_inc(shifted.sem, 1)

            def after(s):
                h, i = steps[s]
                q0, nq, nk = q_tiles(T)[i]
                for m in range(nm):
                    x, st = X[0:nq, s % NX, m, 0:nk], stat[0:nq, s % NX, m]
                    dve.wait_ge(exps.sem, exps.at(s * nm + m + 1))
                    do(dve.reciprocal(st[:, 3:4], st[:, 2:3]))
                    if m == 0:
                        ins = dve.tensor_scalar(x, x, st[:, 3:4], None, ALU.mult)
                        if nm == 2:
                            do(ins)
                        else:
                            ins.then_inc(probs.sem, 1)
                    else:
                        do(dve.tensor_scalar(st[:, 4:5], st[:, 3:4], neg_lam[0:nq, 0:1], None, ALU.mult))
                        x0 = X[0:nq, s % NX, 0, 0:nk]
                        dve.scalar_tensor_tensor(out=x0, in0=x, scalar=st[:, 4:5], in1=x0, op0=ALU.mult,
                                                 op1=ALU.add).then_inc(probs.sem, 1)

            before(0)
            for s in range(N):
                if s + 1 < N:
                    before(s + 1)
                if kind != "stick":
                    after(s)
                if beside:
                    beside.multiply(dve, s)

        @block.scalar
        def _(act):
            do = lambda ins: core.act.do(act, ins)

            def softplus(s):
                h, i = steps[s]
                q0, nq, nk = q_tiles(T)[i]
                got, y = psum_scores(s, 0, nq, nk), Y[0:nq, s % 2, 0:nk]
                act.wait_ge(scores.sem, scores.at(s + 1))
                if s >= 2:
                    act.wait_ge(scores_used.sem, scores_used.at(s - 1))
                do(act.activation(y, got, ACT.Abs))
                do(act.activation(y, y, ACT.Exp, scale=-1.0))
                act.activation(y, y, ACT.Ln, bias=1.0).then_inc(exps.sem, 1)

            def exp(s):
                h, i = steps[s]
                q0, nq, nk = q_tiles(T)[i]
                for m in range(nm):
                    x, st = X[0:nq, s % NX, m, 0:nk], stat[0:nq, s % NX, m]
                    act.wait_ge(shifted.sem, shifted.at(s * nm + m + 1))
                    if kind == "stick":
                        act.activation(x, x, ACT.Exp).then_inc(probs.sem, 1)
                    else:
                        act.activation(x, x, ACT.Exp, bias=st[:, 1:2], accum_out=st[:, 2:3]).then_inc(exps.sem, 1)

            def copy_turned(s):
                h, i = steps[s]
                q0, nq, nk = q_tiles(T)[i]
                act.wait_ge(turned.sem, turned.at(s + 1))
                if s >= 2:
                    act.wait_ge(out_ready.sem, out_ready.at(s - 1))
                full, rest = nk // P * nq, nk % P
                ins = act.activation(PT[:, s % 2, 0:full], core.ps[:, 4 + s % 2, 0:full], ACT.Copy)
                if rest:
                    core.act.do(act, ins)
                    ins = act.activation(PT[0:rest, s % 2, full:full + nq], core.ps[0:rest, 4 + s % 2, full:full + nq], ACT.Copy)
                ins.then_inc(turned_used.sem, 1)

            def copy_out(s):
                h, i = steps[s]
                q0, nq, nk = q_tiles(T)[i]
                lo, n, out = h.out
                act.wait_ge(out_ready.sem, out_ready.at(s + 1))
                act.activation(out[lo:lo + n, q0:q0 + nq], core.ps[lo:lo + n, 6 + s % 2, 0:nq], ACT.Copy).then_inc(out_used.sem, 1)

            if kind == "stick":
                core.nc.scalar.add_instruction(mybir.InstLoadActFuncSet(
                    act_func_set_id=EXP_LN_TABLES, name=core.nc.get_next_instruction_name(),
                    engine=mybir.EngineType.Activation))
                softplus(0)
            for s in range(N):
                if kind == "stick" and s + 1 < N:
                    softplus(s + 1)
                exp(s)
                if s >= 1:
                    copy_turned(s - 1)
                if s >= 2:
                    copy_out(s - 2)
                if beside:
                    beside.sum(act, s)
            copy_turned(N - 1)
            copy_out(N - 2)
            copy_out(N - 1)
    if beside:
        beside.passed(N)
    exps.passed(N * nm)
    scores.passed(N * nm)
    scores_used.passed(N * nm)
    shifted.passed(N * nm)
    for x in (probs, turned, turned_used, out_ready, out_used):
        x.passed(N)


def bias_strips(core, strips, tmp):
    got, made, row, back = (core.sig(n, u) for n, u in (
        ("strip_inputs", 16), ("strip_made", 1), ("strip_row", 1), ("strip_stored", 16)))
    done = [core.sig(f"strip_back{i}", 16) for i in range(2)]
    table = core.area(tmp, 8)
    hot = core.area(tmp + 8, NR)
    rows = core.area(tmp + 8 + NR, NR)
    skew = core.area(tmp + 8 + 2 * NR, 2, STRIP)
    scratch = core.dram["strip_scratch"]
    flipped, used = core.sig("strip_flipped"), core.sig("strip_used")
    with core.nc.Block() as block:
        @block.vector
        def _(dve):
            dve.memset(table[0:64, :], NEG).then_inc(made.sem, 1)
            dve.wait_ge(row.sem, row.at(1))
            dve.tensor_copy(rows[0:8, :], core.flat[0:8, 0:NR]).then_inc(row.sem, 1)
            for h in range(8):
                dve.wait_ge(flipped.sem, flipped.at(h + 1))
                dve.tensor_copy(strips[:, h, :].rearrange("p (s n) -> p s n", s=2),
                                core.ps[:, 2 + 2 * (h % 2):4 + 2 * (h % 2), 0:STRIP // 2]).then_inc(used.sem, 1)

        @block.sync
        def _(sp):
            sp.dma_start(hot[0:BUCKETS + 1, :], core.dram["bucket"]).then_inc(got.sem, 16)
            sp.wait_ge(made.sem, made.at(1))
            sp.dma_start(table[0:BUCKETS, :], core.dram["rel_bias"]).then_inc(got.sem, 16)
            sp.wait_ge(row.sem, row.at(2))
            sp.dma_start(scratch[:, :], rows[0:8, :]).then_inc(back.sem, 16)
            sp.wait_ge(back.sem, back.at(1))
            for h in range(8):
                if h >= 2:
                    sp.wait_ge(flipped.sem, flipped.at(h - 1))
                src = bass.AP(scratch.tensor, scratch.offset + h * NR, [[1, P], [1, STRIP]])
                sp.dma_start(skew[:, h % 2], src).then_inc(done[h % 2].sem, 16)

        @block.tensor
        def _(pe):
            pe.wait_ge(got.sem, got.at(2))
            for o in range(0, NR, 512):
                w = min(512, NR - o)
                last = pe.matmul(core.flat[0:8, o:o + w], table[0:BUCKETS + 1, :], hot[0:BUCKETS + 1, o:o + w],
                                 start=True, stop=True)
            last.then_inc(row.sem, 1)
            for h in range(8):
                pe.wait_ge(done[h % 2].sem, done[h % 2].at(h // 2 + 1))
                if h >= 2:
                    pe.wait_ge(used.sem, used.at(h - 1))
                for s in range(2):
                    n = STRIP // 2
                    last = pe.matmul(core.ps[:, 2 + 2 * (h % 2) + s, 0:n], core.c("flip"), skew[:, h % 2, s * n:(s + 1) * n],
                                     start=True, stop=True)
                last.then_inc(flipped.sem, 1)
    got.passed(2), made.passed(1), row.passed(2), back.passed(1), done[0].passed(4), done[1].passed(4), flipped.passed(8), used.passed(8)


def choose_keys(core, P1, kx, chosen, tmp):
    copied, turned, weighed = core.sig("ix_copied"), core.sig("ix_turned"), core.sig("ix_weights")
    dots, dots_used, relus, relus_used = (core.sig(n) for n in ("ix_dots", "ix_dots_used", "ix_relus", "ix_relus_used"))
    w = core.area(tmp, 5, 8)
    R = core.area(tmp + 40, 2, T1)
    S = core.area(tmp + 40 + 2 * T1, T1)
    W = core.area(tmp + 40 + 3 * T1, T1)
    m8 = core.area(tmp + 40 + 4 * T1, 8)
    need = core.area(tmp + 48 + 4 * T1, 1)
    tiles = q_tiles(T1)
    steps = [(i, j) for i in range(1, 5) for j in range(8)]
    with core.nc.Block() as block:
        @block.gpsimd
        def _(pool):
            for g in range(4):
                ins = pool.tensor_copy(kx[32 * g:32 * g + 32, :], P1[0:32, IX_K, :])
                if g < 3:
                    core.pool.do(pool, ins)
            ins.then_inc(copied.sem, 1)

        @block.tensor
        def _(pe):
            for i, (q0, nq, _) in enumerate(tiles):
                last = pe.transpose(core.ps[0:nq, 4, 8 * i:8 * i + 8], P1[32:40, IX_K, q0:q0 + nq],
                                    core.c("ident")[32:40, 32:40])
            last.then_inc(turned.sem, 1)
            pe.wait_ge(copied.sem, copied.at(1))
            for n, (i, j) in enumerate(steps):
                q0, nq, nk = tiles[i]
                g = 32 * (j % 4)
                if n >= 2:
                    pe.wait_ge(dots_used.sem, dots_used.at(n - 1))
                b = 2 * (n % 2)
                for o in range(0, nk, 512):
                    v = min(512, nk - o)
                    last = pe.matmul(core.flat[0:nq, b * 512 + o:b * 512 + o + v], P1[g:g + 32, IX_Q + j // 4, q0:q0 + nq],
                                     kx[g:g + 32, o:o + v], start=True, stop=True)
                last.then_inc(dots.sem, 1)

        @block.scalar
        def _(act):
            for n, (i, j) in enumerate(steps):
                q0, nq, nk = tiles[i]
                act.wait_ge(dots.sem, dots.at(n + 1))
                if n >= 2:
                    act.wait_ge(relus_used.sem, relus_used.at(n - 1))
                b = 2 * (n % 2)
                act.activation(R[0:nq, n % 2, 0:nk], core.flat[0:nq, b * 512:b * 512 + nk], ACT.Relu).then_inc(dots_used.sem, 1)

        @block.vector
        def _(dve):
            do = lambda ins: core.vec.do(dve, ins)
            dve.wait_ge(turned.sem, turned.at(1))
            do(dve.tensor_copy(w[:, 0:4].rearrange("p a b -> p (a b)"), core.ps[:, 4, 0:32]))
            do(dve.tensor_copy(w[0:16, 4], core.ps[0:16, 4, 32:40]))
            for n, (i, j) in enumerate(steps):
                q0, nq, nk = tiles[i]
                s, wk, c = S[0:nq, 0:nk], W[0:nq, 0:nk], chosen(i)[0:nq, 0:nk]
                dve.wait_ge(dots_used.sem, dots_used.at(n + 1))
                prev = core.c("causal")[0:nq, DIAG - q0:DIAG - q0 + nk] if j == 0 else s
                dve.scalar_tensor_tensor(out=s, in0=R[0:nq, n % 2, 0:nk], scalar=w[0:nq, i, j:j + 1], in1=prev,
                                         op0=ALU.mult, op1=ALU.add).then_inc(relus_used.sem, 1)
                dve.wait_ge(relus_used.sem, relus_used.at(n + 1))
                if j < 7:
                    continue
                m, nd = m8[0:nq, :], need[0:nq, :]
                for k in range(TOPK // 8):
                    src = s if k == 0 else wk
                    do(dve.max(m, src))
                    do(dve.match_replace(wk, m, src, -3e38))
                do(dve.max(m, wk))
                t = m[:, TOPK % 8 - 1:TOPK % 8]
                do(dve.tensor_scalar(c, s, t, None, ALU.is_gt))
                do(dve.tensor_reduce(nd, c, AX, ALU.add))
                do(dve.tensor_scalar(nd, nd, -1.0, float(TOPK), ALU.mult, ALU.add))
                do(dve.tensor_scalar(s, s, t, None, ALU.is_equal))
                do(dve.tensor_tensor_scan(wk, s, s, 0.0, ALU.add, ALU.bypass))
                do(dve.scalar_tensor_tensor(out=s, in0=wk, scalar=nd, in1=s, op0=ALU.is_le, op1=ALU.mult))
                do(dve.tensor_tensor(c, c, s, ALU.add))
                do(dve.tensor_scalar(c, c, -NEG, NEG, ALU.mult, ALU.add))
    assert TOPK % 8
    for x in (copied, turned):
        x.passed(1)
    for x in (dots, dots_used, relus_used):
        x.passed(len(steps))


def difference_weight(core, neg_lam, tmp):
    got, sums, exps, lam, spread = (core.sig(n, u) for n, u in (
        ("lam_loaded", 16), ("lam_sums", 1), ("lam_exps", 1), ("lam_ready", 1), ("lam_spread", 1)))
    v, pr, s = core.area(tmp, 256), core.area(tmp + 256, 2, 64), core.area(tmp + 384, 8)
    init = 0.8 - 0.6 * math.exp(-0.3 * 0)
    with core.nc.Block() as block:
        @block.sync
        def _(sp):
            sp.dma_start(v[0:1, :], core.dram["lam"]).then_inc(got.sem, 16)

        @block.vector
        def _(dve):
            do = lambda ins: core.vec.do(dve, ins)
            dve.wait_ge(got.sem, got.at(1))
            do(dve.tensor_tensor(pr[0:1].rearrange("p a b -> p (a b)"), v[0:1, 0:128], v[0:1, 128:256], ALU.mult))
            dve.tensor_reduce(s[0:1, 0:2], pr[0:1], AX, ALU.add).then_inc(sums.sem, 1)
            dve.wait_ge(exps.sem, exps.at(1))
            do(dve.tensor_tensor(s[0:1, 4:5], s[0:1, 3:4], s[0:1, 2:3], ALU.subtract))
            dve.tensor_scalar(s[0:1, 5:6], s[0:1, 4:5], -init, None, ALU.add).then_inc(lam.sem, 1)
            dve.wait_ge(spread.sem, spread.at(1))
            do(dve.tensor_copy(neg_lam, core.ps[:, 0, 0:1]))
            do(dve.tensor_scalar(core.p("subln_df"), core.p("subln_df"), 1.0 - init, None, ALU.mult))
            do(dve.tensor_scalar(core.p("q_norm_sp"), core.p("q_norm_sp"), 0.125, None, ALU.mult))
            do(dve.tensor_scalar(core.p("q_norm_df"), core.p("q_norm_df"), 0.125, None, ALU.mult))

        @block.scalar
        def _(act):
            act.wait_ge(sums.sem, sums.at(1))
            act.activation(s[0:1, 2:4], s[0:1, 0:2], ACT.Exp).then_inc(exps.sem, 1)

        @block.tensor
        def _(pe):
            pe.wait_ge(lam.sem, lam.at(1))
            pe.matmul(core.ps[:, 0, 0:1], core.c("ones")[0:1, :], s[0:1, 5:6], start=True, stop=True).then_inc(spread.sem, 1)
    for x in (got, sums, exps, lam, spread):
        x.passed(1)


def scale_tiles(core, tiles, factor):
    with core.nc.Block() as block:
        @block.vector
        def _(dve):
            for a in tiles:
                dve.tensor_scalar(a, a, factor, None, ALU.mult)



def merge_branches(core, G, merged, T, tmp):
    branch, branch_used, merge = (core.sig(n) for n in ("branch", "branch_used", "merge_step"))
    m = core.area(tmp, 2, T)
    cuts = [(0, 2), (2, 4), (4, 8)]
    parts = lambda a: a.rearrange("p (s n) -> p s n", s=2)

    with core.nc.Block() as block:
        @block.sync
        def _(sp):
            core.load_units(sp, NC)

        @block.tensor
        def _(pe):
            def body(i, j):
                t = 4 * i + j
                s = core.taken + j
                pe.wait_ge(core.split_done, s + 1 + i * 4)
                wh, wl = core.wh[:, s % 2], core.wl[:, s % 2]
                for b, (lo, hi) in enumerate(cuts):
                    if not isinstance(t, int) or 3 * t + b >= 2:
                        pe.wait_ge(branch_used.sem, branch_used.at(3 * t + b - 1))
                    for k in range(lo, hi):
                        for n, (w, x) in enumerate(((wh, core.xh), (wh, core.xl), (wl, core.xh))):
                            for e, (o, c) in enumerate(halves(T)):
                                last = pe.matmul(core.ps[:, out_slot(3 * j + b) + e, 0:c], w[:, k, :], x[:, k, o:o + c],
                                                 start=(k == lo and n == 0), stop=(k == hi - 1 and n == 2))
                    if b < 2:
                        last.then_inc(branch.sem, 1)
                last.then_inc(core.used, 1)
            tile_loop(pe, NC, 4, body)

        @block.scalar
        def _(act):
            core.split_first(act, core.split_hi)
            tile_loop(act, NC, 4, lambda i, j: core.split_hi(act, j, i, 4))

        @block.vector
        def _(dve):
            core.split_first(dve, core.split_lo)

            def gate(b, t):
                return tile_of(G, b * NC + t, T)

            def body(i, j):
                t = 4 * i + j
                out = tile_of(merged, t, T)
                for b in range(3):
                    if b < 2:
                        dve.wait_ge(branch.sem, branch.at(2 * t + b + 1))
                    else:
                        dve.wait_ge(core.used, core.taken + j + 1 + i * 4)
                    to = out if b == 0 else parts(m[:, b - 1])
                    dve.tensor_tensor(to, banks(core, out_slot(3 * j + b), T), gate(b, t),
                                      ALU.mult).then_inc(branch_used.sem, 1)
                    dve.wait_ge(branch_used.sem, branch_used.at(3 * t + b + 1))
                    if b:
                        dve.tensor_tensor(out, out, to, ALU.add).then_inc(merge.sem, 1)
                        dve.wait_ge(merge.sem, merge.at(2 * t + b))
                core.split_lo(dve, j, i, 4)
            tile_loop(dve, NC, 4, body)
    branch.passed(2 * NC), branch_used.passed(3 * NC), merge.passed(2 * NC)
    core.finished(NC)


def first_block(core, stop=None):
    T = T1
    P1 = core.area(0, N1, T)
    at = N1 * T
    strips = core.area(at, 8, STRIP)
    at += 8 * STRIP
    VT = core.area(at, 5, 8, P)
    at += 40 * P
    Y = core.area(at, NC, T)
    at += NC * T
    neg_lam = core.area(at, 1)
    tmp = TAIL
    after = N1 * T + 8 * STRIP
    core.open_inputs()
    difference_weight(core, neg_lam, after)
    bias_strips(core, strips, after)
    core.open_weights(N1)
    layer_norm_input(core, "attn_norm", T, after)
    project(core, N1, P1, T)
    core.close()
    core.open_tail(SMALL_TAIL)

    to_tokens(core, [([P1[:, SB_V, :], P1[:, SB_V + 1, :], P1[:, SP_V, :], P1[:, SP_V + 1, :]],
                      lambda j: VT[:, j, 0:4].rearrange("p a b -> p (a b)")),
                     ([P1[:, DF_V + t, :] for t in range(4)],
                      lambda j: VT[:, j, 4:8].rearrange("p a b -> p (a b)"))], T)
    normed = [(SP_Q, 2, "q_norm_sp"), (SP_K, 2, "k_norm_sp"), (DF_Q, 4, "q_norm_df"), (DF_K, 4, "k_norm_df")]
    norm(core, [([P1[:, a + t, :]], [P1[:, a + t, :]], [core.p(g)], None) for a, n, g in normed for t in range(n)],
         T, 1.0 / 64, tmp, ones="pair64")
    scale_tiles(core, [P1[:, SB_Q + t, :] for t in range(2)], 0.125)

    kx = P1[:, SB_V, :]
    spots = {i: P1[:, DF_V + i - 1, :] for i in range(1, 5)}
    choose_keys(core, P1, kx, lambda i: spots[i], tmp)

    def half(t, h):
        lo = 64 * (h % 2)
        return lambda base: P1[lo:lo + 64, base + h // 2, :]

    def values(v, lo, n):
        return lambda j, w: VT[0:w, j, v, lo:lo + n]

    sb = [Head([(half(0, h)(SB_Q), half(0, h)(SB_K))], values(h // 2, 64 * (h % 2), 64), (64 * (h % 2), 64, Y[:, h // 2, :]))
          for h in range(4)]
    attention(core, "stick", sb, T, tmp)
    sp_ = [Head([(half(0, h)(SP_Q), half(0, h)(SP_K))], values(2 + h // 2, 64 * (h % 2), 64),
                (64 * (h % 2), 64, Y[:, 2 + h // 2, :]), strips[:, h, :], lambda i: spots[i]) for h in range(4)]
    attention(core, "soft", sp_, T, tmp)
    df = [Head([(P1[lo:lo + 64, DF_Q + h, :], P1[lo:lo + 64, DF_K + h, :]) for lo in (0, 64)], values(4 + h, 0, P),
               (0, P, Y[:, 4 + h, :]), strips[:, 4 + h, :]) for h in range(4)]
    attention(core, "diff", df, T, tmp, neg_lam)
    norm(core, [([Y[:, 4 + h, :]], [Y[:, 4 + h, :]], [core.p("subln_df")], None) for h in range(4)], T, 1.0 / P, tmp)
    if stop == "Y":
        return Y, P1, spots

    core.inner.close()
    core.open_weights(RAW0 - N1)
    G, merged = core.area(0, 3 * NC, T), core.area(3 * NC * T, NC, T)
    project(core, 3 * NC, G, T, ACT.Sigmoid, "b_gate")
    split_input(core, [Y[:, k] for k in range(NC)], T)
    merge_branches(core, G, merged, T, 4 * NC * T)
    add_product(core, NC, merged, T)
    feed_forward(core, T, "ffn_norm", "conv_w", "conv_b")


def feed_forward(core, T, gain, conv_w, conv_b):
    hidden = core.area(0, FT, T)
    tmp = FT * T
    layer_norm_input(core, gain, T, tmp)
    conv_glu_up(core, hidden, tmp, T, conv_w, conv_b)
    add_product(core, FT, hidden, T)


def load_constants(core, names, dram, area):
    got = core.sig("constants", 16)
    with core.nc.Block() as block:
        @block.sync
        def _(sp):
            sp.dma_start(area, core.dram[dram]).then_inc(got.sem, 16)
            sp.wait_ge(got.sem, got.at(1))
    got.passed(1)
    core.place(names, area)


def compress(core, P2, KC, VC, tmp):
    got, blocks, hidden, act_out, out, kept = (core.sig(n, u) for n, u in (
        ("cmp_loaded", 16), ("cmp_blocks", 1), ("cmp_hidden", 1), ("cmp_gelu", 1), ("cmp_out", 1), ("cmp_kept", 1)))
    w1 = core.area(tmp, 2, 16, 256)
    w2 = core.area(tmp + 8192, 2, 2, 64)
    pos = core.area(tmp + 8448, 2, 16)
    X = core.area(tmp + 8480, 2, 16, 2 * NCMP)
    H = core.area(tmp + 8480 + 64 * NCMP, 2, 2, 2 * NCMP)
    with core.nc.Block() as block:
        @block.sync
        def _(sp):
            for e in range(2):
                sp.dma_start(w1[:, e].rearrange("p a b -> p (a b)"), core.dram["cmp_w1"][e]).then_inc(got.sem, 16)
            sp.dma_start(w2.rearrange("p a b c -> p (a b c)"), core.dram["cmp_w2"]).then_inc(got.sem, 16)
            sp.dma_start(pos.rearrange("p a b -> p (a b)"), core.dram["cmp_pos"]).then_inc(got.sem, 16)

        @block.vector
        def _(dve):
            for e in range(2):
                for g in range(2):
                    v = P2[64 * g:64 * g + 64, NKC + e, :].rearrange("p (n l two) -> p two l n", l=8, two=2)
                    for half in range(2):
                        for late in range(2):
                            ins = dve.tensor_copy(
                                X[64 * half:64 * half + 64, e, 8 * late:8 * late + 8, g * NCMP:(g + 1) * NCMP],
                                v[:, half, :, late:late + NCMP])
                core.vec.do(dve, ins)
            dve.wait_ge(got.sem, got.at(4))
            for e in range(2):
                dve.tensor_tensor(X[:, e], X[:, e], pos[:, e].unsqueeze(2).broadcast_to([P, 16, 2 * NCMP]),
                                  ALU.add).then_inc(blocks.sem, 1)
            dve.wait_ge(out.sem, out.at(1))
            dve.tensor_copy(KC, core.ps[:, 4, 0:2 * NCMP]).then_inc(kept.sem, 1)
            dve.tensor_copy(VC[0:NCMP], core.ps[0:NCMP, 5, 0:P].rearrange("p (a b) -> p a b", a=2)).then_inc(kept.sem, 1)

        @block.tensor
        def _(pe):
            pe.wait_ge(got.sem, got.at(4))
            for e in range(2):
                pe.wait_ge(blocks.sem, blocks.at(e + 1))
                for c in range(2):
                    for l in range(16):
                        last = pe.matmul(core.ps[:, 2 * e + c, 0:2 * NCMP], w1[:, e, l, c * P:(c + 1) * P], X[:, e, l],
                                         start=(l == 0), stop=(l == 15))
                    last.then_inc(hidden.sem, 1)
            pe.wait_ge(act_out.sem, act_out.at(4))
            for lo in (0, 64):
                for c in range(2):
                    pe.matmul(core.ps[lo:lo + 64, 4, 0:2 * NCMP], w2[:, 0, c], H[:, 0, c], start=(c == 0), stop=(c == 1))
            for g in range(2):
                for c in range(2):
                    last = pe.matmul(core.ps[0:NCMP, 5, 64 * g:64 * g + 64], H[:, 1, c, g * NCMP:(g + 1) * NCMP], w2[:, 1, c],
                                     start=(c == 0), stop=(c == 1))
            last.then_inc(out.sem, 1)

        @block.scalar
        def _(act):
            for n in range(4):
                act.wait_ge(hidden.sem, hidden.at(n + 1))
                act.activation(H[:, n // 2, n % 2], core.ps[:, n, 0:2 * NCMP], ACT.Gelu_apprx_tanh).then_inc(act_out.sem, 1)
    got.passed(4), blocks.passed(2), hidden.passed(4), act_out.passed(4), out.passed(1), kept.passed(2)


def compressed_attention(core, P2, KC, VC, OC, tmp):
    scores, shifted, exps, probs, turned, pt, out, kept = (core.sig(n) for n in (
        "cmp_scores", "cmp_shifted", "cmp_exps", "cmp_probs", "cmp_turned", "cmp_pt", "cmp_weighed", "cmp_copied"))
    X = core.area(tmp, 24, NCMP)
    st = core.area(tmp + 24 * NCMP, 2, 24)
    PT = core.area(tmp + 24 * NCMP + 48, 2, 6 * P)
    wide = [P, 24, NCMP]
    with core.nc.Block() as block:
        @block.tensor
        def _(pe):
            for i in range(4):
                for h in range(6):
                    lo, g = 64 * (h % 2), h // 3
                    o = h // 2 * NCMP
                    last = pe.matmul(core.ps[:, 4 * (h % 2) + i, o:o + NCMP], P2[lo:lo + 64, NQ + h // 2, i * P:(i + 1) * P],
                                     KC[lo:lo + 64, g * NCMP:(g + 1) * NCMP], start=True, stop=True)
            last.then_inc(scores.sem, 1)
            pe.wait_ge(probs.sem, probs.at(1))
            for i in range(4):
                if i >= 1:
                    pe.wait_ge(pt.sem, pt.at(i))
                for h in range(6):
                    last = pe.transpose(core.flat[0:NCMP, 2048 + h * P:2048 + (h + 1) * P], X[:, i * 6 + h % 2 * 3 + h // 2], core.c("ident"))
                last.then_inc(turned.sem, 1)
                pe.wait_ge(pt.sem, pt.at(i + 1))
                if i >= 2:
                    pe.wait_ge(kept.sem, kept.at(i - 1))
                for h in range(6):
                    lo, g = 64 * (h % 2), h // 3
                    last = pe.matmul(core.ps[lo:lo + 64, 6 + i % 2, h // 2 * P:(h // 2 + 1) * P], VC[0:NCMP, g],
                                     PT[0:NCMP, i % 2, h * P:(h + 1) * P], start=True, stop=True)
                last.then_inc(out.sem, 1)

        @block.vector
        def _(dve):
            do = lambda ins: core.vec.do(dve, ins)
            dve.wait_ge(scores.sem, scores.at(1))
            for odd in range(2):
                ins = dve.tensor_tensor(X.rearrange("p (a o b) c -> p a o (b c)", a=4, o=2)[:, :, odd],
                                        core.ps[:, 4 * odd:4 * odd + 4, 0:3 * NCMP],
                                        core.c("cmp_bias").rearrange("p (a o b) -> p a o b", a=4, o=2)[:, :, odd], ALU.add)
            do(ins)
            do(dve.tensor_reduce(st[:, 0], X, AX, ALU.max))
            dve.tensor_tensor(X, X, st[:, 0].unsqueeze(2).broadcast_to(wide), ALU.subtract).then_inc(shifted.sem, 1)
            dve.wait_ge(exps.sem, exps.at(1))
            do(dve.tensor_tensor(X, X, core.c("cmp_keep").rearrange("p (a b) -> p a b", a=24), ALU.mult))
            do(dve.tensor_reduce(st[:, 1], X, AX, ALU.add))
            do(dve.tensor_scalar(st[:, 1], st[:, 1], 1e-30, None, ALU.max))
            do(dve.reciprocal(st[:, 1], st[:, 1]))
            dve.tensor_tensor(X, X, st[:, 1].unsqueeze(2).broadcast_to(wide), ALU.mult).then_inc(probs.sem, 1)
            for i in range(4):
                dve.wait_ge(out.sem, out.at(i + 1))
                dve.tensor_copy(OC[:, :, i * P:(i + 1) * P],
                                core.ps[:, 6 + i % 2, 0:3 * P].rearrange("p (a b) -> p a b", a=3)).then_inc(kept.sem, 1)

        @block.scalar
        def _(act):
            act.wait_ge(shifted.sem, shifted.at(1))
            act.activation(X, X, ACT.Exp).then_inc(exps.sem, 1)
            for i in range(4):
                act.wait_ge(turned.sem, turned.at(i + 1))
                if i >= 2:
                    act.wait_ge(out.sem, out.at(i - 1))
                act.activation(PT[0:NCMP, i % 2], core.flat[0:NCMP, 2048:2048 + 6 * P], ACT.Copy).then_inc(pt.sem, 1)
    for x in (scores, shifted, exps, probs):
        x.passed(1)
    for x in (turned, pt, out, kept):
        x.passed(4)


def cross_keys(core, P2, KX):
    with core.nc.Block() as block:
        @block.gpsimd
        def _(pool):
            for e, t in enumerate((NKS, NKW)):
                for g in range(2):
                    core.pool.do(pool, pool.tensor_copy(KX[64 - 64 * g:128 - 64 * g, e], P2[64 * g:64 * g + 64, t, :]))


def gate_branches(core, P2, branches, tmp):
    sig, spread, used = core.sig("nsa_gates"), core.sig("nsa_spread"), core.sig("nsa_spread_used")
    g = core.area(tmp, SEQ)
    with core.nc.Block() as block:
        @block.scalar
        def _(act):
            act.activation(g[0:18], P2[0:18, NG, :], ACT.Sigmoid).then_inc(sig.sem, 1)

        @block.tensor
        def _(pe):
            pe.wait_ge(sig.sem, sig.at(1))
            for n in range(9):
                if n >= 4:
                    pe.wait_ge(used.sem, used.at(n - 3))
                pe.matmul(core.ps[:, n % 4, :], core.c("gates")[0:18, n * P:(n + 1) * P], g[0:18], start=True,
                          stop=True).then_inc(spread.sem, 1)

        @block.vector
        def _(dve):
            for n in range(9):
                b, t = n // 3, n % 3
                dve.wait_ge(spread.sem, spread.at(n + 1))
                a = branches[b][:, t]
                dve.tensor_tensor(a, core.ps[:, n % 4, :], a, ALU.mult).then_inc(used.sem, 1)
                if b:
                    dve.wait_ge(used.sem, used.at(n + 1))
                    o = branches[0][:, t]
                    core.vec.do(dve, dve.tensor_tensor(o, o, a, ALU.add))
    sig.passed(1), spread.passed(9), used.passed(9)


def center(core, items, T, inv_n, ones):
    total, gone = core.sig("mean_ready"), core.sig("mean_used")
    with core.nc.Block() as block:
        @block.tensor
        def _(pe):
            for n, x in enumerate(items):
                if n >= 2:
                    pe.wait_ge(gone.sem, gone.at(n - 1))
                for k, a in enumerate(x):
                    last = pe.matmul(core.ps[:, n % 2, 0:T], core.c(ones), a, start=(k == 0), stop=(k == len(x) - 1))
                last.then_inc(total.sem, 1)

        @block.vector
        def _(dve):
            for n, x in enumerate(items):
                dve.wait_ge(total.sem, total.at(n + 1))
                for k, a in enumerate(x):
                    ins = dve.scalar_tensor_tensor(out=a, in0=core.ps[:, n % 2, 0:T], scalar=-inv_n, in1=a, op0=ALU.mult,
                                                   op1=ALU.add)
                ins.then_inc(gone.sem, 1)
    total.passed(len(items)), gone.passed(len(items))


def rwkv_prepare(core, R, K, V, L, A, G, KK, AR, B, KP, CE, bonus, tmp):
    got, up, lora, lora_used, decays, exps, sums, done = (core.sig(n, u) for n, u in (
        ("lora_loaded", 16), ("lora_in", 1), ("lora_out", 1), ("lora_used", 1), ("decay_sums", 1), ("decay_exps", 1),
        ("bonus_sum", 1), ("rwkv_ready", 1)))
    w = core.area(tmp, 256)
    LW = core.area(tmp + 256, 2, SEQ)
    CL = core.area(tmp + 256 + 1024, 2, SEQ)
    E = core.area(tmp + 256 + 2048, 3, 2, SEQ)
    D_ = core.area(tmp + 256 + 2048 + 3072, SEQ)
    tiles = [(R, 0), (R, 1), (K, 0), (K, 1), (V, 0), (V, 1), (L, 0)]
    with core.nc.Block() as block:
        @block.sync
        def _(sp):
            sp.dma_start(w, core.dram["lora"]).then_inc(got.sem, 16)

        @block.vector
        def _(dve):
            do = lambda ins: core.vec.do(dve, ins)
            for n in [6, 0, 1, 2, 3, 4, 5]:
                a, t = tiles[n]
                x = a[:, t]
                do(dve.tensor_scalar(D_[:, 0:1], x[:, 0:1], -1.0, None, ALU.mult))
                do(dve.tensor_tensor(D_[:, 1:], x[:, :-1], x[:, 1:], ALU.subtract))
                ins = dve.scalar_tensor_tensor(out=x, in0=D_, scalar=core.p("rw_mu_2", n), in1=x, op0=ALU.mult, op1=ALU.add)
                if n == 6:
                    ins.then_inc(up.sem, 1)
                    dve.wait_ge(up.sem, up.at(1))
                else:
                    do(ins)
            for t in range(2):
                dve.wait_ge(lora_used.sem, lora_used.at(t + 1))
                do(dve.tensor_scalar(LW[:, t], LW[:, t], -0.606531, None, ALU.mult))
                do(dve.tensor_tensor_scan(CL[:, t], core.c("restart"), LW[:, t], 0.0, ALU.mult, ALU.add))
                dve.tensor_tensor(LW[:, t], CL[:, t], LW[:, t], ALU.subtract).then_inc(decays.sem, 1)
            dve.wait_ge(lora_used.sem, lora_used.at(4))
            for t in range(2):
                do(dve.tensor_scalar(KK[:, t], K[:, t], core.p("rw_k_k_2", t), None, ALU.mult))
                do(dve.tensor_scalar(D_, A[:, t], 1.0, core.p("rw_k_a_2", t), ALU.subtract, ALU.mult))
                do(dve.scalar_tensor_tensor(out=K[:, t], in0=D_, scalar=1.0, in1=K[:, t], op0=ALU.add, op1=ALU.mult))
                do(dve.scalar_tensor_tensor(out=D_, in0=R[:, t], scalar=core.p("rw_r_k_2", t), in1=K[:, t],
                                            op0=ALU.mult, op1=ALU.mult))
                dve.tensor_copy(bonus[:, t], D_).then_inc(done.sem, 1)
                dve.wait_ge(done.sem, done.at(t + 1))
            for t in range(2):
                dve.wait_ge(sums.sem, sums.at(t + 1))
                do(dve.tensor_tensor(bonus[:, t], core.ps[:, 6 + t, :], V[:, t], ALU.mult))
            dve.wait_ge(exps.sem, exps.at(6))
            for t in range(2):
                c, c0, ic = E[:, 0, t], E[:, 1, t], E[:, 2, t]
                by = lambda a: a.rearrange("p (c t) -> p c t", t=CH)
                do(dve.tensor_tensor(AR[:, t, :, 1], by(c), by(R[:, t]), ALU.mult))
                do(dve.tensor_copy(AR[:, t, :, 0], by(c0)))
                do(dve.tensor_tensor(KP[:, t], ic, K[:, t], ALU.mult))
                do(dve.tensor_tensor(B[:, t], ic, A[:, t], ALU.mult))
                do(dve.tensor_copy(CE[:, t], by(c)[:, :, CH - 1]))

        @block.scalar
        def _(act):
            act.wait_ge(up.sem, up.at(1))
            x = L[:, 0]
            act.activation(x[0:32], x[0:32], ACT.Tanh)
            act.activation(x[64:128], x[64:128], ACT.Sigmoid).then_inc(up.sem, 1)
            for n, (dst, bias) in enumerate([(LW, "rw_w0_2"), (A, "rw_a0_2"), (G, None)]):
                for t in range(2):
                    act.wait_ge(lora.sem, lora.at(2 * n + t + 1))
                    got_ = core.ps[:, 2 * n + t, :]
                    if bias:
                        ins = act.activation(dst[:, t], got_, ACT.Sigmoid, bias=core.p(bias, t))
                    else:
                        ins = act.activation(dst[:, t], got_, ACT.Copy)
                    ins.then_inc(lora_used.sem, 1)
            for t in range(2):
                act.wait_ge(decays.sem, decays.at(t + 1))
                act.activation(E[:, 0, t], CL[:, t], ACT.Exp).then_inc(exps.sem, 1)
                act.activation(E[:, 1, t], LW[:, t], ACT.Exp).then_inc(exps.sem, 1)
                act.activation(E[:, 2, t], CL[:, t], ACT.Exp, scale=-1.0).then_inc(exps.sem, 1)

        @block.tensor
        def _(pe):
            pe.wait_ge(got.sem, got.at(1))
            pe.wait_ge(up.sem, up.at(2))
            for n, (lo, hi) in enumerate([(0, 32), (32, 64), (64, 128)]):
                for t in range(2):
                    pe.matmul(core.ps[:, 2 * n + t, :], w[lo:hi, t * P:(t + 1) * P], L[lo:hi, 0], start=True,
                              stop=True).then_inc(lora.sem, 1)
            for t in range(2):
                pe.wait_ge(done.sem, done.at(t + 1))
                pe.matmul(core.ps[:, 6 + t, :], core.c("pair64"), bonus[:, t], start=True, stop=True).then_inc(sums.sem, 1)
    got.passed(1), up.passed(2), lora.passed(6), lora_used.passed(6), decays.passed(2), exps.passed(6), sums.passed(2)
    done.passed(2)


def rwkv_factors(core, KK, AR, B):
    with core.nc.Block() as block:
        @block.vector
        def _(dve):
            for t in range(2):
                by = KK[:, t].rearrange("p (c t) -> p c t", t=CH)
                core.vec.do(dve, dve.tensor_tensor(AR[:, t, :, 0], AR[:, t, :, 0], by, ALU.mult))
                core.vec.do(dve, dve.tensor_tensor(B[:, t], B[:, t], KK[:, t], ALU.mult))


def rwkv_matrices(core, V, AR, B, KP, MM, TOK):
    made, used, turned, kept = (core.sig(n) for n in ("chunk_products", "chunk_masked", "chunk_turned", "chunk_kept"))
    NCH = SEQ // CH
    with core.nc.Block() as block:
        @block.tensor
        def _(pe):
            for c in range(NCH):
                if c >= 2:
                    pe.wait_ge(used.sem, used.at(c - 1))
                t0 = c * CH
                for h in range(4):
                    lo, t = 64 * (h % 2), h // 2
                    for e, F in enumerate((B, KP)):
                        o = (t * 2 + e) * 64
                        last = pe.matmul(core.ps[0:CH, 2 * (c % 2) + h % 2, o:o + 64], F[lo:lo + 64, t, t0:t0 + CH],
                                         AR[lo:lo + 64, t, c].rearrange("p a b -> p (a b)"), start=True, stop=True)
                last.then_inc(made.sem, 1)
                if c >= 2:
                    pe.wait_ge(kept.sem, kept.at(c - 1))
                for e, F in enumerate((B, KP, V)):
                    for t in range(2):
                        o = (4 + 2 * (c % 2)) * 512 + e * 256 + t * P
                        last = pe.transpose(core.flat[0:CH, o:o + P], F[:, t, t0:t0 + CH], core.c("ident"))
                last.then_inc(turned.sem, 1)

        @block.vector
        def _(dve):
            for c in range(NCH):
                dve.wait_ge(made.sem, made.at(c + 1))
                two = lambda a: a.rearrange("p (o n) -> p o n", o=2)
                dve.tensor_tensor(two(MM[0:CH, c]), core.ps[0:CH, 2 * (c % 2):2 * (c % 2) + 2, 0:256],
                                  two(core.c("mask32")[0:CH]), ALU.mult).then_inc(used.sem, 1)

        @block.scalar
        def _(act):
            for c in range(NCH):
                act.wait_ge(turned.sem, turned.at(c + 1))
                o = (4 + 2 * (c % 2)) * 512
                for e in range(3):
                    ins = act.activation(TOK[e][0:CH, c], core.flat[0:CH, o + 256 * e:o + 256 * e + 256], ACT.Copy)
                ins.then_inc(kept.sem, 1)
    for x in (made, used, turned, kept):
        x.passed(NCH)


def rwkv_inverse(core, MM, TT, tmp, rd):
    out, back, solved, out2, back2 = (core.sig(n, u) for n, u in (
        ("chunks_stored", 16), ("chunks_back", 16), ("chunks_solved", 1), ("inverse_stored", 16), ("inverse_back", 16)))
    NP = SEQ // CH * 4
    AT = core.area(tmp, CH, CH)
    Yv = core.area(tmp + CH * CH, CH, 16)
    pr = core.area(tmp + CH * CH + CH * 16, 16 * CH)
    a_dram, y_dram = core.dram["chunk_scratch"], core.dram["inverse_scratch"]
    with core.nc.Block() as block:
        @block.sync
        def _(sp):
            m = MM.rearrange("p c (h e f t) -> p c h e f t", h=4, e=2, f=2)
            for c in range(SEQ // CH):
                sp.dma_start(a_dram[4 * c:4 * c + 4].rearrange("n s t -> s n t"), m[0:CH, c, :, 0, 0, :]).then_inc(out.sem, 16)
            sp.wait_ge(out.sem, out.at(SEQ // CH))
            for half in range(2):
                sp.dma_start(AT[64 * half:64 * half + 64].rearrange("p s t -> p (s t)"),
                             a_dram.rearrange("n s t -> n (s t)")).then_inc(back.sem, 16)
            sp.wait_ge(solved.sem, solved.at(1))
            for half in range(2):
                sp.dma_start(y_dram[:, :, 16 * half:16 * half + 16], Yv[64 * half:64 * half + 64]).then_inc(out2.sem, 16)
            sp.wait_ge(out2.sem, out2.at(2))
            sp.dma_start(TT[0:CH], y_dram.rearrange("n s i -> s n i")).then_inc(back2.sem, 16)
            sp.wait_ge(back2.sem, back2.at(1))

        @block.vector
        def _(dve):
            do = lambda ins: core.vec.do(dve, ins)
            do(dve.tensor_copy(Yv.rearrange("p s i -> p (s i)"), core.c("eye16")))
            dve.wait_ge(back.sem, back.at(2))
            for s in range(CH - 2, -1, -1):
                n = CH - 1 - s
                p3 = pr[:, 0:16 * n].rearrange("p (i t) -> p i t", i=16)
                do(dve.tensor_tensor(p3, Yv[:, s + 1:, :].rearrange("p t i -> p i t"),
                                     AT[:, s, s + 1:].unsqueeze(1).broadcast_to([P, 16, n]), ALU.mult))
                do(dve.tensor_reduce(rd, p3, AX, ALU.add))
                ins = dve.tensor_tensor(Yv[:, s, :], Yv[:, s, :], rd, ALU.subtract)
                if s:
                    do(ins)
                else:
                    ins.then_inc(solved.sem, 1)
    out.passed(SEQ // CH), back.passed(2), solved.passed(1), out2.passed(2), back2.passed(1)
    assert NP == 64


def rwkv_chunks(core, AR, MM, TOK, TT, CE, RO, tmp):
    init, x_ready, x_kept, u_ready, u_kept, o_ready, o_kept, s_ready, s_kept = (core.sig(n) for n in (
        "state_zero", "x_ready", "x_kept", "u_ready", "u_kept", "o_ready", "o_kept", "s_ready", "s_kept"))
    NCH = SEQ // CH
    ST = core.area(tmp, 2, 64)
    SC = core.area(tmp + 128, 2, 64)
    X = core.area(tmp + 256, 256)
    U = core.area(tmp + 512, 256)
    order = lambda h: h % 2 * 2 + h // 2
    with core.nc.Block() as block:
        @block.tensor
        def _(pe):
            pe.wait_ge(s_kept.sem, s_kept.at(1))
            for c in range(NCH):
                m = MM[0:CH, c].rearrange("p (h e f t) -> p h e f t", h=4, e=2, f=2)
                tok = [a[0:CH, c] for a in TOK]
                if c:
                    pe.wait_ge(s_kept.sem, s_kept.at(c + 1))
                    pe.wait_ge(x_kept.sem, x_kept.at(c))
                for h in range(4):
                    lo, t, o = 64 * (h % 2), h // 2, 64 * h
                    dst = core.ps[0:CH, h % 2, t * 64:t * 64 + 64]
                    pe.matmul(dst, m[:, order(h), 1, 0], tok[2][:, o:o + 64], start=True, stop=False)
                    last = pe.matmul(dst, AR[lo:lo + 64, t, c, 0], ST[lo:lo + 64, t], start=False,
                                     stop=True)
                last.then_inc(x_ready.sem, 1)
                pe.wait_ge(x_kept.sem, x_kept.at(c + 1))
                for h in range(4):
                    o = 64 * order(h)
                    last = pe.matmul(core.ps[0:CH, 3, o:o + 64], TT[0:CH, 4 * c + order(h)], X[0:CH, o:o + 64], start=True,
                                     stop=True)
                last.then_inc(u_ready.sem, 1)
                pe.wait_ge(u_kept.sem, u_kept.at(c + 1))
                for h in range(4):
                    lo, t, o = 64 * (h % 2), h // 2, 64 * h
                    dst = core.ps[lo:lo + 64, 2, t * 64:t * 64 + 64]
                    pe.matmul(dst, tok[1][:, o:o + 64], tok[2][:, o:o + 64], start=True, stop=False)
                    last = pe.matmul(dst, tok[0][:, o:o + 64], U[0:CH, 64 * order(h):64 * order(h) + 64], start=False, stop=True)
                if c >= 2:
                    pe.wait_ge(o_kept.sem, o_kept.at(c - 1))
                for h in range(4):
                    lo, t, o = 64 * (h % 2), h // 2, 64 * h
                    dst = core.ps[lo:lo + 64, 4 + c % 2, t * CH:(t + 1) * CH]
                    pe.matmul(dst, ST[lo:lo + 64, t], AR[lo:lo + 64, t, c, 1], start=True, stop=False)
                    pe.matmul(dst, tok[2][:, o:o + 64], m[:, order(h), 1, 1], start=False, stop=False)
                    last = pe.matmul(dst, U[0:CH, 64 * order(h):64 * order(h) + 64], m[:, order(h), 0, 1], start=False, stop=True)
                last.then_inc(s_ready.sem, 1)

        @block.vector
        def _(dve):
            do = lambda ins: core.vec.do(dve, ins)
            dve.memset(ST, 0.0).then_inc(s_kept.sem, 1)
            dve.wait_ge(s_kept.sem, s_kept.at(1))
            for c in range(NCH):
                for t in range(2):
                    ins = dve.tensor_scalar(SC[:, t], ST[:, t], CE[:, t, c:c + 1], None, ALU.mult)
                do(ins)
                dve.wait_ge(x_ready.sem, x_ready.at(c + 1))
                dve.tensor_scalar(X[0:CH].rearrange("p (o n) -> p o n", o=2), core.ps[0:CH, 0:2, 0:128], -1.0, None, ALU.mult).then_inc(x_kept.sem, 1)
                dve.wait_ge(u_ready.sem, u_ready.at(c + 1))
                dve.tensor_copy(U[0:CH], core.ps[0:CH, 3, 0:256]).then_inc(u_kept.sem, 1)
                dve.wait_ge(s_ready.sem, s_ready.at(c + 1))
                for t in range(2):
                    ins = dve.scalar_tensor_tensor(out=ST[:, t], in0=core.ps[:, 2, t * 64:t * 64 + 64], scalar=CE[:, t, c:c + 1],
                                                   in1=SC[:, t], op0=ALU.mult, op1=ALU.add)
                ins.then_inc(s_kept.sem, 1)
                dve.wait_ge(s_kept.sem, s_kept.at(c + 2))

        @block.scalar
        def _(act):
            for c in range(NCH):
                act.wait_ge(s_ready.sem, s_ready.at(c + 1))
                act.activation(RO[:, :, c * CH:(c + 1) * CH], core.ps[:, 4 + c % 2, 0:2 * CH].rearrange("p (a b) -> p a b", a=2),
                               ACT.Copy).then_inc(o_kept.sem, 1)
    s_kept.passed(NCH + 1)
    for x in (x_ready, x_kept, u_ready, u_kept, o_kept, s_ready):
        x.passed(NCH)


def second_block(core, stop=None):
    T = SEQ
    P2 = core.area(0, N2, T)
    at = N2 * T
    Y = core.area(at, NC, T)
    at += NC * T
    VT = core.area(at, 4, 5, P)
    at += 20 * P
    KX = core.area(at, 2, T)
    OC, OS = core.area(at + 2 * T, 3, T), core.area(at + 5 * T, 3, T)
    KC, VC = core.area(at + 8 * T, 2 * NCMP), core.area(at + 8 * T + 2 * NCMP, 2, 64)
    late = at + 8 * T + 2 * NCMP + P
    nsa = sum(m for _, m in NSA_CONSTS)
    tmp = TAIL
    core.h = core.h_all[:, :, META:META + SEQ]
    layer_norm_input(core, "attn_norm_2", T, late)
    project(core, N2, P2, T)
    core.close(inputs=True)
    core.open_tail(SMALL_TAIL + 2 * NC * T1)
    to_tokens(core, [([P2[:, t, :] for t in (NVS, NVW, MV, MV + 1)], lambda j: VT[:, j, 0:4].rearrange("p a b -> p (a b)")),
                     ([P2[:, MV + 2, :]], lambda j: VT[:, j, 4])], T)
    scale_tiles(core, [P2[:, t, :] for t in (NQ, NQ + 1, NQ + 2, MQ, MQ + 1, MQ + 2)], 0.125)
    compress(core, P2, KC, VC, TAIL)
    load_constants(core, NSA_CONSTS, "nsa_consts", core.area(late, nsa))
    cross_keys(core, P2, KX)
    compressed_attention(core, P2, KC, VC, OC, tmp)
    causal = core.c("causal")
    side = Modulation(core, core.area(TAIL + SMALL_TAIL, D))
    side.load()

    def values(v, lo):
        return lambda j, w: VT[0:w, j, v, lo:lo + 64]

    for e, (kt, out) in enumerate(((NKS, OS), (NKW, Y))):
        heads = []
        for h in range(6):
            lo, g = 64 * (h % 2), h // 3
            k = P2[lo:lo + 64, kt, :] if h % 2 == g else KX[lo:lo + 64, e]
            heads.append(Head([(P2[lo:lo + 64, NQ + h // 2, :], k)], values(e, 64 * g), (lo, 64, out[:, h // 2]), causal))
        attention(core, "soft", heads, T, tmp, beside=side)
    gate_branches(core, P2, [OC, OS, Y], tmp)
    heads = []
    for h in range(6):
        lo = 64 * (h % 2)
        heads.append(Head([(P2[lo:lo + 64, MQ + h // 2, :], P2[lo:lo + 64, MK + h // 2, :])], values(2 + h // 2, lo),
                          (lo, 64, Y[:, 5 + h // 2]), causal))
    attention(core, "soft", heads, T, tmp)
    norm(core, [([OC[:, t]], [Y[:, t]], [core.p("nsa_out_gain_2", t)], None) for t in range(3)]
         + [([Y[:, 5 + t]], [Y[:, 5 + t]], [core.p("moba_out_gain_2", t)], None) for t in range(3)], T, 1.0 / 64, tmp,
         ones="pair64")

    R, K, V, L = (P2[:, a:b, :] for a, b in ((RR, RR + 2), (RK, RK + 2), (RV, RV + 2), (RL, RL + 1)))
    A, KK, G, B, KP = (core.area(i * 2 * T, 2, T) for i in range(5))
    at = (N2 + NC) * T
    bonus = core.area(at, 2, T)
    RO = core.area(at + 2 * T, 2, T)
    AR = core.area(at + 4 * T, 2, SEQ // CH, 2, CH)
    MM = core.area(TAIL, SEQ // CH, 512)
    tmp = at + 8 * T
    late = tmp + 8 * T
    end = late + 3 * 512
    spare = core.area(TAIL + 16 * 512, 4144)
    TOK = [core.area((RL + 1) * T, SEQ // CH, 256), core.area(tmp, SEQ // CH, 256),
           spare[:, 0:16 * 256].rearrange("p (c n) -> p c n", n=256)]
    CE = spare[:, 4096:4096 + 32].rearrange("p (a b) -> p a b", a=2)
    rd = spare[:, 4128:4144]
    TT = core.area(0, SEQ // CH * 4, CH)
    load_constants(core, RWKV_CONSTS, "rwkv_consts", core.area(late, end - late))
    rwkv_prepare(core, R, K, V, L, A, G, KK, AR, B, KP, CE, bonus, TAIL)
    norm(core, [([KK[:, t]], [KK[:, t]], None, None) for t in range(2)], T, 1.0, tmp, eps="zero", ones="pair64", least=1e-12)
    rwkv_factors(core, KK, AR, B)
    rwkv_matrices(core, V, AR, B, KP, MM, TOK)
    rwkv_inverse(core, MM, TT, 6 * T, rd)
    rwkv_chunks(core, AR, MM, TOK, TT, CE, RO, end)
    center(core, [[RO[:, t]] for t in range(2)], T, 1.0 / 64, "pair64")
    norm(core, [([RO[:, t]], [RO[:, t]], [core.p("rw_lnx_w_2", t)], [core.p("rw_lnx_b_2", t)]) for t in range(2)], T, 1.0 / 64,
         tmp, eps="eps_rw", ones="pair64")
    rwkv_output(core, RO, bonus, G, Y[:, 3:5, :])
    if stop == "Y":
        return Y
    core.inner.close()
    core.open_inputs()
    core.open_weights(core.total - RAW - core.taken)
    add_product(core, NC, Y, T)
    feed_forward(core, T, "ffn_norm_2", "ffn_conv_w_2", "ffn_conv_b_2")
    x = [core.h[:, k] for k in range(NC)]
    norm(core, [(x, x, [core.p("final_norm_2", k) for k in range(NC)], None)], T, 1.0 / D, 0)


def rwkv_output(core, RO, bonus, G, Y):
    with core.nc.Block() as block:
        @block.vector
        def _(dve):
            core.vec.do(dve, dve.tensor_tensor(RO, RO, bonus, ALU.add))
            dve.tensor_tensor(Y, RO, G, ALU.mult)


class Modulation:

    def __init__(self, core, spread):
        self.core, self.spread = core, spread
        self.product = core.sig("modulation_product")

    def load(self):
        core, got = self.core, self.core.sig("c_loaded", 16)
        with core.nc.Block() as block:
            @block.sync
            def _(sp):
                sp.dma_start(self.spread, core.dram["c"].broadcast_to([P, D])).then_inc(got.sem, 16)

            @block.scalar
            def _(act):
                act.wait_ge(got.sem, got.at(1))
                act.activation(self.spread, self.spread, ACT.Silu)
        got.passed(1)

    def multiply(self, dve, s):
        core, u = self.core, self.core.stream + s
        w = core.ring[:, u % RING].rearrange("p c n -> p (c n)")
        dve.wait_ge(core.arrived[u % RING], 16 * (u // RING + 1))
        dve.tensor_tensor(w, w, self.spread, ALU.mult).then_inc(self.product.sem, 1)

    def sum(self, act, s):
        core, u = self.core, self.core.stream + s
        w = core.ring[:, u % RING].rearrange("p c n -> p (c n)")
        act.wait_ge(self.product.sem, self.product.at(s + 1))
        act.activation(w, w, ACT.Copy, accum_out=core.mod[:, u - RAW0:u - RAW0 + 1]).then_inc(core.raw_used, 1)

    def passed(self, n):
        self.core.stream += n
        self.product.passed(n)


def scale_columns(core):
    mod = core.mod[:, :]
    with core.nc.Block() as block:
        @block.vector
        def _(dve):
            b = PCOL["b_ada_3"]
            core.vec.do(dve, dve.tensor_tensor(mod, mod, core.par[:, b:b + RAW], ALU.add))
            for at, name in ((NC, "norm1_g_3"), (4 * NC, "norm2_g_3")):
                g = PCOL[name]
                dve.scalar_tensor_tensor(out=mod[:, at:at + NC], in0=mod[:, at:at + NC], scalar=1.0,
                                         in1=core.par[:, g:g + NC], op0=ALU.add, op1=ALU.mult)


def mix_tokens(core, VT, MX, tmp):
    got, ready, mixed, kept = (core.sig(n, u) for n, u in (("ws_loaded", 16), ("ws_masked", 1), ("mixed", 1), ("mixed_kept", 1)))
    WS = core.area(tmp, NC, P)
    BS = core.area(tmp + NC * P, NC, P)
    with core.nc.Block() as block:
        @block.sync
        def _(sp):
            sp.dma_start(WS.rearrange("p a b -> p (a b)"), core.dram["gmlp_ws"]).then_inc(got.sem, 16)
            sp.dma_start(BS[0:1].rearrange("p a b -> p (a b)"), core.dram["gmlp_bs"]).then_inc(got.sem, 16)

        @block.vector
        def _(dve):
            dve.wait_ge(got.sem, got.at(2))
            dve.memset(WS[64:128, :, 0:64], 0.0).then_inc(ready.sem, 1)

        @block.tensor
        def _(pe):
            pe.wait_ge(ready.sem, ready.at(1))
            for g in range(NC):
                if g >= 2:
                    pe.wait_ge(kept.sem, kept.at(g - 1))
                for n in range(4):
                    dst = core.ps[:, g % 2, n * P:(n + 1) * P]
                    pe.matmul(dst, VT[:, n, g], WS[:, g], start=True, stop=False)
                    last = pe.matmul(dst, core.c("ones")[0:1, :], BS[0:1, g], start=False, stop=True)
                last.then_inc(mixed.sem, 1)

        @block.scalar
        def _(act):
            for g in range(NC):
                act.wait_ge(mixed.sem, mixed.at(g + 1))
                act.activation(MX[:, g], core.ps[:, g % 2, :], ACT.Copy).then_inc(kept.sem, 1)
    got.passed(2), ready.passed(1), mixed.passed(NC), kept.passed(NC)


def project_conv(core, n, dst, tmp):
    T = SEQ
    copied, conv, act_out = core.sig("tile_free"), core.sig("conv_out"), core.sig("silu_out")
    pad = core.area(tmp, 2, T + 3)
    mid = core.area(tmp + 2 * (T + 3), 2, 2, T)
    step = core.vec
    with core.nc.Block() as block:
        @block.sync
        def _(sp):
            core.load_units(sp, n)

        @block.tensor
        def _(pe):
            gemm(core, pe, n, 4, T, copied)

        @block.scalar
        def _(act):
            core.split_first(act, core.split_hi)
            core.act.do(act, act.activation(pad[:, :, 0:3], core.c("ones", 6).rearrange("p (b n) -> p b n", b=2),
                                            ACT.Copy, scale=0.0))

            def body(i, j):
                t = i * 4 + j
                tile_done(core, act, i, j, 4)
                core.split_hi(act, j, i, 4)
                if not isinstance(t, int) or t >= 2:
                    act.wait_ge(conv.sem, conv.at(t - 1))
                act.activation(pad[:, j % 2, 3:], core.ps[:, out_slot(j), :], ACT.Copy).then_inc(copied.sem, 1)
                act.wait_ge(conv.sem, conv.at(t + 1))
                out = dst[:, t] if isinstance(t, int) else dst[:, bass.ds(t, 1)].rearrange("p o n -> p (o n)")
                act.activation(out, mid[:, j % 2, 1], ACT.Silu).then_inc(act_out.sem, 1)
            tile_loop(act, n, 4, body)

        @block.vector
        def _(dve):
            base = step.value
            core.split_first(dve, core.split_lo)

            def body(i, j):
                t = i * 4 + j
                core.split_lo(dve, j, i, 4)
                x, y, z = pad[:, j % 2], mid[:, j % 2, 0], mid[:, j % 2, 1]

                def ordered(k, ins):
                    ins.then_inc(step.sem, 1)
                    dve.wait_ge(step.sem, base + 3 * t + k)
                dve.wait_ge(copied.sem, copied.at(t + 1))
                ordered(1, dve.tensor_scalar(y, x[:, 3:], core.p("conv_w_3", 48 + t), core.p("conv_b_3", t), ALU.mult, ALU.add))
                ordered(2, dve.scalar_tensor_tensor(out=y, in0=x[:, 2:2 + T], scalar=core.p("conv_w_3", 32 + t), in1=y,
                                                    op0=ALU.mult, op1=ALU.add))
                ordered(3, dve.scalar_tensor_tensor(out=y, in0=x[:, 1:1 + T], scalar=core.p("conv_w_3", 16 + t), in1=y,
                                                    op0=ALU.mult, op1=ALU.add))
                if not isinstance(t, int) or t >= 2:
                    dve.wait_ge(act_out.sem, act_out.at(t - 1))
                dve.scalar_tensor_tensor(out=z, in0=x[:, 0:T], scalar=core.p("conv_w_3", t), in1=y, op0=ALU.mult,
                                         op1=ALU.add).then_inc(conv.sem, 1)
                dve.wait_ge(conv.sem, conv.at(t + 1))
            tile_loop(dve, n, 4, body)
            step.value = base + 3 * n
    for x in (copied, conv, act_out):
        x.passed(n)
    core.finished(n)


def mlstm_gates(core, FI, M4, EB, GC, tmp):
    soft, rows, turned, spread, kept = (core.sig(n) for n in ("f_softplus", "gate_rows", "g_turned", "m_spread", "m_kept"))
    T = SEQ
    S, F, G, FM = (core.area(tmp + i * T, T) for i in range(4))
    with core.nc.Block() as block:
        @block.scalar
        def _(act):
            do = lambda ins: core.act.do(act, ins)
            f = FI[32:36, 0]
            do(act.activation(S[32:36], f, ACT.Abs))
            do(act.activation(S[32:36], S[32:36], ACT.Exp, scale=-1.0))
            act.activation(S[32:36], S[32:36], ACT.Ln, bias=1.0).then_inc(soft.sem, 1)
            for h in range(4):
                act.wait_ge(spread.sem, spread.at(h + 1))
                act.activation(EB[:, h], core.ps[:, h % 2, :], ACT.Exp, scale=-1.0).then_inc(kept.sem, 1)

        @block.vector
        def _(dve):
            do = lambda ins: core.vec.do(dve, ins)
            dve.wait_ge(soft.sem, soft.at(1))
            lf = S[32:36]
            do(dve.scalar_tensor_tensor(out=lf, in0=FI[32:36, 0], scalar=0.0, in1=lf, op0=ALU.min, op1=ALU.subtract))
            do(dve.tensor_tensor_scan(F[32:36], lf, lf, 0.0, ALU.add, ALU.bypass))
            do(dve.tensor_copy(F[0:4], F[32:36]))
            do(dve.tensor_tensor(G[0:4], FI[0:4, 0], F[0:4], ALU.subtract))
            do(dve.tensor_tensor_scan(M4[0:4], G[0:4], G[0:4], 0.0, ALU.max, ALU.bypass))
            dve.tensor_tensor(FM[0:4], F[0:4], M4[0:4], ALU.add).then_inc(rows.sem, 1)
            dve.wait_ge(turned.sem, turned.at(1))
            do(dve.tensor_copy(GC.rearrange("p a b -> p (a b)"), core.ps[:, 2, 0:16]))

        @block.tensor
        def _(pe):
            pe.wait_ge(rows.sem, rows.at(1))
            for j in range(4):
                last = pe.transpose(core.ps[:, 2, 4 * j:4 * j + 4], G[0:4, j * P:(j + 1) * P], core.c("ident")[0:4, 0:4])
            last.then_inc(turned.sem, 1)
            for h in range(4):
                if h >= 2:
                    pe.wait_ge(kept.sem, kept.at(h - 1))
                pe.matmul(core.ps[:, h % 2, :], core.c("heads")[0:4, h * P:(h + 1) * P], FM[0:4], start=True,
                          stop=True).then_inc(spread.sem, 1)
    soft.passed(1), rows.passed(1), turned.passed(1), spread.passed(4), kept.passed(4)


def mlstm(core, Q, K, VT, M4, EB, GC, H, tmp):
    spread, arg, exps, scores, probs, sums, absd, done = (core.sig(n) for n in (
        "m_rows", "weight_arg", "weight_exp", "key_scores", "key_probs", "head_sums", "norm_abs", "head_done"))
    T = SEQ
    MB = core.area(tmp, 2, T)
    W = core.area(tmp + 2 * T, 2, T)
    PT = core.area(tmp + 4 * T, 2, T)
    N = core.area(tmp + 6 * T, 2, T)
    steps = [(h, j) for h in range(4) for j in range(4)]
    with core.nc.Block() as block:
        @block.tensor
        def _(pe):
            def score(n):
                h, j = steps[n]
                if j == 0:
                    if h:
                        pe.wait_ge(spread.sem, spread.at(2 * h))
                    pe.matmul(core.ps[:, 2, :], core.c("heads")[0:4, h * P:(h + 1) * P], M4[0:4], start=True,
                              stop=True).then_inc(spread.sem, 1)
                if n >= 2:
                    pe.wait_ge(probs.sem, probs.at(n - 1))
                for e in range(2):
                    last = pe.matmul(core.ps[:, n % 2, 0:T - j * P], K[:, 2 * h + e, j * P:(j + 1) * P], Q[:, 2 * h + e, j * P:],
                                     start=(e == 0), stop=(e == 1))
                last.then_inc(scores.sem, 1)

            def add(n):
                h, j = steps[n]
                w = T - j * P
                pe.wait_ge(probs.sem, probs.at(n + 1))
                if j == 0 and h:
                    pe.wait_ge(done.sem, done.at(h))
                p = PT[:, n % 2, 0:w]
                for b, lhs in ((3, core.c("ones")), (4, VT[:, j, 2 * h]), (5, VT[:, j, 2 * h + 1])):
                    last = pe.matmul(core.ps[:, b, j * P:], lhs, p, start=(j == 0), stop=(j == 3))
                last.then_inc(sums.sem, 1)

            score(0)
            for n in range(16):
                if n + 1 < 16:
                    score(n + 1)
                add(n)

        @block.vector
        def _(dve):
            do = lambda ins: core.vec.do(dve, ins)

            def argument(n):
                h, j = steps[n]
                w = T - j * P
                if j == 0:
                    dve.wait_ge(spread.sem, spread.at(2 * h + 1))
                    dve.tensor_copy(MB[:, h % 2], core.ps[:, 2, :]).then_inc(spread.sem, 1)
                    dve.wait_ge(spread.sem, spread.at(2 * h + 2))
                dve.tensor_scalar(W[:, n % 2, 0:w], MB[:, h % 2, j * P:], GC[:, j, h:h + 1], 0.0, ALU.subtract,
                                  ALU.max).then_inc(arg.sem, 1)

            argument(0)
            for n, (h, j) in enumerate(steps):
                w = T - j * P
                if n + 1 < 16:
                    if n >= 1:
                        dve.wait_ge(probs.sem, probs.at(n))
                    argument(n + 1)
                dve.wait_ge(exps.sem, exps.at(n + 1))
                dve.wait_ge(scores.sem, scores.at(n + 1))
                if n >= 2:
                    dve.wait_ge(sums.sem, sums.at(n - 1))
                wt, p = W[:, n % 2, 0:w], PT[:, n % 2, 0:w]
                do(dve.tensor_tensor(wt[:, 0:P], wt[:, 0:P], core.c("upper"), ALU.mult))
                dve.scalar_tensor_tensor(out=p, in0=core.ps[:, n % 2, 0:w], scalar=1.0 / 16, in1=wt, op0=ALU.mult,
                                         op1=ALU.mult).then_inc(probs.sem, 1)
                if j < 3:
                    continue
                nh = N[:, h % 2]
                dve.wait_ge(absd.sem, absd.at(h + 1))
                do(dve.tensor_tensor(nh, nh, EB[:, h], ALU.max))
                do(dve.reciprocal(nh, nh))
                do(dve.tensor_tensor(H[:, 2 * h], core.ps[:, 4, :], nh, ALU.mult))
                dve.tensor_tensor(H[:, 2 * h + 1], core.ps[:, 5, :], nh, ALU.mult).then_inc(done.sem, 1)

        @block.scalar
        def _(act):
            for n, (h, j) in enumerate(steps):
                w = T - j * P
                act.wait_ge(arg.sem, arg.at(n + 1))
                act.activation(W[:, n % 2, 0:w], W[:, n % 2, 0:w], ACT.Exp, scale=-1.0).then_inc(exps.sem, 1)
                if j == 0 and h:
                    act.wait_ge(sums.sem, sums.at(4 * h))
                    if h >= 3:
                        act.wait_ge(done.sem, done.at(h - 2))
                    act.activation(N[:, (h - 1) % 2], core.ps[:, 3, :], ACT.Abs).then_inc(absd.sem, 1)
            act.wait_ge(sums.sem, sums.at(16))
            act.activation(N[:, 1], core.ps[:, 3, :], ACT.Abs).then_inc(absd.sem, 1)
    spread.passed(8)
    for x in (arg, exps, scores, probs, sums):
        x.passed(16)
    absd.passed(4), done.passed(4)


def third_block(core, stop=None):
    T = SEQ
    merged = core.area(0, NC, T)
    QK = core.area(NC * T, 2 * NC, T)
    V = core.area(3 * NC * T, NC, T)
    VT = core.area(4 * NC * T, 4, NC, P)
    at = 5 * NC * T
    mod = core.mod
    EB, M4, GC, FI = core.area(at + 64, 4, T), core.area(at + 64 + 4 * T, T), core.area(at + 64 + 5 * T, 4, 4), core.area(
        at + 80 + 5 * T, 1, T)
    tmp = at + 96 + 6 * T
    cols = lambda o: [mod[:, o + k:o + k + 1] for k in range(NC)]
    scale_columns(core)
    input_norm(core, cols(NC), cols(0), T, tmp)

    project(core, NC, V, T, ACT.Gelu_apprx_tanh)
    v = [V[:, k] for k in range(NC)]
    center(core, [v], T, 1.0 / D, "ones")
    norm(core, [(v, v, [core.p("gmlp_ln_g_3", k) for k in range(NC)], [core.p("gmlp_ln_b_3", k) for k in range(NC)])], T,
         1.0 / D, tmp)
    quads = lambda a: [([a[:, 4 * g + k] for k in range(4)], lambda j, g=g: VT[:, j, 4 * g:4 * g + 4].rearrange("p a b -> p (a b)"))
                       for g in range(2)]
    to_tokens(core, quads(V), T)
    mix_tokens(core, VT, merged, tmp)
    act_mul(core, [(ACT.Gelu_apprx_tanh, merged, merged, False), (ACT.Sigmoid, merged, merged, False)], T, tmp)

    project_conv(core, 2 * NC, QK, tmp)
    project(core, NC, V, T)
    to_tokens(core, quads(V), T)
    project(core, 1, FI, T, ACT.Identity, "mlstm_gate_b_3")
    mlstm_gates(core, FI, M4, EB, GC, tmp)
    mlstm(core, QK[:, 0:NC], QK[:, NC:2 * NC], VT, M4, EB, GC, V, tmp)
    center(core, [[V[:, 2 * h], V[:, 2 * h + 1]] for h in range(4)], T, 1.0 / 256, "ones")
    norm(core, [([V[:, 2 * h], V[:, 2 * h + 1]],) * 2 + ([core.p("mlstm_hn_g_3", 2 * h + e) for e in range(2)], None)
                for h in range(4)], T, 1.0 / 256, tmp)
    act_mul(core, [(ACT.Sigmoid, V, V, False), (ACT.Sigmoid, V, merged, True)], T, tmp)
    add_product(core, NC, merged, T, lambda t: column(mod, 2 * NC, t))

    input_norm(core, cols(4 * NC), cols(3 * NC), T, tmp)
    hidden = core.area(0, 4 * NC, T)
    act_mul(core, [(ACT.Relu, None, hidden, False)], T, tmp, 4 * NC)
    add_product(core, 4 * NC, hidden, T, lambda t: column(mod, 5 * NC, t))
    core.close(inputs=True)
    x, out = [core.h[:, k] for k in range(NC)], [core.area(k * T, T) for k in range(NC)]
    norm(core, [(x, out, [core.p("final_g_3", k) for k in range(NC)], None)], T, 1.0 / D, tmp)


def column(a, o, t):
    return a[:, o + t:o + t + 1] if isinstance(t, int) else a[:, bass.ds(o + t, 1)]


def store(core, out):
    got = core.sig("stored", 16)
    with core.nc.Block() as block:
        @block.sync
        def _(sp):
            sp.dma_start(out, core.area(0, NC, SEQ)).then_inc(got.sem, 16)
            sp.wait_ge(got.sem, got.at(1))
    got.passed(1)


def build(nc, dram, out):
    with ExitStack() as ctx:
        core = Core(nc, ctx, dram)
        load_small(core)
        first_block(core)
        second_block(core)
        third_block(core)
        store(core, out)


def kernel(**inputs):
    import concourse.bacc as bacc
    from concourse.bass_utils import run_bass_kernel_spmd

    arrays = {f"in_{n}": np.ascontiguousarray(v) for n, v in lay_out({n: np.asarray(v) for n, v in inputs.items()}).items()}
    nc = bacc.Bacc("TRN2", target_bir_lowering=False, num_devices=1)
    dram = {n[3:]: nc.dram_tensor(n, v.shape, F32, kind="ExternalInput").ap() for n, v in arrays.items()}
    for n, shape in (("strip_scratch", (8, NR)), ("chunk_scratch", (64, CH, CH)), ("inverse_scratch", (64, CH, CH))):
        dram[n] = nc.dram_tensor(n, shape, F32, kind="Internal").ap()
    out = nc.dram_tensor("out_features", (P, NC, SEQ), F32, kind="ExternalOutput").ap()
    build(nc, dram, out)
    r = run_bass_kernel_spmd(nc, [arrays], core_ids=[0])
    return r.results[0]["out_features"].transpose(2, 1, 0).reshape(1, SEQ, D)
```

```python
from contextlib import ExitStack
import math

import numpy as np
import concourse.bass as bass
from concourse import mybir

F32 = mybir.dt.float32
F32R = mybir.dt.float32r
ALU = mybir.AluOpType
ACT = mybir.ActivationFunctionType
AX = mybir.AxisListType.X

P = 128
D = 1024
NC = D // P
META = 16
SEQ = 512
T1 = META + SEQ
D_FF = 2816
FT = D_FF // P
NG_DOWN = -(-FT // NC)
RING = 4
MAIN = 29576
TAIL = 1 << 20
SMALL_TAIL = 4240
NEG = -1e30
EPS = 1e-6
TOPK = T1 // 4
STRIP = 640
DIAG = 512
NR = STRIP + P - 1
BUCKETS = 32
EXP_LN_TABLES = 6
NCMP = (SEQ - 32) // 16 + 1
CH = 32

SB_Q, SB_K, SB_V, SP_Q, SP_K, SP_V, IX_Q, IX_K, DF_Q, DF_K, DF_V, N1 = 0, 2, 4, 6, 8, 10, 12, 14, 15, 19, 23, 27
NQ, NKC, NVC, NKS, NVS, NKW, NVW, NG, RR, RK, RV, RL, MQ, MK, MV, N2 = (
    0, 3, 4, 5, 6, 7, 8, 9, 10, 12, 14, 16, 17, 20, 23, 26)
RAW0 = N1 + 3 * NC + 2 * NC + 2 * FT + NC * NG_DOWN + N2
RAW = 6 * NC


def pack_units(w):
    k, n = w.shape
    ku, nt = -(-k // D), -(-n // P)
    full = np.zeros((ku * D, nt * P), w.dtype)
    full[:k, :n] = w
    return full.reshape(ku, NC, P, nt, P).transpose(3, 0, 2, 1, 4).reshape(nt * ku, P, D)


def pack_groups(w):
    return np.concatenate([pack_units(w[k:k + D]) for k in range(0, w.shape[0], D)], 0)


def interleave(*parts):
    return np.stack(parts, 1).reshape(-1, P, D)


def columns(v):
    v = np.asarray(v).reshape(-1)
    m = -(-v.size // P)
    full = np.zeros(m * P, v.dtype)
    full[:v.size] = v
    return full.reshape(m, P).T


PARAMS = [
    ("attn_norm", 8), ("b_gate", 24), ("q_norm_sp", 1), ("k_norm_sp", 1), ("q_norm_df", 1), ("k_norm_df", 1),
    ("subln_df", 1), ("ffn_norm", 8), ("conv_w", 66), ("conv_b", 22),
    ("attn_norm_2", 8), ("nsa_out_gain_2", 3), ("rw_mu_2", 7), ("rw_w0_2", 2), ("rw_a0_2", 2), ("rw_k_k_2", 2),
    ("rw_k_a_2", 2), ("rw_r_k_2", 2), ("rw_lnx_w_2", 2), ("rw_lnx_b_2", 2), ("moba_out_gain_2", 3),
    ("ffn_norm_2", 8), ("ffn_conv_w_2", 66), ("ffn_conv_b_2", 22), ("final_norm_2", 8),
    ("b_ada_3", 48), ("norm1_g_3", 8), ("conv_w_3", 64), ("conv_b_3", 16), ("mlstm_gate_b_3", 1),
    ("gmlp_ln_g_3", 8), ("gmlp_ln_b_3", 8), ("mlstm_hn_g_3", 8), ("norm2_g_3", 8), ("final_g_3", 8),
]
PCOL, NPAR = {}, 0
for _name, _m in PARAMS:
    PCOL[_name] = NPAR
    NPAR += _m


def params(a):
    v = {n: a[n] for n, _ in PARAMS}
    for n in ("q_norm_sp", "k_norm_sp", "q_norm_df", "k_norm_df"):
        v[n] = np.concatenate([a[n].reshape(-1)] * 2)
    g = a["mlstm_gate_b_3"].reshape(2, 4)
    rows = np.zeros(P, g.dtype)
    rows[0:4], rows[32:36] = g[0], g[1]
    v["mlstm_gate_b_3"] = rows
    return np.concatenate([columns(v[n]) for n, _ in PARAMS], 1)


HEAD_ROWS = 22
CONSTS = [("ident", P), ("ones", P), ("pair64", P), ("flip", P), ("causal", STRIP), ("strict", P), ("strict_neg", P),
          ("heads", 4 * P), ("upper", P), ("pair_rows", 2 * HEAD_ROWS + 2), ("eps6", 1), ("eps_rw", 1), ("zero", 1)]
NSA_CONSTS = [("cmp_bias", 24 * NCMP), ("cmp_keep", 24 * NCMP), ("gates", 9 * P)]
RWKV_CONSTS = [("mask32", 512), ("restart", SEQ), ("eye16", 512)]
WIDTH = dict(CONSTS + NSA_CONSTS + RWKV_CONSTS)
NCON = sum(m for _, m in CONSTS)


def constants():
    p, c = np.arange(P)[:, None], np.arange(P)[None, :]
    k = {}
    k["ident"] = p == c
    k["ones"] = np.ones((P, P))
    k["pair64"] = p // 64 == c // 64
    k["pair_rows"] = np.arange(2 * HEAD_ROWS + 2)[None, :] == HEAD_ROWS + p // 64
    k["flip"] = p + c == P - 1
    k["causal"] = np.where(np.arange(STRIP)[None, :] <= p + DIAG, 0.0, NEG)
    k["strict"] = c < p
    k["strict_neg"] = np.where(c < p, 0.0, NEG)
    heads = np.zeros((P, 4, P))
    for h in range(4):
        heads[h, h], heads[32 + h, h] = 1, 1
    k["heads"] = heads.reshape(P, -1)
    q = np.arange(4)[None, :, None, None] * P + np.arange(P)[:, None, None, None]
    seen = (np.arange(NCMP) * 16 + 31 <= q) & np.ones((1, 1, 6, 1), bool)
    k["cmp_bias"] = np.where(seen, 0.0, NEG).reshape(P, -1)
    k["cmp_keep"] = seen.reshape(P, -1)
    b, t, f = np.arange(3)[None, :, None, None], np.arange(3)[None, None, :, None], np.arange(P)[None, None, None, :]
    k["gates"] = (np.arange(P)[:, None, None, None] == (2 * t + f // 64) * 3 + b).reshape(P, -1)
    s, t = np.arange(P)[:, None, None], np.arange(CH)[None, None, :]
    m = np.concatenate([s < t, s <= t], 1) & (s < CH)
    k["mask32"] = (m[:, None] & np.ones((1, 8, 1, 1), bool)).reshape(P, -1)
    k["restart"] = np.arange(SEQ)[None, :] % CH != 0
    k["restart"] = k["restart"] & np.ones((P, 1), bool)
    k["eye16"] = (np.arange(CH)[None, :, None] == 16 * (np.arange(P)[:, None, None] // 64) + np.arange(16)[None, None, :]).reshape(P, -1)
    k["upper"] = p <= c
    k["eps6"], k["eps_rw"], k["zero"] = np.full(P, EPS), np.full(P, 64e-5), np.zeros(P)
    return [np.concatenate([np.asarray(k[n], np.float32).reshape(P, -1) for n, _ in names], 1)
            for names in (CONSTS, NSA_CONSTS, RWKV_CONSTS)]


def bucket_rows():
    n = STRIP - 1 - np.arange(NR)
    m = np.maximum(n, 1).astype(np.float32)
    large = 16 + (np.log(m / np.float32(16)) / np.float32(math.log(8)) * 16).astype(np.int32)
    b = np.where(n < 16, np.maximum(n, 0), np.minimum(large, 31))
    out = np.zeros((BUCKETS + 1, NR), np.float32)
    out[b, np.arange(NR)] = 1
    out[:BUCKETS, n < 0] = 0
    out[BUCKETS] = n < 0
    return out


def lay_out(a):
    w = a["w_in"][0]
    cut = np.cumsum([0, 256, 256, 256, 256, 256, 256, 256, 32, 8, 512, 512, 512, D, D, D])
    col = [w[:, cut[i]:cut[i + 1]] for i in range(15)]
    units = [pack_units(c) for c in col[:7]]
    units += [pack_units(np.concatenate(col[7:9], 1))]
    units += [pack_units(c) for c in col[9:12]]
    br = np.concatenate([a["w_br_sb"][0], a["w_br_sp"][0], a["w_br_df"][0]], 0)
    units += [pack_units(c) for c in col[12:15]] + [pack_units(br)]
    units += [pack_units(a["w_out"][0])]
    up = a["w_up"][0]
    units += [interleave(pack_units(up[:, :D_FF]), pack_units(up[:, D_FF:]))]
    units += [pack_groups(a["w_down"][0])]
    w = a["w_in_2"][0]
    cut = np.cumsum([0, 384, 128, 128, 128, 128, 128, 128, 18, 256, 256, 256, 128, 384, 384, 384])
    units += [pack_units(w[:, cut[i]:cut[i + 1]]) for i in range(15)]
    units += [a["w_ada_3"][0].T.reshape(RAW, P, D)]
    units += [pack_units(a["w_out_2"][0])]
    up = a["ffn_w_in_2"][0]
    units += [interleave(pack_units(up[:, D_FF:]), pack_units(up[:, :D_FF]))]
    units += [pack_groups(a["ffn_w_out_2"][0])]
    w = a["w_in_3"][0]
    u, v, qk, mv, o = w[:, :D], w[:, D:2 * D], w[:, 2 * D:4 * D], w[:, 4 * D:5 * D], w[:, 5 * D:6 * D]
    fi = np.zeros((D, P), w.dtype)
    fi[:, 0:4], fi[:, 32:36] = w[:, 6 * D:6 * D + 4], w[:, 6 * D + 4:6 * D + 8]
    ga, gb = w[:, 6 * D + 8:7 * D + 8], w[:, 7 * D + 8:]
    units += [pack_units(c) for c in (v, u, ga, qk, mv, fi, o, gb)]
    units += [pack_units(a["w_out_3"][0]), pack_units(a["w_ff1_3"][0]), pack_groups(a["w_ff2_3"][0])]
    fixed = constants()
    seq = np.concatenate([a["meta_tokens"], a["x"][0]], 0)
    return {
        "weights": np.concatenate(units, 0),
        "x": np.ascontiguousarray(seq.T.reshape(NC, P, T1).transpose(1, 0, 2)).reshape(P, -1),
        "params": params(a),
        "consts": fixed[0],
        "nsa_consts": fixed[1],
        "rwkv_consts": fixed[2],
        "c": a["c_3"].reshape(1, D),
        "bucket": bucket_rows(),
        "rel_bias": a["rel_bias"],
        "lam": np.concatenate([a[n].reshape(1, 64) for n in ("lam_q1", "lam_q2", "lam_k1", "lam_k2")], 1),
        "cmp_pos": a["nsa_cmp_pos_2"][0].reshape(2, 16, 2, 64).transpose(2, 3, 0, 1).reshape(P, 32),
        "cmp_w1": a["nsa_cmp_w1_2"][0].reshape(2, 16, P, 256).transpose(0, 2, 1, 3).reshape(2, P, 4096),
        "cmp_w2": a["nsa_cmp_w2_2"][0].reshape(2, 2, P, 64).transpose(2, 0, 1, 3).reshape(P, 256),
        "lora": np.concatenate([a["rw_w2_2"][0], a["rw_a2_2"][0], a["rw_g2_2"][0]], 0),
        "gmlp_ws": a["gmlp_ws_3"][0].transpose(2, 0, 1).reshape(P, -1),
        "gmlp_bs": a["gmlp_bs_3"][0].reshape(1, -1),
    }


class Signal:

    def __init__(self, sem, unit=1):
        self.sem, self.unit, self.base = sem, unit, 0

    def at(self, k):
        return self.base + self.unit * k

    def passed(self, k):
        self.base += self.unit * k


class Chain:

    def __init__(self, sem):
        self.sem, self.value = sem, 0

    def do(self, eng, ins):
        self.value += 1
        ins.then_inc(self.sem, 1)
        eng.wait_ge(self.sem, self.value)


def tile_loop(eng, n, tb, body):
    full = n // tb
    for j in range(min(tb, n)):
        body(0, j)
    if full > 3:
        with eng.Fori(1, full - 1) as i:
            for j in range(tb):
                body(i, j)
    elif full == 3:
        for j in range(tb):
            body(1, j)
    if full > 1:
        for j in range(tb):
            body(full - 1, j)
    if full:
        for j in range(n % tb):
            body(full, j)


def halves(T):
    return [(0, 264), (264, 264)] if T == T1 else [(0, T)]


class Core:

    def __init__(self, nc, ctx, dram):
        self.nc, self.ctx, self.dram = nc, ctx, dram
        self.signals = {}
        self.h_all = self.sb("h", [P, NC, T1])
        self.h = self.h_all[:, :, :]
        self.ring = self.sb("ring", [P, RING, NC, P])
        self.con = self.sb("con", [P, NCON])
        self.where = {}
        self.place(CONSTS, self.con)
        self.par = self.sb("par", [P, NPAR])
        self.mod = self.sb("mod", [P, 6 * NC])
        self.arena = self.sb("arena", [P, MAIN])
        self.inner, self.outer, self.tail = ExitStack(), ExitStack(), None
        self.ps = ctx.enter_context(nc.psum_tensor("ps", [P, 8, 512], F32))
        self.flat = self.ps[:, :, :].rearrange("p b n -> p (b n)")
        self.arrived = [self.sem(f"weights_arrived{i}") for i in range(RING)]
        self.used = self.sem("weights_used")
        self.split_done = self.sem("weights_split")
        self.hi_ready = self.sem("weights_hi_ready")
        self.raw_used = self.sem("raw_weights_used")
        self.issued, self.stream, self.taken, self.split, self.limit = 0, 0, 0, 0, 0
        self.total = dram["weights"].shape[0]
        self.vec = Chain(self.sem("vector_step"))
        self.act = Chain(self.sem("scalar_step"))
        self.pool = Chain(self.sem("pool_step"))

    def sb(self, name, shape):
        return self.ctx.enter_context(self.nc.sbuf_tensor(name, shape, F32))

    def sem(self, name):
        return self.ctx.enter_context(self.nc.semaphore(name))

    def sig(self, name, unit=1):
        if name not in self.signals:
            self.signals[name] = Signal(self.sem(name), unit)
        return self.signals[name]

    def place(self, names, area):
        o = 0
        for n, m in names:
            self.where[n] = area[:, o:o + m]
            o += m

    def c(self, name, n=None):
        return self.where[name][:, 0:n or WIDTH[name]]

    def p(self, name, j=0):
        o = PCOL[name]
        return self.par[:, bass.ds(o + j, 1)] if not isinstance(j, int) else self.par[:, o + j:o + j + 1]

    def area(self, start, *dims):
        n = int(np.prod(dims))
        if start >= TAIL:
            v = self.tail[:, start - TAIL:start - TAIL + n]
            assert start - TAIL + n <= self.tail_size, (start - TAIL, dims)
        else:
            assert start + n <= MAIN, (start, dims)
            v = self.arena[:, start:start + n]
        if len(dims) == 1:
            return v
        names = "abcd"[:len(dims)]
        return v.rearrange(f"p ({' '.join(names)}) -> p {' '.join(names)}", **dict(zip(names[1:], dims[1:])))

    def open_inputs(self):
        self.outer = ExitStack()
        self.xh, self.xl = (self.outer.enter_context(self.nc.sbuf_tensor(f"{n}{self.taken}", [P, NC, T1], F32R)) for n in ("xh", "xl"))

    def open_weights(self, units):
        self.inner = ExitStack()
        self.wh, self.wl = (self.inner.enter_context(self.nc.sbuf_tensor(f"{n}{self.taken}", [P, 2, NC, P], F32R)) for n in ("wh", "wl"))
        self.limit = self.taken + units

    def close(self, inputs=False):
        assert self.taken == self.split == self.limit
        self.inner.close()
        if inputs:
            self.outer.close()

    def open_tail(self, size):
        self.inner, self.tail_size = ExitStack(), size
        self.tail = self.inner.enter_context(self.nc.sbuf_tensor(f"tail{size}", [P, size], F32))

    def load_units(self, sp, units):
        a, b = self.issued, min(self.stream + units + RING, self.total)
        w = self.dram["weights"]

        def load(u, i):
            slot = u % RING
            old = u - RING
            if old >= 0:
                if old < RAW0:
                    sp.wait_ge(self.split_done, old + 1 + i * RING)
                elif old < RAW0 + RAW:
                    sp.wait_ge(self.raw_used, old - RAW0 + 1 + i * RING)
                else:
                    sp.wait_ge(self.split_done, old - RAW + 1 + i * RING)
            src = w[u:u + 1] if isinstance(i, int) else w[bass.ds(u + i * RING, 1)]
            sp.dma_start(self.ring[:, slot:slot + 1], src.rearrange("o p (c n) -> p o c n", c=NC)).then_inc(
                self.arrived[slot], 16)

        cuts = sorted({min(max(c, a), b) for c in (a, RING, RAW0 + RING, RAW0 + RAW + RING, b)})
        for u, end in zip(cuts, cuts[1:]):
            rounds = (end - u) // RING
            if rounds > 1 and u >= RING:
                with sp.Fori(0, rounds) as i:
                    for j in range(RING):
                        load(u + j, i)
                u += rounds * RING
            while u < end:
                load(u, 0)
                u += 1
        self.issued = max(b, a)

    def place_of(self, s):
        return s if s < RAW0 else s + RAW

    def split_hi(self, act, off, i=0, per=0):
        s = self.taken + off + 2
        if isinstance(i, int):
            s += i * per
            i = 0
            if s >= self.limit:
                return
        if s < self.split:
            return
        u = self.place_of(s)
        act.wait_ge(self.arrived[u % RING], 16 * (u // RING + 1) + i * (16 * per // RING))
        if s >= 2:
            act.wait_ge(self.used, s - 1 + i * per)
        flat = lambda a: a.rearrange("p c n -> p (c n)")
        act.activation(flat(self.wh[:, s % 2]), flat(self.ring[:, u % RING]), ACT.Copy).then_inc(self.hi_ready, 1)

    def split_lo(self, dve, off, i=0, per=0):
        s = self.taken + off + 2
        if isinstance(i, int):
            s += i * per
            i = 0
            if s >= self.limit:
                return
        if s < self.split:
            return
        u = self.place_of(s)
        dve.wait_ge(self.hi_ready, s + 1 + i * per)
        flat = lambda a: a.rearrange("p c n -> p (c n)")
        dve.tensor_tensor(flat(self.wl[:, s % 2]), flat(self.ring[:, u % RING]), flat(self.wh[:, s % 2]).bitcast(F32),
                          ALU.subtract).then_inc(self.split_done, 1)

    def split_first(self, eng, split):
        for off in range(2):
            split(eng, off - 2)

    def product(self, pe, out, T, off, i=0, per=0, chunks=NC, input_ready=None, chunk_used=None):
        s = self.taken + off
        pe.wait_ge(self.split_done, s + 1 + i * per)
        wh, wl = self.wh[:, s % 2], self.wl[:, s % 2]
        for k in range(chunks):
            if input_ready:
                input_ready(k)
            for n, (w, x) in enumerate(((wh, self.xh), (wh, self.xl), (wl, self.xh))):
                for e, (o, m) in enumerate(halves(T)):
                    last = pe.matmul(out(e), w[:, k, :], x[:, k, o:o + m], start=(k == 0 and n == 0),
                                     stop=(k == chunks - 1 and n == 2))
            if chunk_used and k < chunks - 1:
                last.then_inc(chunk_used.sem, 1)
        return last

    def finished(self, units):
        self.split = max(self.split, min(self.taken + units + 2, self.limit))
        self.stream += units
        self.taken += units


def tile_of(buf, t, T):
    s = len(halves(T))
    if isinstance(t, int):
        return buf[:, t, 0:T].rearrange("p (s n) -> p s n", s=s)
    return buf[:, bass.ds(t, 1), 0:T].rearrange("p o (s n) -> p (o s) n", s=s)


def banks(core, slot, T):
    s, w = len(halves(T)), halves(T)[0][1]
    return core.ps[:, slot:slot + s, 0:w]


def out_slot(j, bank=0):
    return bank + 2 * (j % 2)


def gemm(core, pe, n, tb, T, free, free2=None, input_ready=None):
    def body(i, j):
        t = i * tb + j
        if not isinstance(t, int) or t >= 2:
            if free2 is None:
                pe.wait_ge(free.sem, free.at(t - 1))
            else:
                own = free2 if j % 2 else free
                pe.wait_ge(own.sem, own.at(i * (tb // 2) + j // 2))
        core.product(pe, lambda s: core.ps[:, out_slot(j) + s, 0:halves(T)[s][1]], T, j, i, tb,
                     input_ready=input_ready if isinstance(i, int) and i * tb + j == 0 else None).then_inc(core.used, 1)
    tile_loop(pe, n, tb, body)


def tile_done(core, eng, i, j, tb):
    eng.wait_ge(core.used, core.taken + j + 1 + i * tb)


def project(core, n, dst, T, func=ACT.Copy, bias=None, x=None):
    x = x or SplitInput(core)
    free = core.sig("tile_free")
    with core.nc.Block() as block:
        @block.sync
        def _(sp):
            core.load_units(sp, n)

        @block.tensor
        def _(pe):
            gemm(core, pe, n, 4, T, free, input_ready=x.ready(pe))

        @block.scalar
        def _(act):
            x.high(act)

            def body(i, j):
                t = i * 4 + j
                tile_done(core, act, i, j, 4)
                core.split_hi(act, j, i, 4)
                act.activation(tile_of(dst, t, T), banks(core, out_slot(j), T), func,
                               bias=core.p(bias, t) if bias else 0.0).then_inc(free.sem, 1)
            tile_loop(act, n, 4, body)

        @block.vector
        def _(dve):
            x.low(dve)
            tile_loop(dve, n, 4, lambda i, j: core.split_lo(dve, j, i, 4))
    free.passed(n)
    x.passed()
    core.finished(n)


def split_input(core, tiles, T):
    hi = core.sig("input_hi")
    with core.nc.Block() as block:
        @block.scalar
        def _(act):
            for k, a in enumerate(tiles):
                act.activation(core.xh[:, k, 0:T], a, ACT.Copy).then_inc(hi.sem, 1)

        @block.vector
        def _(dve):
            for k, a in enumerate(tiles):
                dve.wait_ge(hi.sem, hi.at(k + 1))
                dve.tensor_tensor(core.xl[:, k, 0:T], a, core.xh[:, k, 0:T].bitcast(F32), ALU.subtract)
    hi.passed(len(tiles))


def add_product(core, kc, src, T, tmp=None, scale=None, skip=0):
    free, hi, lo, left = (core.sig(n) for n in ("tile_free", "input_hi", "input_lo", "input_used"))
    groups = [(g, min(NC, kc - g)) for g in range(0, kc, NC)]
    G = len(groups)
    sq = None if tmp is None else core.area(tmp, 2, T)
    with core.nc.Block() as block:
        @block.sync
        def _(sp):
            core.load_units(sp, NC * G)

        @block.tensor
        def _(pe):
            for n, (g, m) in enumerate(groups):
                for t in range(NC):
                    if g + t >= 2:
                        pe.wait_ge(free.sem, free.at(g + t - 1))
                    core.product(pe, lambda s: core.ps[:, out_slot(t) + s, 0:halves(T)[s][1]], T, g + t, chunks=m,
                                 input_ready=(lambda k: pe.wait_ge(lo.sem, lo.at(g + k + 1))) if t == 0 else None,
                                 chunk_used=left if t == NC - 1 and n < G - 1 else None).then_inc(core.used, 1)
                    if sq is not None and n == G - 1 and t:
                        add_square(core, pe, sq, t - 1, T, skip)
            if sq is not None:
                add_square(core, pe, sq, NC - 1, T, skip)

        @block.scalar
        def _(act):
            core.split_first(act, core.split_hi)

            def high(n):
                g, m = groups[n]
                for k in range(m):
                    if n:
                        if k < NC - 1:
                            act.wait_ge(left.sem, left.at((n - 1) * (NC - 1) + k + 1))
                        else:
                            act.wait_ge(core.used, core.taken + g)
                    act.activation(core.xh[:, k, 0:T], src[:, g + k, 0:T], ACT.Copy).then_inc(hi.sem, 1)
            high(0)
            for n in range(G):
                for t in range(NC):
                    if t == NC - 1 and n < G - 1:
                        high(n + 1)
                    core.split_hi(act, n * NC + t)
                    if sq is not None and n == G - 1:
                        act.wait_ge(free.sem, free.at(n * NC + t + 1))
                        square(core, act, sq, t, T)

        @block.vector
        def _(dve):
            core.split_first(dve, core.split_lo)

            def low(n):
                g, m = groups[n]
                for k in range(m):
                    dve.wait_ge(hi.sem, hi.at(g + k + 1))
                    dve.tensor_tensor(core.xl[:, k, 0:T], src[:, g + k, 0:T], core.xh[:, k, 0:T].bitcast(F32),
                                      ALU.subtract).then_inc(lo.sem, 1)
            low(0)
            for n in range(G):
                for t in range(NC):
                    if t == NC - 1 and n < G - 1:
                        low(n + 1)
                    dve.wait_ge(core.used, core.taken + n * NC + t + 1)
                    out, got = tile_of(core.h, t, T), banks(core, out_slot(t), T)
                    if scale is None:
                        dve.tensor_tensor(out, got, out, ALU.add).then_inc(free.sem, 1)
                    else:
                        dve.scalar_tensor_tensor(out=out, in0=got, scalar=scale(t), in1=out, op0=ALU.mult,
                                                 op1=ALU.add).then_inc(free.sem, 1)
                    core.split_lo(dve, n * NC + t)
    free.passed(NC * G)
    hi.passed(kc)
    lo.passed(kc)
    left.passed((NC - 1) * (G - 1))
    if sq is not None:
        core.sig("square_ready").passed(NC)
        core.sig("square_used").passed(NC)
    core.finished(NC * G)


def conv_glu_up(core, x, dst, tmp, T, conv_w, conv_b):
    free, gate_in, conv_out, act_out = (core.sig(n) for n in ("tile_free", "gate_in", "conv_out", "silu_out"))
    gate = core.area(tmp, 2, T + 2)
    mid = core.area(tmp + 2 * (T + 2), 2, 3, T)
    step = core.vec
    with core.nc.Block() as block:
        @block.sync
        def _(sp):
            core.load_units(sp, 2 * FT)

        @block.tensor
        def _(pe):
            gemm(core, pe, 2 * FT, 4, T, gate_in, free, input_ready=x.ready(pe))

        @block.scalar
        def _(act):
            x.high(act)
            core.act.do(act, act.activation(gate[:, :, 0:2], core.c("ones", 4).rearrange("p (b n) -> p b n", b=2),
                                            ACT.Copy, scale=0.0))

            def body(i, j):
                p = i * 2 + j
                act.wait_ge(core.used, core.taken + 2 * j + 1 + i * 4)
                core.split_hi(act, 2 * j, i, 4)
                if not isinstance(p, int) or p >= 2:
                    act.wait_ge(conv_out.sem, conv_out.at(p - 1))
                o = gate[:, j, 2:2 + T].rearrange("p (s n) -> p s n", s=len(halves(T)))
                act.activation(o, banks(core, out_slot(0), T), ACT.Copy).then_inc(gate_in.sem, 1)
                act.wait_ge(conv_out.sem, conv_out.at(p + 1))
                act.activation(mid[:, j, 2], mid[:, j, 1], ACT.Silu).then_inc(act_out.sem, 1)
                core.split_hi(act, 2 * j + 1, i, 4)
            tile_loop(act, FT, 2, body)

        @block.vector
        def _(dve):
            x.low(dve)
            base = step.value

            def body(i, j):
                p = i * 2 + j

                def ordered(k, ins):
                    ins.then_inc(step.sem, 1)
                    dve.wait_ge(step.sem, base + 2 * p + k)
                core.split_lo(dve, 2 * j, i, 4)
                dve.wait_ge(gate_in.sem, gate_in.at(p + 1))
                ordered(1, dve.tensor_scalar(mid[:, j, 0], gate[:, j, 2:2 + T], core.p(conv_w, 2 * FT + p),
                                             core.p(conv_b, p), ALU.mult, ALU.add))
                ordered(2, dve.scalar_tensor_tensor(out=mid[:, j, 1], in0=gate[:, j, 1:1 + T],
                                                    scalar=core.p(conv_w, FT + p), in1=mid[:, j, 0], op0=ALU.mult,
                                                    op1=ALU.add))
                dve.scalar_tensor_tensor(out=mid[:, j, 1], in0=gate[:, j, 0:T], scalar=core.p(conv_w, p),
                                         in1=mid[:, j, 1], op0=ALU.mult, op1=ALU.add).then_inc(conv_out.sem, 1)
                dve.wait_ge(act_out.sem, act_out.at(p + 1))
                dve.wait_ge(core.used, core.taken + 2 * j + 2 + i * 4)
                s = mid[:, j, 2].rearrange("p (s n) -> p s n", s=len(halves(T)))
                dve.tensor_tensor(tile_of(dst, p, T), banks(core, out_slot(1), T), s, ALU.mult).then_inc(free.sem, 1)
                core.split_lo(dve, 2 * j + 1, i, 4)
            tile_loop(dve, FT, 2, body)
            step.value = base + 2 * FT
    for s in (free, gate_in, conv_out, act_out):
        s.passed(FT)
    x.passed()
    core.finished(2 * FT)


def act_mul(core, parts, T, tmp, tiles=NC, x=None):
    x = x or SplitInput(core)
    free, mul = core.sig("tile_free"), core.sig("multiplied")
    mid = core.area(tmp, 2, T)
    prod = core.area(tmp + 2 * T, 2, T)
    S = len(halves(T))

    for func, other, dst, add in parts:
        with core.nc.Block() as block:
            @block.sync
            def _(sp):
                core.load_units(sp, tiles)

            @block.tensor
            def _(pe):
                gemm(core, pe, tiles, 4, T, free, input_ready=x.ready(pe))

            @block.scalar
            def _(act):
                x.high(act)

                def body(i, j):
                    t = i * 4 + j
                    tile_done(core, act, i, j, 4)
                    core.split_hi(act, j, i, 4)
                    if not isinstance(t, int) or t >= 2:
                        act.wait_ge(mul.sem, mul.at(t - 1))
                    act.activation(mid[:, j % 2].rearrange("p (s n) -> p s n", s=S), banks(core, out_slot(j), T),
                                   func).then_inc(free.sem, 1)
                tile_loop(act, tiles, 4, body)

            @block.vector
            def _(dve):
                x.low(dve)

                def body(i, j):
                    t = i * 4 + j
                    core.split_lo(dve, j, i, 4)
                    dve.wait_ge(free.sem, free.at(t + 1))
                    m = mid[:, j % 2].rearrange("p (s n) -> p s n", s=S)
                    o = m if other is None else tile_of(other, t, T)
                    if not add:
                        dve.tensor_tensor(tile_of(dst, t, T), m, o, ALU.mult).then_inc(mul.sem, 1)
                        return
                    pr = prod[:, j % 2].rearrange("p (s n) -> p s n", s=S)
                    dve.tensor_tensor(pr, m, o, ALU.mult).then_inc(mul.sem, 1)
                    dve.wait_ge(mul.sem, mul.at(t + 1))
                    out = tile_of(dst, t, T)
                    dve.tensor_tensor(out, out, pr, ALU.add)
                tile_loop(dve, tiles, 4, body)
        free.passed(tiles)
        mul.passed(tiles)
        core.finished(tiles)
        x.passed()
        x = SplitInput(core)


def norm(core, items, T, inv_n, tmp, eps="eps6", ones="ones", least=None):
    sq_ready, sq_used, sum_used, root_used = (core.sig(n) for n in ("square_ready", "square_used", "sum_used", "root_used"))
    sq = core.area(tmp, 2, T)
    r = core.area(tmp + 2 * T, 2, T)
    tiles = sum(len(x[0]) for x in items)
    with core.nc.Block() as block:
        @block.scalar
        def _(act):
            def root(n, t):
                act.wait_ge(sq_used.sem, sq_used.at(t))
                if n >= 2:
                    act.wait_ge(root_used.sem, root_used.at(n - 1))
                act.activation(r[:, n % 2].rearrange("p (s n) -> p s n", s=len(halves(T))), banks(core, out_slot(n), T),
                               ACT.Sqrt, bias=core.c(eps), scale=inv_n).then_inc(sum_used.sem, 1)

            t = 0
            for n, (x, _, _, _) in enumerate(items):
                for k, a in enumerate(x):
                    if t >= 2:
                        act.wait_ge(sq_used.sem, sq_used.at(t - 1))
                    act.activation(sq[:, t % 2], a, ACT.Square).then_inc(sq_ready.sem, 1)
                    t += 1
                    if n and k == 0:
                        root(n - 1, t - 1)
            root(len(items) - 1, t)

        @block.tensor
        def _(pe):
            t = 0
            for n, (x, _, _, _) in enumerate(items):
                if n >= 2:
                    pe.wait_ge(sum_used.sem, sum_used.at(n - 1))
                for k in range(len(x)):
                    pe.wait_ge(sq_ready.sem, sq_ready.at(t + 1))
                    for s, (o, w) in enumerate(halves(T)):
                        last = pe.matmul(core.ps[:, out_slot(n) + s, 0:w], core.c(ones), sq[:, t % 2, o:o + w],
                                         start=(k == 0), stop=(k == len(x) - 1))
                    last.then_inc(sq_used.sem, 1)
                    t += 1

        @block.vector
        def _(dve):
            do = lambda ins: core.vec.do(dve, ins)
            for n, (x, out, gains, shifts) in enumerate(items):
                rn = r[:, n % 2]
                dve.wait_ge(sum_used.sem, sum_used.at(n + 1))
                if least is not None:
                    do(dve.tensor_scalar(rn, rn, least, None, ALU.max))
                do(dve.reciprocal(rn, rn))
                for k, a in enumerate(x):
                    if gains is None:
                        ins = dve.tensor_tensor(out[k], a, rn, ALU.mult)
                    else:
                        ins = dve.scalar_tensor_tensor(out=out[k], in0=a, scalar=gains[k], in1=rn, op0=ALU.mult,
                                                       op1=ALU.mult)
                    if shifts is not None:
                        do(ins)
                        ins = dve.tensor_scalar(out[k], out[k], shifts[k], None, ALU.add)
                    if k < len(x) - 1:
                        do(ins)
                    else:
                        ins.then_inc(root_used.sem, 1)
    sq_ready.passed(tiles)
    sq_used.passed(tiles)
    sum_used.passed(len(items))
    root_used.passed(len(items))


def square(core, act, sq, k, T):
    ready, used = core.sig("square_ready"), core.sig("square_used")
    if k >= 2:
        act.wait_ge(used.sem, used.at(k - 1))
    act.activation(sq[:, k % 2], core.h[:, k, 0:T], ACT.Square).then_inc(ready.sem, 1)


def add_square(core, pe, sq, k, T, skip=0):
    ready, used = core.sig("square_ready"), core.sig("square_used")
    pe.wait_ge(ready.sem, ready.at(k + 1))
    for s, (o, w) in enumerate(halves(T - skip)):
        last = pe.matmul(core.ps[:, 4 + s, 0:w], core.c("ones"), sq[:, k % 2, skip + o:skip + o + w], start=(k == 0), stop=(k == NC - 1))
    last.then_inc(used.sem, 1)


def sum_squares(core, T, tmp):
    sq = core.area(tmp, 2, T)
    with core.nc.Block() as block:
        @block.sync
        def _(sp):
            core.load_units(sp, 0)

        @block.scalar
        def _(act):
            act.wait_ge(core.sig("x_loaded", 16).sem, 16)
            for k in range(NC):
                square(core, act, sq, k, T)

        @block.tensor
        def _(pe):
            for k in range(NC):
                add_square(core, pe, sq, k, T)
    core.sig("square_ready").passed(NC)
    core.sig("square_used").passed(NC)


class NormedInput:

    def __init__(self, core, gains, shifts, T, tmp):
        self.core, self.gains, self.shifts, self.T = core, gains, shifts, T
        self.root, self.made, self.hi, self.lo = (core.sig(n) for n in ("root_ready", "normed", "input_hi", "input_lo"))
        self.r, self.out = core.area(tmp, T), core.area(tmp + T, 2, T)

    def high(self, act):
        core, T = self.core, self.T
        act.activation(self.r.rearrange("p (s n) -> p s n", s=len(halves(T))), banks(core, 4, T), ACT.Sqrt,
                       bias=core.c("eps6"), scale=1.0 / D).then_inc(self.root.sem, 1)
        core.split_first(act, core.split_hi)
        for k in range(NC):
            act.wait_ge(self.made.sem, self.made.at(k + 1))
            act.activation(core.xh[:, k, 0:T], self.out[:, k % 2], ACT.Identity,
                           bias=self.shifts[k] if self.shifts else 0.0).then_inc(self.hi.sem, 1)

    def low(self, dve):
        core, T, out = self.core, self.T, self.out

        def part(k):
            dve.wait_ge(self.hi.sem, self.hi.at(k + 1))
            to, a, b = core.xl[:, k, 0:T], out[:, k % 2], core.xh[:, k, 0:T].bitcast(F32)
            if self.shifts:
                ins = dve.scalar_tensor_tensor(out=to, in0=a, scalar=self.shifts[k], in1=b, op0=ALU.add, op1=ALU.subtract)
            else:
                ins = dve.tensor_tensor(to, a, b, ALU.subtract)
            ins.then_inc(self.lo.sem, 1)
        dve.wait_ge(self.root.sem, self.root.at(1))
        core.vec.do(dve, dve.reciprocal(self.r, self.r))
        for k in range(NC):
            if k >= 2:
                part(k - 2)
                dve.wait_ge(self.lo.sem, self.lo.at(k - 1))
            dve.scalar_tensor_tensor(out=out[:, k % 2], in0=core.h[:, k, 0:T], scalar=self.gains[k], in1=self.r,
                                     op0=ALU.mult, op1=ALU.mult).then_inc(self.made.sem, 1)
            if k == 1:
                core.split_first(dve, core.split_lo)
        part(NC - 2)
        part(NC - 1)

    def ready(self, pe):
        return lambda k: pe.wait_ge(self.lo.sem, self.lo.at(k + 1))

    def passed(self):
        self.root.passed(1)
        for a in (self.made, self.hi, self.lo):
            a.passed(NC)


class SplitInput:

    def __init__(self, core):
        self.core = core

    def high(self, act):
        self.core.split_first(act, self.core.split_hi)

    def low(self, dve):
        self.core.split_first(dve, self.core.split_lo)

    def ready(self, pe):
        return None

    def passed(self):
        pass


def layer_norm_input(core, gain, T, tmp):
    return NormedInput(core, [core.p(gain, k) for k in range(NC)], None, T, tmp)


def load_small(core):
    d, got, x_loaded = core.dram, core.sig("loaded", 16), core.sig("x_loaded", 16)
    with core.nc.Block() as block:
        @block.sync
        def _(sp):
            sp.dma_start(core.con[:, :], d["consts"]).then_inc(got.sem, 16)
            sp.dma_start(core.par[:, :], d["params"]).then_inc(got.sem, 16)
            sp.wait_ge(got.sem, got.at(2))

        @block.scalar
        def _(act):
            act.dma_start(core.h.rearrange("p c t -> p (c t)"), d["x"]).then_inc(x_loaded.sem, 16)
    got.passed(2)


def renorm(core, gains, T, tmp, out=None):
    root, made, stored = core.sig("root_ready"), core.sig("normed"), core.sig("stored", 16)
    r, sq, final = core.area(tmp, T), core.area(tmp + T, 2, T), core.area(tmp + T, NC, T)
    with core.nc.Block() as block:
        @block.sync
        def _(sp):
            if out is None:
                core.load_units(sp, 0)
                return
            for k in range(NC):
                sp.wait_ge(made.sem, made.at(k + 1))
                sp.dma_start(out[:, k, :], final[:, k]).then_inc(stored.sem, 16)
            sp.wait_ge(stored.sem, stored.at(NC))

        @block.scalar
        def _(act):
            act.activation(r.rearrange("p (s n) -> p s n", s=len(halves(T))), banks(core, 4, T), ACT.Sqrt,
                           bias=core.c("eps6"), scale=1.0 / D).then_inc(root.sem, 1)
            if out is None:
                for k in range(NC):
                    act.wait_ge(made.sem, made.at(k + 1))
                    square(core, act, sq, k, T)

        @block.vector
        def _(dve):
            dve.wait_ge(root.sem, root.at(1))
            core.vec.do(dve, dve.reciprocal(r, r))
            for k in range(NC):
                x = core.h[:, k, 0:T]
                dve.scalar_tensor_tensor(out=x if out is None else final[:, k], in0=x, scalar=gains[k], in1=r,
                                         op0=ALU.mult, op1=ALU.mult).then_inc(made.sem, 1)

        if out is None:
            @block.tensor
            def _(pe):
                for k in range(NC):
                    add_square(core, pe, sq, k, T)
    root.passed(1)
    made.passed(NC)
    if out is None:
        core.sig("square_ready").passed(NC)
        core.sig("square_used").passed(NC)


def head_norm(core, items, T, inv_n, tmp):
    sq_ready, sq_used, root, inverse, spread, applied = (core.sig(n) for n in (
        "square_ready", "square_used", "root_ready", "inverse_ready", "inverse_spread", "normed"))
    sq, r = core.area(tmp, 2, T), core.area(tmp + 2 * T, T)
    N = len(items)
    rows = 2 * N
    S = len(halves(T))
    ident = core.c("ident")
    wide = core.area(tmp + 3 * T, rows, 64)
    with core.nc.Block() as block:
        @block.scalar
        def _(act):
            for n, (x, _, _) in enumerate(items):
                if n >= 2:
                    act.wait_ge(sq_used.sem, sq_used.at(n - 1))
                act.activation(sq[:, n % 2], x, ACT.Square).then_inc(sq_ready.sem, 1)
            act.wait_ge(sq_used.sem, sq_used.at(N))
            act.activation(r[0:rows].rearrange("p (s n) -> p s n", s=S), core.ps[0:rows, 6:6 + S, 0:halves(T)[0][1]], ACT.Sqrt,
                           bias=core.c("eps6")[0:rows], scale=inv_n).then_inc(root.sem, 1)

        @block.tensor
        def _(pe):
            for n in range(N):
                pe.wait_ge(sq_ready.sem, sq_ready.at(n + 1))
                to = core.c("pair_rows")[:, HEAD_ROWS - 2 * n:HEAD_ROWS - 2 * n + rows]
                for s, (o, w) in enumerate(halves(T)):
                    last = pe.matmul(core.ps[0:rows, 6 + s, 0:w], to, sq[:, n % 2, o:o + w], start=(n == 0), stop=(n == N - 1))
                last.then_inc(sq_used.sem, 1)
            pe.wait_ge(inverse.sem, inverse.at(1))
            for n in range(N):
                if n >= 2:
                    pe.wait_ge(applied.sem, applied.at(n - 1))
                to = wide[0:rows, 2 * n:2 * n + 2].rearrange("p a b -> p (a b)")
                for s, (o, w) in enumerate(halves(T)):
                    last = pe.matmul(core.ps[:, out_slot(n) + s, 0:w], to, r[0:rows, o:o + w], start=True, stop=True)
                last.then_inc(spread.sem, 1)

        @block.vector
        def _(dve):
            core.vec.do(dve, dve.tensor_copy(wide[0:rows], ident[0:rows, 0:rows].unsqueeze(2).broadcast_to([rows, rows, 64])))
            dve.wait_ge(root.sem, root.at(1))
            dve.reciprocal(r[0:rows], r[0:rows]).then_inc(inverse.sem, 1)
            for n, (x, out, gain) in enumerate(items):
                dve.wait_ge(spread.sem, spread.at(n + 1))
                parts = lambda a: a.rearrange("p (s n) -> p s n", s=S)
                dve.scalar_tensor_tensor(out=parts(out), in0=parts(x), scalar=gain, in1=banks(core, out_slot(n), T),
                                         op0=ALU.mult, op1=ALU.mult).then_inc(applied.sem, 1)
    for x in (sq_ready, sq_used, spread, applied):
        x.passed(N)
    for x in (root, inverse):
        x.passed(1)


def q_tiles(T):
    return [(q, min(P, T - q), min(q + P, T)) for q in range(0, T, P)]


def to_tokens(core, pairs, T):
    turned, turned_used = core.sig("turned"), core.sig("turned_used")
    nj = len(q_tiles(T))
    with core.nc.Block() as block:
        @block.tensor
        def _(pe):
            n = 0
            for tiles, _ in pairs:
                for q, nq, _ in q_tiles(T):
                    if n >= 2:
                        pe.wait_ge(turned_used.sem, turned_used.at(n - 1))
                    for m, a in enumerate(tiles):
                        last = pe.transpose(core.ps[0:nq, 4 + n % 2, m * P:(m + 1) * P], a[:, q:q + nq], core.c("ident"))
                    last.then_inc(turned.sem, 1)
                    n += 1

        @block.vector
        def _(dve):
            n = 0
            for tiles, dst in pairs:
                for j, (q, nq, _) in enumerate(q_tiles(T)):
                    dve.wait_ge(turned.sem, turned.at(n + 1))
                    dve.tensor_copy(dst(j)[0:nq], core.ps[0:nq, 4 + n % 2, 0:len(tiles) * P]).then_inc(turned_used.sem, 1)
                    n += 1
    turned.passed(nj * len(pairs))
    turned_used.passed(nj * len(pairs))


class Head:

    def __init__(self, maps, values, out, strip=None, chosen=None):
        self.maps, self.values, self.out, self.strip, self.chosen = maps, values, out, strip, chosen


def attention(core, kind, heads, T, tmp, neg_lam=None, beside=None):
    names = ("scores", "scores_used", "shifted", "exps", "probs", "turned", "turned_used", "out_ready", "out_used")
    scores, scores_used, shifted, exps, probs, turned, turned_used, out_ready, out_used = (core.sig(n) for n in names)
    nm = len(heads[0].maps)
    steps = [(h, i) for h in heads for i in range(len(q_tiles(T)))]
    N = len(steps)
    ahead, NX = 2, 3
    softplus_size = 2 * T if kind == "stick" else 0
    X = core.area(tmp, NX, nm, T)
    Y = core.area(tmp + NX * nm * T, 2, T) if kind == "stick" else None
    PT = core.area(tmp + NX * nm * T + softplus_size, 2, 512)
    stat = core.area(tmp + NX * nm * T + softplus_size + 1024, NX, 2, 8)

    def psum_scores(s, m, nq, nk):
        b = 2 * ((s * nm + m) % 2)
        return core.flat[0:nq, b * 512:b * 512 + nk]

    with core.nc.Block() as block:
        if beside:
            @block.sync
            def _(sp):
                core.load_units(sp, N)

            @block.gpsimd
            def _(pool):
                for s in range(N):
                    beside.multiply(pool, s)

        @block.tensor
        def _(pe):
            def score(s):
                h, i = steps[s]
                q0, nq, nk = q_tiles(T)[i]
                for m, (q, k) in enumerate(h.maps):
                    n = s * nm + m
                    if n >= 2:
                        pe.wait_ge(scores_used.sem, scores_used.at(n - 1))
                    dst = psum_scores(s, m, nq, nk)
                    for o in range(0, nk, 512):
                        w = min(512, nk - o)
                        last = pe.matmul(dst[:, o:o + w], q[:, q0:q0 + nq], k[:, o:o + w], start=True, stop=True)
                    last.then_inc(scores.sem, 1)

            def turn(s):
                h, i = steps[s]
                q0, nq, nk = q_tiles(T)[i]
                pe.wait_ge(probs.sem, probs.at(s + 1))
                if s >= 2:
                    pe.wait_ge(turned_used.sem, turned_used.at(s - 1))
                for j, o in enumerate(range(0, nk, P)):
                    w = min(P, nk - o)
                    last = pe.transpose(core.ps[0:w, 4 + s % 2, j * nq:(j + 1) * nq], X[0:nq, s % NX, 0, o:o + w],
                                        core.c("ident")[0:nq, 0:nq])
                last.then_inc(turned.sem, 1)

            def weigh(s):
                h, i = steps[s]
                q0, nq, nk = q_tiles(T)[i]
                pe.wait_ge(turned_used.sem, turned_used.at(s + 1))
                if s >= 2:
                    pe.wait_ge(out_used.sem, out_used.at(s - 1))
                lo, n = h.out[0], h.out[1]
                for j, o in enumerate(range(0, nk, P)):
                    w = min(P, nk - o)
                    last = pe.matmul(core.ps[lo:lo + n, 6 + s % 2, 0:nq], h.values(j, w), PT[0:w, s % 2, j * nq:(j + 1) * nq],
                                     start=(j == 0), stop=(o + P >= nk))
                last.then_inc(out_ready.sem, 1)

            for s in range(ahead):
                score(s)
            for s in range(N):
                if s + ahead < N:
                    score(s + ahead)
                turn(s)
                if s:
                    weigh(s - 1)
            weigh(N - 1)

        @block.vector
        def _(dve):
            do = lambda ins: core.vec.do(dve, ins)

            def before(s):
                h, i = steps[s]
                q0, nq, nk = q_tiles(T)[i]
                o = DIAG - q0
                if s >= NX:
                    dve.wait_ge(turned.sem, turned.at(s - NX + 1))
                for m in range(nm):
                    n = s * nm + m
                    x, got, st = X[0:nq, s % NX, m, 0:nk], psum_scores(s, m, nq, nk), stat[0:nq, s % NX, m]
                    if kind == "stick":
                        y = Y[0:nq, s % 2, 0:nk]
                        dve.wait_ge(exps.sem, exps.at(s + 1))
                        do(dve.scalar_tensor_tensor(out=y, in0=got, scalar=0.0, in1=y, op0=ALU.max, op1=ALU.add))
                        do(dve.tensor_tensor(y[:, q0:nk], y[:, q0:nk], core.c("strict")[0:nq, 0:nk - q0], ALU.mult))
                        do(dve.tensor_tensor_scan(x[:, ::-1], y[:, ::-1], y[:, ::-1], 0.0, ALU.add, ALU.bypass))
                        dve.tensor_tensor(x, got, x, ALU.subtract).then_inc(scores_used.sem, 1)
                        dve.wait_ge(scores_used.sem, scores_used.at(n + 1))
                        dve.tensor_tensor(x[:, q0:nk], x[:, q0:nk], core.c("strict_neg")[0:nq, 0:nk - q0],
                                          ALU.add).then_inc(shifted.sem, 1)
                        continue
                    strip = h.strip[0:nq, o:o + nk]
                    dve.wait_ge(scores.sem, scores.at(n + 1))
                    if h.chosen is not None and i:
                        dve.tensor_tensor(x, got, strip, ALU.add).then_inc(scores_used.sem, 1)
                        dve.wait_ge(scores_used.sem, scores_used.at(n + 1))
                        do(dve.tensor_tensor(x, x, h.chosen(i)[0:nq, 0:nk], ALU.add))
                    else:
                        dve.tensor_tensor(x, got, strip, ALU.add).then_inc(scores_used.sem, 1)
                        dve.wait_ge(scores_used.sem, scores_used.at(n + 1))
                    do(dve.tensor_reduce(st[:, 0:1], x, AX, ALU.max))
                    dve.tensor_scalar(st[:, 1:2], st[:, 0:1], -1.0, None, ALU.mult).then_inc(shifted.sem, 1)

            def after(s):
                h, i = steps[s]
                q0, nq, nk = q_tiles(T)[i]
                for m in range(nm):
                    x, st = X[0:nq, s % NX, m, 0:nk], stat[0:nq, s % NX, m]
                    dve.wait_ge(exps.sem, exps.at(s * nm + m + 1))
                    do(dve.reciprocal(st[:, 3:4], st[:, 2:3]))
                    if m == 0:
                        ins = dve.tensor_scalar(x, x, st[:, 3:4], None, ALU.mult)
                        if nm == 2:
                            do(ins)
                        else:
                            ins.then_inc(probs.sem, 1)
                    else:
                        do(dve.tensor_scalar(st[:, 4:5], st[:, 3:4], neg_lam[0:nq, 0:1], None, ALU.mult))
                        x0 = X[0:nq, s % NX, 0, 0:nk]
                        dve.scalar_tensor_tensor(out=x0, in0=x, scalar=st[:, 4:5], in1=x0, op0=ALU.mult,
                                                 op1=ALU.add).then_inc(probs.sem, 1)

            before(0)
            for s in range(N):
                if s + 1 < N:
                    before(s + 1)
                if kind != "stick":
                    after(s)

        @block.scalar
        def _(act):
            do = lambda ins: core.act.do(act, ins)

            def softplus(s):
                h, i = steps[s]
                q0, nq, nk = q_tiles(T)[i]
                got, y = psum_scores(s, 0, nq, nk), Y[0:nq, s % 2, 0:nk]
                act.wait_ge(scores.sem, scores.at(s + 1))
                if s >= 2:
                    act.wait_ge(scores_used.sem, scores_used.at(s - 1))
                do(act.activation(y, got, ACT.Abs))
                do(act.activation(y, y, ACT.Exp, scale=-1.0))
                act.activation(y, y, ACT.Ln, bias=1.0).then_inc(exps.sem, 1)

            def exp(s):
                h, i = steps[s]
                q0, nq, nk = q_tiles(T)[i]
                for m in range(nm):
                    x, st = X[0:nq, s % NX, m, 0:nk], stat[0:nq, s % NX, m]
                    act.wait_ge(shifted.sem, shifted.at(s * nm + m + 1))
                    if kind == "stick":
                        act.activation(x, x, ACT.Exp).then_inc(probs.sem, 1)
                    else:
                        act.activation(x, x, ACT.Exp, bias=st[:, 1:2], accum_out=st[:, 2:3]).then_inc(exps.sem, 1)

            def copy_turned(s):
                h, i = steps[s]
                q0, nq, nk = q_tiles(T)[i]
                act.wait_ge(turned.sem, turned.at(s + 1))
                if s >= 2:
                    act.wait_ge(out_ready.sem, out_ready.at(s - 1))
                full, rest = nk // P * nq, nk % P
                ins = act.activation(PT[:, s % 2, 0:full], core.ps[:, 4 + s % 2, 0:full], ACT.Copy)
                if rest:
                    core.act.do(act, ins)
                    ins = act.activation(PT[0:rest, s % 2, full:full + nq], core.ps[0:rest, 4 + s % 2, full:full + nq], ACT.Copy)
                ins.then_inc(turned_used.sem, 1)

            def copy_out(s):
                h, i = steps[s]
                q0, nq, nk = q_tiles(T)[i]
                lo, n, out = h.out
                act.wait_ge(out_ready.sem, out_ready.at(s + 1))
                act.activation(out[lo:lo + n, q0:q0 + nq], core.ps[lo:lo + n, 6 + s % 2, 0:nq], ACT.Copy).then_inc(out_used.sem, 1)

            if kind == "stick":
                core.nc.scalar.add_instruction(mybir.InstLoadActFuncSet(
                    act_func_set_id=EXP_LN_TABLES, name=core.nc.get_next_instruction_name(),
                    engine=mybir.EngineType.Activation))
                softplus(0)
            for s in range(N):
                if kind == "stick" and s + 1 < N:
                    softplus(s + 1)
                exp(s)
                if s >= 1:
                    copy_turned(s - 1)
                if s >= 2:
                    copy_out(s - 2)
                if beside:
                    beside.sum(act, s)
            copy_turned(N - 1)
            copy_out(N - 2)
            copy_out(N - 1)
    if beside:
        beside.passed(N)
    exps.passed(N * nm)
    scores.passed(N * nm)
    scores_used.passed(N * nm)
    shifted.passed(N * nm)
    for x in (probs, turned, turned_used, out_ready, out_used):
        x.passed(N)


def bias_strips(core, strips, tmp):
    got, made, row, back = (core.sig(n, u) for n, u in (
        ("strip_inputs", 16), ("strip_made", 1), ("strip_row", 1), ("strip_stored", 16)))
    done = [core.sig(f"strip_back{i}", 16) for i in range(2)]
    table = core.area(tmp, 8)
    hot = core.area(tmp + 8, NR)
    rows = core.area(tmp + 8 + NR, NR)
    skew = core.area(tmp + 8 + 2 * NR, 2, STRIP)
    scratch = core.dram["strip_scratch"]
    flipped, used = core.sig("strip_flipped"), core.sig("strip_used")
    with core.nc.Block() as block:
        @block.vector
        def _(dve):
            dve.memset(table[0:64, :], NEG).then_inc(made.sem, 1)
            dve.wait_ge(row.sem, row.at(1))
            dve.tensor_copy(rows[0:8, :], core.flat[0:8, 0:NR]).then_inc(row.sem, 1)
            for h in range(8):
                dve.wait_ge(flipped.sem, flipped.at(h + 1))
                dve.tensor_copy(strips[:, h, :].rearrange("p (s n) -> p s n", s=2),
                                core.ps[:, 2 + 2 * (h % 2):4 + 2 * (h % 2), 0:STRIP // 2]).then_inc(used.sem, 1)

        @block.sync
        def _(sp):
            sp.dma_start(hot[0:BUCKETS + 1, :], core.dram["bucket"]).then_inc(got.sem, 16)
            sp.wait_ge(made.sem, made.at(1))
            sp.dma_start(table[0:BUCKETS, :], core.dram["rel_bias"]).then_inc(got.sem, 16)
            sp.wait_ge(row.sem, row.at(2))
            sp.dma_start(scratch[:, :], rows[0:8, :]).then_inc(back.sem, 16)
            sp.wait_ge(back.sem, back.at(1))
            for h in range(8):
                if h >= 2:
                    sp.wait_ge(flipped.sem, flipped.at(h - 1))
                src = bass.AP(scratch.tensor, scratch.offset + h * NR, [[1, P], [1, STRIP]])
                sp.dma_start(skew[:, h % 2], src).then_inc(done[h % 2].sem, 16)

        @block.tensor
        def _(pe):
            pe.wait_ge(got.sem, got.at(2))
            for o in range(0, NR, 512):
                w = min(512, NR - o)
                last = pe.matmul(core.flat[0:8, o:o + w], table[0:BUCKETS + 1, :], hot[0:BUCKETS + 1, o:o + w],
                                 start=True, stop=True)
            last.then_inc(row.sem, 1)
            for h in range(8):
                pe.wait_ge(done[h % 2].sem, done[h % 2].at(h // 2 + 1))
                if h >= 2:
                    pe.wait_ge(used.sem, used.at(h - 1))
                for s in range(2):
                    n = STRIP // 2
                    last = pe.matmul(core.ps[:, 2 + 2 * (h % 2) + s, 0:n], core.c("flip"), skew[:, h % 2, s * n:(s + 1) * n],
                                     start=True, stop=True)
                last.then_inc(flipped.sem, 1)
    got.passed(2), made.passed(1), row.passed(2), back.passed(1), done[0].passed(4), done[1].passed(4), flipped.passed(8), used.passed(8)


def choose_keys(core, P1, kx, chosen, tmp):
    copied, turned, weighed = core.sig("ix_copied"), core.sig("ix_turned"), core.sig("ix_weights")
    dots, dots_used, relus, relus_used = (core.sig(n) for n in ("ix_dots", "ix_dots_used", "ix_relus", "ix_relus_used"))
    w = core.area(tmp, 5, 8)
    R = core.area(tmp + 40, 2, T1)
    S = core.area(tmp + 40 + 2 * T1, T1)
    W = core.area(tmp + 40 + 3 * T1, T1)
    m8 = core.area(tmp + 40 + 4 * T1, 8)
    need = core.area(tmp + 48 + 4 * T1, 1)
    tiles = q_tiles(T1)
    steps = [(i, j) for i in range(1, 5) for j in range(8)]
    with core.nc.Block() as block:
        @block.gpsimd
        def _(pool):
            for g in range(4):
                ins = pool.tensor_copy(kx[32 * g:32 * g + 32, :], P1[0:32, IX_K, :])
                if g < 3:
                    core.pool.do(pool, ins)
            ins.then_inc(copied.sem, 1)

        @block.tensor
        def _(pe):
            for i, (q0, nq, _) in enumerate(tiles):
                last = pe.transpose(core.ps[0:nq, 4, 8 * i:8 * i + 8], P1[32:40, IX_K, q0:q0 + nq],
                                    core.c("ident")[32:40, 32:40])
            last.then_inc(turned.sem, 1)
            pe.wait_ge(copied.sem, copied.at(1))
            for n, (i, j) in enumerate(steps):
                q0, nq, nk = tiles[i]
                g = 32 * (j % 4)
                if n >= 2:
                    pe.wait_ge(dots_used.sem, dots_used.at(n - 1))
                b = 2 * (n % 2)
                for o in range(0, nk, 512):
                    v = min(512, nk - o)
                    last = pe.matmul(core.flat[0:nq, b * 512 + o:b * 512 + o + v], P1[g:g + 32, IX_Q + j // 4, q0:q0 + nq],
                                     kx[g:g + 32, o:o + v], start=True, stop=True)
                last.then_inc(dots.sem, 1)

        @block.scalar
        def _(act):
            for n, (i, j) in enumerate(steps):
                q0, nq, nk = tiles[i]
                act.wait_ge(dots.sem, dots.at(n + 1))
                if n >= 2:
                    act.wait_ge(relus_used.sem, relus_used.at(n - 1))
                b = 2 * (n % 2)
                act.activation(R[0:nq, n % 2, 0:nk], core.flat[0:nq, b * 512:b * 512 + nk], ACT.Relu).then_inc(dots_used.sem, 1)

        @block.vector
        def _(dve):
            do = lambda ins: core.vec.do(dve, ins)
            dve.wait_ge(turned.sem, turned.at(1))
            do(dve.tensor_copy(w[:, 0:4].rearrange("p a b -> p (a b)"), core.ps[:, 4, 0:32]))
            do(dve.tensor_copy(w[0:16, 4], core.ps[0:16, 4, 32:40]))
            for n, (i, j) in enumerate(steps):
                q0, nq, nk = tiles[i]
                s, wk, c = S[0:nq, 0:nk], W[0:nq, 0:nk], chosen(i)[0:nq, 0:nk]
                dve.wait_ge(dots_used.sem, dots_used.at(n + 1))
                prev = core.c("causal")[0:nq, DIAG - q0:DIAG - q0 + nk] if j == 0 else s
                dve.scalar_tensor_tensor(out=s, in0=R[0:nq, n % 2, 0:nk], scalar=w[0:nq, i, j:j + 1], in1=prev,
                                         op0=ALU.mult, op1=ALU.add).then_inc(relus_used.sem, 1)
                dve.wait_ge(relus_used.sem, relus_used.at(n + 1))
                if j < 7:
                    continue
                m, nd = m8[0:nq, :], need[0:nq, :]
                for k in range(TOPK // 8):
                    src = s if k == 0 else wk
                    do(dve.max(m, src))
                    do(dve.match_replace(wk, m, src, -3e38))
                do(dve.max(m, wk))
                t = m[:, TOPK % 8 - 1:TOPK % 8]
                do(dve.tensor_scalar(c, s, t, None, ALU.is_gt))
                do(dve.tensor_reduce(nd, c, AX, ALU.add))
                do(dve.tensor_scalar(nd, nd, -1.0, float(TOPK), ALU.mult, ALU.add))
                do(dve.tensor_scalar(s, s, t, None, ALU.is_equal))
                do(dve.tensor_tensor_scan(wk, s, s, 0.0, ALU.add, ALU.bypass))
                do(dve.scalar_tensor_tensor(out=s, in0=wk, scalar=nd, in1=s, op0=ALU.is_le, op1=ALU.mult))
                do(dve.tensor_tensor(c, c, s, ALU.add))
                do(dve.tensor_scalar(c, c, -NEG, NEG, ALU.mult, ALU.add))
    assert TOPK % 8
    for x in (copied, turned):
        x.passed(1)
    for x in (dots, dots_used, relus_used):
        x.passed(len(steps))


def difference_weight(core, neg_lam, tmp):
    got, sums, exps, lam, spread = (core.sig(n, u) for n, u in (
        ("lam_loaded", 16), ("lam_sums", 1), ("lam_exps", 1), ("lam_ready", 1), ("lam_spread", 1)))
    v, pr, s = core.area(tmp, 256), core.area(tmp + 256, 2, 64), core.area(tmp + 384, 8)
    init = 0.8 - 0.6 * math.exp(-0.3 * 0)
    with core.nc.Block() as block:
        @block.sync
        def _(sp):
            sp.dma_start(v[0:1, :], core.dram["lam"]).then_inc(got.sem, 16)

        @block.vector
        def _(dve):
            do = lambda ins: core.vec.do(dve, ins)
            dve.wait_ge(got.sem, got.at(1))
            do(dve.tensor_tensor(pr[0:1].rearrange("p a b -> p (a b)"), v[0:1, 0:128], v[0:1, 128:256], ALU.mult))
            dve.tensor_reduce(s[0:1, 0:2], pr[0:1], AX, ALU.add).then_inc(sums.sem, 1)
            dve.wait_ge(exps.sem, exps.at(1))
            do(dve.tensor_tensor(s[0:1, 4:5], s[0:1, 3:4], s[0:1, 2:3], ALU.subtract))
            dve.tensor_scalar(s[0:1, 5:6], s[0:1, 4:5], -init, None, ALU.add).then_inc(lam.sem, 1)
            dve.wait_ge(spread.sem, spread.at(1))
            do(dve.tensor_copy(neg_lam, core.ps[:, 0, 0:1]))
            do(dve.tensor_scalar(core.p("subln_df"), core.p("subln_df"), 1.0 - init, None, ALU.mult))
            do(dve.tensor_scalar(core.p("q_norm_sp"), core.p("q_norm_sp"), 0.125, None, ALU.mult))
            do(dve.tensor_scalar(core.p("q_norm_df"), core.p("q_norm_df"), 0.125, None, ALU.mult))

        @block.scalar
        def _(act):
            act.wait_ge(sums.sem, sums.at(1))
            act.activation(s[0:1, 2:4], s[0:1, 0:2], ACT.Exp).then_inc(exps.sem, 1)

        @block.tensor
        def _(pe):
            pe.wait_ge(lam.sem, lam.at(1))
            pe.matmul(core.ps[:, 0, 0:1], core.c("ones")[0:1, :], s[0:1, 5:6], start=True, stop=True).then_inc(spread.sem, 1)
    for x in (got, sums, exps, lam, spread):
        x.passed(1)


def scale_tiles(core, tiles, factor):
    with core.nc.Block() as block:
        @block.vector
        def _(dve):
            for a in tiles:
                dve.tensor_scalar(a, a, factor, None, ALU.mult)



def merge_branches(core, G, merged, T, tmp):
    branch, branch_used, merge = (core.sig(n) for n in ("branch", "branch_used", "merge_step"))
    m = core.area(tmp, 2, T)
    cuts = [(0, 2), (2, 4), (4, 8)]
    parts = lambda a: a.rearrange("p (s n) -> p s n", s=2)

    with core.nc.Block() as block:
        @block.sync
        def _(sp):
            core.load_units(sp, NC)

        @block.tensor
        def _(pe):
            def body(i, j):
                t = 4 * i + j
                s = core.taken + j
                pe.wait_ge(core.split_done, s + 1 + i * 4)
                wh, wl = core.wh[:, s % 2], core.wl[:, s % 2]
                for b, (lo, hi) in enumerate(cuts):
                    if not isinstance(t, int) or 3 * t + b >= 2:
                        pe.wait_ge(branch_used.sem, branch_used.at(3 * t + b - 1))
                    for k in range(lo, hi):
                        for n, (w, x) in enumerate(((wh, core.xh), (wh, core.xl), (wl, core.xh))):
                            for e, (o, c) in enumerate(halves(T)):
                                last = pe.matmul(core.ps[:, out_slot(3 * j + b) + e, 0:c], w[:, k, :], x[:, k, o:o + c],
                                                 start=(k == lo and n == 0), stop=(k == hi - 1 and n == 2))
                    if b < 2:
                        last.then_inc(branch.sem, 1)
                last.then_inc(core.used, 1)
            tile_loop(pe, NC, 4, body)

        @block.scalar
        def _(act):
            core.split_first(act, core.split_hi)
            tile_loop(act, NC, 4, lambda i, j: core.split_hi(act, j, i, 4))

        @block.vector
        def _(dve):
            core.split_first(dve, core.split_lo)

            def gate(b, t):
                return tile_of(G, b * NC + t, T)

            def body(i, j):
                t = 4 * i + j
                out = tile_of(merged, t, T)
                for b in range(3):
                    if b < 2:
                        dve.wait_ge(branch.sem, branch.at(2 * t + b + 1))
                    else:
                        dve.wait_ge(core.used, core.taken + j + 1 + i * 4)
                    to = out if b == 0 else parts(m[:, b - 1])
                    dve.tensor_tensor(to, banks(core, out_slot(3 * j + b), T), gate(b, t),
                                      ALU.mult).then_inc(branch_used.sem, 1)
                    dve.wait_ge(branch_used.sem, branch_used.at(3 * t + b + 1))
                    if b:
                        dve.tensor_tensor(out, out, to, ALU.add).then_inc(merge.sem, 1)
                        dve.wait_ge(merge.sem, merge.at(2 * t + b))
                core.split_lo(dve, j, i, 4)
            tile_loop(dve, NC, 4, body)
    branch.passed(2 * NC), branch_used.passed(3 * NC), merge.passed(2 * NC)
    core.finished(NC)


def first_block(core, stop=None):
    T = T1
    P1 = core.area(0, N1, T)
    at = N1 * T
    strips = core.area(at, 8, STRIP)
    at += 8 * STRIP
    VT = core.area(at, 5, 8, P)
    at += 40 * P
    Y = core.area(at, NC, T)
    at += NC * T
    neg_lam = core.area(at, 1)
    tmp = TAIL
    after = N1 * T + 8 * STRIP
    core.open_inputs()
    difference_weight(core, neg_lam, after)
    bias_strips(core, strips, after)
    core.open_weights(N1)
    sum_squares(core, T, after)
    project(core, N1, P1, T, x=layer_norm_input(core, "attn_norm", T, after))
    core.close()
    core.open_tail(SMALL_TAIL)

    to_tokens(core, [([P1[:, SB_V, :], P1[:, SB_V + 1, :], P1[:, SP_V, :], P1[:, SP_V + 1, :]],
                      lambda j: VT[:, j, 0:4].rearrange("p a b -> p (a b)")),
                     ([P1[:, DF_V + t, :] for t in range(4)],
                      lambda j: VT[:, j, 4:8].rearrange("p a b -> p (a b)"))], T)
    normed = [(SP_Q, 2, "q_norm_sp"), (SP_K, 2, "k_norm_sp"), (DF_Q, 4, "q_norm_df"), (DF_K, 4, "k_norm_df")]
    head_norm(core, [(P1[:, a + t, :], P1[:, a + t, :], core.p(g)) for a, n, g in normed for t in range(n)], T, 1.0 / 64, tmp)
    scale_tiles(core, [P1[:, SB_Q + t, :] for t in range(2)], 0.125)

    kx = P1[:, SB_V, :]
    spots = {i: P1[:, DF_V + i - 1, :] for i in range(1, 5)}
    choose_keys(core, P1, kx, lambda i: spots[i], tmp)

    def half(t, h):
        lo = 64 * (h % 2)
        return lambda base: P1[lo:lo + 64, base + h // 2, :]

    def values(v, lo, n):
        return lambda j, w: VT[0:w, j, v, lo:lo + n]

    sb = [Head([(half(0, h)(SB_Q), half(0, h)(SB_K))], values(h // 2, 64 * (h % 2), 64), (64 * (h % 2), 64, Y[:, h // 2, :]))
          for h in range(4)]
    attention(core, "stick", sb, T, tmp)
    sp_ = [Head([(half(0, h)(SP_Q), half(0, h)(SP_K))], values(2 + h // 2, 64 * (h % 2), 64),
                (64 * (h % 2), 64, Y[:, 2 + h // 2, :]), strips[:, h, :], lambda i: spots[i]) for h in range(4)]
    attention(core, "soft", sp_, T, tmp)
    df = [Head([(P1[lo:lo + 64, DF_Q + h, :], P1[lo:lo + 64, DF_K + h, :]) for lo in (0, 64)], values(4 + h, 0, P),
               (0, P, Y[:, 4 + h, :]), strips[:, 4 + h, :]) for h in range(4)]
    attention(core, "diff", df, T, tmp, neg_lam)
    norm(core, [([Y[:, 4 + h, :]], [Y[:, 4 + h, :]], [core.p("subln_df")], None) for h in range(4)], T, 1.0 / P, tmp)
    if stop == "Y":
        return Y, P1, spots

    core.inner.close()
    core.open_weights(RAW0 - N1)
    G, merged = core.area(0, 3 * NC, T), core.area(3 * NC * T, NC, T)
    project(core, 3 * NC, G, T, ACT.Sigmoid, "b_gate")
    split_input(core, [Y[:, k] for k in range(NC)], T)
    merge_branches(core, G, merged, T, 4 * NC * T)
    add_product(core, NC, merged, T, 4 * NC * T)
    feed_forward(core, T, "ffn_norm", "conv_w", "conv_b", META)


def feed_forward(core, T, gain, conv_w, conv_b, skip=0):
    hidden = core.area(0, FT, T)
    tmp = FT * T
    tmp2 = tmp + 8 * T + 8
    conv_glu_up(core, layer_norm_input(core, gain, T, tmp2), hidden, tmp, T, conv_w, conv_b)
    add_product(core, FT, hidden, T, tmp, skip=skip)


def load_constants(core, names, dram, area):
    got = core.sig("constants", 16)
    with core.nc.Block() as block:
        @block.sync
        def _(sp):
            sp.dma_start(area, core.dram[dram]).then_inc(got.sem, 16)
            sp.wait_ge(got.sem, got.at(1))
    got.passed(1)
    core.place(names, area)


def compress(core, P2, KC, VC, tmp):
    got, blocks, hidden, act_out, out, kept = (core.sig(n, u) for n, u in (
        ("cmp_loaded", 16), ("cmp_blocks", 1), ("cmp_hidden", 1), ("cmp_gelu", 1), ("cmp_out", 1), ("cmp_kept", 1)))
    w1 = core.area(tmp, 2, 16, 256)
    w2 = core.area(tmp + 8192, 2, 2, 64)
    pos = core.area(tmp + 8448, 2, 16)
    X = core.area(tmp + 8480, 2, 16, 2 * NCMP)
    H = core.area(tmp + 8480 + 64 * NCMP, 2, 2, 2 * NCMP)
    with core.nc.Block() as block:
        @block.sync
        def _(sp):
            for e in range(2):
                sp.dma_start(w1[:, e].rearrange("p a b -> p (a b)"), core.dram["cmp_w1"][e]).then_inc(got.sem, 16)
            sp.dma_start(w2.rearrange("p a b c -> p (a b c)"), core.dram["cmp_w2"]).then_inc(got.sem, 16)
            sp.dma_start(pos.rearrange("p a b -> p (a b)"), core.dram["cmp_pos"]).then_inc(got.sem, 16)

        @block.vector
        def _(dve):
            for e in range(2):
                for g in range(2):
                    v = P2[64 * g:64 * g + 64, NKC + e, :].rearrange("p (n l two) -> p two l n", l=8, two=2)
                    for half in range(2):
                        for late in range(2):
                            ins = dve.tensor_copy(
                                X[64 * half:64 * half + 64, e, 8 * late:8 * late + 8, g * NCMP:(g + 1) * NCMP],
                                v[:, half, :, late:late + NCMP])
                core.vec.do(dve, ins)
            dve.wait_ge(got.sem, got.at(4))
            for e in range(2):
                dve.tensor_tensor(X[:, e], X[:, e], pos[:, e].unsqueeze(2).broadcast_to([P, 16, 2 * NCMP]),
                                  ALU.add).then_inc(blocks.sem, 1)
            dve.wait_ge(out.sem, out.at(1))
            dve.tensor_copy(KC, core.ps[:, 4, 0:2 * NCMP]).then_inc(kept.sem, 1)
            dve.tensor_copy(VC[0:NCMP], core.ps[0:NCMP, 5, 0:P].rearrange("p (a b) -> p a b", a=2)).then_inc(kept.sem, 1)

        @block.tensor
        def _(pe):
            pe.wait_ge(got.sem, got.at(4))
            for e in range(2):
                pe.wait_ge(blocks.sem, blocks.at(e + 1))
                for c in range(2):
                    for l in range(16):
                        last = pe.matmul(core.ps[:, 2 * e + c, 0:2 * NCMP], w1[:, e, l, c * P:(c + 1) * P], X[:, e, l],
                                         start=(l == 0), stop=(l == 15))
                    last.then_inc(hidden.sem, 1)
            pe.wait_ge(act_out.sem, act_out.at(4))
            for lo in (0, 64):
                for c in range(2):
                    pe.matmul(core.ps[lo:lo + 64, 4, 0:2 * NCMP], w2[:, 0, c], H[:, 0, c], start=(c == 0), stop=(c == 1))
            for g in range(2):
                for c in range(2):
                    last = pe.matmul(core.ps[0:NCMP, 5, 64 * g:64 * g + 64], H[:, 1, c, g * NCMP:(g + 1) * NCMP], w2[:, 1, c],
                                     start=(c == 0), stop=(c == 1))
            last.then_inc(out.sem, 1)

        @block.scalar
        def _(act):
            for n in range(4):
                act.wait_ge(hidden.sem, hidden.at(n + 1))
                act.activation(H[:, n // 2, n % 2], core.ps[:, n, 0:2 * NCMP], ACT.Gelu_apprx_tanh).then_inc(act_out.sem, 1)
    got.passed(4), blocks.passed(2), hidden.passed(4), act_out.passed(4), out.passed(1), kept.passed(2)


def compressed_attention(core, P2, KC, VC, OC, tmp):
    scores, shifted, exps, probs, turned, pt, out, kept = (core.sig(n) for n in (
        "cmp_scores", "cmp_shifted", "cmp_exps", "cmp_probs", "cmp_turned", "cmp_pt", "cmp_weighed", "cmp_copied"))
    X = core.area(tmp, 24, NCMP)
    st = core.area(tmp + 24 * NCMP, 2, 24)
    PT = core.area(tmp + 24 * NCMP + 48, 2, 6 * P)
    wide = [P, 24, NCMP]
    with core.nc.Block() as block:
        @block.tensor
        def _(pe):
            for i in range(4):
                for h in range(6):
                    lo, g = 64 * (h % 2), h // 3
                    o = h // 2 * NCMP
                    last = pe.matmul(core.ps[:, 4 * (h % 2) + i, o:o + NCMP], P2[lo:lo + 64, NQ + h // 2, i * P:(i + 1) * P],
                                     KC[lo:lo + 64, g * NCMP:(g + 1) * NCMP], start=True, stop=True)
            last.then_inc(scores.sem, 1)
            pe.wait_ge(probs.sem, probs.at(1))
            for i in range(4):
                if i >= 1:
                    pe.wait_ge(pt.sem, pt.at(i))
                for h in range(6):
                    last = pe.transpose(core.flat[0:NCMP, 2048 + h * P:2048 + (h + 1) * P], X[:, i * 6 + h % 2 * 3 + h // 2], core.c("ident"))
                last.then_inc(turned.sem, 1)
                pe.wait_ge(pt.sem, pt.at(i + 1))
                if i >= 2:
                    pe.wait_ge(kept.sem, kept.at(i - 1))
                for h in range(6):
                    lo, g = 64 * (h % 2), h // 3
                    last = pe.matmul(core.ps[lo:lo + 64, 6 + i % 2, h // 2 * P:(h // 2 + 1) * P], VC[0:NCMP, g],
                                     PT[0:NCMP, i % 2, h * P:(h + 1) * P], start=True, stop=True)
                last.then_inc(out.sem, 1)

        @block.vector
        def _(dve):
            do = lambda ins: core.vec.do(dve, ins)
            dve.wait_ge(scores.sem, scores.at(1))
            for odd in range(2):
                ins = dve.tensor_tensor(X.rearrange("p (a o b) c -> p a o (b c)", a=4, o=2)[:, :, odd],
                                        core.ps[:, 4 * odd:4 * odd + 4, 0:3 * NCMP],
                                        core.c("cmp_bias").rearrange("p (a o b) -> p a o b", a=4, o=2)[:, :, odd], ALU.add)
            do(ins)
            do(dve.tensor_reduce(st[:, 0], X, AX, ALU.max))
            dve.tensor_tensor(X, X, st[:, 0].unsqueeze(2).broadcast_to(wide), ALU.subtract).then_inc(shifted.sem, 1)
            dve.wait_ge(exps.sem, exps.at(1))
            do(dve.tensor_tensor(X, X, core.c("cmp_keep").rearrange("p (a b) -> p a b", a=24), ALU.mult))
            do(dve.tensor_reduce(st[:, 1], X, AX, ALU.add))
            do(dve.tensor_scalar(st[:, 1], st[:, 1], 1e-30, None, ALU.max))
            do(dve.reciprocal(st[:, 1], st[:, 1]))
            dve.tensor_tensor(X, X, st[:, 1].unsqueeze(2).broadcast_to(wide), ALU.mult).then_inc(probs.sem, 1)
            for i in range(4):
                dve.wait_ge(out.sem, out.at(i + 1))
                dve.tensor_copy(OC[:, :, i * P:(i + 1) * P],
                                core.ps[:, 6 + i % 2, 0:3 * P].rearrange("p (a b) -> p a b", a=3)).then_inc(kept.sem, 1)

        @block.scalar
        def _(act):
            act.wait_ge(shifted.sem, shifted.at(1))
            act.activation(X, X, ACT.Exp).then_inc(exps.sem, 1)
            for i in range(4):
                act.wait_ge(turned.sem, turned.at(i + 1))
                if i >= 2:
                    act.wait_ge(out.sem, out.at(i - 1))
                act.activation(PT[0:NCMP, i % 2], core.flat[0:NCMP, 2048:2048 + 6 * P], ACT.Copy).then_inc(pt.sem, 1)
    for x in (scores, shifted, exps, probs):
        x.passed(1)
    for x in (turned, pt, out, kept):
        x.passed(4)


def cross_keys(core, P2, KX):
    with core.nc.Block() as block:
        @block.gpsimd
        def _(pool):
            for e, t in enumerate((NKS, NKW)):
                for g in range(2):
                    core.pool.do(pool, pool.tensor_copy(KX[64 - 64 * g:128 - 64 * g, e], P2[64 * g:64 * g + 64, t, :]))


def gate_branches(core, P2, branches, tmp):
    sig, spread, used = core.sig("nsa_gates"), core.sig("nsa_spread"), core.sig("nsa_spread_used")
    g = core.area(tmp, SEQ)
    with core.nc.Block() as block:
        @block.scalar
        def _(act):
            act.activation(g[0:18], P2[0:18, NG, :], ACT.Sigmoid).then_inc(sig.sem, 1)

        @block.tensor
        def _(pe):
            pe.wait_ge(sig.sem, sig.at(1))
            for n in range(9):
                if n >= 4:
                    pe.wait_ge(used.sem, used.at(n - 3))
                pe.matmul(core.ps[:, n % 4, :], core.c("gates")[0:18, n * P:(n + 1) * P], g[0:18], start=True,
                          stop=True).then_inc(spread.sem, 1)

        @block.vector
        def _(dve):
            for n in range(9):
                b, t = n // 3, n % 3
                dve.wait_ge(spread.sem, spread.at(n + 1))
                a = branches[b][:, t]
                dve.tensor_tensor(a, core.ps[:, n % 4, :], a, ALU.mult).then_inc(used.sem, 1)
                if b:
                    dve.wait_ge(used.sem, used.at(n + 1))
                    o = branches[0][:, t]
                    core.vec.do(dve, dve.tensor_tensor(o, o, a, ALU.add))
    sig.passed(1), spread.passed(9), used.passed(9)


def center(core, items, T, inv_n, ones):
    total, gone = core.sig("mean_ready"), core.sig("mean_used")
    with core.nc.Block() as block:
        @block.tensor
        def _(pe):
            for n, x in enumerate(items):
                if n >= 2:
                    pe.wait_ge(gone.sem, gone.at(n - 1))
                for k, a in enumerate(x):
                    last = pe.matmul(core.ps[:, n % 2, 0:T], core.c(ones), a, start=(k == 0), stop=(k == len(x) - 1))
                last.then_inc(total.sem, 1)

        @block.vector
        def _(dve):
            for n, x in enumerate(items):
                dve.wait_ge(total.sem, total.at(n + 1))
                for k, a in enumerate(x):
                    ins = dve.scalar_tensor_tensor(out=a, in0=core.ps[:, n % 2, 0:T], scalar=-inv_n, in1=a, op0=ALU.mult,
                                                   op1=ALU.add)
                ins.then_inc(gone.sem, 1)
    total.passed(len(items)), gone.passed(len(items))


def rwkv_prepare(core, R, K, V, L, A, G, KK, AR, B, KP, CE, bonus, tmp):
    got, up, lora, lora_used, decays, exps, sums, done = (core.sig(n, u) for n, u in (
        ("lora_loaded", 16), ("lora_in", 1), ("lora_out", 1), ("lora_used", 1), ("decay_sums", 1), ("decay_exps", 1),
        ("bonus_sum", 1), ("rwkv_ready", 1)))
    w = core.area(tmp, 256)
    LW = core.area(tmp + 256, 2, SEQ)
    CL = core.area(tmp + 256 + 1024, 2, SEQ)
    E = core.area(tmp + 256 + 2048, 3, 2, SEQ)
    D_ = core.area(tmp + 256 + 2048 + 3072, SEQ)
    tiles = [(R, 0), (R, 1), (K, 0), (K, 1), (V, 0), (V, 1), (L, 0)]
    with core.nc.Block() as block:
        @block.sync
        def _(sp):
            sp.dma_start(w, core.dram["lora"]).then_inc(got.sem, 16)

        @block.vector
        def _(dve):
            do = lambda ins: core.vec.do(dve, ins)
            for n in [6, 0, 1, 2, 3, 4, 5]:
                a, t = tiles[n]
                x = a[:, t]
                do(dve.tensor_scalar(D_[:, 0:1], x[:, 0:1], -1.0, None, ALU.mult))
                do(dve.tensor_tensor(D_[:, 1:], x[:, :-1], x[:, 1:], ALU.subtract))
                ins = dve.scalar_tensor_tensor(out=x, in0=D_, scalar=core.p("rw_mu_2", n), in1=x, op0=ALU.mult, op1=ALU.add)
                if n == 6:
                    ins.then_inc(up.sem, 1)
                    dve.wait_ge(up.sem, up.at(1))
                else:
                    do(ins)
            for t in range(2):
                dve.wait_ge(lora_used.sem, lora_used.at(t + 1))
                do(dve.tensor_scalar(LW[:, t], LW[:, t], -0.606531, None, ALU.mult))
                do(dve.tensor_tensor_scan(CL[:, t], core.c("restart"), LW[:, t], 0.0, ALU.mult, ALU.add))
                dve.tensor_tensor(LW[:, t], CL[:, t], LW[:, t], ALU.subtract).then_inc(decays.sem, 1)
            dve.wait_ge(lora_used.sem, lora_used.at(4))
            for t in range(2):
                do(dve.tensor_scalar(KK[:, t], K[:, t], core.p("rw_k_k_2", t), None, ALU.mult))
                do(dve.tensor_scalar(D_, A[:, t], 1.0, core.p("rw_k_a_2", t), ALU.subtract, ALU.mult))
                do(dve.scalar_tensor_tensor(out=K[:, t], in0=D_, scalar=1.0, in1=K[:, t], op0=ALU.add, op1=ALU.mult))
                do(dve.scalar_tensor_tensor(out=D_, in0=R[:, t], scalar=core.p("rw_r_k_2", t), in1=K[:, t],
                                            op0=ALU.mult, op1=ALU.mult))
                dve.tensor_copy(bonus[:, t], D_).then_inc(done.sem, 1)
                dve.wait_ge(done.sem, done.at(t + 1))
            for t in range(2):
                dve.wait_ge(sums.sem, sums.at(t + 1))
                do(dve.tensor_tensor(bonus[:, t], core.ps[:, 6 + t, :], V[:, t], ALU.mult))
            dve.wait_ge(exps.sem, exps.at(6))
            for t in range(2):
                c, c0, ic = E[:, 0, t], E[:, 1, t], E[:, 2, t]
                by = lambda a: a.rearrange("p (c t) -> p c t", t=CH)
                do(dve.tensor_tensor(AR[:, t, :, 1], by(c), by(R[:, t]), ALU.mult))
                do(dve.tensor_copy(AR[:, t, :, 0], by(c0)))
                do(dve.tensor_tensor(KP[:, t], ic, K[:, t], ALU.mult))
                do(dve.tensor_tensor(B[:, t], ic, A[:, t], ALU.mult))
                do(dve.tensor_copy(CE[:, t], by(c)[:, :, CH - 1]))

        @block.scalar
        def _(act):
            act.wait_ge(up.sem, up.at(1))
            x = L[:, 0]
            act.activation(x[0:32], x[0:32], ACT.Tanh)
            act.activation(x[64:128], x[64:128], ACT.Sigmoid).then_inc(up.sem, 1)
            for n, (dst, bias) in enumerate([(LW, "rw_w0_2"), (A, "rw_a0_2"), (G, None)]):
                for t in range(2):
                    act.wait_ge(lora.sem, lora.at(2 * n + t + 1))
                    got_ = core.ps[:, 2 * n + t, :]
                    if bias:
                        ins = act.activation(dst[:, t], got_, ACT.Sigmoid, bias=core.p(bias, t))
                    else:
                        ins = act.activation(dst[:, t], got_, ACT.Copy)
                    ins.then_inc(lora_used.sem, 1)
            for t in range(2):
                act.wait_ge(decays.sem, decays.at(t + 1))
                act.activation(E[:, 0, t], CL[:, t], ACT.Exp).then_inc(exps.sem, 1)
                act.activation(E[:, 1, t], LW[:, t], ACT.Exp).then_inc(exps.sem, 1)
                act.activation(E[:, 2, t], CL[:, t], ACT.Exp, scale=-1.0).then_inc(exps.sem, 1)

        @block.tensor
        def _(pe):
            pe.wait_ge(got.sem, got.at(1))
            pe.wait_ge(up.sem, up.at(2))
            for n, (lo, hi) in enumerate([(0, 32), (32, 64), (64, 128)]):
                for t in range(2):
                    pe.matmul(core.ps[:, 2 * n + t, :], w[lo:hi, t * P:(t + 1) * P], L[lo:hi, 0], start=True,
                              stop=True).then_inc(lora.sem, 1)
            for t in range(2):
                pe.wait_ge(done.sem, done.at(t + 1))
                pe.matmul(core.ps[:, 6 + t, :], core.c("pair64"), bonus[:, t], start=True, stop=True).then_inc(sums.sem, 1)
    got.passed(1), up.passed(2), lora.passed(6), lora_used.passed(6), decays.passed(2), exps.passed(6), sums.passed(2)
    done.passed(2)


def rwkv_factors(core, KK, AR, B):
    with core.nc.Block() as block:
        @block.vector
        def _(dve):
            for t in range(2):
                by = KK[:, t].rearrange("p (c t) -> p c t", t=CH)
                core.vec.do(dve, dve.tensor_tensor(AR[:, t, :, 0], AR[:, t, :, 0], by, ALU.mult))
                core.vec.do(dve, dve.tensor_tensor(B[:, t], B[:, t], KK[:, t], ALU.mult))


def rwkv_matrices(core, V, AR, B, KP, MM, TOK):
    made, used, turned, kept = (core.sig(n) for n in ("chunk_products", "chunk_masked", "chunk_turned", "chunk_kept"))
    NCH = SEQ // CH
    with core.nc.Block() as block:
        @block.tensor
        def _(pe):
            for c in range(NCH):
                if c >= 2:
                    pe.wait_ge(used.sem, used.at(c - 1))
                t0 = c * CH
                for h in range(4):
                    lo, t = 64 * (h % 2), h // 2
                    for e, F in enumerate((B, KP)):
                        o = (t * 2 + e) * 64
                        last = pe.matmul(core.ps[0:CH, 2 * (c % 2) + h % 2, o:o + 64], F[lo:lo + 64, t, t0:t0 + CH],
                                         AR[lo:lo + 64, t, c].rearrange("p a b -> p (a b)"), start=True, stop=True)
                last.then_inc(made.sem, 1)
                if c >= 2:
                    pe.wait_ge(kept.sem, kept.at(c - 1))
                for e, F in enumerate((B, KP, V)):
                    for t in range(2):
                        o = (4 + 2 * (c % 2)) * 512 + e * 256 + t * P
                        last = pe.transpose(core.flat[0:CH, o:o + P], F[:, t, t0:t0 + CH], core.c("ident"))
                last.then_inc(turned.sem, 1)

        @block.vector
        def _(dve):
            for c in range(NCH):
                dve.wait_ge(made.sem, made.at(c + 1))
                two = lambda a: a.rearrange("p (o n) -> p o n", o=2)
                dve.tensor_tensor(two(MM[0:CH, c]), core.ps[0:CH, 2 * (c % 2):2 * (c % 2) + 2, 0:256],
                                  two(core.c("mask32")[0:CH]), ALU.mult).then_inc(used.sem, 1)

        @block.scalar
        def _(act):
            for c in range(NCH):
                act.wait_ge(turned.sem, turned.at(c + 1))
                o = (4 + 2 * (c % 2)) * 512
                for e in range(3):
                    ins = act.activation(TOK[e][0:CH, c], core.flat[0:CH, o + 256 * e:o + 256 * e + 256], ACT.Copy)
                ins.then_inc(kept.sem, 1)
    for x in (made, used, turned, kept):
        x.passed(NCH)


def rwkv_inverse(core, MM, TT, tmp, rd):
    out, back, solved, out2, back2 = (core.sig(n, u) for n, u in (
        ("chunks_stored", 16), ("chunks_back", 16), ("chunks_solved", 1), ("inverse_stored", 16), ("inverse_back", 16)))
    NP = SEQ // CH * 4
    AT = core.area(tmp, CH, CH)
    Yv = core.area(tmp + CH * CH, CH, 16)
    pr = core.area(tmp + CH * CH + CH * 16, 16 * CH)
    a_dram, y_dram = core.dram["chunk_scratch"], core.dram["inverse_scratch"]
    with core.nc.Block() as block:
        @block.sync
        def _(sp):
            m = MM.rearrange("p c (h e f t) -> p c h e f t", h=4, e=2, f=2)
            for c in range(SEQ // CH):
                sp.dma_start(a_dram[4 * c:4 * c + 4].rearrange("n s t -> s n t"), m[0:CH, c, :, 0, 0, :]).then_inc(out.sem, 16)
            sp.wait_ge(out.sem, out.at(SEQ // CH))
            for half in range(2):
                sp.dma_start(AT[64 * half:64 * half + 64].rearrange("p s t -> p (s t)"),
                             a_dram.rearrange("n s t -> n (s t)")).then_inc(back.sem, 16)
            sp.wait_ge(solved.sem, solved.at(1))
            for half in range(2):
                sp.dma_start(y_dram[:, :, 16 * half:16 * half + 16], Yv[64 * half:64 * half + 64]).then_inc(out2.sem, 16)
            sp.wait_ge(out2.sem, out2.at(2))
            sp.dma_start(TT[0:CH], y_dram.rearrange("n s i -> s n i")).then_inc(back2.sem, 16)
            sp.wait_ge(back2.sem, back2.at(1))

        @block.vector
        def _(dve):
            do = lambda ins: core.vec.do(dve, ins)
            do(dve.tensor_copy(Yv.rearrange("p s i -> p (s i)"), core.c("eye16")))
            dve.wait_ge(back.sem, back.at(2))
            for s in range(CH - 2, -1, -1):
                n = CH - 1 - s
                p3 = pr[:, 0:16 * n].rearrange("p (i t) -> p i t", i=16)
                do(dve.tensor_tensor(p3, Yv[:, s + 1:, :].rearrange("p t i -> p i t"),
                                     AT[:, s, s + 1:].unsqueeze(1).broadcast_to([P, 16, n]), ALU.mult))
                do(dve.tensor_reduce(rd, p3, AX, ALU.add))
                ins = dve.tensor_tensor(Yv[:, s, :], Yv[:, s, :], rd, ALU.subtract)
                if s:
                    do(ins)
                else:
                    ins.then_inc(solved.sem, 1)
    out.passed(SEQ // CH), back.passed(2), solved.passed(1), out2.passed(2), back2.passed(1)
    assert NP == 64


def rwkv_chunks(core, AR, MM, TOK, TT, CE, RO, tmp):
    o_ready, x_ready, x_kept, u_ready, u_kept, o_kept, s_ready, s_kept = (core.sig(n) for n in (
        "out_ready", "x_ready", "x_kept", "u_ready", "u_kept", "o_kept", "s_ready", "s_kept"))
    NCH = SEQ // CH
    STATE = core.area(tmp, 2, 2, 64)
    SC = core.area(tmp + 256, 2, 64)
    X = core.area(tmp + 384, 256)
    U = core.area(tmp + 640, 256)
    order = lambda h: h % 2 * 2 + h // 2
    with core.nc.Block() as block:
        @block.tensor
        def _(pe):
            heads = [(64 * (h % 2), h // 2, 64 * h, order(h)) for h in range(4)]
            x_bank = lambda h, t: core.ps[0:CH, h % 2, t * 64:t * 64 + 64]
            parts = lambda c: MM[0:CH, c].rearrange("p (h e f t) -> p h e f t", h=4, e=2, f=2)

            def x_first(c):
                for h, (lo, t, o, r) in enumerate(heads):
                    pe.matmul(x_bank(h, t), parts(c)[:, r, 1, 0], TOK[2][0:CH, c][:, o:o + 64], start=(t == 0), stop=False)

            def out_first(c, some):
                for lo, t, o, r in some:
                    dst = core.ps[lo:lo + 64, 4 + c % 2, t * CH:(t + 1) * CH]
                    pe.matmul(dst, STATE[lo:lo + 64, c % 2, t], AR[lo:lo + 64, t, c, 1], start=(t == 0), stop=False)
                    pe.matmul(dst, TOK[2][0:CH, c][:, o:o + 64], parts(c)[:, r, 1, 1], start=False, stop=False)

            def out_last(c):
                for lo, t, o, r in heads:
                    last = pe.matmul(core.ps[lo:lo + 64, 4 + c % 2, t * CH:(t + 1) * CH], U[0:CH, 64 * r:64 * r + 64],
                                     parts(c)[:, r, 0, 1], start=False, stop=(t == 1))
                last.then_inc(o_ready.sem, 1)

            x_first(0)
            for c in range(NCH):
                tok, ST = [a[0:CH, c] for a in TOK], STATE[:, c % 2]
                pe.wait_ge(s_kept.sem, s_kept.at(c + 1))
                for h, (lo, t, o, r) in enumerate(heads):
                    last = pe.matmul(x_bank(h, t), AR[lo:lo + 64, t, c, 0], ST[lo:lo + 64, t], start=False, stop=(t == 1))
                last.then_inc(x_ready.sem, 1)
                if c:
                    out_last(c - 1)
                s_bank = lambda lo, t: core.ps[lo:lo + 64, 2, t * 64:t * 64 + 64]
                pe.wait_ge(x_kept.sem, x_kept.at(c + 1))
                for lo, t, o, r in heads:
                    last = pe.matmul(core.ps[0:CH, 3, 64 * r:64 * r + 64], TT[0:CH, 4 * c + r], X[0:CH, 64 * r:64 * r + 64],
                                     start=True, stop=True)
                last.then_inc(u_ready.sem, 1)
                for lo, t, o, r in heads:
                    pe.matmul(s_bank(lo, t), tok[1][:, o:o + 64], tok[2][:, o:o + 64], start=(t == 0), stop=False)
                if c >= 2:
                    pe.wait_ge(o_kept.sem, o_kept.at(c - 1))
                out_first(c, heads[0:2])
                pe.wait_ge(u_kept.sem, u_kept.at(c + 1))
                for lo, t, o, r in heads:
                    last = pe.matmul(s_bank(lo, t), tok[0][:, o:o + 64], U[0:CH, 64 * r:64 * r + 64], start=False, stop=(t == 1))
                last.then_inc(s_ready.sem, 1)
                out_first(c, heads[2:4])
                if c + 1 < NCH:
                    x_first(c + 1)
            out_last(NCH - 1)

        @block.vector
        def _(dve):
            do = lambda ins: core.vec.do(dve, ins)
            dve.memset(STATE[:, 0], 0.0).then_inc(s_kept.sem, 1)
            dve.wait_ge(s_kept.sem, s_kept.at(1))
            for c in range(NCH):
                ST, new = STATE[:, c % 2], STATE[:, (c + 1) % 2]
                for t in range(2):
                    ins = dve.tensor_scalar(SC[:, t], ST[:, t], CE[:, t, c:c + 1], None, ALU.mult)
                do(ins)
                dve.wait_ge(x_ready.sem, x_ready.at(c + 1))
                dve.tensor_scalar(X[0:CH].rearrange("p (o n) -> p o n", o=2), core.ps[0:CH, 0:2, 0:128], -1.0, None, ALU.mult).then_inc(x_kept.sem, 1)
                dve.wait_ge(u_ready.sem, u_ready.at(c + 1))
                dve.tensor_copy(U[0:CH], core.ps[0:CH, 3, 0:256]).then_inc(u_kept.sem, 1)
                dve.wait_ge(s_ready.sem, s_ready.at(c + 1))
                for t in range(2):
                    ins = dve.scalar_tensor_tensor(out=new[:, t], in0=core.ps[:, 2, t * 64:t * 64 + 64], scalar=CE[:, t, c:c + 1],
                                                   in1=SC[:, t], op0=ALU.mult, op1=ALU.add)
                ins.then_inc(s_kept.sem, 1)
                dve.wait_ge(s_kept.sem, s_kept.at(c + 2))

        @block.scalar
        def _(act):
            for c in range(NCH):
                act.wait_ge(o_ready.sem, o_ready.at(c + 1))
                act.activation(RO[:, :, c * CH:(c + 1) * CH], core.ps[:, 4 + c % 2, 0:2 * CH].rearrange("p (a b) -> p a b", a=2),
                               ACT.Copy).then_inc(o_kept.sem, 1)
    s_kept.passed(NCH + 1)
    for x in (x_ready, x_kept, u_ready, u_kept, o_kept, s_ready, o_ready):
        x.passed(NCH)


def second_block(core, stop=None):
    T = SEQ
    P2 = core.area(0, N2, T)
    at = N2 * T
    Y = core.area(at, NC, T)
    at += NC * T
    VT = core.area(at, 4, 5, P)
    at += 20 * P
    KX = core.area(at, 2, T)
    OC, OS = core.area(at + 2 * T, 3, T), core.area(at + 5 * T, 3, T)
    KC, VC = core.area(at + 8 * T, 2 * NCMP), core.area(at + 8 * T + 2 * NCMP, 2, 64)
    late = at + 8 * T + 2 * NCMP + P
    nsa = sum(m for _, m in NSA_CONSTS)
    tmp = TAIL
    core.h = core.h_all[:, :, META:META + SEQ]
    project(core, N2, P2, T, x=layer_norm_input(core, "attn_norm_2", T, late))
    core.close(inputs=True)
    core.open_tail(SMALL_TAIL + 2 * NC * T1)
    to_tokens(core, [([P2[:, t, :] for t in (NVS, NVW, MV, MV + 1)], lambda j: VT[:, j, 0:4].rearrange("p a b -> p (a b)")),
                     ([P2[:, MV + 2, :]], lambda j: VT[:, j, 4])], T)
    scale_tiles(core, [P2[:, t, :] for t in (NQ, NQ + 1, NQ + 2, MQ, MQ + 1, MQ + 2)], 0.125)
    compress(core, P2, KC, VC, TAIL)
    load_constants(core, NSA_CONSTS, "nsa_consts", core.area(late, nsa))
    cross_keys(core, P2, KX)
    compressed_attention(core, P2, KC, VC, OC, tmp)
    causal = core.c("causal")
    side = Modulation(core, core.area(TAIL + SMALL_TAIL, D))
    side.load()

    def values(v, lo):
        return lambda j, w: VT[0:w, j, v, lo:lo + 64]

    for e, (kt, out) in enumerate(((NKS, OS), (NKW, Y))):
        heads = []
        for h in range(6):
            lo, g = 64 * (h % 2), h // 3
            k = P2[lo:lo + 64, kt, :] if h % 2 == g else KX[lo:lo + 64, e]
            heads.append(Head([(P2[lo:lo + 64, NQ + h // 2, :], k)], values(e, 64 * g), (lo, 64, out[:, h // 2]), causal))
        attention(core, "soft", heads, T, tmp, beside=side)
    gate_branches(core, P2, [OC, OS, Y], tmp)
    heads = []
    for h in range(6):
        lo = 64 * (h % 2)
        heads.append(Head([(P2[lo:lo + 64, MQ + h // 2, :], P2[lo:lo + 64, MK + h // 2, :])], values(2 + h // 2, lo),
                          (lo, 64, Y[:, 5 + h // 2]), causal))
    attention(core, "soft", heads, T, tmp)
    head_norm(core, [(OC[:, t], Y[:, t], core.p("nsa_out_gain_2", t)) for t in range(3)]
              + [(Y[:, 5 + t], Y[:, 5 + t], core.p("moba_out_gain_2", t)) for t in range(3)], T, 1.0 / 64, tmp)

    R, K, V, L = (P2[:, a:b, :] for a, b in ((RR, RR + 2), (RK, RK + 2), (RV, RV + 2), (RL, RL + 1)))
    A, KK, G, B, KP = (core.area(i * 2 * T, 2, T) for i in range(5))
    at = (N2 + NC) * T
    bonus = core.area(at, 2, T)
    RO = core.area(at + 2 * T, 2, T)
    AR = core.area(at + 4 * T, 2, SEQ // CH, 2, CH)
    MM = core.area(TAIL, SEQ // CH, 512)
    tmp = at + 8 * T
    late = tmp + 8 * T
    end = late + 3 * 512
    spare = core.area(TAIL + 16 * 512, 4144)
    TOK = [core.area((RL + 1) * T, SEQ // CH, 256), core.area(tmp, SEQ // CH, 256),
           spare[:, 0:16 * 256].rearrange("p (c n) -> p c n", n=256)]
    CE = spare[:, 4096:4096 + 32].rearrange("p (a b) -> p a b", a=2)
    rd = spare[:, 4128:4144]
    TT = core.area(0, SEQ // CH * 4, CH)
    load_constants(core, RWKV_CONSTS, "rwkv_consts", core.area(late, end - late))
    rwkv_prepare(core, R, K, V, L, A, G, KK, AR, B, KP, CE, bonus, TAIL)
    norm(core, [([KK[:, t]], [KK[:, t]], None, None) for t in range(2)], T, 1.0, tmp, eps="zero", ones="pair64", least=1e-12)
    rwkv_factors(core, KK, AR, B)
    rwkv_matrices(core, V, AR, B, KP, MM, TOK)
    rwkv_inverse(core, MM, TT, 6 * T, rd)
    rwkv_chunks(core, AR, MM, TOK, TT, CE, RO, end)
    center(core, [[RO[:, t]] for t in range(2)], T, 1.0 / 64, "pair64")
    norm(core, [([RO[:, t]], [RO[:, t]], [core.p("rw_lnx_w_2", t)], [core.p("rw_lnx_b_2", t)]) for t in range(2)], T, 1.0 / 64,
         tmp, eps="eps_rw", ones="pair64")
    rwkv_output(core, RO, bonus, G, Y[:, 3:5, :])
    if stop == "Y":
        return Y
    core.inner.close()
    core.open_inputs()
    core.open_weights(core.total - RAW - core.taken)
    add_product(core, NC, Y, T, 0)
    feed_forward(core, T, "ffn_norm_2", "ffn_conv_w_2", "ffn_conv_b_2")
    renorm(core, [core.p("final_norm_2", k) for k in range(NC)], T, 0)


def rwkv_output(core, RO, bonus, G, Y):
    with core.nc.Block() as block:
        @block.vector
        def _(dve):
            core.vec.do(dve, dve.tensor_tensor(RO, RO, bonus, ALU.add))
            dve.tensor_tensor(Y, RO, G, ALU.mult)


class Modulation:

    def __init__(self, core, spread):
        self.core, self.spread = core, spread
        self.product = core.sig("modulation_product")

    def load(self):
        core, got = self.core, self.core.sig("c_loaded", 16)
        with core.nc.Block() as block:
            @block.sync
            def _(sp):
                sp.dma_start(self.spread, core.dram["c"].broadcast_to([P, D])).then_inc(got.sem, 16)

            @block.scalar
            def _(act):
                act.wait_ge(got.sem, got.at(1))
                act.activation(self.spread, self.spread, ACT.Silu)
        got.passed(1)

    def multiply(self, pool, s):
        core, u = self.core, self.core.stream + s
        w = core.ring[:, u % RING].rearrange("p c n -> p (c n)")
        pool.wait_ge(core.arrived[u % RING], 16 * (u // RING + 1))
        pool.tensor_tensor(w, w, self.spread, ALU.mult).then_inc(self.product.sem, 1)

    def sum(self, act, s):
        core, u = self.core, self.core.stream + s
        w = core.ring[:, u % RING].rearrange("p c n -> p (c n)")
        act.wait_ge(self.product.sem, self.product.at(s + 1))
        act.activation(w, w, ACT.Copy, accum_out=core.mod[:, u - RAW0:u - RAW0 + 1]).then_inc(core.raw_used, 1)

    def passed(self, n):
        self.core.stream += n
        self.product.passed(n)


def scale_columns(core):
    mod = core.mod[:, :]
    with core.nc.Block() as block:
        @block.vector
        def _(dve):
            b = PCOL["b_ada_3"]
            core.vec.do(dve, dve.tensor_tensor(mod, mod, core.par[:, b:b + RAW], ALU.add))
            for at, name in ((NC, "norm1_g_3"), (4 * NC, "norm2_g_3")):
                g = PCOL[name]
                dve.scalar_tensor_tensor(out=mod[:, at:at + NC], in0=mod[:, at:at + NC], scalar=1.0,
                                         in1=core.par[:, g:g + NC], op0=ALU.add, op1=ALU.mult)


def mix_tokens(core, VT, MX, tmp):
    got, ready, mixed, kept = (core.sig(n, u) for n, u in (("ws_loaded", 16), ("ws_masked", 1), ("mixed", 1), ("mixed_kept", 1)))
    WS = core.area(tmp, NC, P)
    BS = core.area(tmp + NC * P, NC, P)
    with core.nc.Block() as block:
        @block.sync
        def _(sp):
            sp.dma_start(WS.rearrange("p a b -> p (a b)"), core.dram["gmlp_ws"]).then_inc(got.sem, 16)
            sp.dma_start(BS[0:1].rearrange("p a b -> p (a b)"), core.dram["gmlp_bs"]).then_inc(got.sem, 16)

        @block.vector
        def _(dve):
            dve.wait_ge(got.sem, got.at(2))
            dve.memset(WS[64:128, :, 0:64], 0.0).then_inc(ready.sem, 1)

        @block.tensor
        def _(pe):
            pe.wait_ge(ready.sem, ready.at(1))
            for g in range(NC):
                if g >= 2:
                    pe.wait_ge(kept.sem, kept.at(g - 1))
                for n in range(4):
                    dst = core.ps[:, g % 2, n * P:(n + 1) * P]
                    pe.matmul(dst, VT[:, n, g], WS[:, g], start=True, stop=False)
                    last = pe.matmul(dst, core.c("ones")[0:1, :], BS[0:1, g], start=False, stop=True)
                last.then_inc(mixed.sem, 1)

        @block.scalar
        def _(act):
            for g in range(NC):
                act.wait_ge(mixed.sem, mixed.at(g + 1))
                act.activation(MX[:, g], core.ps[:, g % 2, :], ACT.Copy).then_inc(kept.sem, 1)
    got.passed(2), ready.passed(1), mixed.passed(NC), kept.passed(NC)


def project_conv(core, n, dst, tmp):
    T = SEQ
    copied, conv, act_out = core.sig("tile_free"), core.sig("conv_out"), core.sig("silu_out")
    pad = core.area(tmp, 2, T + 3)
    mid = core.area(tmp + 2 * (T + 3), 2, 2, T)
    step = core.vec
    with core.nc.Block() as block:
        @block.sync
        def _(sp):
            core.load_units(sp, n)

        @block.tensor
        def _(pe):
            gemm(core, pe, n, 4, T, copied)

        @block.scalar
        def _(act):
            core.split_first(act, core.split_hi)
            core.act.do(act, act.activation(pad[:, :, 0:3], core.c("ones", 6).rearrange("p (b n) -> p b n", b=2),
                                            ACT.Copy, scale=0.0))

            def body(i, j):
                t = i * 4 + j
                tile_done(core, act, i, j, 4)
                core.split_hi(act, j, i, 4)
                if not isinstance(t, int) or t >= 2:
                    act.wait_ge(conv.sem, conv.at(t - 1))
                act.activation(pad[:, j % 2, 3:], core.ps[:, out_slot(j), :], ACT.Copy).then_inc(copied.sem, 1)
                act.wait_ge(conv.sem, conv.at(t + 1))
                out = dst[:, t] if isinstance(t, int) else dst[:, bass.ds(t, 1)].rearrange("p o n -> p (o n)")
                act.activation(out, mid[:, j % 2, 1], ACT.Silu).then_inc(act_out.sem, 1)
            tile_loop(act, n, 4, body)

        @block.vector
        def _(dve):
            base = step.value
            core.split_first(dve, core.split_lo)

            def body(i, j):
                t = i * 4 + j
                core.split_lo(dve, j, i, 4)
                x, y, z = pad[:, j % 2], mid[:, j % 2, 0], mid[:, j % 2, 1]

                def ordered(k, ins):
                    ins.then_inc(step.sem, 1)
                    dve.wait_ge(step.sem, base + 3 * t + k)
                dve.wait_ge(copied.sem, copied.at(t + 1))
                ordered(1, dve.tensor_scalar(y, x[:, 3:], core.p("conv_w_3", 48 + t), core.p("conv_b_3", t), ALU.mult, ALU.add))
                ordered(2, dve.scalar_tensor_tensor(out=y, in0=x[:, 2:2 + T], scalar=core.p("conv_w_3", 32 + t), in1=y,
                                                    op0=ALU.mult, op1=ALU.add))
                ordered(3, dve.scalar_tensor_tensor(out=y, in0=x[:, 1:1 + T], scalar=core.p("conv_w_3", 16 + t), in1=y,
                                                    op0=ALU.mult, op1=ALU.add))
                if not isinstance(t, int) or t >= 2:
                    dve.wait_ge(act_out.sem, act_out.at(t - 1))
                dve.scalar_tensor_tensor(out=z, in0=x[:, 0:T], scalar=core.p("conv_w_3", t), in1=y, op0=ALU.mult,
                                         op1=ALU.add).then_inc(conv.sem, 1)
                dve.wait_ge(conv.sem, conv.at(t + 1))
            tile_loop(dve, n, 4, body)
            step.value = base + 3 * n
    for x in (copied, conv, act_out):
        x.passed(n)
    core.finished(n)


def mlstm_gates(core, FI, M4, EB, GC, tmp):
    soft, rows, turned, spread, kept = (core.sig(n) for n in ("f_softplus", "gate_rows", "g_turned", "m_spread", "m_kept"))
    T = SEQ
    S, F, G, FM = (core.area(tmp + i * T, T) for i in range(4))
    with core.nc.Block() as block:
        @block.scalar
        def _(act):
            do = lambda ins: core.act.do(act, ins)
            f = FI[32:36, 0]
            do(act.activation(S[32:36], f, ACT.Abs))
            do(act.activation(S[32:36], S[32:36], ACT.Exp, scale=-1.0))
            act.activation(S[32:36], S[32:36], ACT.Ln, bias=1.0).then_inc(soft.sem, 1)
            for h in range(4):
                act.wait_ge(spread.sem, spread.at(h + 1))
                act.activation(EB[:, h], core.ps[:, h % 2, :], ACT.Exp, scale=-1.0).then_inc(kept.sem, 1)

        @block.vector
        def _(dve):
            do = lambda ins: core.vec.do(dve, ins)
            dve.wait_ge(soft.sem, soft.at(1))
            lf = S[32:36]
            do(dve.scalar_tensor_tensor(out=lf, in0=FI[32:36, 0], scalar=0.0, in1=lf, op0=ALU.min, op1=ALU.subtract))
            do(dve.tensor_tensor_scan(F[32:36], lf, lf, 0.0, ALU.add, ALU.bypass))
            do(dve.tensor_copy(F[0:4], F[32:36]))
            do(dve.tensor_tensor(G[0:4], FI[0:4, 0], F[0:4], ALU.subtract))
            do(dve.tensor_tensor_scan(M4[0:4], G[0:4], G[0:4], 0.0, ALU.max, ALU.bypass))
            dve.tensor_tensor(FM[0:4], F[0:4], M4[0:4], ALU.add).then_inc(rows.sem, 1)
            dve.wait_ge(turned.sem, turned.at(1))
            do(dve.tensor_copy(GC.rearrange("p a b -> p (a b)"), core.ps[:, 2, 0:16]))

        @block.tensor
        def _(pe):
            pe.wait_ge(rows.sem, rows.at(1))
            for j in range(4):
                last = pe.transpose(core.ps[:, 2, 4 * j:4 * j + 4], G[0:4, j * P:(j + 1) * P], core.c("ident")[0:4, 0:4])
            last.then_inc(turned.sem, 1)
            for h in range(4):
                if h >= 2:
                    pe.wait_ge(kept.sem, kept.at(h - 1))
                pe.matmul(core.ps[:, h % 2, :], core.c("heads")[0:4, h * P:(h + 1) * P], FM[0:4], start=True,
                          stop=True).then_inc(spread.sem, 1)
    soft.passed(1), rows.passed(1), turned.passed(1), spread.passed(4), kept.passed(4)


def mlstm(core, Q, K, VT, M4, EB, GC, H, tmp):
    spread, arg, exps, scores, probs, sums, absd, done = (core.sig(n) for n in (
        "m_rows", "weight_arg", "weight_exp", "key_scores", "key_probs", "head_sums", "norm_abs", "head_done"))
    T = SEQ
    MB = core.area(tmp, 2, T)
    W = core.area(tmp + 2 * T, 2, T)
    PT = core.area(tmp + 4 * T, 2, T)
    N = core.area(tmp + 6 * T, 2, T)
    steps = [(h, j) for h in range(4) for j in range(4)]
    with core.nc.Block() as block:
        @block.tensor
        def _(pe):
            def score(n):
                h, j = steps[n]
                if j == 0:
                    if h:
                        pe.wait_ge(spread.sem, spread.at(2 * h))
                    pe.matmul(core.ps[:, 2, :], core.c("heads")[0:4, h * P:(h + 1) * P], M4[0:4], start=True,
                              stop=True).then_inc(spread.sem, 1)
                if n >= 2:
                    pe.wait_ge(probs.sem, probs.at(n - 1))
                for e in range(2):
                    last = pe.matmul(core.ps[:, n % 2, 0:T - j * P], K[:, 2 * h + e, j * P:(j + 1) * P], Q[:, 2 * h + e, j * P:],
                                     start=(e == 0), stop=(e == 1))
                last.then_inc(scores.sem, 1)

            def add(n):
                h, j = steps[n]
                w = T - j * P
                pe.wait_ge(probs.sem, probs.at(n + 1))
                if j == 0 and h:
                    pe.wait_ge(done.sem, done.at(h))
                p = PT[:, n % 2, 0:w]
                for b, lhs in ((3, core.c("ones")), (4, VT[:, j, 2 * h]), (5, VT[:, j, 2 * h + 1])):
                    last = pe.matmul(core.ps[:, b, j * P:], lhs, p, start=(j == 0), stop=(j == 3))
                last.then_inc(sums.sem, 1)

            score(0)
            for n in range(16):
                if n + 1 < 16:
                    score(n + 1)
                add(n)

        @block.vector
        def _(dve):
            do = lambda ins: core.vec.do(dve, ins)

            def argument(n):
                h, j = steps[n]
                w = T - j * P
                if j == 0:
                    dve.wait_ge(spread.sem, spread.at(2 * h + 1))
                    dve.tensor_copy(MB[:, h % 2], core.ps[:, 2, :]).then_inc(spread.sem, 1)
                    dve.wait_ge(spread.sem, spread.at(2 * h + 2))
                dve.tensor_scalar(W[:, n % 2, 0:w], MB[:, h % 2, j * P:], GC[:, j, h:h + 1], 0.0, ALU.subtract,
                                  ALU.max).then_inc(arg.sem, 1)

            argument(0)
            for n, (h, j) in enumerate(steps):
                w = T - j * P
                if n + 1 < 16:
                    if n >= 1:
                        dve.wait_ge(probs.sem, probs.at(n))
                    argument(n + 1)
                dve.wait_ge(exps.sem, exps.at(n + 1))
                dve.wait_ge(scores.sem, scores.at(n + 1))
                if n >= 2:
                    dve.wait_ge(sums.sem, sums.at(n - 1))
                wt, p = W[:, n % 2, 0:w], PT[:, n % 2, 0:w]
                do(dve.tensor_tensor(wt[:, 0:P], wt[:, 0:P], core.c("upper"), ALU.mult))
                dve.scalar_tensor_tensor(out=p, in0=core.ps[:, n % 2, 0:w], scalar=1.0 / 16, in1=wt, op0=ALU.mult,
                                         op1=ALU.mult).then_inc(probs.sem, 1)
                if j < 3:
                    continue
                nh = N[:, h % 2]
                dve.wait_ge(absd.sem, absd.at(h + 1))
                do(dve.tensor_tensor(nh, nh, EB[:, h], ALU.max))
                do(dve.reciprocal(nh, nh))
                do(dve.tensor_tensor(H[:, 2 * h], core.ps[:, 4, :], nh, ALU.mult))
                dve.tensor_tensor(H[:, 2 * h + 1], core.ps[:, 5, :], nh, ALU.mult).then_inc(done.sem, 1)

        @block.scalar
        def _(act):
            for n, (h, j) in enumerate(steps):
                w = T - j * P
                act.wait_ge(arg.sem, arg.at(n + 1))
                act.activation(W[:, n % 2, 0:w], W[:, n % 2, 0:w], ACT.Exp, scale=-1.0).then_inc(exps.sem, 1)
                if j == 0 and h:
                    act.wait_ge(sums.sem, sums.at(4 * h))
                    if h >= 3:
                        act.wait_ge(done.sem, done.at(h - 2))
                    act.activation(N[:, (h - 1) % 2], core.ps[:, 3, :], ACT.Abs).then_inc(absd.sem, 1)
            act.wait_ge(sums.sem, sums.at(16))
            act.activation(N[:, 1], core.ps[:, 3, :], ACT.Abs).then_inc(absd.sem, 1)
    spread.passed(8)
    for x in (arg, exps, scores, probs, sums):
        x.passed(16)
    absd.passed(4), done.passed(4)


def third_block(core, out):
    T = SEQ
    merged = core.area(0, NC, T)
    QK = core.area(NC * T, 2 * NC, T)
    V = core.area(3 * NC * T, NC, T)
    VT = core.area(4 * NC * T, 4, NC, P)
    at = 5 * NC * T
    mod = core.mod
    EB, M4, GC, FI = core.area(at + 64, 4, T), core.area(at + 64 + 4 * T, T), core.area(at + 64 + 5 * T, 4, 4), core.area(
        at + 80 + 5 * T, 1, T)
    tmp = at + 96 + 6 * T
    cols = lambda o: [mod[:, o + k:o + k + 1] for k in range(NC)]
    scale_columns(core)

    project(core, NC, V, T, ACT.Gelu_apprx_tanh, x=NormedInput(core, cols(NC), cols(0), T, tmp))
    v = [V[:, k] for k in range(NC)]
    center(core, [v], T, 1.0 / D, "ones")
    norm(core, [(v, v, [core.p("gmlp_ln_g_3", k) for k in range(NC)], [core.p("gmlp_ln_b_3", k) for k in range(NC)])], T,
         1.0 / D, tmp)
    quads = lambda a: [([a[:, 4 * g + k] for k in range(4)], lambda j, g=g: VT[:, j, 4 * g:4 * g + 4].rearrange("p a b -> p (a b)"))
                       for g in range(2)]
    to_tokens(core, quads(V), T)
    mix_tokens(core, VT, merged, tmp)
    act_mul(core, [(ACT.Gelu_apprx_tanh, merged, merged, False), (ACT.Sigmoid, merged, merged, False)], T, tmp)

    project_conv(core, 2 * NC, QK, tmp)
    project(core, NC, V, T)
    to_tokens(core, quads(V), T)
    project(core, 1, FI, T, ACT.Identity, "mlstm_gate_b_3")
    mlstm_gates(core, FI, M4, EB, GC, tmp)
    mlstm(core, QK[:, 0:NC], QK[:, NC:2 * NC], VT, M4, EB, GC, V, tmp)
    center(core, [[V[:, 2 * h], V[:, 2 * h + 1]] for h in range(4)], T, 1.0 / 256, "ones")
    norm(core, [([V[:, 2 * h], V[:, 2 * h + 1]],) * 2 + ([core.p("mlstm_hn_g_3", 2 * h + e) for e in range(2)], None)
                for h in range(4)], T, 1.0 / 256, tmp)
    act_mul(core, [(ACT.Sigmoid, V, V, False), (ACT.Sigmoid, V, merged, True)], T, tmp)
    add_product(core, NC, merged, T, tmp, lambda t: column(mod, 2 * NC, t))

    hidden = core.area(0, 4 * NC, T)
    act_mul(core, [(ACT.Relu, None, hidden, False)], T, tmp, 4 * NC,
            NormedInput(core, cols(4 * NC), cols(3 * NC), T, tmp + 4 * T))
    add_product(core, 4 * NC, hidden, T, tmp, lambda t: column(mod, 5 * NC, t))
    core.close(inputs=True)
    renorm(core, [core.p("final_g_3", k) for k in range(NC)], T, 0, out)


def column(a, o, t):
    return a[:, o + t:o + t + 1] if isinstance(t, int) else a[:, bass.ds(o + t, 1)]


def build(nc, dram, out):
    with ExitStack() as ctx:
        core = Core(nc, ctx, dram)
        load_small(core)
        first_block(core)
        second_block(core)
        third_block(core, out)


def kernel(**inputs):
    import concourse.bacc as bacc
    from concourse.bass_utils import run_bass_kernel_spmd

    arrays = {f"in_{n}": np.ascontiguousarray(v) for n, v in lay_out({n: np.asarray(v) for n, v in inputs.items()}).items()}
    nc = bacc.Bacc("TRN2", target_bir_lowering=False, num_devices=1)
    dram = {n[3:]: nc.dram_tensor(n, v.shape, F32, kind="ExternalInput").ap() for n, v in arrays.items()}
    for n, shape in (("strip_scratch", (8, NR)), ("chunk_scratch", (64, CH, CH)), ("inverse_scratch", (64, CH, CH))):
        dram[n] = nc.dram_tensor(n, shape, F32, kind="Internal").ap()
    out = nc.dram_tensor("out_features", (P, NC, SEQ), F32, kind="ExternalOutput").ap()
    build(nc, dram, out)
    r = run_bass_kernel_spmd(nc, [arrays], core_ids=[0])
    return r.results[0]["out_features"].transpose(2, 1, 0).reshape(1, SEQ, D)
```
